# Optimizing a Trainium2 kernel written in Bass

```python
import jax, jax.numpy as jnp
from jax import lax
import numpy as np
import jax
import jax.numpy as jnp

D_MODEL = 1024
BATCH = 1
SEQ = 512
DEPTH = 1

PLE_DIM = 256
EPS = 1e-6
RET_HEADS = 4
RET_QK_DIM = 256
RET_V_DIM = 512
RET_CHUNK = 128
RET_ROPE_BASE = 10000.0
DIL_GROUPS = ((128, 1), (512, 4), (2048, 16))
DIL_SLOTS = 8
DIL_HEAD_DIM = 64
DIL_BLOCK = 128
ROPE_THETA = 500000.0
ROPE_DIM = DIL_HEAD_DIM // 4
D_FF = 4 * D_MODEL

RET_QK_W = RET_HEADS * RET_QK_DIM
RET_V_W = RET_HEADS * RET_V_DIM
DIL_HEADS = len(DIL_GROUPS) * DIL_SLOTS
DIL_W = DIL_HEADS * DIL_HEAD_DIM
DIL_OUT_W = DIL_SLOTS * DIL_HEAD_DIM
SPLITS = (RET_QK_W, RET_QK_W, RET_V_W, RET_V_W, DIL_W, DIL_W, DIL_W, D_MODEL, D_MODEL)
IN_W = RET_QK_W * 2 + RET_V_W * 2 + DIL_W * 3 + D_MODEL * 2


def rmsnorm(x, g=None):
    xf = x.astype(jnp.float32)
    y = xf * lax.rsqrt(jnp.mean(xf * xf, axis=-1, keepdims=True) + EPS)
    if g is not None:
        y = y * g.astype(jnp.float32)
    return y.astype(x.dtype)

def rope(x, cos, sin, rot_dim):
    half = rot_dim // 2
    x1 = x[..., :half]
    x2 = x[..., half:rot_dim]
    return jnp.concatenate([x1 * cos - x2 * sin, x2 * cos + x1 * sin, x[..., rot_dim:]], axis=-1)

def retention(q, k, v, pos):
    B, S, H, dk = q.shape
    dv = v.shape[-1]
    f32 = jnp.float32
    half = dk // 2
    inv_freq = 1.0 / (RET_ROPE_BASE ** jnp.linspace(0.0, 1.0, half, dtype=f32))
    ang = pos.astype(f32)[:, :, None, None] * inv_freq
    cos, sin = jnp.cos(ang), jnp.sin(ang)
    q = rope(q.astype(f32), cos, sin, dk)
    k = rope(k.astype(f32), cos, sin, dk) * (dk ** -0.5)
    v = v.astype(f32)
    C = RET_CHUNK
    Sp = -(-S // C) * C
    padw = ((0, 0), (0, Sp - S), (0, 0), (0, 0))
    nc = Sp // C
    qc = jnp.pad(q, padw).reshape(B, nc, C, H, dk)
    kc = jnp.pad(k, padw).reshape(B, nc, C, H, dk)
    vc = jnp.pad(v, padw).reshape(B, nc, C, H, dv)
    log_gamma = jnp.log1p(-(2.0 ** (-5.0 - jnp.arange(H, dtype=f32))))
    idx = jnp.arange(C, dtype=f32)
    diff = idx[:, None] - idx[None, :]
    decay = jnp.where(diff[None] >= 0, jnp.exp(jnp.maximum(diff, 0.0)[None] * log_gamma[:, None, None]), 0.0)
    scores = jnp.einsum('bnihd,bnjhd->bnhij', qc, kc) * decay[None, None]
    inner = jnp.einsum('bnhij,bnjhe->bnihe', scores, vc)
    q_dec = jnp.exp((idx + 1.0)[:, None] * log_gamma[None, :])
    k_dec = jnp.exp((C - 1.0 - idx)[:, None] * log_gamma[None, :])
    chunk_dec = jnp.exp(C * log_gamma)

    def step(R, inp):
        qn, kn, vn = inp
        cross = jnp.einsum('bihd,bhde->bihe', qn * q_dec[None, :, :, None], R)
        R = R * chunk_dec[None, :, None, None] + jnp.einsum('bjhd,bjhe->bhde', kn * k_dec[None, :, :, None], vn)
        return R, cross

    R0 = jnp.zeros((B, H, dk, dv), f32)
    _, cross = lax.scan(step, R0, (jnp.moveaxis(qc, 1, 0), jnp.moveaxis(kc, 1, 0), jnp.moveaxis(vc, 1, 0)))
    y = inner + jnp.moveaxis(cross, 0, 1)
    return y.reshape(B, Sp, H, dv)[:, :S]

def dilated_group(q, k, v, window, dilation):
    B, S, Hg, hd = q.shape
    f32 = jnp.float32
    band = window // dilation
    QB = DIL_BLOCK
    seg = dilation * QB
    Sp = -(-S // seg) * seg
    L = Sp // dilation
    nb = L // QB
    padw = ((0, 0), (0, Sp - S), (0, 0), (0, 0))

    def to_streams(t):
        t = jnp.pad(t.astype(f32), padw).reshape(B, L, dilation, Hg, hd)
        return t.transpose(0, 2, 1, 3, 4).reshape(B, dilation, nb, QB, Hg, hd)

    def with_prev(t):
        prev = jnp.pad(t[:, :, :-1], ((0, 0), (0, 0), (1, 0), (0, 0), (0, 0), (0, 0)))
        return jnp.concatenate([prev, t], axis=3)

    qs = to_streams(q)
    kk = with_prev(to_streams(k))
    vv = with_prev(to_streams(v))
    s = jnp.einsum('bcnqhe,bcnkhe->bcnhqk', qs, kk) * (hd ** -0.5)
    qi = jnp.arange(QB)[:, None]
    kj = jnp.arange(2 * QB)[None, :] - QB
    dist = qi - kj
    in_band = (dist >= 0) & (dist <= band)
    key_exists = (jnp.arange(nb)[:, None, None] * QB + kj[None]) >= 0
    mask = in_band[None] & key_exists
    s = jnp.where(mask[None, None, :, None], s, -1e30)
    lse = jax.nn.logsumexp(s, axis=-1)
    pr = jnp.exp(s - lse[..., None])
    o = jnp.einsum('bcnhqk,bcnkhe->bcnqhe', pr, vv)
    o = o.reshape(B, dilation, L, Hg, hd).transpose(0, 2, 1, 3, 4).reshape(B, Sp, Hg, hd)[:, :S]
    lse = lse.transpose(0, 1, 2, 4, 3).reshape(B, dilation, L, Hg).transpose(0, 2, 1, 3).reshape(B, Sp, Hg)[:, :S]
    return o, lse

def dilated_attention(q, k, v, pos):
    f32 = jnp.float32
    freqs = ROPE_THETA ** (-jnp.arange(0, ROPE_DIM, 2, dtype=f32) / ROPE_DIM)
    ang = pos.astype(f32)[:, :, None, None] * freqs
    cos, sin = jnp.cos(ang), jnp.sin(ang)
    q = rope(q.astype(f32), cos, sin, ROPE_DIM)
    k = rope(k.astype(f32), cos, sin, ROPE_DIM)
    outs, lses = [], []
    for g, (window, dilation) in enumerate(DIL_GROUPS):
        sl = slice(g * DIL_SLOTS, (g + 1) * DIL_SLOTS)
        o, l = dilated_group(q[:, :, sl], k[:, :, sl], v[:, :, sl], window, dilation)
        outs.append(o)
        lses.append(l)
    w = jax.nn.softmax(jnp.stack(lses, axis=0), axis=0)
    return jnp.sum(w[..., None] * jnp.stack(outs, axis=0), axis=0)

def first_inputs(seed: int = 0) -> dict:
    key = jax.random.key(seed)
    ks = jax.random.split(key, 24)
    f32 = jnp.float32
    nrm = lambda k, shape, fan_in: jax.random.normal(k, shape, f32) * (fan_in ** -0.5)
    gain = lambda k: 1.0 + 0.02 * jax.random.normal(k, (DEPTH, D_MODEL), f32)
    x = jax.random.normal(ks[0], (BATCH, SEQ, D_MODEL), f32)
    p = jax.random.normal(ks[1], (DEPTH, BATCH, SEQ, PLE_DIM), f32)
    positions = jnp.broadcast_to(jnp.arange(SEQ, dtype=jnp.int32)[None, :], (BATCH, SEQ))
    return {
        "x": x,
        "p": p,
        "positions": positions,
        "w_in": nrm(ks[2], (DEPTH, D_MODEL, IN_W), D_MODEL),
        "b_gate": 0.01 * jax.random.normal(ks[3], (DEPTH, 2, D_MODEL), f32),
        "w_ret_out": nrm(ks[4], (DEPTH, RET_V_W, D_MODEL), RET_V_W),
        "w_dil_out": nrm(ks[5], (DEPTH, DIL_OUT_W, D_MODEL), DIL_OUT_W),
        "w_o": nrm(ks[6], (DEPTH, D_MODEL, D_MODEL), D_MODEL),
        "g_pre_mix": gain(ks[7]),
        "g_post_mix": gain(ks[8]),
        "g_pre_mlp": gain(ks[9]),
        "g_post_mlp": gain(ks[10]),
        "w_up": nrm(ks[11], (DEPTH, D_MODEL, D_FF), D_MODEL),
        "w_down": nrm(ks[12], (DEPTH, D_FF, D_MODEL), D_FF),
        "g_pre_ple": gain(ks[13]),
        "w_ple_gate": nrm(ks[14], (DEPTH, D_MODEL, D_MODEL), D_MODEL),
        "b_ple_gate": 0.01 * jax.random.normal(ks[15], (DEPTH, D_MODEL), f32),
        "w_ple_in": nrm(ks[16], (DEPTH, PLE_DIM, D_MODEL), PLE_DIM),
        "g_post_ple": gain(ks[17]),
    }

def first_block(x, p, positions, w_in, b_gate, w_ret_out, w_dil_out, w_o, g_pre_mix, g_post_mix,
              g_pre_mlp, g_post_mlp, w_up, w_down, g_pre_ple, w_ple_gate, b_ple_gate, w_ple_in,
              g_post_ple):
    B, S, _ = x.shape
    split_points = [int(s) for s in np.cumsum(SPLITS)[:-1]]
    h = x
    for i in range(DEPTH):
        u = rmsnorm(h, g_pre_mix[i])
        proj = u @ w_in[i]
        rq, rk, rv, rg, aq, ak, av, gr, ga = jnp.split(proj, split_points, axis=-1)
        yr = retention(rq.reshape(B, S, RET_HEADS, RET_QK_DIM), rk.reshape(B, S, RET_HEADS, RET_QK_DIM),
                       rv.reshape(B, S, RET_HEADS, RET_V_DIM), positions)
        yr = rmsnorm(yr) * jax.nn.silu(rg.reshape(B, S, RET_HEADS, RET_V_DIM).astype(jnp.float32))
        ya_branch = yr.reshape(B, S, RET_V_W).astype(h.dtype) @ w_ret_out[i]
        ya = dilated_attention(aq.reshape(B, S, DIL_HEADS, DIL_HEAD_DIM), ak.reshape(B, S, DIL_HEADS, DIL_HEAD_DIM),
                               av.reshape(B, S, DIL_HEADS, DIL_HEAD_DIM), positions)
        yb_branch = ya.reshape(B, S, DIL_OUT_W).astype(h.dtype) @ w_dil_out[i]
        mixed = jax.nn.sigmoid(gr + b_gate[i, 0]) * ya_branch + jax.nn.sigmoid(ga + b_gate[i, 1]) * yb_branch
        h = h + rmsnorm(mixed @ w_o[i], g_post_mix[i])
        v2 = rmsnorm(h, g_pre_mlp[i])
        f = jnp.square(jax.nn.relu(v2 @ w_up[i])) @ w_down[i]
        h = h + rmsnorm(f, g_post_mlp[i])
        gate = jax.nn.sigmoid(rmsnorm(h, g_pre_ple[i]) @ w_ple_gate[i] + b_ple_gate[i])
        e = p[i].astype(h.dtype) @ w_ple_in[i]
        h = h + rmsnorm(gate * e, g_post_ple[i])
    return h


DEPTH_2 = 2

GRID_W = 64
CTX_LEN = 256
N_MIXERS = 4
ROPE_BASE = 10000.0
NORM_EPS = 1e-6
NEG_INF = -1e30
Q_BLOCK = 128

NA_HEADS = 16
NA_HEAD_DIM = D_MODEL // NA_HEADS
NA_WIN_ROWS = 8
NA_WIN_COLS = 16

RW_HEAD = 64
RW_HEADS = D_MODEL // RW_HEAD
RW_DECAY_LORA = 64
RW_ICLR_LORA = 64
RW_GATE_LORA = 128
RW_GN_EPS = 64e-5

MLA_HEADS = 16
MLA_Q_RANK = 384
MLA_KV_RANK = 256
MLA_NOPE = 64
MLA_ROPE = 32
MLA_V = 64

SWA_Q_HEADS = 16
SWA_KV_HEADS = 4
SWA_GROUP = SWA_Q_HEADS // SWA_KV_HEADS
SWA_HEAD_DIM = 64
SWA_WINDOW = 128

N_EXPERTS = 16
EC_CAPACITY = 2
D_FF_EXPERT = 1024


def rms_norm(x, g):
    xf = x.astype(jnp.float32)
    y = xf * lax.rsqrt(jnp.mean(xf * xf, axis=-1, keepdims=True) + NORM_EPS)
    return (y * g.astype(jnp.float32)).astype(x.dtype)

def modulate(h, shift, scale):
    return h * (1 + scale) + shift

def ada_modulation(cond, w, b):
    m = jax.nn.silu(cond) @ w + b
    return jnp.split(m, 6, axis=-1)

def axial_rope(n, d_rot):
    t = jnp.arange(n)
    row = (t // GRID_W).astype(jnp.float32)
    col = (t % GRID_W).astype(jnp.float32)
    d_axis = d_rot // 2
    inv = ROPE_BASE ** (-jnp.arange(0, d_axis, 2, dtype=jnp.float32) / d_axis)
    ang = jnp.concatenate([row[:, None] * inv, col[:, None] * inv], axis=-1)
    return jnp.cos(ang), jnp.sin(ang)

def apply_rope(x, cos, sin):
    half = x.shape[-1] // 2
    xf = x.astype(jnp.float32)
    x1, x2 = xf[..., :half], xf[..., half:]
    return jnp.concatenate([x1 * cos - x2 * sin, x2 * cos + x1 * sin], axis=-1).astype(x.dtype)

def context_attention(q, k, v, scale, sink=None):
    L = k.shape[1]
    s = jnp.einsum('bqhgd,bkhd->bhgqk', q, k).astype(jnp.float32) * scale
    if sink is not None:
        snk = jnp.broadcast_to(sink.astype(jnp.float32)[None, :, :, None, None], s.shape[:-1] + (1,))
        s = jnp.concatenate([s, snk], axis=-1)
    p = jax.nn.softmax(s, axis=-1)[..., :L]
    return jnp.einsum('bhgqk,bkhd->bqhgd', p.astype(v.dtype), v)

def neighbourhood_attention(hc, hl, w_qkv, q_g, k_g, rpb, w_o, ctx_out):
    B, n, D = hl.shape
    L = hc.shape[1]
    rows = n // GRID_W
    H, dh = NA_HEADS, NA_HEAD_DIM
    scale = dh ** -0.5

    def project(h):
        qkv = (h @ w_qkv).reshape(h.shape[0], h.shape[1], 3, H, dh)
        return rms_norm(qkv[:, :, 0], q_g), rms_norm(qkv[:, :, 1], k_g), qkv[:, :, 2]

    qc, kc, vc = project(hc)
    ql, kl, vl = project(hl)

    kr = min(NA_WIN_ROWS, rows)
    n_cb = GRID_W // NA_WIN_COLS
    strip = 2 * NA_WIN_COLS
    qcol = np.arange(GRID_W).reshape(n_cb, NA_WIN_COLS)
    strip0 = np.clip(np.arange(n_cb) * NA_WIN_COLS - NA_WIN_COLS // 2, 0, GRID_W - strip)
    kcol = strip0[:, None] + np.arange(strip)
    cstart = np.clip(qcol - NA_WIN_COLS // 2, 0, GRID_W - NA_WIN_COLS)
    kc3 = kcol[:, None, :]
    col_ok = (kc3 >= cstart[:, :, None]) & (kc3 < cstart[:, :, None] + NA_WIN_COLS)
    dcol_idx = np.clip(kc3 - qcol[:, :, None] + NA_WIN_COLS - 1, 0, 2 * NA_WIN_COLS - 2)
    rpb_cols = rpb[:, :, dcol_idx]
    col_ok = jnp.asarray(col_ok)[:, :, None, :]

    qg = ql.reshape(B, rows, GRID_W, H, dh)
    kg = kl.reshape(B, rows, GRID_W, H, dh)
    vg = vl.reshape(B, rows, GRID_W, H, dh)

    def row_step(r):
        r0 = jnp.clip(r - kr // 2, 0, rows - kr)
        kw = lax.dynamic_slice_in_dim(kg, r0, kr, axis=1)[:, :, kcol]
        vw = lax.dynamic_slice_in_dim(vg, r0, kr, axis=1)[:, :, kcol]
        q = lax.dynamic_index_in_dim(qg, r, axis=1, keepdims=False)[:, qcol]
        dr_idx = r0 + jnp.arange(kr) - r + (NA_WIN_ROWS - 1)
        bias = jnp.transpose(rpb_cols[:, dr_idx], (0, 2, 3, 1, 4)).astype(jnp.float32)
        s_lat = jnp.einsum('bjqhd,brjkhd->bhjqrk', q, kw).astype(jnp.float32) * scale + bias[None]
        s_lat = jnp.where(col_ok, s_lat, NEG_INF).reshape(B, H, n_cb, NA_WIN_COLS, kr * strip)
        s_ctx = jnp.einsum('bjqhd,bkhd->bhjqk', q, kc).astype(jnp.float32) * scale
        p = jax.nn.softmax(jnp.concatenate([s_lat, s_ctx], axis=-1), axis=-1).astype(vl.dtype)
        p_lat = p[..., :kr * strip].reshape(B, H, n_cb, NA_WIN_COLS, kr, strip)
        o = (jnp.einsum('bhjqrk,brjkhd->bjqhd', p_lat, vw)
             + jnp.einsum('bhjqk,bkhd->bjqhd', p[..., kr * strip:], vc))
        return o.reshape(B, GRID_W, H, dh)

    o = lax.map(row_step, jnp.arange(rows))
    ol = jnp.moveaxis(o, 0, 1).reshape(B, n, H * dh) @ w_o
    oc = None
    if ctx_out:
        oc = context_attention(qc[:, :, :, None], kc, vc, scale).reshape(B, L, H * dh) @ w_o
    return oc, ol

def centred_shift(h):
    hp = jnp.pad(h, ((0, 0), (1, 1), (0, 0)))
    return 0.5 * (hp[:, :-2] + hp[:, 2:])

def _rwkv_step(S, inp):
    r, w, kk, kka, kt, v = inp
    sk = jnp.einsum('bhij,bhj->bhi', S, kk)
    S = S * w[:, :, None, :] - sk[..., None] * kka[:, :, None, :] + v[..., None] * kt[:, :, None, :]
    return S, jnp.einsum('bhij,bhj->bhi', S, r)

def _rwkv_scan(S0, seqs, reverse):
    xs = tuple(jnp.swapaxes(t, 0, 1) for t in seqs)
    S, y = lax.scan(_rwkv_step, S0, xs, reverse=reverse)
    return S, jnp.swapaxes(y, 0, 1)

def rwkv7_bidirectional(hc, hl, mix, w_r, w_k, w_v, w0, w1, w2, a0, a1, a2, g1, g2,
                        k_k, k_a, r_k, ln_g, ln_b, w_o, ctx_out):
    f32 = jnp.float32
    H, N = RW_HEADS, RW_HEAD

    def heads(t):
        return t.reshape(t.shape[:-1] + (H, N))

    def stream(h, S0):
        B = h.shape[0]
        xx = centred_shift(h) - h
        xr, xw, xk, xv, xa, xg = (h + xx * mix[s] for s in range(6))
        r = heads((xr @ w_r).astype(f32))
        k = (xk @ w_k).astype(f32)
        v = heads((xv @ w_v).astype(f32))
        g = jax.nn.sigmoid(xg @ g1) @ g2
        dec = w0[:, None, None, :] + jnp.einsum('zbtr,zrd->zbtd', jnp.tanh(jnp.einsum('btd,zdr->zbtr', xw, w1)), w2)
        logw = -jax.nn.softplus(-dec.astype(f32)) - 0.5
        w = heads(jnp.exp(-jnp.exp(logw)))
        a = heads(jax.nn.sigmoid((a0[:, None, None, :] + jnp.einsum(
            'zbtr,zrd->zbtd', jnp.einsum('btd,zdr->zbtr', xa, a1), a2)).astype(f32)))
        kk = heads(k * k_k.astype(f32))
        kk = kk / jnp.maximum(jnp.linalg.norm(kk, axis=-1, keepdims=True), 1e-12)
        kt = heads(k)[None] * (1 + (a - 1) * heads(k_a.astype(f32)))
        if S0 is None:
            z = jnp.zeros((B, H, N, N), f32)
            S0 = (z, z)
        S_f, y_f = _rwkv_scan(S0[0], (r, w[0], kk, kk * a[0], kt[0], v), False)
        S_b, y_b = _rwkv_scan(S0[1], (r, w[1], kk, kk * a[1], kt[1], v), True)
        return (S_f, S_b), (y_f + y_b, r, kt, v, g)

    def readout(y, r, kt, v, g, dtype):
        B, T = y.shape[:2]
        mu = jnp.mean(y, axis=-1, keepdims=True)
        var = jnp.mean(jnp.square(y - mu), axis=-1, keepdims=True)
        yn = ((y - mu) * lax.rsqrt(var + RW_GN_EPS)).reshape(B, T, -1) * ln_g.astype(f32) + ln_b.astype(f32)
        bonus = jnp.sum(jnp.sum(r[None] * kt * r_k.astype(f32), axis=-1, keepdims=True), axis=0) * v
        return ((yn + bonus.reshape(B, T, -1)).astype(dtype) * g) @ w_o

    ctx_state, ctx_feats = stream(hc, None)
    _, lat_feats = stream(hl, ctx_state)
    ol = readout(*lat_feats, hl.dtype)
    oc = readout(*ctx_feats, hc.dtype) if ctx_out else None
    return oc, ol

def multi_head_latent_attention(hc, hl, w_down, q_norm_g, kv_norm_g, w_uq, w_ukv,
                                qn_g, qr_g, kn_g, kr_g, w_o, cos, sin, ctx_out):
    f32 = jnp.float32
    H = MLA_HEADS
    scale = (MLA_NOPE + MLA_ROPE) ** -0.5

    def project(h, rope):
        B, T, _ = h.shape
        d = h @ w_down
        cq = rms_norm(d[..., :MLA_Q_RANK], q_norm_g)
        ckv = rms_norm(d[..., MLA_Q_RANK:MLA_Q_RANK + MLA_KV_RANK], kv_norm_g)
        k_r = rms_norm(d[..., MLA_Q_RANK + MLA_KV_RANK:], kr_g)
        q = (cq @ w_uq).reshape(B, T, H, MLA_NOPE + MLA_ROPE)
        kv = (ckv @ w_ukv).reshape(B, T, H, MLA_NOPE + MLA_V)
        q_n = rms_norm(q[..., :MLA_NOPE], qn_g)
        q_r = rms_norm(q[..., MLA_NOPE:], qr_g)
        k_n = rms_norm(kv[..., :MLA_NOPE], kn_g)
        v = kv[..., MLA_NOPE:]
        if rope:
            q_r = apply_rope(q_r, cos[:, None], sin[:, None])
            k_r = apply_rope(k_r, cos, sin)
        return q_n, q_r, k_n, k_r, v

    qn_l, qr_l, kn_l, kr_l, v_l = project(hl, True)
    qn_c, qr_c, kn_c, kr_c, v_c = project(hc, False)
    B, n = hl.shape[:2]
    L = hc.shape[1]

    def block(b):
        s0 = b * Q_BLOCK
        qn = lax.dynamic_slice_in_dim(qn_l, s0, Q_BLOCK, axis=1)
        qr = lax.dynamic_slice_in_dim(qr_l, s0, Q_BLOCK, axis=1)
        s_lat = jnp.einsum('bqhd,bkhd->bhqk', qn, kn_l) + jnp.einsum('bqhd,bkd->bhqk', qr, kr_l)
        s_ctx = jnp.einsum('bqhd,bkhd->bhqk', qn, kn_c) + jnp.einsum('bqhd,bkd->bhqk', qr, kr_c)
        s = jnp.concatenate([s_lat, s_ctx], axis=-1).astype(f32) * scale
        p = jax.nn.softmax(s, axis=-1).astype(v_l.dtype)
        return (jnp.einsum('bhqk,bkhd->bqhd', p[..., :n], v_l)
                + jnp.einsum('bhqk,bkhd->bqhd', p[..., n:], v_c))

    o = lax.map(block, jnp.arange(n // Q_BLOCK))
    ol = jnp.moveaxis(o, 0, 1).reshape(B, n, H * MLA_V) @ w_o
    oc = None
    if ctx_out:
        q = jnp.concatenate([qn_c, qr_c], axis=-1)
        k = jnp.concatenate([kn_c, jnp.broadcast_to(kr_c[:, :, None, :], (B, L, H, MLA_ROPE))], axis=-1)
        oc = context_attention(q[:, :, :, None], k, v_c, scale).reshape(B, L, H * MLA_V) @ w_o
    return oc, ol

def window_gqa_sink(hc, hl, w_qkv, q_g, k_g, sink, w_o, cos, sin, ctx_out):
    f32 = jnp.float32
    Hk, G, dh = SWA_KV_HEADS, SWA_GROUP, SWA_HEAD_DIM
    scale = dh ** -0.5
    sink_hg = sink.reshape(Hk, G)
    nq = Hk * G * dh

    def project(h, rope):
        B, T, _ = h.shape
        qkv = h @ w_qkv
        q = rms_norm(qkv[..., :nq].reshape(B, T, Hk, G, dh), q_g)
        k = rms_norm(qkv[..., nq:nq + Hk * dh].reshape(B, T, Hk, dh), k_g)
        v = qkv[..., nq + Hk * dh:].reshape(B, T, Hk, dh)
        if rope:
            q = apply_rope(q, cos[:, None, None], sin[:, None, None])
            k = apply_rope(k, cos[:, None], sin[:, None])
        return q, k, v

    ql, kl, vl = project(hl, True)
    qc, kc, vc = project(hc, False)
    B, n = hl.shape[:2]
    L = hc.shape[1]
    pad = ((0, 0), (Q_BLOCK, Q_BLOCK), (0, 0), (0, 0))
    kp, vp = jnp.pad(kl, pad), jnp.pad(vl, pad)
    q_off = jnp.arange(Q_BLOCK)
    k_off = jnp.arange(3 * Q_BLOCK) - Q_BLOCK

    def block(b):
        s0 = b * Q_BLOCK
        q = lax.dynamic_slice_in_dim(ql, s0, Q_BLOCK, axis=1)
        k = lax.dynamic_slice_in_dim(kp, s0, 3 * Q_BLOCK, axis=1)
        v = lax.dynamic_slice_in_dim(vp, s0, 3 * Q_BLOCK, axis=1)
        qpos, kpos = s0 + q_off, s0 + k_off
        ok = ((kpos >= 0) & (kpos < n))[None, :] & (jnp.abs(qpos[:, None] - kpos[None, :]) <= SWA_WINDOW)
        s_loc = jnp.where(ok, jnp.einsum('bqhgd,bkhd->bhgqk', q, k).astype(f32) * scale, NEG_INF)
        s_ctx = jnp.einsum('bqhgd,bkhd->bhgqk', q, kc).astype(f32) * scale
        s_snk = jnp.broadcast_to(sink_hg.astype(f32)[None, :, :, None, None], s_loc.shape[:-1] + (1,))
        p = jax.nn.softmax(jnp.concatenate([s_loc, s_ctx, s_snk], axis=-1), axis=-1).astype(vl.dtype)
        return (jnp.einsum('bhgqk,bkhd->bqhgd', p[..., :3 * Q_BLOCK], v)
                + jnp.einsum('bhgqk,bkhd->bqhgd', p[..., 3 * Q_BLOCK:-1], vc))

    o = lax.map(block, jnp.arange(n // Q_BLOCK))
    ol = jnp.moveaxis(o, 0, 1).reshape(B, n, nq) @ w_o
    oc = None
    if ctx_out:
        oc = context_attention(qc, kc, vc, scale, sink_hg).reshape(B, L, nq) @ w_o
    return oc, ol

def expert_choice_ffn(h, w_router, w1, w3, w2):
    B, T, D = h.shape
    cap = max(1, EC_CAPACITY * T // N_EXPERTS)
    aff = jax.nn.softmax((h @ w_router).astype(jnp.float32), axis=-1)
    gate, idx = lax.top_k(jnp.swapaxes(aff, 1, 2), cap)
    xin = jax.vmap(lambda hb, ib: hb[ib])(h, idx)
    hid = jax.nn.silu(jnp.einsum('becd,edf->becf', xin, w1)) * jnp.einsum('becd,edf->becf', xin, w3)
    y = jnp.einsum('becf,efd->becd', hid, w2) * gate[..., None].astype(h.dtype)
    return jax.vmap(lambda yb, ib: jax.ops.segment_sum(
        yb.reshape(-1, D), ib.reshape(-1), num_segments=T))(y, idx)

def _layers_of(mixer):
    return len(range(mixer, DEPTH_2, N_MIXERS))

def second_inputs(seed: int = 0) -> dict:
    key = jax.random.key(seed)
    keys = iter(jax.random.split(key, 96))
    f32 = jnp.float32
    D = D_MODEL

    def normal(shape, scale):
        return jax.random.normal(next(keys), shape, f32) * scale

    def gain(shape):
        return 1.0 + 0.1 * jax.random.normal(next(keys), shape, f32)

    def uniform(shape, lo, hi):
        return jax.random.uniform(next(keys), shape, f32, lo, hi)

    nA, nB, nC, nD = (_layers_of(m) for m in range(N_MIXERS))
    swa_cols = (SWA_Q_HEADS + 2 * SWA_KV_HEADS) * SWA_HEAD_DIM
    return {
        'x': normal((BATCH, SEQ, D), 1.0),
        'c': normal((BATCH, D), 1.0),
        'ctx': normal((BATCH, CTX_LEN, D), 1.0),
        'c_ctx': normal((D,), 1.0),
        'norm1_g': gain((DEPTH_2, D)),
        'norm2_g': gain((DEPTH_2, D)),
        'ada_w': normal((DEPTH_2, D, 6 * D), 0.5 * D ** -0.5),
        'ada_b': normal((DEPTH_2, 6 * D), 0.02),
        'na_w_qkv': normal((nA, D, 3 * D), D ** -0.5),
        'na_q_g': gain((nA, NA_HEAD_DIM)),
        'na_k_g': gain((nA, NA_HEAD_DIM)),
        'na_rpb': normal((nA, NA_HEADS, 2 * NA_WIN_ROWS - 1, 2 * NA_WIN_COLS - 1), 0.5),
        'na_w_o': normal((nA, D, D), D ** -0.5),
        'rw_mix': uniform((nB, 6, D), 0.0, 1.0),
        'rw_w_r': normal((nB, D, D), D ** -0.5),
        'rw_w_k': normal((nB, D, D), D ** -0.5),
        'rw_w_v': normal((nB, D, D), D ** -0.5),
        'rw_w0': uniform((nB, 2, D), -6.0, -1.0),
        'rw_w1': normal((nB, 2, D, RW_DECAY_LORA), D ** -0.5),
        'rw_w2': normal((nB, 2, RW_DECAY_LORA, D), 0.5 * RW_DECAY_LORA ** -0.5),
        'rw_a0': normal((nB, 2, D), 0.5),
        'rw_a1': normal((nB, 2, D, RW_ICLR_LORA), D ** -0.5),
        'rw_a2': normal((nB, 2, RW_ICLR_LORA, D), 0.5 * RW_ICLR_LORA ** -0.5),
        'rw_g1': normal((nB, D, RW_GATE_LORA), D ** -0.5),
        'rw_g2': normal((nB, RW_GATE_LORA, D), RW_GATE_LORA ** -0.5),
        'rw_k_k': uniform((nB, D), 0.7, 1.0),
        'rw_k_a': uniform((nB, D), 0.8, 1.2),
        'rw_r_k': normal((nB, RW_HEADS, RW_HEAD), 0.1),
        'rw_ln_g': gain((nB, D)),
        'rw_ln_b': normal((nB, D), 0.02),
        'rw_w_o': normal((nB, D, D), D ** -0.5),
        'mla_w_down': normal((nC, D, MLA_Q_RANK + MLA_KV_RANK + MLA_ROPE), D ** -0.5),
        'mla_q_norm_g': gain((nC, MLA_Q_RANK)),
        'mla_kv_norm_g': gain((nC, MLA_KV_RANK)),
        'mla_w_uq': normal((nC, MLA_Q_RANK, MLA_HEADS * (MLA_NOPE + MLA_ROPE)), MLA_Q_RANK ** -0.5),
        'mla_w_ukv': normal((nC, MLA_KV_RANK, MLA_HEADS * (MLA_NOPE + MLA_V)), MLA_KV_RANK ** -0.5),
        'mla_qn_g': gain((nC, MLA_NOPE)),
        'mla_qr_g': gain((nC, MLA_ROPE)),
        'mla_kn_g': gain((nC, MLA_NOPE)),
        'mla_kr_g': gain((nC, MLA_ROPE)),
        'mla_w_o': normal((nC, MLA_HEADS * MLA_V, D), (MLA_HEADS * MLA_V) ** -0.5),
        'swa_w_qkv': normal((nD, D, swa_cols), D ** -0.5),
        'swa_q_g': gain((nD, SWA_HEAD_DIM)),
        'swa_k_g': gain((nD, SWA_HEAD_DIM)),
        'swa_sink': normal((nD, SWA_Q_HEADS), 0.5),
        'swa_w_o': normal((nD, SWA_Q_HEADS * SWA_HEAD_DIM, D), (SWA_Q_HEADS * SWA_HEAD_DIM) ** -0.5),
        'moe_router': normal((DEPTH_2, D, N_EXPERTS), D ** -0.5),
        'moe_w1': normal((DEPTH_2, N_EXPERTS, D, D_FF_EXPERT), D ** -0.5),
        'moe_w3': normal((DEPTH_2, N_EXPERTS, D, D_FF_EXPERT), D ** -0.5),
        'moe_w2': normal((DEPTH_2, N_EXPERTS, D_FF_EXPERT, D), D_FF_EXPERT ** -0.5),
    }

def second_block(x, c, ctx, c_ctx, norm1_g, norm2_g, ada_w, ada_b,
              na_w_qkv, na_q_g, na_k_g, na_rpb, na_w_o,
              rw_mix, rw_w_r, rw_w_k, rw_w_v, rw_w0, rw_w1, rw_w2, rw_a0, rw_a1, rw_a2,
              rw_g1, rw_g2, rw_k_k, rw_k_a, rw_r_k, rw_ln_g, rw_ln_b, rw_w_o,
              mla_w_down, mla_q_norm_g, mla_kv_norm_g, mla_w_uq, mla_w_ukv,
              mla_qn_g, mla_qr_g, mla_kn_g, mla_kr_g, mla_w_o,
              swa_w_qkv, swa_q_g, swa_k_g, swa_sink, swa_w_o,
              moe_router, moe_w1, moe_w3, moe_w2):
    n = x.shape[1]
    cos_mla, sin_mla = axial_rope(n, MLA_ROPE)
    cos_swa, sin_swa = axial_rope(n, SWA_HEAD_DIM)
    xl, xc = x, ctx
    for i in range(DEPTH_2):
        mixer, j = i % N_MIXERS, i // N_MIXERS
        ctx_needed = i < DEPTH_2 - 1
        sh1, sc1, gt1, sh2, sc2, gt2 = (t[:, None, :] for t in ada_modulation(c, ada_w[i], ada_b[i]))
        csh1, csc1, cgt1, csh2, csc2, cgt2 = ada_modulation(c_ctx, ada_w[i], ada_b[i])
        hl = modulate(rms_norm(xl, norm1_g[i]), sh1, sc1)
        hc = modulate(rms_norm(xc, norm1_g[i]), csh1, csc1)
        if mixer == 0:
            oc, ol = neighbourhood_attention(hc, hl, na_w_qkv[j], na_q_g[j], na_k_g[j], na_rpb[j],
                                             na_w_o[j], ctx_needed)
        elif mixer == 1:
            oc, ol = rwkv7_bidirectional(hc, hl, rw_mix[j], rw_w_r[j], rw_w_k[j], rw_w_v[j],
                                         rw_w0[j], rw_w1[j], rw_w2[j], rw_a0[j], rw_a1[j], rw_a2[j],
                                         rw_g1[j], rw_g2[j], rw_k_k[j], rw_k_a[j], rw_r_k[j],
                                         rw_ln_g[j], rw_ln_b[j], rw_w_o[j], ctx_needed)
        elif mixer == 2:
            oc, ol = multi_head_latent_attention(hc, hl, mla_w_down[j], mla_q_norm_g[j], mla_kv_norm_g[j],
                                                 mla_w_uq[j], mla_w_ukv[j], mla_qn_g[j], mla_qr_g[j],
                                                 mla_kn_g[j], mla_kr_g[j], mla_w_o[j],
                                                 cos_mla, sin_mla, ctx_needed)
        else:
            oc, ol = window_gqa_sink(hc, hl, swa_w_qkv[j], swa_q_g[j], swa_k_g[j], swa_sink[j],
                                     swa_w_o[j], cos_swa, sin_swa, ctx_needed)
        xl = xl + gt1 * ol
        hl = modulate(rms_norm(xl, norm2_g[i]), sh2, sc2)
        xl = xl + gt2 * expert_choice_ffn(hl, moe_router[i], moe_w1[i], moe_w3[i], moe_w2[i])
        if ctx_needed:
            xc = xc + cgt1 * oc
            hc = modulate(rms_norm(xc, norm2_g[i]), csh2, csc2)
            xc = xc + cgt2 * expert_choice_ffn(hc, moe_router[i], moe_w1[i], moe_w3[i], moe_w2[i])
    return xl


def setup_inputs(seed=0):
    out = dict(first_inputs(seed))
    for name, value in second_inputs(seed + 1).items():
        if name != "x":
            out[name + "_2"] = value
    return out


def reference(
    x, p, positions, w_in, b_gate, w_ret_out, w_dil_out, w_o, g_pre_mix, g_post_mix, g_pre_mlp,
    g_post_mlp, w_up, w_down, g_pre_ple, w_ple_gate, b_ple_gate, w_ple_in, g_post_ple, c_2,
    ctx_2, c_ctx_2, norm1_g_2, norm2_g_2, ada_w_2, ada_b_2, na_w_qkv_2, na_q_g_2, na_k_g_2,
    na_rpb_2, na_w_o_2, rw_mix_2, rw_w_r_2, rw_w_k_2, rw_w_v_2, rw_w0_2, rw_w1_2, rw_w2_2,
    rw_a0_2, rw_a1_2, rw_a2_2, rw_g1_2, rw_g2_2, rw_k_k_2, rw_k_a_2, rw_r_k_2, rw_ln_g_2,
    rw_ln_b_2, rw_w_o_2, mla_w_down_2, mla_q_norm_g_2, mla_kv_norm_g_2, mla_w_uq_2, mla_w_ukv_2,
    mla_qn_g_2, mla_qr_g_2, mla_kn_g_2, mla_kr_g_2, mla_w_o_2, swa_w_qkv_2, swa_q_g_2,
    swa_k_g_2, swa_sink_2, swa_w_o_2, moe_router_2, moe_w1_2, moe_w3_2, moe_w2_2,
):
    x = first_block(
        x, p, positions, w_in, b_gate, w_ret_out, w_dil_out, w_o, g_pre_mix, g_post_mix,
        g_pre_mlp, g_post_mlp, w_up, w_down, g_pre_ple, w_ple_gate, b_ple_gate, w_ple_in,
        g_post_ple,
    )
    return second_block(
        x, c_2, ctx_2, c_ctx_2, norm1_g_2, norm2_g_2, ada_w_2, ada_b_2, na_w_qkv_2, na_q_g_2,
        na_k_g_2, na_rpb_2, na_w_o_2, rw_mix_2, rw_w_r_2, rw_w_k_2, rw_w_v_2, rw_w0_2, rw_w1_2,
        rw_w2_2, rw_a0_2, rw_a1_2, rw_a2_2, rw_g1_2, rw_g2_2, rw_k_k_2, rw_k_a_2, rw_r_k_2,
        rw_ln_g_2, rw_ln_b_2, rw_w_o_2, mla_w_down_2, mla_q_norm_g_2, mla_kv_norm_g_2,
        mla_w_uq_2, mla_w_ukv_2, mla_qn_g_2, mla_qr_g_2, mla_kn_g_2, mla_kr_g_2, mla_w_o_2,
        swa_w_qkv_2, swa_q_g_2, swa_k_g_2, swa_sink_2, swa_w_o_2, moe_router_2, moe_w1_2,
        moe_w3_2, moe_w2_2,
    )


_drawn_inputs = setup_inputs


def setup_inputs(seed=0):
    import zlib

    import numpy as np

    out = dict(_drawn_inputs(seed))
    spreads = {}
    factors = {'b_gate': 8.0,
     'g_post_mix': 4.268,
     'g_pre_mlp': 4.537,
     'g_post_mlp': 5.379,
     'g_pre_ple': 8.0,
     'b_ple_gate': 8.0,
     'g_post_ple': 5.427,
     'norm1_g_2': 3.559,
     'norm2_g_2': 4.53,
     'ada_b_2': 5.082,
     'na_q_g_2': 8.0,
     'na_k_g_2': 8.0,
     'na_rpb_2': 8.0,
     'rw_w1_2': 8.0,
     'rw_w2_2': 8.0,
     'rw_a0_2': 3.246,
     'rw_a1_2': 3.929,
     'rw_a2_2': 3.831,
     'rw_k_k_2': 11.959,
     'rw_ln_g_2': 22.198,
     'rw_ln_b_2': 64.0}
    for name, (base, spread) in spreads.items():
        noise = np.random.default_rng([zlib.crc32(name.encode()), seed]).standard_normal(out[name].shape)
        drawn = base * np.exp(spread * noise) if base else spread * noise
        out[name] = jnp.asarray(drawn.astype(out[name].dtype))
    for name, factor in factors.items():
        out[name] = (out[name] * factor).astype(out[name].dtype)
    return out
```

```python
from contextlib import ExitStack

import numpy as np
import concourse.bass as bass
from concourse import mybir

F32 = mybir.dt.float32
I32 = mybir.dt.int32
ALU = mybir.AluOpType
ACT = mybir.ActivationFunctionType
AX = mybir.AxisListType.X

P = 128
D = 1024
KD = D // P
SEQ = 512
LT = SEQ // P
CTX = 256
CT = CTX // P
NT = LT + CT
TOK = SEQ + CTX
W = 512
EPS = 1e-6
BIG = 1e30

RET_HEADS, RET_QK, RET_V = 4, 256, 512
DIL_SLOTS, DIL_GROUPS, HD = 8, 3, 64
DIL_STRIDE = 4
ROPE8 = 8
D_FF = 4096
PLE = 256
COL_RQ, COL_RK, COL_RV, COL_RG = 0, 1024, 2048, 4096
COL_DIL = 6144
COL_GATE = COL_DIL + 3 * DIL_GROUPS * DIL_SLOTS * HD

NA_HEADS = 16
STRIP = 32
BLOCKS = 4
GRID = 64
ROWS = SEQ // GRID

EXPERTS = 16
CAP_L, CAP_C = 2 * SEQ // EXPERTS, 2 * CTX // EXPERTS
SLOTS = CAP_L + CAP_C
D_EXP = 1024

RW_PAIRS = 8
CH = 64
GN_EPS = 64e-5
RPB_PAD = 32
RING = 3
SLOT = KD * W


def constants():
    c = {}
    eye = np.eye(P, dtype=np.float64)
    c["ident"] = eye
    f = np.arange(P)
    c["ret_freq"] = (1.0 / (10000.0 ** (f / (P - 1.0))))[:, None]
    c["dil_freq"] = np.broadcast_to(500000.0 ** (-np.arange(0, 16, 2) / 16.0), (P, ROPE8))
    dec = np.zeros((P, RET_HEADS, SEQ))
    for h in range(RET_HEADS):
        g = np.log1p(-(2.0 ** (-5.0 - h)))
        dist = np.arange(SEQ)[None, :] - np.arange(P)[:, None]
        dec[:, h] = np.where(dist >= 0, np.exp(np.maximum(dist, 0) * g), 0.0) * RET_QK ** -0.5
    c["ret_decay"] = dec
    m = np.full((P, DIL_STRIDE, 6, P), -BIG)
    l = np.arange(P)
    for s in range(DIL_STRIDE):
        t = DIL_STRIDE * l + s
        for s2 in range(DIL_STRIDE):
            d = t[:, None] - (DIL_STRIDE * l + s2)[None, :]
            m[:, s, s2][(d >= 0) & (d <= 128)] = 0
        d = l[:, None] - l[None, :]
        m[:, s, 4][d >= 0] = 0
        m[:, s, 5][(d >= 0) & (d % 4 == 0)] = 0
    c["dil_mask"] = m
    m = np.full((P, 3, ROWS, STRIP), -BIG)
    cc = np.arange(P) % 16
    kk = np.arange(STRIP)[None, :]
    for n, j in enumerate((0, 1, 3)):
        qcol = 16 * j + cc
        lo = np.clip(qcol - 8, 0, GRID - 16) - np.clip(16 * j - 8, 0, GRID - STRIP)
        ok = (kk >= lo[:, None]) & (kk < lo[:, None] + 16)
        m[:, n][np.broadcast_to(ok[:, None, :], (P, ROWS, STRIP))] = 0
    c["na_mask"] = m
    c["slot_no"] = np.broadcast_to(np.arange(CAP_L), (P, CAP_L))
    a, b = np.arange(P)[:, None], np.arange(P)[None, :]
    same = a // CH == b // CH
    k = np.exp(-0.5)
    c["rw_sum"] = np.stack([(same & (a <= b)) * k, (same & (a >= b)) * k], 1)
    c["rw_sum_ex"] = np.stack([(same & (a < b)) * k, (same & (a > b)) * k], 1)
    c["rw_blocks"] = same
    c["rw_ind"] = np.stack([(f // CH == n) * k for n in range(2)], 1)
    c["rw_mask"] = np.stack([np.stack([same & (a < b), same & (a <= b)], 1), np.stack([same & (a > b), same & (a >= b)], 1)], 1)
    lv, lvt = np.zeros((P, 2, 6, P)), np.zeros((P, 2, 6, P))
    for n in range(6):
        half = 1 << n
        join = (a // (2 * half) == b // (2 * half)) & (a // half % 2 == 1) & (b // half % 2 == 0)
        lv[:, 0, n], lv[:, 1, n] = join, join.T
        lvt[:, 0, n], lvt[:, 1, n] = join.T, join
    c["rw_join"], c["rw_join_t"] = lv[:, :, 0], lvt
    return {k: np.ascontiguousarray(np.asarray(v, np.float32).reshape(P, -1)) for k, v in c.items()}


class Job:

    def __init__(self, number, bank, width, engine, count, before):
        self.number, self.bank, self.width = number, bank, width
        self.engine, self.count, self.before = engine, count, before


class JobPlan:

    def __init__(self):
        self.jobs, self.at, self.holder, self.taken = {}, 0, [None] * 8, {"act": 0, "dve": 0}

    def add(self, engine, *key, width=1):
        if width == 2 and self.at % 2:
            self.at += 1
        bank = self.at % 8
        before = [self.holder[bank + i] for i in range(width) if self.holder[bank + i]]
        self.taken[engine] += 1
        job = Job(len(self.jobs), bank, width, engine, self.taken[engine], before)
        for i in range(width):
            self.holder[bank + i] = job
        self.at += width
        assert key not in self.jobs, key
        self.jobs[key] = job

    def __getitem__(self, key):
        return self.jobs[key]


DIL_STEPS = [(g, kind) for g in range(DIL_GROUPS) for kind in range(3)]
DIL_TILES = DIL_SLOTS * DIL_STRIDE
TILES = [NT, LT]
NA_STEPS = 4 * NT
NA_UNITS = NA_HEADS * NT
NORMS = {"dil": LT, "mlp": LT, "ple": LT, "na": NT, "moe0": NT, "rw": NT, "moe1": LT}


def plan_jobs():
    plan = JobPlan()

    def norm(use):
        for k in range(KD):
            plan.add("act", "turn", use, 0, k)
        if NORMS[use] == NT:
            for k in range(KD):
                plan.add("act", "turn", use, 1, k)

    norm("dil")
    for i in range(len(DIL_STEPS) + 1):
        if i < len(DIL_STEPS):
            for c in range(DIL_STRIDE):
                plan.add("act", "dil_proj", i, c)
        if i >= 1 and DIL_STEPS[i - 1][1] < 2:
            for c in range(DIL_STRIDE):
                plan.add("act", "dil_turn", i - 1, c)
    for i in range(DIL_TILES + 2):
        if i < DIL_TILES:
            plan.add("dve", "dil_score", i, width=2)
        if 1 <= i <= DIL_TILES:
            plan.add("act", "dil_pt", i - 1, width=2)
        if i >= 2:
            plan.add("dve", "dil_out", i - 2)
    for c in range(DIL_STRIDE):
        plan.add("act", "dil_ot", c)

    for h in range(RET_HEADS):
        for m in range(4):
            plan.add("dve", "ret_qk", h, m)
        for t in range(LT):
            plan.add("act", "ret_v", h, t)
        for t in range(LT):
            plan.add("act", "ret_g", h, t)
        if h >= 1:
            for f in range(4):
                plan.add("act", "ret_turn", h - 1, f)
        for j in range(LT):
            plan.add("dve", "ret_score", h, j)
        for t in range(LT):
            plan.add("dve", "ret_out", h, t)
    for f in range(4):
        plan.add("act", "ret_turn", RET_HEADS - 1, f)

    for n in range(2):
        for b in range(2):
            for f in range(4):
                plan.add("act", "mix_gate", b, n, f)
        for f in range(4):
            plan.add("dve", "mix_ret", n, f)
    for f in range(KD):
        plan.add("dve", "mix_dil", f)
    for n in range(2):
        for t in range(LT):
            plan.add("act", "mix_o", n, t)

    norm("mlp")
    for f in range(D_FF // P):
        plan.add("act", "up", f)
    for n in range(2):
        for t in range(LT):
            plan.add("act", "down", n, t)

    norm("ple")
    for d in range(PLE // P):
        plan.add("act", "ple_turn", d)
    for n in range(2):
        for t in range(LT):
            plan.add("act", "ple_gate", n, t)
    for n in range(2):
        for t in range(LT):
            plan.add("dve", "ple_in", n, t)

    for l in range(2):
        for n in range(6 * D // W):
            plan.add("dve", "ada", l, n)
    for l in range(2):
        plan.add("act", "ada_turn", l)

    norm("na")
    for i in range(NA_STEPS + 2):
        if i < NA_STEPS:
            plan.add("act", "na_proj", i)
        if i >= 2:
            plan.add("act", "na_turn", i - 2)
    for n in range(2):
        for t in range(NT):
            plan.add("act", "na_v", n, t)
    for i in range(NA_UNITS + 2):
        if i < NA_UNITS:
            plan.add("dve", "na_score", i)
        if 1 <= i <= NA_UNITS:
            plan.add("act", "na_pt", i - 1)
        if i >= 2:
            plan.add("dve", "na_out", i - 2)
    for t in range(NT):
        plan.add("act", "na_ot", t, width=2)
    for n in range(2):
        for t in range(NT):
            plan.add("dve", "na_o", n, t)
    plan_experts(plan, norm, 0)
    plan_recurrence(plan, norm)
    plan_experts(plan, norm, 1)
    return plan


def plan_experts(plan, norm, l):
    norm(f"moe{l}")
    plan.add("dve", "moe_logit", l)
    plan.add("dve", "moe_afft", l, width=2)
    plan.add("dve", "moe_slot", l)

    def gather(e):
        for half in range(2):
            plan.add("act", "moe_gather", l, e, half)
        plan.add("act", "moe_selt", l, e, width=2)

    def scatter(e):
        for t in range(TILES[l]):
            for n in range(2):
                plan.add("dve", "moe_add", l, e, t, n)

    gather(0)
    for e in range(EXPERTS):
        for n in range(2):
            plan.add("act", "moe_h1", l, e, n)
            plan.add("dve", "moe_h3", l, e, n)
        if e >= 1:
            scatter(e - 1)
        if e + 1 < EXPERTS:
            gather(e + 1)
        plan.add("act", "moe_ht", l, e, width=2)
        for n in range(2):
            plan.add("act", "moe_y", l, e, n)
    scatter(EXPERTS - 1)


RW_RANK = {"w": 2 * CH, "a": 2 * CH, "g": P}


def plan_recurrence(plan, norm):
    norm("rw")
    for q in "rkv":
        for n in range(2):
            for t in range(LT if q == "r" else NT):
                plan.add("act", "rw_proj", q, n, t)
    for q in "wag":
        plan.add("act", "rw_low", q, width=2)
        for z in range(1 if q == "g" else 2):
            for n in range(2):
                for t in range(LT if q == "g" else NT):
                    plan.add("act", "rw_high", q, z, n, t)
    for p in range(RW_PAIRS):
        for z in range(2):
            plan.add("act", "rw_sum", p, z, width=2)
            plan.add("act", "rw_sum_ex", p, z, width=2)
            plan.add("act", "rw_end", p, z)
            for x in range(4):
                plan.add("act", "rw_turn", p, z, x, width=2)
        for t in range(NT):
            for z in range(2):
                plan.add("dve", "rw_ab", p, t, z, width=2)
                plan.add("dve", "rw_a", p, t, z, width=2)
            for lv in range(1, 6):
                for z in range(2):
                    plan.add("act", "rw_x", p, t, z, lv)
                for z in range(2):
                    plan.add("dve", "rw_join", p, t, z, lv)
            for z in range(2):
                plan.add("act", "rw_gv", p, t, z)
                plan.add("act", "rw_tk", p, t, z)
            for z in range(2):
                plan.add("act", "rw_tgv", p, t, z)
        for i in range(2 * NT):
            for z in range(2):
                plan.add("dve", "rw_u", p, i, z)
            for z in range(2):
                plan.add("dve", "rw_state", p, i, z)
                if rw_chunk(i, z)[0] < LT:
                    plan.add("act", "rw_y", p, i, z)
        plan.add("act", "rw_ot", p)
    for n in range(2):
        for t in range(LT):
            plan.add("dve", "rw_o", n, t)


def rw_chunk(i, z):
    tile, c = divmod(i, 2)
    if z == 0:
        return (LT + tile, c) if tile < CT else (tile - CT, c)
    return (LT + CT - 1 - tile, 1 - c) if tile < CT else (LT - 1 - (tile - CT), 1 - c)


def plan_weights(a):
    def square(w, n):
        return [(w[:, n * W:(n + 1) * W].rearrange("(k p) n -> p k n", p=P), 0, KD, W)]

    loads = []
    w_in = a["w_in"]
    for i, (g, kind) in enumerate(DIL_STEPS):
        c0 = COL_DIL + kind * DIL_GROUPS * W + g * W
        loads.append(("dil_proj", square(w_in[:, c0:c0 + W], 0), ("dil_proj", i, DIL_STRIDE - 1)))
    for h in range(RET_HEADS):
        q, k = (w_in[:, c + h * RET_QK:c + (h + 1) * RET_QK].rearrange("(k p) n -> p k n", p=P) for c in (COL_RQ, COL_RK))
        loads.append(("ret_qk", [(q, 0, KD, RET_QK), (k, KD * RET_QK, KD, RET_QK)], ("ret_qk", h, 3)))
        loads.append(("ret_v", square(w_in[:, COL_RV:], h), ("ret_v", h, LT - 1)))
        loads.append(("ret_g", square(w_in[:, COL_RG:], h), ("ret_g", h, LT - 1)))
    for n in range(2):
        loads.append(("mix_gate", square(w_in[:, COL_GATE:], n), ("mix_gate", 0, n, 3)))
        loads.append(("mix_gate", square(w_in[:, COL_GATE + D:], n), ("mix_gate", 1, n, 3)))
        for half in range(2):
            loads.append(("mix_ret", square(a["w_ret_out"][half * D:(half + 1) * D], n), ("mix_ret", n, 3) if half else None))
    loads.append(("mix_dil", [(a["w_dil_out"].rearrange("(k p) n -> p k n", p=P), 0, 4, D)], ("mix_dil", KD - 1)))
    for n in range(2):
        loads.append(("mix_o", square(a["w_o"], n), ("mix_o", n, LT - 1)))
    for n in range(D_FF // W):
        loads.append(("up", square(a["w_up"], n), ("up", 4 * n + 3)))
    for n in range(2):
        for part in range(4):
            loads.append(("down", square(a["w_down"][part * D:(part + 1) * D], n), ("down", n, LT - 1) if part == 3 else None))
    for n in range(2):
        loads.append(("ple_gate", square(a["w_ple_gate"], n), ("ple_gate", n, LT - 1)))
    loads.append(("ple_in", [(a["w_ple_in"].rearrange("(k p) n -> p k n", p=P), 0, 2, D)], ("ple_in", 1, LT - 1)))
    for l in range(2):
        for n in range(6 * D // W):
            loads.append(("ada", square(a["ada_w"][l], n), ("ada", l, n)))
    for n in range(4):
        loads.append(("na_proj", square(a["na_w_qkv"], n), ("na_proj", (n + 1) * NT - 1)))
    for n in range(2):
        loads.append(("na_v", square(a["na_w_qkv"][:, 2 * D:], n), ("na_v", n, NT - 1)))
    for n in range(2):
        loads.append(("na_o", square(a["na_w_o"], n), ("na_o", n, NT - 1)))

    def experts(l):
        for e in range(EXPERTS):
            for n in range(2):
                loads.append(("moe_w1", square(a["moe_w1"][l, e], n), ("moe_h1", l, e, n)))
                loads.append(("moe_w3", square(a["moe_w3"][l, e], n), ("moe_h3", l, e, n)))
            for n in range(2):
                loads.append(("moe_w2", square(a["moe_w2"][l, e], n), ("moe_y", l, e, n)))

    experts(0)
    for q in "rkv":
        for n in range(2):
            loads.append(("rw_proj", square(a[f"rw_w_{q}"], n), ("rw_proj", q, n, (LT if q == "r" else NT) - 1)))
    for q in "wa":
        pieces = [(a[f"rw_{q}1"].rearrange("(k p) r -> p k r", p=P), 0, KD, 2 * CH),
                  (a[f"rw_{q}2"].rearrange("r (o d) -> r o d", o=1), KD * 2 * CH, 1, D)]
        pieces += [(a[f"rw_{q}0"][z:z + 1], KD * 2 * CH + D, 1, D, z * CH) for z in range(2)]
        loads.append((f"rw_low_{q}", pieces, ("rw_high", q, 1, 1, NT - 1)))
    loads.append(("rw_low_g", [(a["rw_g1"].rearrange("(k p) r -> p k r", p=P), 0, KD, P),
                               (a["rw_g2"].rearrange("r (o d) -> r o d", o=1), KD * P, 1, D)], ("rw_high", "g", 0, 1, LT - 1)))
    for n in range(2):
        loads.append(("rw_o", square(a["rw_w_o"], n), ("rw_o", n, LT - 1)))
    experts(1)
    return loads


COLUMNS = {}
for _name, _n in (("g_pre_mix", KD), ("b_gate_r", KD), ("b_gate_a", KD), ("g_pre_mlp", KD), ("g_pre_ple", KD),
                  ("norm_g", 4 * KD), ("na_q_g", 1), ("na_k_g", 1), ("rw_mix", 6 * KD), ("cond", 2 * KD)):
    COLUMNS[_name] = (sum(n for _, n in COLUMNS.values()), _n)
N_COLUMNS = sum(n for _, n in COLUMNS.values())


def build(nc, a, out, debug=None):
    plan = plan_jobs()
    loads = plan_weights(a)
    ctx = ExitStack()
    signals = {}

    def sem(name):
        if name not in signals:
            signals[name] = nc.alloc_semaphore(name)
        return signals[name]

    def sb(name, *shape, dt=F32):
        return ctx.enter_context(nc.sbuf_tensor(name, [P, *shape], dt))

    h = sb("h", NT, D)
    ring = sb("ring", RING, SLOT)
    ident = sb("ident", P)
    ones = sb("ones", P)
    cols = sb("cols", N_COLUMNS)
    stats = sb("stats", 64)
    psum = [ctx.enter_context(nc.psum_tensor(f"bank{i}", [P, 2 * W], F32)) for i in range(4)]
    ARENA = 32512
    arena = sb("arena", ARENA)

    class Carve:

        def __init__(self, at=0):
            self.at = at

        def take(self, *shape, dt=F32):
            n = int(np.prod(shape))
            assert self.at + n <= ARENA, (self.at, n)
            v = arena[:, self.at:self.at + n]
            self.at += n
            if dt != F32:
                v = v.bitcast(dt)
            names = "abcd"[:len(shape)]
            if len(shape) > 1:
                v = v.rearrange(f"p ({' '.join(names)}) -> p {' '.join(names)}", **dict(zip(names[1:], shape[1:])))
            return v

    def col(name, k=0):
        at, _ = COLUMNS[name]
        return cols[:, at + k:at + k + 1]

    def bank(job):
        lo = job.bank % 2 * W
        return psum[job.bank // 2][:, lo:lo + job.width * W]

    filled = sem("psum_filled")
    freed = {"act": sem("psum_freed_act"), "dve": sem("psum_freed_dve")}
    landed = [sem(f"weights_landed_{i}") for i in range(RING)]
    used = sem("weights_used")

    def full(eng, *key):
        eng.wait_ge(filled, plan[key].number + 1)
        return bank(plan[key])

    def taken(eng, *key):
        eng.wait_ge(freed[plan[key].engine], plan[key].count)

    def free(ins, *key):
        done[plan[key].engine] += 1
        assert done[plan[key].engine] == plan[key].count, key
        ins.then_inc(freed[plan[key].engine], 1)

    done = {"act": 0, "dve": 0, "pe": 0, "weights": 0}

    m = Carve()
    uT = m.take(KD, SEQ)
    yaT = h[:, LT:NT, :].rearrange("p t (f c) -> p (t f) c", f=2)
    ret_cos, ret_sin = m.take(SEQ), m.take(SEQ)
    dil_cos, dil_sin = m.take(DIL_STRIDE, ROPE8), m.take(DIL_STRIDE, ROPE8)
    part = m.at
    n = Carve(part)
    ang, turns, angs = n.take(544), n.take(544), n.take(544)
    pos_i, pos_f = n.take(SEQ, dt=I32), n.take(SEQ)
    pos_ci, pos_cf = n.take(DIL_STRIDE, dt=I32), n.take(DIL_STRIDE)
    ret_freq, dil_freq = n.take(1), n.take(ROPE8)
    n = Carve(part)
    dil_tmp = n.take(DIL_STRIDE, W)
    dil_rot = n.take(4, 2, DIL_SLOTS, ROPE8)
    dil_o = dil_tmp
    qT, kT = n.take(12, SEQ), n.take(12, SEQ)
    v_at = n.at
    vR = n.take(DIL_STRIDE, 3 * W)
    xn_dil = Carve(v_at).take(LT, D)
    dil_mask = n.take(DIL_STRIDE, 6 * P)
    dil_s = n.take(2, 6 * P)
    dil_p = n.take(2, 6 * P)
    n = Carve(part)
    yrT = n.take(16, SEQ)
    mix_from = n.at
    rqT, rkT = n.take(2, SEQ), n.take(2, SEQ)
    rot_a, rot_b = n.take(SEQ), n.take(SEQ)
    rv, rg, rs, ry = (n.take(LT, W) for _ in range(4))
    decay = n.take(RET_HEADS, SEQ)
    n = Carve(mix_from)
    gate_r, gate_a, mixT = n.take(KD, SEQ), n.take(KD, SEQ), n.take(KD, SEQ)
    mix_t = n.take(SEQ)
    F_mix = n.take(LT, D)
    gb_mix = n.take(D)
    n = Carve()
    vT = n.take(KD, SEQ)
    xn_mlp = n.take(LT, D)
    ffT = n.take(D_FF // P, SEQ)
    F_mlp = n.take(LT, D)
    gb_mlp = n.take(D)
    n = Carve()
    wT = n.take(KD, SEQ)
    xn_ple = n.take(LT, D)
    pR, pT = n.take(LT, PLE), n.take(PLE // P, SEQ)
    gate_p = n.take(LT, D)
    F_ple = n.take(LT, D)
    gb_ple = n.take(D)
    b_ple = n.take(D)
    junk = sb("junk", D)
    cond = sb("cond", 2, KD)
    mod = sb("mod", 2, 2, 6, KD)
    mod_a = sb("mod_a", 2, 2, 2, KD)
    n = Carve()
    xn_na, hT_na = n.take(NT, D), n.take(KD, TOK)
    ada_m = n.take(2, 6 * D)
    mod_rows = n.take(2, P)
    n = Carve()
    naq = n.take(KD, TOK)
    n.take(KD, TOK)
    na_o = hT_na.rearrange("p k t -> p (k t)").rearrange("p (t d) -> p t d", d=D)
    nak = n.take(KD, TOK)
    na_vs = n.take(2 * BLOCKS, D)
    na_vc = n.take(CT, D)
    na_v = Carve(n.at).take(LT, W)
    na_s, na_p = n.take(2, W), n.take(2, W)
    na_bias = [n.take(4, 2 * P), junk[:, :].rearrange("p (a b) -> p a b", a=4)]
    na_mask = n.take(3, 2 * P)
    na_oT = naq
    na_gate = nak.rearrange("p k t -> p (k t)")[:, 0:2 * D].rearrange("p (s d) -> p s d", d=D)
    na_t = nak.rearrange("p k t -> p (k t)")[:, 2 * D:3 * D].rearrange("p (s d) -> p s d", d=W)
    n = Carve()
    xn_moe = n.take(NT, D)
    moe_after = n.at
    hT_moe = n.take(KD, TOK)
    router = n.take(KD, EXPERTS)
    logit, aff = n.take(NT, EXPERTS), n.take(NT, EXPERTS)
    affT, workT, sumT = n.take(TOK), n.take(TOK), n.take(TOK)
    top8 = n.take(8)
    slot = n.take(NT, EXPERTS)
    slot_no = n.take(CAP_L)
    moe_gate = n.take(2, D)
    keep = n.at
    acc = Carve(moe_after).take(NT, D)
    n = Carve(keep)
    sel_l, sel_c = n.take(LT, CAP_L), n.take(CT, CAP_C)
    sel_g = n.take(NT, SLOTS)
    selT = n.take(2, NT * P)
    xinT = n.take(2, KD, SLOTS)
    s1, hid, hidT = n.take(D), n.take(D), n.take(KD, SLOTS)
    y_moe = n.take(2, D)
    n = Carve()
    hT_rw = n.take(KD, TOK)
    xx = n.take(KD, TOK)
    xs = [n.take(KD, TOK), n.take(KD, TOK)]
    xn_rw = xs[1].rearrange("p k t -> p (k t)").rearrange("p (t d) -> p t d", d=D)
    lowT = n.take(TOK)
    staging = n.take(4, W)
    ring_flat = ring[:, :, :].rearrange("p a b -> p (a b)")
    RW_IN, at = {}, 0
    for q in ("r", "g", "k", "v", "w0", "w1", "a0", "a1"):
        nt = LT if q in "rg" else NT
        RW_IN[q] = [ring_flat[:, b * 5632 + at:b * 5632 + at + nt * P].rearrange("p (t d) -> p t d", d=P) for b in range(2)]
        at += nt * P
    assert at == 5632
    n = Carve()
    c_sum, c_sum_ex, c_ind = n.take(2, P), n.take(2, P), n.take(2)
    c_mask, c_join, c_join_t = n.take(2, 2, P), n.take(2, P), n.take(2, 6, P)
    c_blocks = n.take(P)
    rw_rows = n.take(2, 5, P)
    kh, bh, th = ([n.take(NT, P) for _ in range(2)] for _ in range(3))
    xT = [n.take(2 * TOK + TOK + SEQ) for _ in range(2)]
    KT, RT, BT, TT = ([x[:, lo:hi] for x in xT] for lo, hi in ((0, TOK), (TOK, TOK + SEQ), (TOK + SEQ, 2 * TOK + SEQ), (2 * TOK + SEQ, 3 * TOK + SEQ)))
    tkT, tgv = ([n.take(NT, P) for _ in range(2)] for _ in range(2))
    rbT, rtT = ([n.take(LT, 2, P) for _ in range(2)] for _ in range(2))
    w_end = [n.take(2 * NT) for _ in range(2)]
    temp = n.at
    e_neg, e_pos, e_ex, kk, rw_t = (n.take(NT, P) for _ in range(5))
    n = Carve(temp)
    at_off = [n.take(2, 5, P) for _ in range(2)]
    aT, gT = ([n.take(2, P) for _ in range(2)] for _ in range(2))
    gv = [n.take(P) for _ in range(2)]
    inv = [n.take(2, 2, P) for _ in range(2)]
    xl = [n.take(5, 2, P) for _ in range(2)]
    state, u = [n.take(2, P) for _ in range(2)], [n.take(P) for _ in range(2)]
    zT_hi = n.take(4, SEQ)
    zT_lo = h[:, LT:NT, :].rearrange("p t (f c) -> p (t f) c", f=2)
    n = Carve(0)
    yz = [BT[z][:, 0:SEQ].rearrange("p (t d) -> p t d", d=P) for z in range(2)]
    yd = [TT[z][:, 0:SEQ].rearrange("p (t d) -> p t d", d=P) for z in range(2)]
    rw_s = sb("rw_s", 48)
    n = Carve(ARENA - 4 * SEQ - 2 * D - D)
    rw_gate, rw_ot = n.take(D), n.take(2, W)

    def zT(f):
        return zT_lo[:, f, :] if f < 4 else zT_hi[:, f - 4, :]

    mod_dram = nc.dram_tensor("mod_dram", [2, 2, 6 * D], F32).ap()
    spill = {q: nc.dram_tensor(f"spill_{q}", [LT if q in "rg" else NT, P, D], F32).ap()
             for q in ("r", "g", "k", "v", "w0", "w1", "a0", "a1")}
    rpb_strip = nc.dram_tensor("rpb_strip", [NA_HEADS, 3, 16, 15 * STRIP], F32).ap()

    norm_of = {"dil": (xn_dil, uT), "mlp": (xn_mlp, vT), "ple": (xn_ple, wT), "na": (xn_na, hT_na), "moe0": (xn_moe, hT_moe),
               "rw": (xn_rw, hT_rw), "moe1": (xn_moe, hT_moe)}
    norm_mod = {"na": (0, 0), "moe0": (0, 1), "rw": (1, 0), "moe1": (1, 1)}

    def modulation(use, s, k):
        l, n = norm_mod[use]
        return mod_a[:, l, s, n, k:k + 1], mod[:, l, s, 3 * n, k:k + 1]

    norm_scale = {"dil": "g_pre_mix", "mlp": "g_pre_mlp", "ple": "g_pre_ple"}
    USES = list(NORMS)
    tiles_before = {u: sum(NORMS[x] for x in USES[:i]) for i, u in enumerate(USES)}
    POSTS = ["mix", "mlp", "ple"]
    post_of = {"mix": (F_mix, gb_mix), "mlp": (F_mlp, gb_mlp), "ple": (F_ple, gb_ple)}
    last_job = {"mix": ("mix_o", 1, LT - 1), "mlp": ("down", 1, LT - 1), "ple": ("ple_in", 1, LT - 1)}

    def h_ready(eng, use):
        i = USES.index(use)
        if i == 0:
            eng.wait_ge(sem("x_landed"), 16)
        elif i <= len(POSTS):
            eng.wait_ge(sem("post_added"), i * LT)
            if use == "na":
                eng.wait_ge(sem("ctx_landed"), 16)
        elif use == "moe0":
            eng.wait_ge(sem("na_added"), 2 * NT)
        elif use == "rw":
            eng.wait_ge(sem("moe_added"), NT)
        else:
            eng.wait_ge(sem("rw_added"), 2 * LT)

    strip0 = [int(np.clip(16 * j - 8, 0, GRID - STRIP)) for j in range(BLOCKS)]

    def spilled_jobs():
        for q in "rkv":
            for n in range(2):
                for t in range(LT if q == "r" else NT):
                    yield q, n, t, ("rw_proj", q, n, t)
        for q in "wag":
            for z in range(1 if q == "g" else 2):
                for n in range(2):
                    for t in range(LT if q == "g" else NT):
                        yield (q if q == "g" else f"{q}{z}"), n, t, ("rw_high", q, z, n, t)

    def unit(step):
        p, rest = divmod(step, 2 * NT)
        return (p, *divmod(rest, 2))

    def halves(x, lv, z, transposed=False):
        b = 1 << lv
        v = x.rearrange("p h (a two b) -> p h a two b", two=2, b=b)
        return v[:, :, :, (z + transposed) % 2, :]

    block = ctx.enter_context(nc.Block())
    first_rw_o = [name for name, _, _ in loads].index("rw_o")

    @block.sync
    def _(sp):
        sp.dma_start(h[:, 0:LT, :], a["x"].rearrange("(t p) d -> p t d", p=P)).then_inc(sem("x_landed"), 16)
        goes_on = 0
        for i, (_, pieces, _) in enumerate(loads):
            if i >= RING:
                last = loads[i - RING][2]
                if last:
                    full(sp, *last)
                else:
                    goes_on += 1
                    sp.wait_ge(used, goes_on)
            if i == first_rw_o:
                taken(sp, "rw_ot", RW_PAIRS - 1)
            for src, at, k, n, *row in pieces:
                if row:
                    dst = ring[row[0]:row[0] + 1, i % RING, at:at + n]
                else:
                    dst = ring[:, i % RING, at:at + k * n].rearrange("p (k n) -> p k n", n=n)
                sp.dma_start(dst, src).then_inc(landed[i % RING], 16)
        for t in range(LT):
            sp.wait_ge(sem("moe_added"), NT + t + 1)
            sp.dma_start(out[t * P:(t + 1) * P, :], h[:, t, :]).then_inc(sem("out_stored"), 16)
        sp.wait_ge(sem("out_stored"), 16 * LT)

    slot_count, landed_at = [0] * RING, []
    for i, (_, pieces, _) in enumerate(loads):
        slot_count[i % RING] += 16 * len(pieces)
        landed_at.append(slot_count[i % RING])

    @block.gpsimd
    def _(pool):
        def load(dst, name, signal, n=None):
            src = a[name]
            pool.dma_start(dst, src).then_inc(sem(signal), 16)

        nc.gpsimd.memset(ones[:, :], 1.0).then_inc(sem("ones_set"), 1)
        load(ident[:, :], "ident", "const_landed")
        load(cols[:, :], "cols", "const_landed")
        load(pos_i, "pos_row", "const_landed")
        load(pos_ci, "pos_col", "const_landed")
        load(ret_freq, "ret_freq", "const_landed")
        load(dil_freq, "dil_freq", "const_landed")
        load(dil_mask.rearrange("p a b -> p (a b)"), "dil_mask", "mask_landed")
        taken(pool, "dil_ot", DIL_STRIDE - 1)
        load(decay.rearrange("p a b -> p (a b)"), "ret_decay", "decay_landed")
        for u in POSTS:
            if u == "mix":
                taken(pool, "ret_turn", RET_HEADS - 1, 3)
            else:
                pool.wait_ge(sem("post_added"), POSTS.index(u) * LT)
            pool.dma_start(post_of[u][1], a[f"g_post_{u}"].partition_broadcast(P)).then_inc(sem("post_gain_landed"), 16)
            if u == "ple":
                pool.dma_start(pR, a["p"].rearrange("(t p) d -> p t d", p=P)).then_inc(sem("ple_landed"), 16)
                pool.dma_start(b_ple[0:1, :], a["b_ple_gate"].rearrange("(o d) -> o d", o=1)).then_inc(sem("ple_landed"), 16)
            if u == "mlp":
                pool.dma_start(h[:, LT:NT, :], a["ctx"].rearrange("(t p) d -> p t d", p=P)).then_inc(sem("ctx_landed"), 16)
        for n, j in enumerate((0, 1, 3)):
            off = int(np.clip(16 * j - 8, 0, GRID - STRIP)) - 16 * j
            for cc in range(16):
                lo = off - cc + 15 + RPB_PAD
                pool.dma_start(rpb_strip[:, n, cc, :].rearrange("h (r k) -> h r k", k=STRIP),
                               a["na_rpb"][:, :, lo:lo + STRIP]).then_inc(sem("strip_stored"), 16)
        pool.wait_ge(sem("post_added"), 3 * LT)
        for l in range(2):
            pool.dma_start(ada_m[0:2, l, :], a["ada_b"][l].partition_broadcast(2)).then_inc(sem("ada_bias_landed"), 16)
        for l in range(2):
            taken(pool, "ada", l, 6 * D // W - 1)
            pool.dma_start(mod_dram[l], ada_m[0:2, l, :]).then_inc(sem("mod_stored"), 16)
            pool.wait_ge(sem("mod_stored"), 16 * (l + 1))
            pool.dma_start(mod_rows[0:96, l, :], mod_dram[l].rearrange("s (r c) -> (s r) c", c=P)).then_inc(sem("mod_rows_landed"), 16)
        taken(pool, "ada_turn", 1)
        for n in range(2):
            for t in range(LT):
                taken(pool, "na_v", n, t)
                for j in range(BLOCKS):
                    for r in range(2):
                        to = (2 * t + r) % 4 * STRIP
                        pool.dma_start(na_vs[to:to + STRIP, 2 * j + t // 2, n * W:(n + 1) * W],
                                       na_v[r * GRID + strip0[j]:r * GRID + strip0[j] + STRIP, t, :]).then_inc(sem("na_strips_landed"), 16)
        pool.dma_start(na_mask.rearrange("p a b -> p (a b)"), a["na_mask"]).then_inc(sem("na_mask_landed"), 16)
        for b in range(2):
            nc.gpsimd.memset(na_bias[b][:, 3, :], 0.0).then_inc(sem("na_zeroed"), 1)
        pool.wait_ge(sem("strip_stored"), 16 * 48)
        pool.wait_ge(sem("na_mask_landed"), 16)
        for hd in range(NA_HEADS):
            if hd >= 2:
                taken(pool, "na_score", (hd - 1) * NT - 1)
            for r in range(ROWS):
                pool.dma_start(na_bias[hd % 2][16 * r:16 * r + 16, 0:3, :],
                               rpb_strip[hd, :, :, (7 - r) * STRIP:(15 - r) * STRIP].rearrange("n c k -> c n k")
                               ).then_inc(sem(f"na_bias_landed_{hd % 2}"), 16)
        taken(pool, "na_out", NA_UNITS - 1)
        for s in range(2):
            pool.dma_start(na_gate[:, s, :], mod_dram[0, s, 2 * D:3 * D].partition_broadcast(P)).then_inc(sem("na_gate_landed"), 16)

        def experts(l):
            h_ready(pool, f"moe{l}")
            pool.dma_start(router, a["moe_router"][l].rearrange("(k p) e -> p k e", p=P)).then_inc(sem("moe_landed"), 16)
            pool.dma_start(slot_no, a["slot_no"]).then_inc(sem("moe_landed"), 16)
            for s in range(2):
                pool.dma_start(moe_gate[:, s, :], mod_dram[l, s, 5 * D:6 * D].partition_broadcast(P)).then_inc(sem("moe_landed"), 16)

        experts(0)
        uses = [0] * 4
        for i, (q, n, t, key) in enumerate(spilled_jobs()):
            taken(pool, *key)
            pool.dma_start(spill[q][t, :, n * W:(n + 1) * W], staging[:, i % 4, :]).then_inc(sem(f"spilled_{i % 4}"), 16)
            uses[i % 4] += 16
        for i in range(4):
            pool.wait_ge(sem(f"spilled_{i}"), uses[i])
        taken(pool, "rw_low", "g")
        for dst, name in ((c_sum, "rw_sum"), (c_sum_ex, "rw_sum_ex"), (c_ind, "rw_ind"), (c_mask, "rw_mask"), (c_join, "rw_join"),
                          (c_join_t, "rw_join_t"), (c_blocks, "rw_blocks")):
            pool.dma_start(dst if len(dst.shape) == 2 else dst.rearrange("p a b -> p (a b)") if len(dst.shape) == 3 else
                           dst.rearrange("p a b c -> p (a b c)"), a[name]).then_inc(sem("rw_const_landed"), 16)
        for z in range(2):
            nc.gpsimd.memset(xl[z], 0.0).then_inc(sem("rw_zeroed"), 1)

        def load_pair(p):
            for q in RW_IN:
                pool.dma_start(RW_IN[q][p % 2], spill[q][:, :, p * P:(p + 1) * P].rearrange("t p d -> p t d")
                               ).then_inc(sem(f"rw_in_landed_{p % 2}"), 16)
            pool.dma_start(rw_rows[:, p % 2], a["rw_rows"][:, p * P:(p + 1) * P].partition_broadcast(P)
                           ).then_inc(sem(f"rw_in_landed_{p % 2}"), 16)

        load_pair(0)
        step = 0
        for p in range(RW_PAIRS):
            if p + 1 < RW_PAIRS:
                if p >= 1:
                    taken(pool, "rw_ot", p - 1)
                load_pair(p + 1)
            pool.wait_ge(sem("rw_const_landed"), 16 * 7)
            for t in range(NT):
                for z in range(2):
                    pool.wait_ge(sem("rw_at"), step + 1)
                    if step >= 2:
                        full(pool, "rw_join", *unit(step - 2), 5)
                    aT_b = [aT[z][:, hd, :].unsqueeze(1).to_broadcast([P, 5, P]) for hd in range(2)]
                    for hd in range(2):
                        nc.gpsimd.tensor_tensor(at_off[z][:, hd], aT_b[hd], c_join_t[:, z, 1:6, :], ALU.mult).then_inc(sem("rw_pool_step"), 1)
                    join = c_join_t[:, z, 0:1, :].to_broadcast([P, 2, P])
                    pool.wait_ge(sem("rw_pool_step"), 3 * step + 2)
                    nc.gpsimd.tensor_tensor(aT[z], aT[z], join, ALU.mult).then_inc(sem("rw_pool_step"), 1)
                    pool.wait_ge(sem("rw_pool_step"), 3 * step + 3)
                    nc.gpsimd.tensor_tensor(inv[z][:, :, 1, :], ident[:, :].unsqueeze(1).to_broadcast([P, 2, P]), aT[z],
                                            ALU.subtract).then_inc(sem("rw_off"), 1)
                    step += 1
        taken(pool, "rw_ot", RW_PAIRS - 1)
        pool.dma_start(rw_gate, mod_dram[1, 0, 2 * D:3 * D].partition_broadcast(P)).then_inc(sem("rw_gate_landed"), 16)
        experts(1)

    @block.scalar
    def _(act):
        A = nc.scalar.activation
        act_step = [0]

        def link(ins):
            act_step[0] += 1
            ins.then_inc(sem("act_step"), 1)
            act.wait_ge(sem("act_step"), act_step[0])

        def norm(use):
            xn, dst = norm_of[use]
            t0, nt = tiles_before[use], NORMS[use]
            h_ready(act, use)
            for t in range(nt):
                A(xn[:, t, :], h[:, t, :], ACT.Square, accum_out=stats[:, t:t + 1]).then_inc(sem("norm_squared"), 1)
            act.wait_ge(sem("norm_var"), USES.index(use) + 1)
            A(stats[:, 16:16 + nt], stats[:, 8:8 + nt], ACT.Sqrt).then_inc(sem("norm_std"), 1)
            if use in norm_mod:
                act.wait_ge(sem("modulation"), 2)
                for s in range(1 if nt == LT else 2):
                    for k in range(KD):
                        scale, shift = modulation(use, s, k)
                        n0, n1 = (0, SEQ) if s == 0 else (SEQ, TOK)
                        ps = full(act, "turn", use, s, k)[:, 0:n1 - n0]
                        free(A(dst[:, k, n0:n1], ps, ACT.Identity, bias=shift, scale=scale), "turn", use, s, k)
                return
            for k in range(KD):
                ps = full(act, "turn", use, 0, k)
                free(A(dst[:, k, 0:SEQ], ps, ACT.Copy, scale=col(norm_scale[use], k)), "turn", use, 0, k)

        def post(use):
            F, _ = post_of[use]
            taken(act, *last_job[use])
            for t in range(LT):
                if t:
                    act.wait_ge(sem("post_squared"), POSTS.index(use) * LT + t)
                A(junk[:, :], F[:, t, :], ACT.Square, accum_out=stats[:, 24 + t:25 + t]).then_inc(sem("post_squared"), 1)
            act.wait_ge(sem("post_var"), POSTS.index(use) + 1)
            A(stats[:, 32:36], stats[:, 28:32], ACT.Sqrt).then_inc(sem("post_std"), 1)

        act.wait_ge(sem("angle_reduced"), 1)
        A(angs, ang, ACT.Sin)
        A(turns, ang, ACT.Sin, scale=0.5).then_inc(sem("angle_sin"), 1)
        norm("dil")

        for i in range(len(DIL_STEPS) + 1):
            if i < len(DIL_STEPS):
                g, kind = DIL_STEPS[i]
                for c in range(DIL_STRIDE):
                    ps = full(act, "dil_proj", i, c)
                    if kind == 2:
                        dst = vR[:, c, g * W:(g + 1) * W]
                    else:
                        dst = dil_tmp[:, c, :]
                        if i >= 1 and DIL_STEPS[i - 1][1] < 2:
                            full(act, "dil_turn", i - 1, c)
                    free(A(dst, ps, ACT.Copy), "dil_proj", i, c)
            if i >= 1 and DIL_STEPS[i - 1][1] < 2:
                g, kind = DIL_STEPS[i - 1]
                for c in range(DIL_STRIDE):
                    ps = full(act, "dil_turn", i - 1, c).rearrange("p (f l) -> p f l", f=4)
                    dst = (qT, kT)[kind][:, 4 * g:4 * g + 4, c * P:(c + 1) * P]
                    free(A(dst, ps, ACT.Copy), "dil_turn", i - 1, c)
        for i in range(DIL_TILES + 1):
            if i < DIL_TILES:
                act.wait_ge(sem("dil_max"), i + 1)
                A(dil_s[:, i % 2, :], dil_s[:, i % 2, :], ACT.Exp, bias=stats[:, 40 + i % 2:41 + i % 2],
                  accum_out=stats[:, 42 + i % 2:43 + i % 2]).then_inc(sem("dil_exp"), 1)
            if i >= 1:
                ps = full(act, "dil_pt", i - 1)[:, 0:6 * P]
                if i >= 3:
                    full(act, "dil_out", i - 3)
                free(A(dil_p[:, (i - 1) % 2, :], ps, ACT.Copy), "dil_pt", i - 1)
        for c in range(DIL_STRIDE):
            ps = full(act, "dil_ot", c).rearrange("p (f l) -> p f l", f=4)
            free(A(yaT[:, :, c::DIL_STRIDE], ps, ACT.Copy), "dil_ot", c)

        def ret_turn(hd):
            for f in range(4):
                ps = full(act, "ret_turn", hd, f)
                free(A(yrT[:, 4 * hd + f, :], ps, ACT.Copy), "ret_turn", hd, f)

        for hd in range(RET_HEADS):
            for t in range(LT):
                free(A(rv[:, t, :], full(act, "ret_v", hd, t), ACT.Copy), "ret_v", hd, t)
            if hd >= 1:
                taken(act, "ret_out", hd - 1, LT - 1)
            for t in range(LT):
                free(A(rg[:, t, :], full(act, "ret_g", hd, t), ACT.Silu), "ret_g", hd, t)
            if hd >= 1:
                ret_turn(hd - 1)
            for t in range(LT):
                ps = full(act, "ret_out", hd, t)
                act.wait_ge(sem("ret_squared"), hd * LT + t) if hd + t else None
                A(junk[:, 0:W], ps, ACT.Square, accum_out=stats[:, 44 + t:45 + t]).then_inc(sem("ret_squared"), 1)
            act.wait_ge(sem("ret_var"), hd + 1)
            A(stats[:, 52:56], stats[:, 48:52], ACT.Sqrt).then_inc(sem("ret_std"), 1)
        ret_turn(RET_HEADS - 1)

        for n in range(2):
            for b, (dst, bias) in enumerate(((gate_r, "b_gate_r"), (gate_a, "b_gate_a"))):
                for f in range(4):
                    ps = full(act, "mix_gate", b, n, f)
                    free(A(dst[:, 4 * n + f, :], ps, ACT.Sigmoid, bias=col(bias, 4 * n + f)), "mix_gate", b, n, f)
        for n in range(2):
            for t in range(LT):
                free(A(F_mix[:, t, n * W:(n + 1) * W], full(act, "mix_o", n, t), ACT.Copy), "mix_o", n, t)
        post("mix")

        norm("mlp")
        for f in range(D_FF // P):
            ps = full(act, "up", f)
            ins = A(ffT[:, f, :], ps, ACT.Relu)
            free(ins, "up", f)
            taken(act, "up", f)
            A(ffT[:, f, :], ffT[:, f, :], ACT.Square).then_inc(sem("ff_squared"), 1)
        for n in range(2):
            for t in range(LT):
                free(A(F_mlp[:, t, n * W:(n + 1) * W], full(act, "down", n, t), ACT.Copy), "down", n, t)
        post("mlp")

        norm("ple")
        for d in range(PLE // P):
            free(A(pT[:, d, :], full(act, "ple_turn", d), ACT.Copy), "ple_turn", d)
        for n in range(2):
            for t in range(LT):
                free(A(gate_p[:, t, n * W:(n + 1) * W], full(act, "ple_gate", n, t), ACT.Sigmoid), "ple_gate", n, t)
        post("ple")

        A(cond[:, :, :], cols[:, COLUMNS["cond"][0]:COLUMNS["cond"][0] + 2 * KD].rearrange("p (s k) -> p s k", s=2),
          ACT.Silu).then_inc(sem("cond_ready"), 1)
        for l in range(2):
            ps = full(act, "ada_turn", l)[:, 0:96]
            free(A(mod[:, l].rearrange("p s j k -> p (s j k)"), ps, ACT.Copy), "ada_turn", l)

        norm("na")
        for i in range(NA_STEPS + 2):
            if i < NA_STEPS:
                if i >= 2:
                    dummy = full(act, "na_turn", i - 2)
                ps = full(act, "na_proj", i)
                A(na_p[:, i % 2, :], ps, ACT.Square).then_inc(sem("na_squared"), 1)
                free(A(na_s[:, i % 2, :], ps, ACT.Copy), "na_proj", i)
                act.wait_ge(sem("na_var"), i + 1)
                A(stats[:, 16 + 8 * (i % 2):24 + 8 * (i % 2)], stats[:, 8 * (i % 2):8 * (i % 2) + 8], ACT.Sqrt).then_inc(sem("na_std"), 1)
            if i >= 2:
                j = i - 2
                half, t = divmod(j, NT)
                ps = full(act, "na_turn", j).rearrange("p (f t) -> p f t", f=4)
                dst, g = (naq, "na_q_g") if half < 2 else (nak, "na_k_g")
                f0 = 4 * (half % 2)
                if half < 2 and t < LT:
                    for r in range(2):
                        to = dst[:, f0:f0 + 4, 0:SEQ].rearrange("p f (j r c) -> p f j r c", j=BLOCKS, r=ROWS)[:, :, :, 2 * t + r, :]
                        ins = A(to, ps.rearrange("p f (r j c) -> p f r j c", r=2, j=BLOCKS)[:, :, r], ACT.Copy, scale=col(g))
                else:
                    ins = A(dst[:, f0:f0 + 4, t * P:(t + 1) * P], ps, ACT.Copy, scale=col(g))
                free(ins, "na_turn", j)
        for n in range(2):
            if n == 1:
                act.wait_ge(sem("na_strips_landed"), 16 * 2 * BLOCKS * LT)
            for t in range(NT):
                ps = full(act, "na_v", n, t)
                dst = na_v[:, t, :] if t < LT else na_vc[:, t - LT, n * W:(n + 1) * W]
                free(A(dst, ps, ACT.Copy), "na_v", n, t)
        for i in range(NA_UNITS + 1):
            if i < NA_UNITS:
                nk = W if i % NT < BLOCKS else CTX
                act.wait_ge(sem("na_max"), i + 1)
                A(na_s[:, i % 2, 0:nk], na_s[:, i % 2, 0:nk], ACT.Exp, bias=stats[:, 40 + i % 2:41 + i % 2],
                  accum_out=stats[:, 42 + i % 2:43 + i % 2]).then_inc(sem("na_exp"), 1)
            if i >= 1:
                nk = W if (i - 1) % NT < BLOCKS else CTX
                ps = full(act, "na_pt", i - 1)[:, 0:nk]
                if i >= 3:
                    full(act, "na_out", i - 3)
                free(A(na_p[:, (i - 1) % 2, 0:nk], ps, ACT.Copy), "na_pt", i - 1)
        for t in range(NT):
            ps = full(act, "na_ot", t)
            if t < BLOCKS:
                for f in range(KD):
                    dst = na_oT[:, f, 0:SEQ].rearrange("p (r c) -> p r c", c=GRID)[:, :, 16 * t:16 * t + 16]
                    ins = A(dst, ps[:, f * P:(f + 1) * P].rearrange("p (r c) -> p r c", c=16), ACT.Copy)
            else:
                ins = A(na_oT[:, :, t * P:(t + 1) * P], ps.rearrange("p (f c) -> p f c", f=KD), ACT.Copy)
            free(ins, "na_ot", t)

        def experts(l):
            use = f"moe{l}"
            norm(use)
            act.wait_ge(sem("moe_logit_less_max"), l + 1)
            A(logit, logit, ACT.Exp).then_inc(sem("moe_exp"), 1)

            def gather(e):
                b = e % 2
                for half in range(2):
                    ps = full(act, "moe_gather", l, e, half).rearrange("p (k s) -> p k s", k=4)
                    if half == 0 and e >= 2:
                        full(act, "moe_h3", l, e - 2, 1)
                    for k in range(4):
                        for s in range(1 if l else 2):
                            lo, hi = (0, CAP_L) if s == 0 else (CAP_L, SLOTS)
                            scale, shift = modulation(use, s, 4 * half + k)
                            ins = A(xinT[:, b, 4 * half + k, lo:hi], ps[:, k, lo:hi], ACT.Identity, bias=shift, scale=scale)
                    free(ins, "moe_gather", l, e, half)
                ps = full(act, "moe_selt", l, e)[:, 0:TILES[l] * P]
                if e >= 2:
                    full(act, "moe_add", l, e - 2, TILES[l] - 1, 1)
                n = SLOTS if l == 0 else CAP_L
                free(A(selT[0:n, b, 0:TILES[l] * P], ps[0:n, :], ACT.Copy), "moe_selt", l, e)

            gather(0)
            m = SLOTS if l == 0 else CAP_L
            for e in range(EXPERTS):
                for n in range(2):
                    ps = full(act, "moe_h1", l, e, n)
                    if e >= 1:
                        taken(act, "moe_h3", l, e - 1, n)
                    free(A(s1[0:m, n * W:(n + 1) * W], ps[0:m, :], ACT.Silu), "moe_h1", l, e, n)
                if e + 1 < EXPERTS:
                    gather(e + 1)
                ps = full(act, "moe_ht", l, e).rearrange("p (k s) -> p k s", k=KD)
                free(A(hidT[:, :, 0:m], ps[:, :, 0:m], ACT.Copy), "moe_ht", l, e)
                for n in range(2):
                    ps = full(act, "moe_y", l, e, n)
                    if e >= 2:
                        full(act, "moe_add", l, e - 2, TILES[l] - 1, 1)
                    free(A(y_moe[0:m, e % 2, n * W:(n + 1) * W], ps[0:m, :], ACT.Copy), "moe_y", l, e, n)

        experts(0)

        norm("rw")
        count = [0]

        def stage(ins_of, key):
            i = count[0]
            if i >= 4:
                act.wait_ge(sem(f"spilled_{i % 4}"), 16 * (i // 4))
            free(ins_of(staging[:, i % 4, :]), *key)
            count[0] += 1

        for q in "rkv":
            for n in range(2):
                for t in range(LT if q == "r" else NT):
                    ps = full(act, "rw_proj", q, n, t)
                    stage(lambda dst: A(dst, ps, ACT.Copy), ("rw_proj", q, n, t))
        for q in "wag":
            ps = full(act, "rw_low", q)[:, 0:TOK]
            free(A(lowT, ps, {"w": ACT.Tanh, "a": ACT.Copy, "g": ACT.Sigmoid}[q]), "rw_low", q)
            for z in range(1 if q == "g" else 2):
                for n in range(2):
                    for t in range(LT if q == "g" else NT):
                        ps = full(act, "rw_high", q, z, n, t)
                        stage(lambda dst: A(dst, ps, ACT.Copy if q == "g" else ACT.Sigmoid), ("rw_high", q, z, n, t))

        def flat(x):
            return x.rearrange("p a b -> p (a b)")

        for p in range(RW_PAIRS):
            act.wait_ge(sem("rw_kk_squared"), p + 1)
            A(rw_s[:, 12:24], rw_s[:, 0:12], ACT.Sqrt).then_inc(sem("rw_kk_norm"), 1)
            for z in range(2):
                ps = full(act, "rw_sum", p, z)[:, 0:TOK]
                if z == 0 and p >= 1:
                    taken(act, "rw_tgv", p - 1, NT - 1, 1)
                if z == 1:
                    act.wait_ge(sem("rw_scaled"), 2 * p + 1)
                A(flat(e_neg), ps, ACT.Exp, scale=-1.0)
                free(A(flat(e_pos), ps, ACT.Exp), "rw_sum", p, z)
                ps = full(act, "rw_sum_ex", p, z)[:, 0:TOK]
                free(A(flat(e_ex), ps, ACT.Exp, scale=-1.0), "rw_sum_ex", p, z)
                ps = full(act, "rw_end", p, z)[:, 0:2 * NT]
                free(A(w_end[z], ps, ACT.Exp, scale=-1.0), "rw_end", p, z)
                for x, dst in enumerate((KT[z], BT[z], TT[z], RT[z])):
                    ps = full(act, "rw_turn", p, z, x)[:, 0:SEQ if x == 3 else TOK]
                    free(A(dst, ps, ACT.Copy), "rw_turn", p, z, x)
            for t in range(NT):
                for lv in range(1, 6):
                    for z in range(2):
                        ps = full(act, "rw_x", p, t, z, lv)[:, 0:P].rearrange("p (h a b) -> p h a b", h=2, b=1 << lv)
                        dst = halves(xl[z][:, lv - 1], lv, z)
                        free(A(dst, ps, ACT.Copy), "rw_x", p, t, z, lv)
                for z in range(2):
                    ps = full(act, "rw_gv", p, t, z)[:, 0:P]
                    free(A(gv[z], ps, ACT.Copy), "rw_gv", p, t, z)
                    ps = full(act, "rw_tk", p, t, z)
                    A(tkT[z][0:CH, t, :], ps[0:CH, 0:P], ACT.Copy)
                    free(A(tkT[z][CH:P, t, :], ps[CH:P, P:2 * P], ACT.Copy), "rw_tk", p, t, z)
                for z in range(2):
                    ps = full(act, "rw_tgv", p, t, z)[:, 0:P]
                    free(A(tgv[z][:, t, :], ps, ACT.Copy), "rw_tgv", p, t, z)
            for i in range(2 * NT):
                for z in range(2):
                    t, c = rw_chunk(i, z)
                    if t < LT:
                        ps = full(act, "rw_y", p, i, z)[:, 0:P]
                        rows = slice(c * CH, (c + 1) * CH)
                        free(A(yz[z][rows, t, :], ps[rows, :], ACT.Copy), "rw_y", p, i, z)
            act.wait_ge(sem("rw_y_var"), p + 1)
            A(rw_s[:, 32:40], rw_s[:, 24:32], ACT.Sqrt).then_inc(sem("rw_y_std"), 1)
            free(A(zT(p), full(act, "rw_ot", p), ACT.Copy), "rw_ot", p)
        experts(1)

    @block.vector
    def _(dve):
        V = nc.vector
        dve_step = [0]

        def link(ins):
            dve_step[0] += 1
            ins.then_inc(sem("dve_step"), 1)
            dve.wait_ge(sem("dve_step"), dve_step[0])

        def norm(use):
            xn, _ = norm_of[use]
            t0, nt = tiles_before[use], NORMS[use]
            dve.wait_ge(sem("norm_squared"), t0 + nt)
            V.tensor_scalar(stats[:, 8:8 + nt], stats[:, 0:nt], 1.0 / D, EPS, ALU.mult, ALU.add).then_inc(sem("norm_var"), 1)
            dve.wait_ge(sem("norm_std"), USES.index(use) + 1)
            link(V.reciprocal(stats[:, 0:nt], stats[:, 16:16 + nt]))
            for t in range(nt):
                V.tensor_scalar(xn[:, t, :], h[:, t, :], stats[:, t:t + 1], None, ALU.mult).then_inc(sem("normed"), 1)

        def post(use):
            F, gb = post_of[use]
            i = POSTS.index(use)
            dve.wait_ge(sem("post_squared"), (i + 1) * LT)
            V.tensor_scalar(stats[:, 28:32], stats[:, 24:28], 1.0 / D, EPS, ALU.mult, ALU.add).then_inc(sem("post_var"), 1)
            dve.wait_ge(sem("post_std"), i + 1)
            link(V.reciprocal(stats[:, 36:40], stats[:, 32:36]))
            dve.wait_ge(sem("post_gain_landed"), 16 * (i + 1))
            for t in range(LT):
                link(V.scalar_tensor_tensor(F[:, t, :], F[:, t, :], stats[:, 36 + t:37 + t], gb, ALU.mult, ALU.mult))
                V.tensor_tensor(h[:, t, :], h[:, t, :], F[:, t, :], ALU.add).then_inc(sem("post_added"), 1)

        dve.wait_ge(sem("const_landed"), 16 * 6)
        V.tensor_copy(pos_f, pos_i)
        link(V.tensor_copy(pos_cf, pos_ci))
        V.tensor_scalar(ang[:, 0:SEQ], pos_f, ret_freq, None, ALU.mult)
        for c in range(DIL_STRIDE):
            ins = V.tensor_scalar(ang[:, SEQ + 8 * c:SEQ + 8 * c + 8], dil_freq, pos_cf[:, c:c + 1], None, ALU.mult)
        link(ins)
        ROUND = 1.5 * 2.0 ** 23
        link(V.tensor_scalar(turns, ang, float(np.float32(1 / (2 * np.pi))), ROUND, ALU.mult, ALU.add))
        link(V.tensor_scalar(turns, turns, ROUND, None, ALU.subtract))
        part1 = 6.28125
        part2 = float(np.float32(np.float64(2 * np.pi) - part1).astype(np.float16))
        part3 = float(np.float32(2 * np.pi - part1 - part2))
        for x in (part1, part2, part3):
            link(V.scalar_tensor_tensor(ang, turns, -x, ang, ALU.mult, ALU.add))
        lim = float(np.nextafter(np.float32(np.pi), np.float32(0)))
        V.tensor_scalar(ang, ang, lim, -lim, ALU.min, ALU.max).then_inc(sem("angle_reduced"), 1)
        dve.wait_ge(sem("angle_sin"), 1)
        link(V.tensor_tensor(turns, turns, turns, ALU.mult))
        V.tensor_copy(ret_sin, angs[:, 0:SEQ])
        V.tensor_copy(dil_sin.rearrange("p a b -> p (a b)"), angs[:, SEQ:544])
        V.tensor_scalar(ret_cos, turns[:, 0:SEQ], -2.0, 1.0, ALU.mult, ALU.add)
        link(V.tensor_scalar(dil_cos.rearrange("p a b -> p (a b)"), turns[:, SEQ:544], -2.0, 1.0, ALU.mult, ALU.add))
        norm("dil")

        n_rot = 0
        for i, (g, kind) in enumerate(DIL_STEPS):
            if kind == 2:
                continue
            for c in range(DIL_STRIDE):
                taken(dve, "dil_proj", i, c)
                x = dil_tmp[:, c, :].rearrange("p (h d) -> p h d", d=HD)
                x1, x2 = x[:, :, 0:ROPE8], x[:, :, ROPE8:2 * ROPE8]
                cos = dil_cos[:, c, :].unsqueeze(1).to_broadcast([P, DIL_SLOTS, ROPE8])
                sin = dil_sin[:, c, :].unsqueeze(1).to_broadcast([P, DIL_SLOTS, ROPE8])
                if n_rot >= 2:
                    dve.wait_ge(sem("dil_rotated"), n_rot - 1)
                r = [dil_rot[:, q, n_rot % 2] for q in range(4)]
                V.tensor_tensor(r[0], x1, cos, ALU.mult)
                V.tensor_tensor(r[1], x2, sin, ALU.mult)
                V.tensor_tensor(r[2], x2, cos, ALU.mult)
                link(V.tensor_tensor(r[3], x1, sin, ALU.mult))
                V.tensor_tensor(x1, r[0], r[1], ALU.subtract)
                V.tensor_tensor(x2, r[2], r[3], ALU.add).then_inc(sem("dil_rotated"), 1)
                n_rot += 1
        dve.wait_ge(sem("mask_landed"), 16)
        for i in range(DIL_TILES + 2):
            if i < DIL_TILES:
                s, c = divmod(i, DIL_STRIDE)
                ps = full(dve, "dil_score", i)[:, 0:6 * P]
                if i >= 2:
                    full(dve, "dil_pt", i - 2)
                    dve.wait_ge(sem("dil_exp"), i - 1)
                x = V.tensor_tensor_reduce(out=dil_s[:, i % 2, :], in0=ps, in1=dil_mask[:, c, :], scale=HD ** -0.5,
                                           scalar=-3e38, op0=ALU.add, op1=ALU.max, accum_out=stats[:, 56 + i % 2:57 + i % 2])
                free(x, "dil_score", i)
                taken(dve, "dil_score", i)
                V.tensor_scalar(stats[:, 40 + i % 2:41 + i % 2], stats[:, 56 + i % 2:57 + i % 2], -1.0, None,
                                ALU.mult).then_inc(sem("dil_max"), 1)
            if 1 <= i <= DIL_TILES:
                j = i - 1
                dve.wait_ge(sem("dil_exp"), j + 1)
                if j >= 2:
                    taken(dve, "dil_out", j - 2)
                link(V.reciprocal(stats[:, 58 + j % 2:59 + j % 2], stats[:, 42 + j % 2:43 + j % 2]))
            if i >= 2:
                j = i - 2
                s, c = divmod(j, DIL_STRIDE)
                ps = full(dve, "dil_out", j)[:, 0:HD]
                free(V.tensor_scalar(dil_o[:, c, s * HD:(s + 1) * HD], ps, stats[:, 58 + j % 2:59 + j % 2], None, ALU.mult),
                     "dil_out", j)

        dve.wait_ge(sem("decay_landed"), 16)
        for hd in range(RET_HEADS):
            for b, dst in enumerate((rqT, rkT)):
                if hd + b:
                    dve.wait_ge(sem("ret_rotated"), 2 * hd + b)
                p0 = full(dve, "ret_qk", hd, 2 * b)
                V.tensor_tensor(dst[:, 0, :], p0, ret_cos, ALU.mult)
                free(V.tensor_tensor(rot_b, p0, ret_sin, ALU.mult), "ret_qk", hd, 2 * b)
                p1 = full(dve, "ret_qk", hd, 2 * b + 1)
                V.tensor_tensor(rot_a, p1, ret_sin, ALU.mult)
                x = V.tensor_tensor(dst[:, 1, :], p1, ret_cos, ALU.mult)
                free(x, "ret_qk", hd, 2 * b + 1)
                taken(dve, "ret_qk", hd, 2 * b + 1)
                V.tensor_tensor(dst[:, 0, :], dst[:, 0, :], rot_a, ALU.subtract)
                V.tensor_tensor(dst[:, 1, :], dst[:, 1, :], rot_b, ALU.add).then_inc(sem("ret_rotated"), 1)
            for j in range(LT):
                n = SEQ - j * P
                ps = full(dve, "ret_score", hd, j)[:, 0:n]
                free(V.tensor_tensor(rs[:, j, 0:n], ps, decay[:, hd, 0:n], ALU.mult), "ret_score", hd, j)
            dve.wait_ge(sem("ret_squared"), (hd + 1) * LT)
            V.tensor_scalar(stats[:, 48:52], stats[:, 44:48], 1.0 / RET_V, EPS, ALU.mult, ALU.add).then_inc(sem("ret_var"), 1)
            dve.wait_ge(sem("ret_std"), hd + 1)
            link(V.reciprocal(stats[:, 60:64], stats[:, 52:56]))
            for t in range(LT):
                taken(dve, "ret_g", hd, t)
                ps = full(dve, "ret_out", hd, t)
                free(V.scalar_tensor_tensor(ry[:, t, :], ps, stats[:, 60 + t:61 + t], rg[:, t, :], ALU.mult, ALU.mult),
                     "ret_out", hd, t)

        for n in range(2):
            for f in range(4):
                taken(dve, "mix_gate", 0, n, f)
                ps = full(dve, "mix_ret", n, f)
                free(V.tensor_tensor(mixT[:, 4 * n + f, :], ps, gate_r[:, 4 * n + f, :], ALU.mult), "mix_ret", n, f)
        for f in range(KD):
            taken(dve, "mix_gate", 1, f // 4, f % 4)
            if f:
                dve.wait_ge(sem("mixed"), f)
            ps = full(dve, "mix_dil", f)
            free(V.tensor_tensor(mix_t, ps, gate_a[:, f, :], ALU.mult), "mix_dil", f)
            taken(dve, "mix_dil", f)
            V.tensor_tensor(mixT[:, f, :], mixT[:, f, :], mix_t, ALU.add).then_inc(sem("mixed"), 1)
        post("mix")

        norm("mlp")
        post("mlp")

        norm("ple")
        for n in range(2):
            for t in range(LT):
                taken(dve, "ple_gate", n, t)
                ps = full(dve, "ple_in", n, t)
                sl = slice(n * W, (n + 1) * W)
                free(V.tensor_tensor(F_ple[:, t, sl], ps, gate_p[:, t, sl], ALU.mult), "ple_in", n, t)
        post("ple")

        dve.wait_ge(sem("ada_bias_landed"), 32)
        for l in range(2):
            for n in range(6 * D // W):
                ps = full(dve, "ada", l, n)
                m = ada_m[0:2, l, n * W:(n + 1) * W]
                free(V.tensor_tensor(m, ps[0:2, :], m, ALU.add), "ada", l, n)
        for l in range(2):
            taken(dve, "ada_turn", l)
            for s in range(2):
                for n in range(2):
                    at = COLUMNS["norm_g"][0] + (2 * l + n) * KD
                    ins = V.scalar_tensor_tensor(mod_a[:, l, s, n, :], mod[:, l, s, 3 * n + 1, :], 1.0, cols[:, at:at + KD], ALU.add, ALU.mult)
            ins.then_inc(sem("modulation"), 1)

        norm("na")
        for i in range(NA_STEPS):
            b = i % 2
            dve.wait_ge(sem("na_squared"), i + 1)
            if i >= 2:
                dve.wait_ge(sem("na_normed"), i - 1)
            link(V.tensor_reduce(rw_s[:, 8 * b:8 * b + 8], na_p[:, b, :].rearrange("p (h d) -> p h d", d=HD), AX, ALU.add))
            V.tensor_scalar(stats[:, 8 * b:8 * b + 8], rw_s[:, 8 * b:8 * b + 8], 1.0 / HD, EPS, ALU.mult, ALU.add).then_inc(sem("na_var"), 1)
            dve.wait_ge(sem("na_std"), i + 1)
            link(V.reciprocal(rw_s[:, 16 + 8 * b:24 + 8 * b], stats[:, 16 + 8 * b:24 + 8 * b]))
            taken(dve, "na_proj", i)
            x = na_s[:, b, :].rearrange("p (h d) -> p h d", d=HD)
            V.tensor_tensor(x, x, rw_s[:, 16 + 8 * b:24 + 8 * b].unsqueeze(2).to_broadcast([P, 8, HD]), ALU.mult).then_inc(sem("na_normed"), 1)
        dve.wait_ge(sem("na_zeroed"), 2)
        dve.wait_ge(sem("na_strips_landed"), 16 * 4 * BLOCKS * LT)
        dve.wait_ge(sem("na_mask_landed"), 16)
        for i in range(NA_UNITS + 2):
            if i < NA_UNITS:
                hd, un = divmod(i, NT)
                bias = na_bias[hd % 2]
                if un == 0:
                    dve.wait_ge(sem(f"na_bias_landed_{hd % 2}"), 16 * ROWS * (hd // 2 + 1))
                    link(V.scalar_tensor_tensor(bias[:, 0:3, :], bias[:, 0:3, :], HD ** 0.5, na_mask, ALU.mult, ALU.add))
                nk = W if un < BLOCKS else CTX
                ps = full(dve, "na_score", i)[:, 0:nk]
                if i >= 2:
                    full(dve, "na_pt", i - 2)
                    dve.wait_ge(sem("na_exp"), i - 1)
                s_ = na_s[:, i % 2, 0:nk]
                mx = stats[:, 56 + i % 2:57 + i % 2]
                if un < BLOCKS:
                    kind = (0, 1, 1, 2)[un]
                    ins = V.tensor_tensor_reduce(out=s_.rearrange("p (a b) -> p a b", a=2), in0=ps.rearrange("p (a b) -> p a b", a=2),
                                                 in1=bias[:, kind::3 - kind, :], scale=HD ** -0.5, scalar=-3e38, op0=ALU.add, op1=ALU.max,
                                                 accum_out=mx)
                else:
                    ins = V.tensor_tensor_reduce(out=s_, in0=ps, in1=bias[:, 3, :], scale=HD ** -0.5, scalar=-3e38, op0=ALU.add,
                                                 op1=ALU.max, accum_out=mx)
                free(ins, "na_score", i)
                taken(dve, "na_score", i)
                V.tensor_scalar(stats[:, 40 + i % 2:41 + i % 2], mx, -1.0, None, ALU.mult).then_inc(sem("na_max"), 1)
            if 1 <= i <= NA_UNITS:
                j = i - 1
                dve.wait_ge(sem("na_exp"), j + 1)
                if j >= 2:
                    taken(dve, "na_out", j - 2)
                link(V.reciprocal(stats[:, 58 + j % 2:59 + j % 2], stats[:, 42 + j % 2:43 + j % 2]))
            if i >= 2:
                j = i - 2
                hd, un = divmod(j, NT)
                ps = full(dve, "na_out", j)[:, 0:HD]
                free(V.tensor_scalar(na_o[:, un, hd * HD:(hd + 1) * HD], ps, stats[:, 58 + j % 2:59 + j % 2], None, ALU.mult), "na_out", j)
        dve.wait_ge(sem("na_gate_landed"), 32)
        for n in range(2):
            for t in range(NT):
                i = n * NT + t
                ps = full(dve, "na_o", n, t)
                sl = slice(n * W, (n + 1) * W)
                if i >= 2:
                    dve.wait_ge(sem("na_added"), i - 1)
                free(V.tensor_tensor(na_t[:, i % 2, :], ps, na_gate[:, int(t >= LT), sl], ALU.mult), "na_o", n, t)
                taken(dve, "na_o", n, t)
                V.tensor_tensor(h[:, t, sl], h[:, t, sl], na_t[:, i % 2, :], ALU.add).then_inc(sem("na_added"), 1)

        def experts(l):
            nt, tok = TILES[l], TILES[l] * P
            streams = [(0, SEQ, CAP_L)] + ([(SEQ, TOK, CAP_C)] if l == 0 else [])
            norm(f"moe{l}")
            ps = full(dve, "moe_logit", l)[:, 0:nt * EXPERTS].rearrange("p (t e) -> p t e", e=EXPERTS)
            link(V.tensor_reduce(stats[:, 24:24 + nt], ps, AX, ALU.max))
            free(V.tensor_tensor(logit[:, 0:nt], ps, stats[:, 24:24 + nt].unsqueeze(2).to_broadcast([P, nt, EXPERTS]), ALU.subtract), "moe_logit", l)
            if l == 1:
                V.memset(logit[:, nt:NT, :], 0.0)
            taken(dve, "moe_logit", l)
            V.memset(sel_g[:, :, :], 0.0).then_inc(sem("moe_logit_less_max"), 1)
            dve.wait_ge(sem("moe_exp"), l + 1)
            link(V.tensor_reduce(stats[:, 32:32 + nt], logit[:, 0:nt], AX, ALU.add))
            link(V.reciprocal(stats[:, 24:24 + nt], stats[:, 32:32 + nt]))
            V.tensor_tensor(aff[:, 0:nt], logit[:, 0:nt], stats[:, 24:24 + nt].unsqueeze(2).to_broadcast([P, nt, EXPERTS]),
                            ALU.mult).then_inc(sem("moe_affinity"), 1)
            E = slice(0, EXPERTS)
            ps = full(dve, "moe_afft", l)[E, 0:tok]
            free(V.tensor_copy(workT[E, 0:tok], ps), "moe_afft", l)
            taken(dve, "moe_afft", l)
            for lo, hi, cap in streams:
                for _ in range(cap // 8):
                    link(V.max(top8[E, :], workT[E, lo:hi]))
                    link(V.match_replace(affT[E, lo:hi], top8[E, :], workT[E, lo:hi], -1.0))
                    link(V.tensor_copy(workT[E, lo:hi], affT[E, lo:hi]))
            link(V.tensor_scalar(workT[E, 0:tok], workT[E, 0:tok], 0.0, None, ALU.is_lt))
            for lo, hi, cap in streams:
                ins = V.tensor_tensor_scan(sumT[E, lo:hi], ones[E, 0:1].to_broadcast([EXPERTS, hi - lo]), workT[E, lo:hi], 0.0,
                                           ALU.mult, ALU.add)
            link(ins)
            link(V.tensor_tensor(sumT[E, 0:tok], sumT[E, 0:tok], workT[E, 0:tok], ALU.mult))
            V.tensor_scalar(sumT[E, 0:tok], sumT[E, 0:tok], -1.0, None, ALU.add).then_inc(sem("moe_numbered"), 1)
            ps = full(dve, "moe_slot", l)[:, 0:nt * EXPERTS]
            free(V.tensor_copy(slot[:, 0:nt].rearrange("p t e -> p (t e)"), ps), "moe_slot", l)
            taken(dve, "moe_slot", l)
            dve.wait_ge(sem("moe_landed"), 64 * (l + 1))

            def select(e):
                if e >= 1:
                    full(dve, "moe_gather", l, e - 1, 1)
                    full(dve, "moe_selt", l, e - 1)
                for t in range(nt):
                    lat = t < LT
                    cap = CAP_L if lat else CAP_C
                    lo = 0 if lat else CAP_L
                    one = slot[:, t, e:e + 1]
                    dst = sel_l[:, t, :] if lat else sel_c[:, t - LT, :]
                    V.tensor_scalar(dst, slot_no[:, 0:cap], one, None, ALU.is_equal)
                    ins = V.tensor_scalar(sel_g[:, t, lo:lo + cap], slot_no[:, 0:cap], one, aff[:, t, e:e + 1], ALU.is_equal, ALU.mult)
                ins.then_inc(sem("moe_selected"), 1)

            def scatter(e):
                for t in range(nt):
                    for n in range(2):
                        ps = full(dve, "moe_add", l, e, t, n)
                        x = acc[:, t, n * W:(n + 1) * W]
                        if e == 0:
                            ins = V.tensor_copy(x, ps)
                        else:
                            taken(dve, "moe_add", l, e - 1, t, n)
                            ins = V.tensor_tensor(x, x, ps, ALU.add)
                        free(ins, "moe_add", l, e, t, n)

            m = SLOTS if l == 0 else CAP_L
            select(0)
            for e in range(EXPERTS):
                if e + 1 < EXPERTS:
                    select(e + 1)
                for n in range(2):
                    taken(dve, "moe_h1", l, e, n)
                    ps = full(dve, "moe_h3", l, e, n)
                    if e >= 1:
                        full(dve, "moe_ht", l, e - 1)
                    free(V.tensor_tensor(hid[0:m, n * W:(n + 1) * W], ps[0:m, :], s1[0:m, n * W:(n + 1) * W], ALU.mult), "moe_h3", l, e, n)
                if e >= 1:
                    scatter(e - 1)
            scatter(EXPERTS - 1)
            for t in range(nt):
                taken(dve, "moe_add", l, EXPERTS - 1, t, 1)
                link(V.tensor_tensor(acc[:, t, :], acc[:, t, :], moe_gate[:, int(t >= LT), :], ALU.mult))
                V.tensor_tensor(h[:, t, :], h[:, t, :], acc[:, t, :], ALU.add).then_inc(sem("moe_added"), 1)

        experts(0)

        norm("rw")
        taken(dve, "turn", "rw", 1, KD - 1)
        for lo, hi in ((0, SEQ), (SEQ, TOK)):
            V.tensor_tensor(xx[:, :, lo + 1:hi - 1], hT_rw[:, :, lo:hi - 2], hT_rw[:, :, lo + 2:hi], ALU.add)
            V.tensor_copy(xx[:, :, lo:lo + 1], hT_rw[:, :, lo + 1:lo + 2])
            ins = V.tensor_copy(xx[:, :, hi - 1:hi], hT_rw[:, :, hi - 2:hi - 1])
        link(ins)
        link(V.scalar_tensor_tensor(xx, xx, 0.5, hT_rw, ALU.mult, ALU.subtract))
        order = "rkvwag"
        for i, q in enumerate(order):
            if i >= 2:
                o = order[i - 2]
                full(dve, *(("rw_proj", o, 1, (LT if o == "r" else NT) - 1) if o in "rkv" else ("rw_low", o)))
            for k in range(KD):
                c = "rwkvag".index(q) * KD + k
                V.scalar_tensor_tensor(xs[i % 2][:, k, :], xx[:, k, :], col("rw_mix", c), hT_rw[:, k, :], ALU.mult, ALU.add
                                       ).then_inc(sem("rw_mixed"), 1)

        def over(row, nt):
            return row.unsqueeze(1).to_broadcast([P, nt, P])

        def heads(x):
            return x.rearrange("p t (h d) -> p (t h) d", d=HD)

        def by_head(x, n):
            return x.unsqueeze(2).to_broadcast([P, n, HD])

        dve.wait_ge(sem("rw_const_landed"), 16 * 7)
        n_step = 0
        for p in range(RW_PAIRS):
            b = p % 2
            I = {q: v[b] for q, v in RW_IN.items()}
            k_k, k_a, r_k, ln_g, ln_b = (rw_rows[:, b, x, :] for x in range(5))
            dve.wait_ge(sem(f"rw_in_landed_{b}"), 16 * 9 * (p // 2 + 1))
            if p >= 1:
                taken(dve, "rw_tgv", p - 1, NT - 1, 1)
                taken(dve, "rw_ot", p - 1)
            link(V.tensor_tensor(kk, I["k"], over(k_k, NT), ALU.mult))
            link(V.tensor_tensor(rw_t, kk, kk, ALU.mult))
            V.tensor_reduce(rw_s[:, 0:12], heads(rw_t), AX, ALU.add).then_inc(sem("rw_kk_squared"), 1)
            dve.wait_ge(sem("rw_kk_norm"), p + 1)
            link(V.tensor_scalar(rw_s[:, 12:24], rw_s[:, 12:24], 1e-12, None, ALU.max))
            link(V.reciprocal(rw_s[:, 0:12], rw_s[:, 12:24]))
            link(V.tensor_tensor(heads(kk), heads(kk), by_head(rw_s[:, 0:12], 12), ALU.mult))
            for z in range(2):
                az = I[f"a{z}"]
                V.tensor_tensor(bh[z], kk, az, ALU.mult)
                link(V.scalar_tensor_tensor(rw_t, az, -1.0, over(k_a, NT), ALU.add, ALU.mult))
                link(V.scalar_tensor_tensor(th[z], rw_t, 1.0, I["k"], ALU.add, ALU.mult))
                taken(dve, "rw_sum_ex", p, z)
                V.tensor_tensor(kh[z], kk, e_ex, ALU.mult)
                V.tensor_tensor(bh[z], bh[z], e_pos, ALU.mult)
                V.tensor_tensor(th[z], th[z], e_pos, ALU.mult)
                V.tensor_tensor(rw_t[:, 0:LT], I["r"], e_neg[:, 0:LT], ALU.mult).then_inc(sem("rw_scaled"), 1)
                full(dve, "rw_turn", p, z, 3)
            for t in range(NT):
                for z in range(2):
                    if n_step >= 2:
                        full(dve, "rw_gv", *unit(n_step - 2))
                        full(dve, "rw_tgv", *unit(n_step - 2))
                    mask = [c_mask[:, z, x:x + 1, :].to_broadcast([P, 2, P]) for x in range(2)]
                    ps = full(dve, "rw_ab", p, t, z).rearrange("p (h x s) -> p h x s", h=2, x=4)
                    V.tensor_tensor(aT[z], ps[:, :, 0, :], mask[0], ALU.mult).then_inc(sem("rw_at"), 1)
                    if t < LT:
                        V.tensor_tensor(rbT[z][:, t], ps[:, :, 1, :], mask[1], ALU.mult)
                        V.tensor_tensor(rtT[z][:, t], ps[:, :, 3, :], mask[1], ALU.mult)
                    free(V.tensor_tensor(gT[z], ps[:, :, 2, :], mask[0], ALU.mult), "rw_ab", p, t, z)
                    ps = full(dve, "rw_a", p, t, z).rearrange("p (h s) -> p h s", h=2)[:, :, 0:P]
                    ins = V.tensor_tensor(inv[z][:, :, 0, :], ps, c_join[:, z:z + 1, :].to_broadcast([P, 2, P]), ALU.mult)
                    free(ins, "rw_a", p, t, z)
                    taken(dve, "rw_a", p, t, z)
                    V.tensor_tensor(inv[z][:, :, 0, :], ident[:, :].unsqueeze(1).to_broadcast([P, 2, P]), inv[z][:, :, 0, :],
                                    ALU.subtract).then_inc(sem("rw_inv_started"), 1)
                    n_step += 1
                for lv in range(1, 6):
                    for z in range(2):
                        ps = full(dve, "rw_join", p, t, z, lv)[:, 0:4 * CH].rearrange("p (h x a b) -> p h x a b", h=2, x=2, b=1 << lv)
                        T = halves(inv[z][:, :, 0, :], lv, z)
                        M = halves(inv[z][:, :, 1, :], lv, z, True)
                        if lv == 1:
                            dve.wait_ge(sem("rw_inv_started"), n_step - 1 + z)
                            dve.wait_ge(sem("rw_off"), n_step - 1 + z)
                        else:
                            taken(dve, "rw_join", p, t, z, lv - 1)
                        V.tensor_tensor(T, T, ps[:, :, 0], ALU.subtract)
                        free(V.tensor_tensor(M, M, ps[:, :, 1], ALU.subtract), "rw_join", p, t, z, lv)
            for z in range(2):
                ins = V.memset(state[z][:, 0, :], 0.0)
            ins.then_inc(sem("rw_state_zeroed"), 1)
            for i in range(2 * NT):
                for z in range(2):
                    t, c = rw_chunk(i, z)
                    rows = slice(c * CH, (c + 1) * CH)
                    ps = full(dve, "rw_u", p, i, z)[:, 0:P]
                    taken(dve, "rw_tgv", p, t, z)
                    free(V.scalar_tensor_tensor(u[z][rows, :], ps[rows, :], -1.0, tgv[z][rows, t, :], ALU.mult, ALU.subtract), "rw_u", p, i, z)
                for z in range(2):
                    t, c = rw_chunk(i, z)
                    ps = full(dve, "rw_state", p, i, z)[:, 0:P]
                    new = state[z][:, (i + 1) % 2, :]
                    if i == 0:
                        dve.wait_ge(sem("rw_state_zeroed"), p + 1)
                    else:
                        taken(dve, "rw_state", p, i - 1, z)
                    if i >= 1 and rw_chunk(i - 1, z)[0] < LT:
                        full(dve, "rw_y", p, i - 1, z)
                    ins = V.tensor_tensor(new, ps, state[z][:, i % 2, :], ALU.add)
                    link(ins)
                    end = w_end[z][:, 2 * t + c:2 * t + c + 1]
                    free(V.scalar_tensor_tensor(new, new, end, c_blocks, ALU.mult, ALU.mult), "rw_state", p, i, z)
            for z in range(2):
                taken(dve, "rw_y", p, 2 * NT - 1, z)
            y, d = yd
            link(V.tensor_tensor(y, yz[0], yz[1], ALU.add))
            link(V.tensor_reduce(rw_s[:, 24:32], heads(y), AX, ALU.add))
            link(V.tensor_scalar(rw_s[:, 24:32], rw_s[:, 24:32], 1.0 / HD, None, ALU.mult))
            link(V.tensor_tensor(heads(d), heads(y), by_head(rw_s[:, 24:32], 8), ALU.subtract))
            link(V.tensor_tensor(y, d, d, ALU.mult))
            link(V.tensor_reduce(rw_s[:, 40:48], heads(y), AX, ALU.add))
            V.tensor_scalar(rw_s[:, 24:32], rw_s[:, 40:48], 1.0 / HD, GN_EPS, ALU.mult, ALU.add).then_inc(sem("rw_y_var"), 1)
            w = yz[0]
            link(V.tensor_tensor(w, I["a0"][:, 0:LT], I["a1"][:, 0:LT], ALU.add))
            link(V.scalar_tensor_tensor(w, w, -2.0, over(k_a, LT), ALU.add, ALU.mult))
            link(V.scalar_tensor_tensor(w, w, 2.0, I["k"][:, 0:LT], ALU.add, ALU.mult))
            link(V.tensor_tensor(w, w, I["r"], ALU.mult))
            link(V.tensor_tensor(w, w, over(r_k, LT), ALU.mult))
            link(V.tensor_reduce(rw_s[:, 40:48], heads(w), AX, ALU.add))
            link(V.tensor_tensor(heads(w), heads(I["v"][:, 0:LT]), by_head(rw_s[:, 40:48], 8), ALU.mult))
            dve.wait_ge(sem("rw_y_std"), p + 1)
            link(V.reciprocal(rw_s[:, 40:48], rw_s[:, 32:40]))
            link(V.tensor_tensor(heads(d), heads(d), by_head(rw_s[:, 40:48], 8), ALU.mult))
            link(V.tensor_tensor(d, d, over(ln_g, LT), ALU.mult))
            link(V.tensor_tensor(d, d, over(ln_b, LT), ALU.add))
            link(V.tensor_tensor(d, d, w, ALU.add))
            V.tensor_tensor(d, d, I["g"], ALU.mult).then_inc(sem("rw_read_out"), 1)
        dve.wait_ge(sem("rw_gate_landed"), 16)
        for n in range(2):
            for t in range(LT):
                i = n * LT + t
                ps = full(dve, "rw_o", n, t)
                sl = slice(n * W, (n + 1) * W)
                if i >= 2:
                    dve.wait_ge(sem("rw_added"), i - 1)
                free(V.tensor_tensor(rw_ot[:, i % 2, :], ps, rw_gate[:, sl], ALU.mult), "rw_o", n, t)
                taken(dve, "rw_o", n, t)
                V.tensor_tensor(h[:, t, sl], h[:, t, sl], rw_ot[:, i % 2, :], ALU.add).then_inc(sem("rw_added"), 1)
        experts(1)

    @block.tensor
    def _(pe):
        mm, turn = nc.tensor.matmul, nc.tensor.transpose
        load_no = [0]

        def weights(name, k=KD, n=W):
            i = load_no[0]
            assert loads[i][0] == name, (loads[i][0], name)
            pe.wait_ge(landed[i % RING], landed_at[i])
            load_no[0] += 1
            return ring[:, i % RING, 0:k * n].rearrange("p (k n) -> p k n", n=n)

        def open_(*key):
            for before in plan[key].before:
                pe.wait_ge(freed[before.engine], before.count)
            return bank(plan[key])

        def close(ins, *key):
            assert done["pe"] == plan[key].number, (key, done["pe"], plan[key].number)
            done["pe"] += 1
            ins.then_inc(filled, 1)

        def product(key, lhs, rhs, nk, ncol=W, first=True):
            ps = open_(*key)
            for k in range(nk):
                ins = mm(ps[:, 0:ncol], lhs(k), rhs(k), start=(k == 0 and first), stop=(k == nk - 1))
            return ins

        def norm(use):
            xn, _ = norm_of[use]
            t0 = tiles_before[use]
            for k in range(KD):
                ps = open_("turn", use, 0, k)
                for t in range(LT):
                    pe.wait_ge(sem("normed"), t0 + t + 1)
                    ins = turn(ps[:, t * P:(t + 1) * P], xn[:, t, k * P:(k + 1) * P], ident[:, :])
                close(ins, "turn", use, 0, k)
            if NORMS[use] == NT:
                for k in range(KD):
                    ps = open_("turn", use, 1, k)
                    for t in range(LT, NT):
                        pe.wait_ge(sem("normed"), t0 + t + 1)
                        ins = turn(ps[:, (t - LT) * P:(t - LT + 1) * P], xn[:, t, k * P:(k + 1) * P], ident[:, :])
                    close(ins, "turn", use, 1, k)
            taken(pe, "turn", use, int(NORMS[use] == NT), KD - 1)

        pe.wait_ge(sem("const_landed"), 16 * 6)
        norm("dil")
        n_rot = 0
        for i in range(len(DIL_STEPS) + 1):
            if i < len(DIL_STEPS):
                w = weights("dil_proj")
                for c in range(DIL_STRIDE):
                    ins = product(("dil_proj", i, c), lambda k: uT[:, k, c::DIL_STRIDE], lambda k: w[:, k, :], KD)
                    close(ins, "dil_proj", i, c)
            if i >= 1 and DIL_STEPS[i - 1][1] < 2:
                for c in range(DIL_STRIDE):
                    n_rot += 1
                    pe.wait_ge(sem("dil_rotated"), n_rot)
                    ps = open_("dil_turn", i - 1, c)
                    for f in range(4):
                        ins = turn(ps[:, f * P:(f + 1) * P], dil_tmp[:, c, f * P:(f + 1) * P], ident[:, :])
                    close(ins, "dil_turn", i - 1, c)
        taken(pe, "dil_turn", len(DIL_STEPS) - 2, DIL_STRIDE - 1)
        taken(pe, "dil_proj", len(DIL_STEPS) - 1, DIL_STRIDE - 1)
        for i in range(DIL_TILES + 2):
            if i < DIL_TILES:
                s, c = divmod(i, DIL_STRIDE)
                rows = slice(s % 2 * HD, s % 2 * HD + HD)
                ps = open_("dil_score", i)
                f = [4 * g + s // 2 for g in range(DIL_GROUPS)]
                own = slice(c * P, (c + 1) * P)
                mm(ps[:, 0:SEQ], qT[rows, f[0], own], kT[rows, f[0], :], start=True, stop=True)
                for g in (1, 2):
                    ins = mm(ps[:, SEQ + (g - 1) * P:SEQ + g * P], qT[rows, f[g], own], kT[rows, f[g], own], start=True, stop=True)
                close(ins, "dil_score", i)
            if 1 <= i <= DIL_TILES:
                j = i - 1
                ps = open_("dil_pt", j)
                pe.wait_ge(sem("dil_exp"), j + 1)
                for b in range(6):
                    ins = turn(ps[:, b * P:(b + 1) * P], dil_s[:, j % 2, b * P:(b + 1) * P], ident[:, :])
                close(ins, "dil_pt", j)
            if i >= 2:
                j = i - 2
                s, c = divmod(j, DIL_STRIDE)
                ps = open_("dil_out", j)
                taken(pe, "dil_pt", j)
                for b in range(6):
                    g, tile = (0, b) if b < 4 else (b - 3, c)
                    ins = mm(ps[:, 0:HD], dil_p[:, j % 2, b * P:(b + 1) * P], vR[:, tile, g * W + s * HD:g * W + (s + 1) * HD],
                             start=(b == 0), stop=(b == 5))
                close(ins, "dil_out", j)
        taken(pe, "dil_out", DIL_TILES - 1)
        for c in range(DIL_STRIDE):
            ps = open_("dil_ot", c)
            for f in range(4):
                ins = turn(ps[:, f * P:(f + 1) * P], dil_o[:, c, f * P:(f + 1) * P], ident[:, :])
            close(ins, "dil_ot", c)

        def ret_turn(hd):
            taken(pe, "ret_out", hd, LT - 1)
            for f in range(4):
                ps = open_("ret_turn", hd, f)
                for t in range(LT):
                    ins = turn(ps[:, t * P:(t + 1) * P], ry[:, t, f * P:(f + 1) * P], ident[:, :])
                close(ins, "ret_turn", hd, f)

        for hd in range(RET_HEADS):
            w = weights("ret_qk", 2 * KD, RET_QK)
            for mt in range(4):
                b, d = divmod(mt, 2)
                ins = product(("ret_qk", hd, mt), lambda k: w[:, b * KD + k, d * P:(d + 1) * P], lambda k: uT[:, k, :], KD)
                close(ins, "ret_qk", hd, mt)
            for name in ("ret_v", "ret_g"):
                w = weights(name)
                for t in range(LT):
                    ins = product((name, hd, t), lambda k: uT[:, k, t * P:(t + 1) * P], lambda k: w[:, k, :], KD)
                    close(ins, name, hd, t)
            if hd >= 1:
                ret_turn(hd - 1)
            pe.wait_ge(sem("ret_rotated"), 2 * (hd + 1))
            for j in range(LT):
                ins = product(("ret_score", hd, j), lambda d: rkT[:, d, j * P:(j + 1) * P], lambda d: rqT[:, d, j * P:SEQ], 2,
                              ncol=SEQ - j * P)
                close(ins, "ret_score", hd, j)
            taken(pe, "ret_v", hd, LT - 1)
            for t in range(LT):
                taken(pe, "ret_score", hd, t)
                ins = product(("ret_out", hd, t), lambda j: rs[:, j, (t - j) * P:(t - j + 1) * P], lambda j: rv[:, j, :], t + 1)
                close(ins, "ret_out", hd, t)
        ret_turn(RET_HEADS - 1)
        taken(pe, "ret_turn", RET_HEADS - 1, 3)

        for n in range(2):
            for b in range(2):
                w = weights("mix_gate")
                for f in range(4):
                    ins = product(("mix_gate", b, n, f), lambda k: w[:, k, f * P:(f + 1) * P], lambda k: uT[:, k, :], KD)
                    close(ins, "mix_gate", b, n, f)
            for half in range(2):
                w = weights("mix_ret")
                for f in range(4):
                    ps = open_("mix_ret", n, f) if half == 0 else bank(plan["mix_ret", n, f])
                    for k in range(KD):
                        ins = mm(ps, w[:, k, f * P:(f + 1) * P], yrT[:, half * KD + k, :], start=(half == 0 and k == 0),
                                 stop=(half == 1 and k == KD - 1))
                    if half == 1:
                        close(ins, "mix_ret", n, f)
                if half == 0:
                    ins.then_inc(used, 1)
        w = weights("mix_dil", 4, D)
        for f in range(KD):
            ins = product(("mix_dil", f), lambda k: w[:, k, f * P:(f + 1) * P], lambda k: yaT[:, k, :], 4)
            close(ins, "mix_dil", f)
        pe.wait_ge(sem("mixed"), KD)
        for n in range(2):
            w = weights("mix_o")
            for t in range(LT):
                ins = product(("mix_o", n, t), lambda k: mixT[:, k, t * P:(t + 1) * P], lambda k: w[:, k, :], KD)
                close(ins, "mix_o", n, t)

        norm("mlp")
        for l in range(D_FF // W):
            w = weights("up")
            for f in range(4):
                ins = product(("up", 4 * l + f), lambda k: w[:, k, f * P:(f + 1) * P], lambda k: vT[:, k, :], KD)
                close(ins, "up", 4 * l + f)
        for n in range(2):
            for q in range(4):
                w = weights("down")
                for t in range(LT):
                    ps = open_("down", n, t) if q == 0 else bank(plan["down", n, t])
                    for k in range(KD):
                        pe.wait_ge(sem("ff_squared"), q * KD + k + 1)
                        ins = mm(ps, ffT[:, q * KD + k, t * P:(t + 1) * P], w[:, k, :], start=(q == 0 and k == 0),
                                 stop=(q == 3 and k == KD - 1))
                    if q == 3:
                        close(ins, "down", n, t)
                if q < 3:
                    ins.then_inc(used, 1)

        norm("ple")
        pe.wait_ge(sem("ple_landed"), 32)
        pe.wait_ge(sem("ones_set"), 1)
        for d in range(PLE // P):
            ps = open_("ple_turn", d)
            for t in range(LT):
                ins = turn(ps[:, t * P:(t + 1) * P], pR[:, t, d * P:(d + 1) * P], ident[:, :])
            close(ins, "ple_turn", d)
        for n in range(2):
            w = weights("ple_gate")
            for t in range(LT):
                ps = open_("ple_gate", n, t)
                mm(ps, ones[0:1, :], b_ple[0:1, n * W:(n + 1) * W], start=True, stop=False)
                for k in range(KD):
                    ins = mm(ps, wT[:, k, t * P:(t + 1) * P], w[:, k, :], start=False, stop=(k == KD - 1))
                close(ins, "ple_gate", n, t)
        taken(pe, "ple_turn", PLE // P - 1)
        w = weights("ple_in", 2, D)
        for n in range(2):
            for t in range(LT):
                ins = product(("ple_in", n, t), lambda k: pT[:, k, t * P:(t + 1) * P], lambda k: w[:, k, n * W:(n + 1) * W], 2)
                close(ins, "ple_in", n, t)

        pe.wait_ge(sem("cond_ready"), 1)
        for l in range(2):
            for n in range(6 * D // W):
                w = weights("ada")
                ps = open_("ada", l, n)
                for k in range(KD):
                    ins = mm(ps[0:2, :], cond[:, :, k], w[:, k, :], start=(k == 0), stop=(k == KD - 1))
                close(ins, "ada", l, n)
        for l in range(2):
            ps = open_("ada_turn", l)
            pe.wait_ge(sem("mod_rows_landed"), 16 * (l + 1))
            close(turn(ps[:, 0:96], mod_rows[0:96, l, :], ident[0:96, 0:96]), "ada_turn", l)

        norm("na")
        for i in range(NA_STEPS + 2):
            if i < NA_STEPS:
                half, t = divmod(i, NT)
                if t == 0:
                    w = weights("na_proj")
                ins = product(("na_proj", i), lambda k: hT_na[:, k, t * P:(t + 1) * P], lambda k: w[:, k, :], KD)
                close(ins, "na_proj", i)
            if i >= 2:
                j = i - 2
                ps = open_("na_turn", j)
                pe.wait_ge(sem("na_normed"), j + 1)
                for f in range(4):
                    ins = turn(ps[:, f * P:(f + 1) * P], na_s[:, j % 2, f * P:(f + 1) * P], ident[:, :])
                close(ins, "na_turn", j)

        def grid(x, c0, n):
            return x[:, 0:SEQ].rearrange("p (r c) -> p r c", c=GRID)[:, :, c0:c0 + n]

        for n in range(2):
            w = weights("na_v")
            for t in range(NT):
                ins = product(("na_v", n, t), lambda k: hT_na[:, k, t * P:(t + 1) * P], lambda k: w[:, k, :], KD)
                close(ins, "na_v", n, t)
        taken(pe, "na_turn", NA_STEPS - 1)
        taken(pe, "na_v", 1, NT - 1)
        pe.wait_ge(sem("na_strips_landed"), 16 * 4 * BLOCKS * LT)
        for i in range(NA_UNITS + 2):
            if i < NA_UNITS:
                hd, un = divmod(i, NT)
                rows, f = slice(hd % 2 * HD, hd % 2 * HD + HD), hd // 2
                ps = open_("na_score", i)
                if un < BLOCKS:
                    q = naq[rows, f, un * P:(un + 1) * P]
                    mm(ps[:, 0:2 * P], q, grid(nak[rows, f, :], strip0[un], STRIP), start=True, stop=True)
                    ins = mm(ps[:, 2 * P:W], q, nak[rows, f, SEQ:TOK], start=True, stop=True)
                else:
                    ins = mm(ps[:, 0:CTX], naq[rows, f, un * P:(un + 1) * P], nak[rows, f, SEQ:TOK], start=True, stop=True)
                close(ins, "na_score", i)
            if 1 <= i <= NA_UNITS:
                j = i - 1
                ps = open_("na_pt", j)
                pe.wait_ge(sem("na_exp"), j + 1)
                for b in range(4 if j % NT < BLOCKS else CT):
                    ins = turn(ps[:, b * P:(b + 1) * P], na_s[:, j % 2, b * P:(b + 1) * P], ident[:, :])
                close(ins, "na_pt", j)
            if i >= 2:
                j = i - 2
                hd, un = divmod(j, NT)
                ps = open_("na_out", j)
                taken(pe, "na_pt", j)
                d = slice(hd * HD, (hd + 1) * HD)
                vals = [na_vc[:, c, d] for c in range(CT)]
                if un < BLOCKS:
                    vals = [na_vs[:, 2 * un + half, d] for half in range(2)] + vals
                for b, v in enumerate(vals):
                    ins = mm(ps[:, 0:HD], na_p[:, j % 2, b * P:(b + 1) * P], v, start=(b == 0), stop=(b == len(vals) - 1))
                close(ins, "na_out", j)
        taken(pe, "na_out", NA_UNITS - 1)
        for t in range(NT):
            ps = open_("na_ot", t)
            for f in range(KD):
                ins = turn(ps[:, f * P:(f + 1) * P], na_o[:, t, f * P:(f + 1) * P], ident[:, :])
            close(ins, "na_ot", t)
        taken(pe, "na_ot", NT - 1)
        for n in range(2):
            w = weights("na_o")
            for t in range(NT):
                ins = product(("na_o", n, t), lambda k: na_oT[:, k, t * P:(t + 1) * P], lambda k: w[:, k, :], KD)
                close(ins, "na_o", n, t)

        def experts(l):
            nt, m = TILES[l], SLOTS if l == 0 else CAP_L
            norm(f"moe{l}")
            pe.wait_ge(sem("moe_landed"), 64 * (l + 1))
            ps = open_("moe_logit", l)
            for t in range(nt):
                for k in range(KD):
                    ins = mm(ps[:, t * EXPERTS:(t + 1) * EXPERTS], hT_moe[:, k, t * P:(t + 1) * P], router[:, k, :],
                             start=(k == 0), stop=(k == KD - 1))
            close(ins, "moe_logit", l)
            ps = open_("moe_afft", l)
            pe.wait_ge(sem("moe_affinity"), l + 1)
            for t in range(nt):
                ins = turn(ps[0:EXPERTS, t * P:(t + 1) * P], aff[:, t, :], ident[:, :])
            close(ins, "moe_afft", l)
            ps = open_("moe_slot", l)
            pe.wait_ge(sem("moe_numbered"), l + 1)
            for t in range(nt):
                ins = turn(ps[:, t * EXPERTS:(t + 1) * EXPERTS], sumT[0:EXPERTS, t * P:(t + 1) * P], ident[0:EXPERTS, 0:EXPERTS])
            close(ins, "moe_slot", l)

            def gather(e):
                pe.wait_ge(sem("moe_selected"), l * EXPERTS + e + 1)
                for half in range(2):
                    ps = open_("moe_gather", l, e, half).rearrange("p (k s) -> p k s", k=4)
                    for k in range(4):
                        d = slice((4 * half + k) * P, (4 * half + k + 1) * P)
                        for t in range(LT):
                            ins = mm(ps[:, k, 0:CAP_L], xn_moe[:, t, d], sel_l[:, t, :], start=(t == 0), stop=(t == LT - 1))
                        for t in range(LT, nt):
                            ins = mm(ps[:, k, CAP_L:SLOTS], xn_moe[:, t, d], sel_c[:, t - LT, :], start=(t == LT), stop=(t == nt - 1))
                    close(ins, "moe_gather", l, e, half)
                ps = open_("moe_selt", l, e)
                for t in range(nt):
                    ins = turn(ps[0:m, t * P:(t + 1) * P], sel_g[:, t, 0:m], ident[:, :])
                close(ins, "moe_selt", l, e)

            def scatter(e):
                taken(pe, "moe_selt", l, e)
                taken(pe, "moe_y", l, e, 1)
                for t in range(nt):
                    for n in range(2):
                        ps = open_("moe_add", l, e, t, n)
                        close(mm(ps, selT[0:m, e % 2, t * P:(t + 1) * P], y_moe[0:m, e % 2, n * W:(n + 1) * W], start=True, stop=True),
                              "moe_add", l, e, t, n)

            gather(0)
            for e in range(EXPERTS):
                taken(pe, "moe_gather", l, e, 1)
                for n in range(2):
                    for name, key in (("moe_w1", "moe_h1"), ("moe_w3", "moe_h3")):
                        w = weights(name)
                        ps = open_(key, l, e, n)
                        for k in range(KD):
                            ins = mm(ps[0:m, :], xinT[:, e % 2, k, 0:m], w[:, k, :], start=(k == 0), stop=(k == KD - 1))
                        close(ins, key, l, e, n)
                if e >= 1:
                    scatter(e - 1)
                if e + 1 < EXPERTS:
                    gather(e + 1)
                taken(pe, "moe_h3", l, e, 1)
                ps = open_("moe_ht", l, e).rearrange("p (k s) -> p k s", k=KD)
                for k in range(KD):
                    ins = turn(ps[:, k, 0:m], hid[0:m, k * P:(k + 1) * P], ident[0:m, 0:m])
                close(ins, "moe_ht", l, e)
                taken(pe, "moe_ht", l, e)
                for n in range(2):
                    w = weights("moe_w2")
                    ps = open_("moe_y", l, e, n)
                    for k in range(KD):
                        ins = mm(ps[0:m, :], hidT[:, k, 0:m], w[:, k, :], start=(k == 0), stop=(k == KD - 1))
                    close(ins, "moe_y", l, e, n)
            scatter(EXPERTS - 1)

        experts(0)

        norm("rw")
        for i, q in enumerate("rkvwag"):
            x = xs[i % 2]
            if q in "rkv":
                for n in range(2):
                    w = weights("rw_proj")
                    for t in range(LT if q == "r" else NT):
                        pe.wait_ge(sem("rw_mixed"), (i + 1) * KD)
                        ins = product(("rw_proj", q, n, t), lambda k: x[:, k, t * P:(t + 1) * P], lambda k: w[:, k, :], KD)
                        close(ins, "rw_proj", q, n, t)
                continue
            w = weights(f"rw_low_{q}", 1, SLOT)[:, 0, :]
            pe.wait_ge(sem("rw_mixed"), (i + 1) * KD)
            ps = open_("rw_low", q)
            for lo, hi in ((0, SEQ), (SEQ, TOK)):
                for k in range(KD):
                    ins = mm(ps[:, lo:hi], w[:, k * P:(k + 1) * P], x[:, k, lo:hi], start=(k == 0), stop=(k == KD - 1))
            close(ins, "rw_low", q)
            taken(pe, "rw_low", q)
            for z in range(1 if q == "g" else 2):
                rows = slice(0, P) if q == "g" else slice(z * CH, (z + 1) * CH)
                for n in range(2):
                    at = KD * P + n * W
                    for t in range(LT if q == "g" else NT):
                        ps = open_("rw_high", q, z, n, t)
                        if q != "g":
                            mm(ps, ones[z * CH:z * CH + 1, :], w[z * CH:z * CH + 1, at + D:at + D + W], start=True, stop=False)
                        ins = mm(ps, lowT[rows, t * P:(t + 1) * P], w[rows, at:at + W], start=(q == "g"), stop=True)
                        close(ins, "rw_high", q, z, n, t)

        n_step = 0
        pe.wait_ge(sem("rw_const_landed"), 16 * 7)
        pe.wait_ge(sem("rw_zeroed"), 2)
        for p in range(RW_PAIRS):
            I = {q: v[p % 2] for q, v in RW_IN.items()}
            pe.wait_ge(sem(f"rw_in_landed_{p % 2}"), 16 * 9 * (p // 2 + 1))
            for z in range(2):
                lam = I[f"w{z}"]
                lam_f = lam.rearrange("p t d -> p (t d)")
                for key, c in (("rw_sum", c_sum), ("rw_sum_ex", c_sum_ex)):
                    ps = open_(key, p, z)
                    for lo, hi in ((0, SEQ), (SEQ, TOK)):
                        ins = mm(ps[:, lo:hi], c[:, z, :], lam_f[:, lo:hi], start=True, stop=True)
                    close(ins, key, p, z)
                ps = open_("rw_end", p, z)
                for t in range(NT):
                    ins = mm(ps[:, 2 * t:2 * t + 2], lam[:, t, :], c_ind, start=True, stop=True)
                close(ins, "rw_end", p, z)
                pe.wait_ge(sem("rw_scaled"), 2 * p + z + 1)
                for x, src in enumerate((kh[z], bh[z], th[z], rw_t)):
                    ps = open_("rw_turn", p, z, x)
                    for t in range(LT if x == 3 else NT):
                        ins = turn(ps[:, t * P:(t + 1) * P], src[:, t, :], ident[:, :])
                    close(ins, "rw_turn", p, z, x)
            taken(pe, "rw_turn", p, 1, 3)
            for t in range(NT):
                tile = slice(t * P, (t + 1) * P)
                for z in range(2):
                    kr = xT[z][:, 0:2 * TOK].rearrange("p (x s) -> p x s", x=2)[:, 0:2 if t < LT else 1, tile]
                    n = 2 * P if t < LT else P
                    ps = open_("rw_ab", p, t, z).rearrange("p (h s) -> p h s", h=2)
                    for hd in range(2):
                        rows = slice(hd * CH, (hd + 1) * CH)
                        mm(ps[:, hd, 0:n], BT[z][rows, tile], kr[rows], start=True, stop=True)
                        ins = mm(ps[:, hd, 2 * P:2 * P + n], TT[z][rows, tile], kr[rows], start=True, stop=True)
                    close(ins, "rw_ab", p, t, z)
                    ps = open_("rw_a", p, t, z).rearrange("p (h s) -> p h s", h=2)
                    for hd in range(2):
                        rows = slice(hd * CH, (hd + 1) * CH)
                        ins = mm(ps[:, hd, 0:P], KT[z][rows, tile], BT[z][rows, tile], start=True, stop=True)
                    close(ins, "rw_a", p, t, z)
                    n_step += 1
                for lv in range(1, 6):
                    for z in range(2):
                        ps = open_("rw_x", p, t, z, lv)
                        if lv == 1:
                            pe.wait_ge(sem("rw_inv_started"), n_step - 1 + z)
                            pe.wait_ge(sem("rw_off"), n_step - 1 + z)
                        else:
                            taken(pe, "rw_join", p, t, z, lv - 1)
                        T = halves(inv[z][:, :, 0, :], lv, z)
                        for hd in range(2):
                            ins = mm(ps[:, hd * CH:(hd + 1) * CH], at_off[z][:, hd, lv - 1, :], T[:, hd], start=True, stop=True)
                        close(ins, "rw_x", p, t, z, lv)
                    for z in range(2):
                        ps = open_("rw_join", p, t, z, lv)[:, 0:4 * CH].rearrange("p (h x s) -> p h x s", h=2, x=2)
                        taken(pe, "rw_x", p, t, z, lv)
                        X = halves(xl[z][:, lv - 1], lv, z)
                        M = halves(inv[z][:, :, 1, :], lv, z, True)
                        for hd in range(2):
                            mm(ps[:, hd, 0, :], inv[z][:, hd, 1, :], X[:, hd], start=True, stop=True)
                            ins = mm(ps[:, hd, 1, :], xl[z][:, lv - 1, hd, :], M[:, hd], start=True, stop=True)
                        close(ins, "rw_join", p, t, z, lv)
                for z in range(2):
                    ps = open_("rw_gv", p, t, z)
                    taken(pe, "rw_ab", p, t, z)
                    for hd in range(2):
                        ins = mm(ps[:, hd * CH:(hd + 1) * CH], gT[z][:, hd, :], I["v"][:, t, hd * CH:(hd + 1) * CH], start=True, stop=True)
                    close(ins, "rw_gv", p, t, z)
                    ps = open_("rw_tk", p, t, z)
                    taken(pe, "rw_join", p, t, z, 5)
                    for hd in range(2):
                        ins = mm(ps[:, hd * P:(hd + 1) * P], kh[z][:, t, :], inv[z][:, hd, 1, :], start=True, stop=True)
                    close(ins, "rw_tk", p, t, z)
                for z in range(2):
                    ps = open_("rw_tgv", p, t, z)
                    taken(pe, "rw_gv", p, t, z)
                    for hd in range(2):
                        d = slice(hd * CH, (hd + 1) * CH)
                        ins = mm(ps[:, d], inv[z][:, hd, 1, :], gv[z][:, d], start=True, stop=True)
                    close(ins, "rw_tgv", p, t, z)
            pe.wait_ge(sem("rw_state_zeroed"), p + 1)
            taken(pe, "rw_tk", p, NT - 1, 1)
            for i in range(2 * NT):
                for z in range(2):
                    t, c = rw_chunk(i, z)
                    ps = open_("rw_u", p, i, z)
                    if i >= 1:
                        taken(pe, "rw_state", p, i - 1, z)
                    close(mm(ps[:, 0:P], tkT[z][:, t, :], state[z][:, i % 2, :], start=True, stop=True), "rw_u", p, i, z)
                for z in range(2):
                    t, c = rw_chunk(i, z)
                    rows = slice(c * CH, (c + 1) * CH)
                    ps = open_("rw_state", p, i, z)[:, 0:P]
                    mm(ps, th[z][rows, t, :], I["v"][rows, t, :], start=True, stop=False)
                    taken(pe, "rw_u", p, i, z)
                    close(mm(ps, bh[z][rows, t, :], u[z][rows, :], start=False, stop=True), "rw_state", p, i, z)
                    if t < LT:
                        ps = open_("rw_y", p, i, z)[:, 0:P]
                        mm(ps, RT[z][:, t * P:(t + 1) * P], state[z][:, i % 2, :], start=True, stop=False)
                        for hd in range(2):
                            d = slice(hd * CH, (hd + 1) * CH)
                            mm(ps[:, d], rtT[z][rows, t, hd, :], I["v"][rows, t, d], start=False, stop=False)
                            ins = mm(ps[:, d], rbT[z][rows, t, hd, :], u[z][rows, d], start=False, stop=(hd == 1))
                        close(ins, "rw_y", p, i, z)
            ps = open_("rw_ot", p)
            pe.wait_ge(sem("rw_read_out"), p + 1)
            for t in range(LT):
                ins = turn(ps[:, t * P:(t + 1) * P], yd[1][:, t, :], ident[:, :])
            close(ins, "rw_ot", p)
        taken(pe, "rw_ot", RW_PAIRS - 1)
        for n in range(2):
            w = weights("rw_o")
            for t in range(LT):
                ins = product(("rw_o", n, t), lambda k: zT(k)[:, t * P:(t + 1) * P], lambda k: w[:, k, :], KD)
                close(ins, "rw_o", n, t)
        experts(1)


def columns_of(x):
    x = np.asarray(x).reshape(-1, P)
    return x.T


def kernel(**inputs):
    from concourse import bacc
    from concourse.bass_utils import run_bass_kernel_spmd

    nc = bacc.Bacc("TRN2", target_bir_lowering=False, num_devices=1)
    i = {k: np.asarray(v) for k, v in inputs.items()}
    arrays = dict(constants())
    vectors = {"g_pre_mix": i["g_pre_mix"], "b_gate_r": i["b_gate"][0, 0], "b_gate_a": i["b_gate"][0, 1],
               "g_pre_mlp": i["g_pre_mlp"], "g_pre_ple": i["g_pre_ple"],
               "norm_g": np.stack([i["norm1_g_2"], i["norm2_g_2"]], 1), "na_q_g": np.tile(i["na_q_g_2"][0], 2),
               "na_k_g": np.tile(i["na_k_g_2"][0], 2), "rw_mix": i["rw_mix_2"][0], "cond": np.stack([i["c_2"][0], i["c_ctx_2"]])}
    arrays["cols"] = np.concatenate([columns_of(vectors[k]) for k in COLUMNS], 1)
    arrays["x"] = i["x"][0]
    arrays["p"] = i["p"][0, 0]
    arrays["pos_row"] = np.broadcast_to(i["positions"], (P, SEQ))
    arrays["pos_col"] = i["positions"].reshape(P, DIL_STRIDE)
    for k in ("w_in", "w_ret_out", "w_dil_out", "w_o", "w_up", "w_down", "w_ple_gate", "w_ple_in", "g_post_mix", "g_post_mlp",
              "g_post_ple", "b_ple_gate"):
        arrays[k] = i[k][0]
    arrays["ctx"] = i["ctx_2"][0]
    for k in ("ada_w", "ada_b", "moe_router", "moe_w1", "moe_w3", "moe_w2"):
        arrays[k] = i[k + "_2"]
    for k in ("na_w_qkv", "na_w_o", "rw_w_r", "rw_w_k", "rw_w_v", "rw_w0", "rw_a0", "rw_g1", "rw_g2", "rw_w_o"):
        arrays[k] = i[k + "_2"][0]
    arrays["na_rpb"] = np.pad(i["na_rpb_2"][0], ((0, 0), (0, 0), (RPB_PAD, RPB_PAD)))
    for q in "wa":
        arrays[f"rw_{q}1"] = i[f"rw_{q}1_2"][0].transpose(1, 0, 2).reshape(D, 2 * CH)
        arrays[f"rw_{q}2"] = i[f"rw_{q}2_2"][0].reshape(2 * CH, D)
    arrays["rw_rows"] = np.stack([i["rw_k_k_2"][0], i["rw_k_a_2"][0], i["rw_r_k_2"][0].reshape(D), i["rw_ln_g_2"][0], i["rw_ln_b_2"][0]])
    arrays = {f"in_{k}": np.ascontiguousarray(v) for k, v in arrays.items()}
    a = {k[3:]: nc.dram_tensor(k, v.shape, mybir.dt.from_np(v.dtype), kind="ExternalInput").ap() for k, v in arrays.items()}
    out = nc.dram_tensor("out", (SEQ, D), F32, kind="ExternalOutput").ap()
    build(nc, a, out)
    got = run_bass_kernel_spmd(nc, [arrays], core_ids=[0])
    return got.results[0]["out"].reshape(1, SEQ, D)
```

```python
from contextlib import ExitStack

import numpy as np
import concourse.bass as bass
from concourse import mybir

F32 = mybir.dt.float32
I32 = mybir.dt.int32
ALU = mybir.AluOpType
ACT = mybir.ActivationFunctionType
AX = mybir.AxisListType.X

P = 128
D = 1024
KD = D // P
SEQ = 512
LT = SEQ // P
CTX = 256
CT = CTX // P
NT = LT + CT
TOK = SEQ + CTX
W = 512
EPS = 1e-6
BIG = 1e30

RET_HEADS, RET_QK, RET_V = 4, 256, 512
DIL_SLOTS, DIL_GROUPS, HD = 8, 3, 64
DIL_STRIDE = 4
ROPE8 = 8
D_FF = 4096
PLE = 256
COL_RQ, COL_RK, COL_RV, COL_RG = 0, 1024, 2048, 4096
COL_DIL = 6144
COL_GATE = COL_DIL + 3 * DIL_GROUPS * DIL_SLOTS * HD

NA_HEADS = 16
STRIP = 32
BLOCKS = 4
GRID = 64
ROWS = SEQ // GRID

EXPERTS = 16
CAP_L, CAP_C = 2 * SEQ // EXPERTS, 2 * CTX // EXPERTS
SLOTS = CAP_L + CAP_C
D_EXP = 1024

RW_PAIRS = 8
CH = 64
RW_LEVELS = 6
RW_CHAINS = 4
RW_GROUPS = NT * 2 // RW_CHAINS
RW_STEPS = 2 * NT
RW_READ_STD = 3
GN_EPS = 64e-5
RPB_PAD = 32
RING = 3
SLOT = KD * W


def constants():
    c = {}
    eye = np.eye(P, dtype=np.float64)
    c["ident"] = eye
    f = np.arange(P)
    c["ret_freq"] = (1.0 / (10000.0 ** (f / (P - 1.0))))[:, None]
    c["dil_freq"] = np.broadcast_to(500000.0 ** (-np.arange(0, 16, 2) / 16.0), (P, ROPE8))
    dec = np.zeros((P, RET_HEADS, SEQ))
    for h in range(RET_HEADS):
        g = np.log1p(-(2.0 ** (-5.0 - h)))
        dist = np.arange(SEQ)[None, :] - np.arange(P)[:, None]
        dec[:, h] = np.where(dist >= 0, np.exp(np.maximum(dist, 0) * g), 0.0) * RET_QK ** -0.5
    c["ret_decay"] = dec
    m = np.full((P, DIL_STRIDE, 6, P), -BIG)
    l = np.arange(P)
    for s in range(DIL_STRIDE):
        t = DIL_STRIDE * l + s
        for s2 in range(DIL_STRIDE):
            d = t[:, None] - (DIL_STRIDE * l + s2)[None, :]
            m[:, s, s2][(d >= 0) & (d <= 128)] = 0
        d = l[:, None] - l[None, :]
        m[:, s, 4][d >= 0] = 0
        m[:, s, 5][(d >= 0) & (d % 4 == 0)] = 0
    c["dil_mask"] = m
    m = np.full((P, 3, ROWS, STRIP), -BIG)
    cc = np.arange(P) % 16
    kk = np.arange(STRIP)[None, :]
    for n, j in enumerate((0, 1, 3)):
        qcol = 16 * j + cc
        lo = np.clip(qcol - 8, 0, GRID - 16) - np.clip(16 * j - 8, 0, GRID - STRIP)
        ok = (kk >= lo[:, None]) & (kk < lo[:, None] + 16)
        m[:, n][np.broadcast_to(ok[:, None, :], (P, ROWS, STRIP))] = 0
    c["na_mask"] = m
    c["slot_no"] = np.broadcast_to(np.arange(CAP_L), (P, CAP_L))
    a, b = np.arange(P)[:, None], np.arange(P)[None, :]
    same = a // CH == b // CH
    k = np.exp(-0.5)
    c["rw_sum"] = np.stack([(same & (a <= b)) * k, (same & (a >= b)) * k], 1)
    c["rw_sum_ex"] = np.stack([(same & (a < b)) * k, (same & (a > b)) * k], 1)
    c["rw_blocks"] = same
    c["rw_ind"] = np.stack([(f // CH == n) * k for n in range(2)], 1)
    c["rw_mask"] = np.stack([np.stack([same & (a < b), same & (a <= b)], 1), np.stack([same & (a > b), same & (a >= b)], 1)], 1)
    joins = np.zeros((P, 2, RW_LEVELS, P))
    for n in range(RW_LEVELS):
        half = 1 << n
        join = (a // (2 * half) == b // (2 * half)) & (a // half % 2 == 1) & (b // half % 2 == 0)
        joins[:, 0, n], joins[:, 1, n] = join, join.T
    c["rw_join"] = joins[:, :, 1:]
    c["rw_pairs"] = -np.stack([joins[:, :, 0], joins[:, ::-1, 0]], 2)
    return {k: np.ascontiguousarray(np.asarray(v, np.float32).reshape(P, -1)) for k, v in c.items()}


class Job:

    def __init__(self, number, bank, width, engine, count, before):
        self.number, self.bank, self.width = number, bank, width
        self.engine, self.count, self.before = engine, count, before


class JobPlan:

    def __init__(self):
        self.jobs, self.at, self.holder, self.taken = {}, 0, [None] * 8, {"act": 0, "dve": 0}

    def add(self, engine, *key, width=1):
        if width == 2 and self.at % 2:
            self.at += 1
        bank = self.at % 8
        before = [self.holder[bank + i] for i in range(width) if self.holder[bank + i]]
        self.taken[engine] += 1
        job = Job(len(self.jobs), bank, width, engine, self.taken[engine], before)
        for i in range(width):
            self.holder[bank + i] = job
        self.at += width
        assert key not in self.jobs, key
        self.jobs[key] = job

    def __getitem__(self, key):
        return self.jobs[key]


DIL_STEPS = [(g, kind) for g in range(DIL_GROUPS) for kind in range(3)]
DIL_TILES = DIL_SLOTS * DIL_STRIDE
TILES = [NT, LT]
NA_STEPS = 4 * NT
NA_UNITS = NA_HEADS * NT
NORMS = {"dil": LT, "mlp": LT, "ple": LT, "na": NT, "moe0": NT, "rw": NT, "moe1": LT}


def plan_jobs():
    plan = JobPlan()

    def norm(use):
        for k in range(KD):
            plan.add("act", "turn", use, 0, k)
        if NORMS[use] == NT:
            for k in range(KD):
                plan.add("act", "turn", use, 1, k)

    norm("dil")
    for i in range(len(DIL_STEPS) + 1):
        if i < len(DIL_STEPS):
            for c in range(DIL_STRIDE):
                plan.add("act", "dil_proj", i, c)
        if i >= 1 and DIL_STEPS[i - 1][1] < 2:
            for c in range(DIL_STRIDE):
                plan.add("act", "dil_turn", i - 1, c)
    for i in range(DIL_TILES + 2):
        if i < DIL_TILES:
            plan.add("dve", "dil_score", i, width=2)
        if 1 <= i <= DIL_TILES:
            plan.add("act", "dil_pt", i - 1, width=2)
        if i >= 2:
            plan.add("dve", "dil_out", i - 2)
    for c in range(DIL_STRIDE):
        plan.add("act", "dil_ot", c)

    for h in range(RET_HEADS):
        for m in range(4):
            plan.add("dve", "ret_qk", h, m)
        for t in range(LT):
            plan.add("act", "ret_v", h, t)
        for t in range(LT):
            plan.add("act", "ret_g", h, t)
        if h >= 1:
            for f in range(4):
                plan.add("act", "ret_turn", h - 1, f)
        for j in range(LT):
            plan.add("dve", "ret_score", h, j)
        for t in range(LT):
            plan.add("dve", "ret_out", h, t)
    for f in range(4):
        plan.add("act", "ret_turn", RET_HEADS - 1, f)

    for n in range(2):
        for b in range(2):
            for f in range(4):
                plan.add("act", "mix_gate", b, n, f)
        for f in range(4):
            plan.add("dve", "mix_ret", n, f)
    for f in range(KD):
        plan.add("dve", "mix_dil", f)
    for n in range(2):
        for t in range(LT):
            plan.add("act", "mix_o", n, t)

    norm("mlp")
    for f in range(D_FF // P):
        plan.add("act", "up", f)
    for n in range(2):
        for t in range(LT):
            plan.add("act", "down", n, t)

    norm("ple")
    for d in range(PLE // P):
        plan.add("act", "ple_turn", d)
    for n in range(2):
        for t in range(LT):
            plan.add("act", "ple_gate", n, t)
    for n in range(2):
        for t in range(LT):
            plan.add("dve", "ple_in", n, t)

    for l in range(2):
        for n in range(6 * D // W):
            plan.add("dve", "ada", l, n)
    for l in range(2):
        plan.add("act", "ada_turn", l)

    norm("na")
    for i in range(NA_STEPS + 2):
        if i < NA_STEPS:
            plan.add("act", "na_proj", i)
        if i >= 2:
            plan.add("act", "na_turn", i - 2)
    for n in range(2):
        for t in range(NT):
            plan.add("act", "na_v", n, t)
    for i in range(NA_UNITS + 2):
        if i < NA_UNITS:
            plan.add("dve", "na_score", i)
        if 1 <= i <= NA_UNITS:
            plan.add("act", "na_pt", i - 1)
        if i >= 2:
            plan.add("dve", "na_out", i - 2)
    for t in range(NT):
        plan.add("act", "na_ot", t, width=2)
    for n in range(2):
        for t in range(NT):
            plan.add("dve", "na_o", n, t)
    plan_experts(plan, norm, 0)
    plan_recurrence(plan, norm)
    plan_experts(plan, norm, 1)
    return plan


def plan_experts(plan, norm, l):
    norm(f"moe{l}")
    plan.add("dve", "moe_logit", l)
    plan.add("dve", "moe_afft", l, width=2)
    plan.add("dve", "moe_slot", l)

    def gather(e):
        for half in range(2):
            plan.add("act", "moe_gather", l, e, half)
        plan.add("act", "moe_selt", l, e, width=2)

    def scatter(e):
        for t in range(TILES[l]):
            for n in range(2):
                plan.add("dve", "moe_add", l, e, t, n)

    gather(0)
    for e in range(EXPERTS):
        for n in range(2):
            plan.add("act", "moe_h1", l, e, n)
            plan.add("dve", "moe_h3", l, e, n)
        if e >= 1:
            scatter(e - 1)
        if e + 1 < EXPERTS:
            gather(e + 1)
        plan.add("act", "moe_ht", l, e, width=2)
        for n in range(2):
            plan.add("act", "moe_y", l, e, n)
    scatter(EXPERTS - 1)


RW_RANK = {"w": 2 * CH, "a": 2 * CH, "g": P}


def plan_recurrence(plan, norm):
    norm("rw")
    for q in "rkv":
        for n in range(2):
            for t in range(LT if q == "r" else NT):
                plan.add("act", "rw_proj", q, n, t)
    for q in "wag":
        plan.add("act", "rw_low", q, width=2)
        for z in range(1 if q == "g" else 2):
            for n in range(2):
                for t in range(LT if q == "g" else NT):
                    plan.add("act", "rw_high", q, z, n, t)

    def sums(p, z):
        plan.add("act", "rw_sum", p, z, width=2)
        plan.add("act", "rw_sum_ex", p, z, width=2)
        plan.add("act", "rw_end", p, z)

    def turn_factors(p, z):
        for x in range(4):
            plan.add("act", "rw_turn", p, z, x, width=2)

    def scan_u(p, i):
        for z in range(2):
            plan.add("dve", "rw_u", p, i, z)

    def scan_state(p, i):
        for z in range(2):
            if i + 1 < RW_STEPS:
                plan.add("dve", "rw_state", p, i, z)
            if rw_chunk(i, z)[0] < LT:
                plan.add("act", "rw_y", p, i, z)

    def scan(p, i):
        if p >= 0:
            scan_u(p, i)
            scan_state(p, i)

    for p in range(RW_PAIRS):
        sums(p, 0)
        scan(p - 1, RW_STEPS - 4)
        turn_factors(p, 0)
        sums(p, 1)
        scan(p - 1, RW_STEPS - 3)
        scan(p - 1, RW_STEPS - 2)
        turn_factors(p, 1)
        scan(p - 1, RW_STEPS - 1)
        for g in range(RW_GROUPS):
            for c in range(RW_CHAINS):
                plan.add("dve", "rw_ab", p, g, c, width=2)
                plan.add("dve", "rw_a", p, g, c, width=2)
            for c in range(RW_CHAINS):
                plan.add("act", "rw_gv", p, g, c)
            for lv in range(1, RW_LEVELS):
                i = rw_step_beside(g, lv)
                for c in range(RW_CHAINS):
                    plan.add("dve", "rw_x", p, g, c, lv)
                if i is not None:
                    scan_u(p, i)
                for c in range(RW_CHAINS):
                    plan.add("dve", "rw_join", p, g, c, lv)
                if i is not None:
                    scan_state(p, i)
            for c in range(RW_CHAINS):
                plan.add("act", "rw_tk", p, g, c)
            for c in range(RW_CHAINS):
                plan.add("act", "rw_tgv", p, g, c)
            if g == 0 and p >= 1:
                plan.add("act", "rw_ot", p - 1)
    for i in range(RW_STEPS - 4, RW_STEPS):
        scan(RW_PAIRS - 1, i)
    plan.add("act", "rw_ot", RW_PAIRS - 1)
    for n in range(2):
        for t in range(LT):
            plan.add("dve", "rw_o", n, t)


def rw_chunk(i, z):
    tile, c = divmod(i, 2)
    if z == 0:
        return (LT + tile, c) if tile < CT else (tile - CT, c)
    return (LT + CT - 1 - tile, 1 - c) if tile < CT else (LT - 1 - (tile - CT), 1 - c)


def rw_tile(g, c):
    return rw_chunk(2 * (2 * g + c // 2), c % 2)[0], c % 2


def rw_step_beside(g, lv):
    return 4 * (g - 1) + lv - 1 if g and lv <= 4 else None


def plan_weights(a):
    def square(w, n):
        return [(w[:, n * W:(n + 1) * W].rearrange("(k p) n -> p k n", p=P), 0, KD, W)]

    loads = []
    w_in = a["w_in"]
    for i, (g, kind) in enumerate(DIL_STEPS):
        c0 = COL_DIL + kind * DIL_GROUPS * W + g * W
        loads.append(("dil_proj", square(w_in[:, c0:c0 + W], 0), ("dil_proj", i, DIL_STRIDE - 1)))
    for h in range(RET_HEADS):
        q, k = (w_in[:, c + h * RET_QK:c + (h + 1) * RET_QK].rearrange("(k p) n -> p k n", p=P) for c in (COL_RQ, COL_RK))
        loads.append(("ret_qk", [(q, 0, KD, RET_QK), (k, KD * RET_QK, KD, RET_QK)], ("ret_qk", h, 3)))
        loads.append(("ret_v", square(w_in[:, COL_RV:], h), ("ret_v", h, LT - 1)))
        loads.append(("ret_g", square(w_in[:, COL_RG:], h), ("ret_g", h, LT - 1)))
    for n in range(2):
        loads.append(("mix_gate", square(w_in[:, COL_GATE:], n), ("mix_gate", 0, n, 3)))
        loads.append(("mix_gate", square(w_in[:, COL_GATE + D:], n), ("mix_gate", 1, n, 3)))
        for half in range(2):
            loads.append(("mix_ret", square(a["w_ret_out"][half * D:(half + 1) * D], n), ("mix_ret", n, 3) if half else None))
    loads.append(("mix_dil", [(a["w_dil_out"].rearrange("(k p) n -> p k n", p=P), 0, 4, D)], ("mix_dil", KD - 1)))
    for n in range(2):
        loads.append(("mix_o", square(a["w_o"], n), ("mix_o", n, LT - 1)))
    for n in range(D_FF // W):
        loads.append(("up", square(a["w_up"], n), ("up", 4 * n + 3)))
    for n in range(2):
        for part in range(4):
            loads.append(("down", square(a["w_down"][part * D:(part + 1) * D], n), ("down", n, LT - 1) if part == 3 else None))
    for n in range(2):
        loads.append(("ple_gate", square(a["w_ple_gate"], n), ("ple_gate", n, LT - 1)))
    loads.append(("ple_in", [(a["w_ple_in"].rearrange("(k p) n -> p k n", p=P), 0, 2, D)], ("ple_in", 1, LT - 1)))
    for l in range(2):
        for n in range(6 * D // W):
            loads.append(("ada", square(a["ada_w"][l], n), ("ada", l, n)))
    for n in range(4):
        loads.append(("na_proj", square(a["na_w_qkv"], n), ("na_proj", (n + 1) * NT - 1)))
    for n in range(2):
        loads.append(("na_v", square(a["na_w_qkv"][:, 2 * D:], n), ("na_v", n, NT - 1)))
    for n in range(2):
        loads.append(("na_o", square(a["na_w_o"], n), ("na_o", n, NT - 1)))

    def experts(l):
        for e in range(EXPERTS):
            for n in range(2):
                loads.append(("moe_w1", square(a["moe_w1"][l, e], n), ("moe_h1", l, e, n)))
                loads.append(("moe_w3", square(a["moe_w3"][l, e], n), ("moe_h3", l, e, n)))
            for n in range(2):
                loads.append(("moe_w2", square(a["moe_w2"][l, e], n), ("moe_y", l, e, n)))

    experts(0)
    for q in "rkv":
        for n in range(2):
            loads.append(("rw_proj", square(a[f"rw_w_{q}"], n), ("rw_proj", q, n, (LT if q == "r" else NT) - 1)))
    for q in "wa":
        pieces = [(a[f"rw_{q}1"].rearrange("(k p) r -> p k r", p=P), 0, KD, 2 * CH),
                  (a[f"rw_{q}2"].rearrange("r (o d) -> r o d", o=1), KD * 2 * CH, 1, D)]
        pieces += [(a[f"rw_{q}0"][z:z + 1], KD * 2 * CH + D, 1, D, z * CH) for z in range(2)]
        loads.append((f"rw_low_{q}", pieces, ("rw_high", q, 1, 1, NT - 1)))
    loads.append(("rw_low_g", [(a["rw_g1"].rearrange("(k p) r -> p k r", p=P), 0, KD, P),
                               (a["rw_g2"].rearrange("r (o d) -> r o d", o=1), KD * P, 1, D)], ("rw_high", "g", 0, 1, LT - 1)))
    for n in range(2):
        loads.append(("rw_o", square(a["rw_w_o"], n), ("rw_o", n, LT - 1)))
    experts(1)
    return loads


COLUMNS = {}
for _name, _n in (("g_pre_mix", KD), ("b_gate_r", KD), ("b_gate_a", KD), ("g_pre_mlp", KD), ("g_pre_ple", KD),
                  ("norm_g", 4 * KD), ("na_q_g", 1), ("na_k_g", 1), ("rw_mix", 6 * KD), ("cond", 2 * KD)):
    COLUMNS[_name] = (sum(n for _, n in COLUMNS.values()), _n)
N_COLUMNS = sum(n for _, n in COLUMNS.values())


def build(nc, a, out, debug=None):
    plan = plan_jobs()
    loads = plan_weights(a)
    ctx = ExitStack()
    signals = {}

    def sem(name):
        if name not in signals:
            signals[name] = nc.alloc_semaphore(name)
        return signals[name]

    def sb(name, *shape, dt=F32):
        return ctx.enter_context(nc.sbuf_tensor(name, [P, *shape], dt))

    h = sb("h", NT, D)
    ring = sb("ring", RING, SLOT)
    ident = sb("ident", P)
    ones = sb("ones", P)
    cols = sb("cols", N_COLUMNS)
    stats = sb("stats", 64)
    psum = [ctx.enter_context(nc.psum_tensor(f"bank{i}", [P, 2 * W], F32)) for i in range(4)]
    ARENA = 32512
    arena = sb("arena", ARENA)

    class Carve:

        def __init__(self, at=0):
            self.at = at

        def take(self, *shape, dt=F32):
            n = int(np.prod(shape))
            assert self.at + n <= ARENA, (self.at, n)
            v = arena[:, self.at:self.at + n]
            self.at += n
            if dt != F32:
                v = v.bitcast(dt)
            names = "abcd"[:len(shape)]
            if len(shape) > 1:
                v = v.rearrange(f"p ({' '.join(names)}) -> p {' '.join(names)}", **dict(zip(names[1:], shape[1:])))
            return v

    def col(name, k=0):
        at, _ = COLUMNS[name]
        return cols[:, at + k:at + k + 1]

    def bank(job):
        lo = job.bank % 2 * W
        return psum[job.bank // 2][:, lo:lo + job.width * W]

    filled = sem("psum_filled")
    freed = {"act": sem("psum_freed_act"), "dve": sem("psum_freed_dve")}
    landed = [sem(f"weights_landed_{i}") for i in range(RING)]
    used = sem("weights_used")

    def full(eng, *key):
        eng.wait_ge(filled, plan[key].number + 1)
        return bank(plan[key])

    def taken(eng, *key):
        eng.wait_ge(freed[plan[key].engine], plan[key].count)

    def free(ins, *key):
        done[plan[key].engine] += 1
        assert done[plan[key].engine] == plan[key].count, key
        ins.then_inc(freed[plan[key].engine], 1)

    done = {"act": 0, "dve": 0, "pe": 0, "weights": 0}

    m = Carve()
    uT = m.take(KD, SEQ)
    yaT = h[:, LT:NT, :].rearrange("p t (f c) -> p (t f) c", f=2)
    ret_cos, ret_sin = m.take(SEQ), m.take(SEQ)
    dil_cos, dil_sin = m.take(DIL_STRIDE, ROPE8), m.take(DIL_STRIDE, ROPE8)
    part = m.at
    n = Carve(part)
    ang, turns, angs = n.take(544), n.take(544), n.take(544)
    pos_i, pos_f = n.take(SEQ, dt=I32), n.take(SEQ)
    pos_ci, pos_cf = n.take(DIL_STRIDE, dt=I32), n.take(DIL_STRIDE)
    ret_freq, dil_freq = n.take(1), n.take(ROPE8)
    n = Carve(part)
    dil_tmp = n.take(DIL_STRIDE, W)
    dil_rot = n.take(4, 2, DIL_SLOTS, ROPE8)
    dil_o = dil_tmp
    qT, kT = n.take(12, SEQ), n.take(12, SEQ)
    v_at = n.at
    vR = n.take(DIL_STRIDE, 3 * W)
    xn_dil = Carve(v_at).take(LT, D)
    dil_mask = n.take(DIL_STRIDE, 6 * P)
    dil_s = n.take(2, 6 * P)
    dil_p = n.take(2, 6 * P)
    n = Carve(part)
    yrT = n.take(16, SEQ)
    mix_from = n.at
    rqT, rkT = n.take(2, SEQ), n.take(2, SEQ)
    rot_a, rot_b = n.take(SEQ), n.take(SEQ)
    rv, rg, rs, ry = (n.take(LT, W) for _ in range(4))
    decay = n.take(RET_HEADS, SEQ)
    n = Carve(mix_from)
    gate_r, gate_a, mixT = n.take(KD, SEQ), n.take(KD, SEQ), n.take(KD, SEQ)
    mix_t = n.take(SEQ)
    F_mix = n.take(LT, D)
    gb_mix = n.take(D)
    n = Carve()
    vT = n.take(KD, SEQ)
    xn_mlp = n.take(LT, D)
    ffT = n.take(D_FF // P, SEQ)
    F_mlp = n.take(LT, D)
    gb_mlp = n.take(D)
    n = Carve()
    wT = n.take(KD, SEQ)
    xn_ple = n.take(LT, D)
    pR, pT = n.take(LT, PLE), n.take(PLE // P, SEQ)
    gate_p = n.take(LT, D)
    F_ple = n.take(LT, D)
    gb_ple = n.take(D)
    b_ple = n.take(D)
    junk = sb("junk", D)
    cond = sb("cond", 2, KD)
    mod = sb("mod", 2, 2, 6, KD)
    mod_a = sb("mod_a", 2, 2, 2, KD)
    n = Carve()
    xn_na, hT_na = n.take(NT, D), n.take(KD, TOK)
    ada_m = n.take(2, 6 * D)
    mod_rows = n.take(2, P)
    n = Carve()
    naq = n.take(KD, TOK)
    n.take(KD, TOK)
    na_o = hT_na.rearrange("p k t -> p (k t)").rearrange("p (t d) -> p t d", d=D)
    nak = n.take(KD, TOK)
    na_vs = n.take(2 * BLOCKS, D)
    na_vc = n.take(CT, D)
    na_v = Carve(n.at).take(LT, W)
    na_s, na_p = n.take(2, W), n.take(2, W)
    na_bias = [n.take(4, 2 * P), junk[:, :].rearrange("p (a b) -> p a b", a=4)]
    na_mask = n.take(3, 2 * P)
    na_oT = naq
    na_gate = nak.rearrange("p k t -> p (k t)")[:, 0:2 * D].rearrange("p (s d) -> p s d", d=D)
    na_t = nak.rearrange("p k t -> p (k t)")[:, 2 * D:3 * D].rearrange("p (s d) -> p s d", d=W)
    n = Carve()
    xn_moe = n.take(NT, D)
    moe_after = n.at
    hT_moe = n.take(KD, TOK)
    router = n.take(KD, EXPERTS)
    logit, aff = n.take(NT, EXPERTS), n.take(NT, EXPERTS)
    affT, workT, sumT = n.take(TOK), n.take(TOK), n.take(TOK)
    top8 = n.take(8)
    slot = n.take(NT, EXPERTS)
    slot_no = n.take(CAP_L)
    moe_gate = n.take(2, D)
    keep = n.at
    acc = Carve(moe_after).take(NT, D)
    n = Carve(keep)
    sel_l, sel_c = n.take(LT, CAP_L), n.take(CT, CAP_C)
    sel_g = n.take(NT, SLOTS)
    selT = n.take(2, NT * P)
    xinT = n.take(2, KD, SLOTS)
    s1, hid, hidT = n.take(D), n.take(D), n.take(KD, SLOTS)
    y_moe = n.take(2, D)
    n = Carve()
    hT_rw = n.take(KD, TOK)
    xx = n.take(KD, TOK)
    xs = [n.take(KD, TOK), n.take(KD, TOK)]
    xn_rw = xs[1].rearrange("p k t -> p (k t)").rearrange("p (t d) -> p t d", d=D)
    lowT = n.take(TOK)
    staging = n.take(4, W)
    ring_flat = ring[:, :, :].rearrange("p a b -> p (a b)")
    RW_IN, at = {}, 0
    for q in ("r", "g", "k", "v", "w0", "w1", "a0", "a1"):
        nt = LT if q in "rg" else NT
        RW_IN[q] = [ring_flat[:, b * 5632 + at:b * 5632 + at + nt * P].rearrange("p (t d) -> p t d", d=P) for b in range(2)]
        at += nt * P
    assert at == 5632
    n = Carve()
    c_sum, c_sum_ex, c_ind = n.take(2, P), n.take(2, P), n.take(2)
    c_mask, c_join, c_pairs = n.take(2, 2, P), n.take(2, RW_LEVELS - 1, P), n.take(2, 2, P)
    c_blocks = n.take(P)
    rw_rows = n.take(2, 5, P)
    kh = [n.take(NT, P) for _ in range(2)]
    bh, th = ([[n.take(NT, P) for _ in range(2)] for _ in range(2)] for _ in range(2))
    xT = [n.take(2 * TOK + 2 * SEQ) for _ in range(2)]
    TT = [n.take(TOK) for _ in range(2)]
    KT, BT = ([x[:, lo:lo + TOK] for x in xT] for lo in (0, TOK + 2 * SEQ))
    RT = [[x[:, TOK + b * SEQ:TOK + (b + 1) * SEQ] for x in xT] for b in range(2)]
    tkT, tgv = ([n.take(NT, P) for _ in range(2)] for _ in range(2))
    rbT, rtT = ([n.take(LT, 2, CH) for _ in range(2)] for _ in range(2))
    w_end = [[n.take(RW_STEPS) for _ in range(2)] for _ in range(2)]
    state, u = [n.take(2, P) for _ in range(2)], [n.take(P) for _ in range(2)]
    zT_hi = n.take(4, SEQ)
    temp = n.at
    e_neg, e_pos, e_ex, kk, rw_t = (n.take(NT, P) for _ in range(5))
    n = Carve(temp)
    aT, gT = ([n.take(2, P) for _ in range(RW_CHAINS)] for _ in range(2))
    gv = [n.take(P) for _ in range(RW_CHAINS)]
    inv = [n.take(2, 2, P) for _ in range(RW_CHAINS)]
    xl = [n.take(2, P) for _ in range(RW_CHAINS)]
    zT_lo = h[:, LT:NT, :].rearrange("p t (f c) -> p (t f) c", f=2)
    yz = [junk[:, z * SEQ:(z + 1) * SEQ].rearrange("p (t d) -> p t d", d=P) for z in range(2)]
    yd = [ring_flat[:, RING * SLOT - (z + 1) * SEQ:RING * SLOT - z * SEQ].rearrange("p (t d) -> p t d", d=P) for z in range(2)]
    rw_s = sb("rw_s", 48)
    n = Carve(ARENA - 4 * SEQ - 2 * D - D)
    rw_gate, rw_ot = n.take(D), n.take(2, W)

    def zT(f):
        return zT_lo[:, f, :] if f < 4 else zT_hi[:, f - 4, :]

    mod_dram = nc.dram_tensor("mod_dram", [2, 2, 6 * D], F32).ap()
    spill = {q: nc.dram_tensor(f"spill_{q}", [LT if q in "rg" else NT, P, D], F32).ap()
             for q in ("r", "g", "k", "v", "w0", "w1", "a0", "a1")}
    rpb_strip = nc.dram_tensor("rpb_strip", [NA_HEADS, 3, 16, 15 * STRIP], F32).ap()

    norm_of = {"dil": (xn_dil, uT), "mlp": (xn_mlp, vT), "ple": (xn_ple, wT), "na": (xn_na, hT_na), "moe0": (xn_moe, hT_moe),
               "rw": (xn_rw, hT_rw), "moe1": (xn_moe, hT_moe)}
    norm_mod = {"na": (0, 0), "moe0": (0, 1), "rw": (1, 0), "moe1": (1, 1)}

    def modulation(use, s, k):
        l, n = norm_mod[use]
        return mod_a[:, l, s, n, k:k + 1], mod[:, l, s, 3 * n, k:k + 1]

    norm_scale = {"dil": "g_pre_mix", "mlp": "g_pre_mlp", "ple": "g_pre_ple"}
    USES = list(NORMS)
    tiles_before = {u: sum(NORMS[x] for x in USES[:i]) for i, u in enumerate(USES)}
    POSTS = ["mix", "mlp", "ple"]
    post_of = {"mix": (F_mix, gb_mix), "mlp": (F_mlp, gb_mlp), "ple": (F_ple, gb_ple)}
    last_job = {"mix": ("mix_o", 1, LT - 1), "mlp": ("down", 1, LT - 1), "ple": ("ple_in", 1, LT - 1)}

    def h_ready(eng, use):
        i = USES.index(use)
        if i == 0:
            eng.wait_ge(sem("x_landed"), 16)
        elif i <= len(POSTS):
            eng.wait_ge(sem("post_added"), i * LT)
            if use == "na":
                eng.wait_ge(sem("ctx_landed"), 16)
        elif use == "moe0":
            eng.wait_ge(sem("na_added"), 2 * NT)
        elif use == "rw":
            eng.wait_ge(sem("moe_added"), NT)
        else:
            eng.wait_ge(sem("rw_added"), 2 * LT)

    strip0 = [int(np.clip(16 * j - 8, 0, GRID - STRIP)) for j in range(BLOCKS)]

    def spilled_jobs():
        for q in "rkv":
            for n in range(2):
                for t in range(LT if q == "r" else NT):
                    yield q, n, t, ("rw_proj", q, n, t)
        for q in "wag":
            for z in range(1 if q == "g" else 2):
                for n in range(2):
                    for t in range(LT if q == "g" else NT):
                        yield (q if q == "g" else f"{q}{z}"), n, t, ("rw_high", q, z, n, t)

    def chains():
        for i in range(RW_PAIRS * RW_GROUPS * RW_CHAINS):
            yield (i, i // (RW_GROUPS * RW_CHAINS), i // RW_CHAINS % RW_GROUPS, i % RW_CHAINS)

    def last_unit(p, g, c):
        i = p * RW_GROUPS + g - 1
        return (i // RW_GROUPS, i % RW_GROUPS, c) if i >= 0 else None

    def halves(x, lv, z, transposed=False):
        b = 1 << lv
        v = x.rearrange("p h (a two b) -> p h a two b", two=2, b=b)
        return v[:, :, :, (z + transposed) % 2, :]

    block = ctx.enter_context(nc.Block())
    first_rw_o = [name for name, _, _ in loads].index("rw_o")

    @block.sync
    def _(sp):
        sp.dma_start(h[:, 0:LT, :], a["x"].rearrange("(t p) d -> p t d", p=P)).then_inc(sem("x_landed"), 16)
        goes_on = 0
        for i, (_, pieces, _) in enumerate(loads):
            if i >= RING:
                last = loads[i - RING][2]
                if last:
                    full(sp, *last)
                else:
                    goes_on += 1
                    sp.wait_ge(used, goes_on)
            if i == first_rw_o:
                taken(sp, "rw_ot", RW_PAIRS - 1)
            for src, at, k, n, *row in pieces:
                if row:
                    dst = ring[row[0]:row[0] + 1, i % RING, at:at + n]
                else:
                    dst = ring[:, i % RING, at:at + k * n].rearrange("p (k n) -> p k n", n=n)
                sp.dma_start(dst, src).then_inc(landed[i % RING], 16)
        for t in range(LT):
            sp.wait_ge(sem("moe_added"), NT + t + 1)
            sp.dma_start(out[t * P:(t + 1) * P, :], h[:, t, :]).then_inc(sem("out_stored"), 16)
        sp.wait_ge(sem("out_stored"), 16 * LT)

    slot_count, landed_at = [0] * RING, []
    for i, (_, pieces, _) in enumerate(loads):
        slot_count[i % RING] += 16 * len(pieces)
        landed_at.append(slot_count[i % RING])

    @block.gpsimd
    def _(pool):
        def load(dst, name, signal):
            pool.dma_start(dst, a[name]).then_inc(sem(signal), 16)

        nc.gpsimd.memset(ones[:, :], 1.0).then_inc(sem("ones_set"), 1)
        load(ident[:, :], "ident", "const_landed")
        load(cols[:, :], "cols", "const_landed")
        load(pos_i, "pos_row", "const_landed")
        load(pos_ci, "pos_col", "const_landed")
        load(ret_freq, "ret_freq", "const_landed")
        load(dil_freq, "dil_freq", "const_landed")
        load(dil_mask.rearrange("p a b -> p (a b)"), "dil_mask", "mask_landed")
        taken(pool, "dil_ot", DIL_STRIDE - 1)
        load(decay.rearrange("p a b -> p (a b)"), "ret_decay", "decay_landed")
        for u in POSTS:
            if u == "mix":
                taken(pool, "ret_turn", RET_HEADS - 1, 3)
            else:
                pool.wait_ge(sem("post_added"), POSTS.index(u) * LT)
            pool.dma_start(post_of[u][1], a[f"g_post_{u}"].partition_broadcast(P)).then_inc(sem("post_gain_landed"), 16)
            if u == "ple":
                pool.dma_start(pR, a["p"].rearrange("(t p) d -> p t d", p=P)).then_inc(sem("ple_landed"), 16)
                pool.dma_start(b_ple[0:1, :], a["b_ple_gate"].rearrange("(o d) -> o d", o=1)).then_inc(sem("ple_landed"), 16)
            if u == "mlp":
                pool.dma_start(h[:, LT:NT, :], a["ctx"].rearrange("(t p) d -> p t d", p=P)).then_inc(sem("ctx_landed"), 16)
        for n, j in enumerate((0, 1, 3)):
            off = int(np.clip(16 * j - 8, 0, GRID - STRIP)) - 16 * j
            for cc in range(16):
                lo = off - cc + 15 + RPB_PAD
                pool.dma_start(rpb_strip[:, n, cc, :].rearrange("h (r k) -> h r k", k=STRIP),
                               a["na_rpb"][:, :, lo:lo + STRIP]).then_inc(sem("strip_stored"), 16)
        pool.wait_ge(sem("post_added"), 3 * LT)
        for l in range(2):
            pool.dma_start(ada_m[0:2, l, :], a["ada_b"][l].partition_broadcast(2)).then_inc(sem("ada_bias_landed"), 16)
        for l in range(2):
            taken(pool, "ada", l, 6 * D // W - 1)
            pool.dma_start(mod_dram[l], ada_m[0:2, l, :]).then_inc(sem("mod_stored"), 16)
            pool.wait_ge(sem("mod_stored"), 16 * (l + 1))
            pool.dma_start(mod_rows[0:96, l, :], mod_dram[l].rearrange("s (r c) -> (s r) c", c=P)).then_inc(sem("mod_rows_landed"), 16)
        taken(pool, "ada_turn", 1)
        for n in range(2):
            for t in range(LT):
                taken(pool, "na_v", n, t)
                for j in range(BLOCKS):
                    for r in range(2):
                        to = (2 * t + r) % 4 * STRIP
                        pool.dma_start(na_vs[to:to + STRIP, 2 * j + t // 2, n * W:(n + 1) * W],
                                       na_v[r * GRID + strip0[j]:r * GRID + strip0[j] + STRIP, t, :]).then_inc(sem("na_strips_landed"), 16)
        pool.dma_start(na_mask.rearrange("p a b -> p (a b)"), a["na_mask"]).then_inc(sem("na_mask_landed"), 16)
        for b in range(2):
            nc.gpsimd.memset(na_bias[b][:, 3, :], 0.0).then_inc(sem("na_zeroed"), 1)
        pool.wait_ge(sem("strip_stored"), 16 * 48)
        pool.wait_ge(sem("na_mask_landed"), 16)
        for hd in range(NA_HEADS):
            if hd >= 2:
                taken(pool, "na_score", (hd - 1) * NT - 1)
            for r in range(ROWS):
                pool.dma_start(na_bias[hd % 2][16 * r:16 * r + 16, 0:3, :],
                               rpb_strip[hd, :, :, (7 - r) * STRIP:(15 - r) * STRIP].rearrange("n c k -> c n k")
                               ).then_inc(sem(f"na_bias_landed_{hd % 2}"), 16)
        taken(pool, "na_out", NA_UNITS - 1)
        for s in range(2):
            pool.dma_start(na_gate[:, s, :], mod_dram[0, s, 2 * D:3 * D].partition_broadcast(P)).then_inc(sem("na_gate_landed"), 16)

        def experts(l):
            h_ready(pool, f"moe{l}")
            pool.dma_start(router, a["moe_router"][l].rearrange("(k p) e -> p k e", p=P)).then_inc(sem("moe_landed"), 16)
            pool.dma_start(slot_no, a["slot_no"]).then_inc(sem("moe_landed"), 16)
            for s in range(2):
                pool.dma_start(moe_gate[:, s, :], mod_dram[l, s, 5 * D:6 * D].partition_broadcast(P)).then_inc(sem("moe_landed"), 16)

        experts(0)
        uses = [0] * 4
        for i, (q, n, t, key) in enumerate(spilled_jobs()):
            taken(pool, *key)
            pool.dma_start(spill[q][t, :, n * W:(n + 1) * W], staging[:, i % 4, :]).then_inc(sem(f"spilled_{i % 4}"), 16)
            uses[i % 4] += 16
        for i in range(4):
            pool.wait_ge(sem(f"spilled_{i}"), uses[i])
        taken(pool, "rw_low", "g")
        for dst, name in ((c_sum, "rw_sum"), (c_sum_ex, "rw_sum_ex"), (c_ind, "rw_ind"), (c_mask, "rw_mask"), (c_join, "rw_join"),
                          (c_pairs, "rw_pairs"), (c_blocks, "rw_blocks")):
            pool.dma_start(dst if len(dst.shape) == 2 else dst.rearrange("p a b -> p (a b)") if len(dst.shape) == 3 else
                           dst.rearrange("p a b c -> p (a b c)"), a[name]).then_inc(sem("rw_const_landed"), 16)

        def load_pair(p):
            for q in RW_IN:
                pool.dma_start(RW_IN[q][p % 2], spill[q][:, :, p * P:(p + 1) * P].rearrange("t p d -> p t d")
                               ).then_inc(sem(f"rw_in_landed_{p % 2}"), 16)
            pool.dma_start(rw_rows[:, p % 2], a["rw_rows"][:, p * P:(p + 1) * P].partition_broadcast(P)
                           ).then_inc(sem(f"rw_in_landed_{p % 2}"), 16)

        load_pair(0)
        load_pair(1)
        pool.wait_ge(sem("rw_const_landed"), 16 * 7)
        for i, p, g, c in chains():
            z = c % 2
            pool.wait_ge(sem("rw_at"), i + 1)
            if last_unit(p, g, c):
                full(pool, "rw_tgv", *last_unit(p, g, c))
            M = inv[c][:, :, 1, :]
            nc.gpsimd.tensor_tensor(M, aT[c], c_pairs[:, z, 1:2, :].to_broadcast([P, 2, P]), ALU.mult).then_inc(sem("rw_pool_step"), 1)
            pool.wait_ge(sem("rw_pool_step"), i + 1)
            nc.gpsimd.tensor_tensor(M, M, ident[:, :].unsqueeze(1).to_broadcast([P, 2, P]), ALU.add).then_inc(sem("rw_off"), 1)
            if (g, c) == (0, RW_CHAINS - 1) and 1 <= p < RW_PAIRS - 1:
                taken(pool, "rw_ot", p - 1)
                load_pair(p + 1)
        taken(pool, "rw_ot", RW_PAIRS - 1)
        pool.dma_start(rw_gate, mod_dram[1, 0, 2 * D:3 * D].partition_broadcast(P)).then_inc(sem("rw_gate_landed"), 16)
        experts(1)

    @block.scalar
    def _(act):
        A = nc.scalar.activation
        act_step = [0]

        def link(ins):
            act_step[0] += 1
            ins.then_inc(sem("act_step"), 1)
            act.wait_ge(sem("act_step"), act_step[0])

        def norm(use):
            xn, dst = norm_of[use]
            t0, nt = tiles_before[use], NORMS[use]
            h_ready(act, use)
            for t in range(nt):
                A(xn[:, t, :], h[:, t, :], ACT.Square, accum_out=stats[:, t:t + 1]).then_inc(sem("norm_squared"), 1)
            act.wait_ge(sem("norm_var"), USES.index(use) + 1)
            A(stats[:, 16:16 + nt], stats[:, 8:8 + nt], ACT.Sqrt).then_inc(sem("norm_std"), 1)
            if use in norm_mod:
                act.wait_ge(sem("modulation"), 2)
                for s in range(1 if nt == LT else 2):
                    for k in range(KD):
                        scale, shift = modulation(use, s, k)
                        n0, n1 = (0, SEQ) if s == 0 else (SEQ, TOK)
                        ps = full(act, "turn", use, s, k)[:, 0:n1 - n0]
                        free(A(dst[:, k, n0:n1], ps, ACT.Identity, bias=shift, scale=scale), "turn", use, s, k)
                return
            for k in range(KD):
                ps = full(act, "turn", use, 0, k)
                free(A(dst[:, k, 0:SEQ], ps, ACT.Copy, scale=col(norm_scale[use], k)), "turn", use, 0, k)

        def post(use):
            F, _ = post_of[use]
            taken(act, *last_job[use])
            for t in range(LT):
                if t:
                    act.wait_ge(sem("post_squared"), POSTS.index(use) * LT + t)
                A(junk[:, :], F[:, t, :], ACT.Square, accum_out=stats[:, 24 + t:25 + t]).then_inc(sem("post_squared"), 1)
            act.wait_ge(sem("post_var"), POSTS.index(use) + 1)
            A(stats[:, 32:36], stats[:, 28:32], ACT.Sqrt).then_inc(sem("post_std"), 1)

        act.wait_ge(sem("angle_reduced"), 1)
        A(angs, ang, ACT.Sin)
        A(turns, ang, ACT.Sin, scale=0.5).then_inc(sem("angle_sin"), 1)
        norm("dil")

        for i in range(len(DIL_STEPS) + 1):
            if i < len(DIL_STEPS):
                g, kind = DIL_STEPS[i]
                for c in range(DIL_STRIDE):
                    ps = full(act, "dil_proj", i, c)
                    if kind == 2:
                        dst = vR[:, c, g * W:(g + 1) * W]
                    else:
                        dst = dil_tmp[:, c, :]
                        if i >= 1 and DIL_STEPS[i - 1][1] < 2:
                            full(act, "dil_turn", i - 1, c)
                    free(A(dst, ps, ACT.Copy), "dil_proj", i, c)
            if i >= 1 and DIL_STEPS[i - 1][1] < 2:
                g, kind = DIL_STEPS[i - 1]
                for c in range(DIL_STRIDE):
                    ps = full(act, "dil_turn", i - 1, c).rearrange("p (f l) -> p f l", f=4)
                    dst = (qT, kT)[kind][:, 4 * g:4 * g + 4, c * P:(c + 1) * P]
                    free(A(dst, ps, ACT.Copy), "dil_turn", i - 1, c)
        for i in range(DIL_TILES + 1):
            if i < DIL_TILES:
                act.wait_ge(sem("dil_max"), i + 1)
                A(dil_s[:, i % 2, :], dil_s[:, i % 2, :], ACT.Exp, bias=stats[:, 40 + i % 2:41 + i % 2],
                  accum_out=stats[:, 42 + i % 2:43 + i % 2]).then_inc(sem("dil_exp"), 1)
            if i >= 1:
                ps = full(act, "dil_pt", i - 1)[:, 0:6 * P]
                if i >= 3:
                    full(act, "dil_out", i - 3)
                free(A(dil_p[:, (i - 1) % 2, :], ps, ACT.Copy), "dil_pt", i - 1)
        for c in range(DIL_STRIDE):
            ps = full(act, "dil_ot", c).rearrange("p (f l) -> p f l", f=4)
            free(A(yaT[:, :, c::DIL_STRIDE], ps, ACT.Copy), "dil_ot", c)

        def ret_turn(hd):
            for f in range(4):
                ps = full(act, "ret_turn", hd, f)
                free(A(yrT[:, 4 * hd + f, :], ps, ACT.Copy), "ret_turn", hd, f)

        for hd in range(RET_HEADS):
            for t in range(LT):
                free(A(rv[:, t, :], full(act, "ret_v", hd, t), ACT.Copy), "ret_v", hd, t)
            if hd >= 1:
                taken(act, "ret_out", hd - 1, LT - 1)
            for t in range(LT):
                free(A(rg[:, t, :], full(act, "ret_g", hd, t), ACT.Silu), "ret_g", hd, t)
            if hd >= 1:
                ret_turn(hd - 1)
            for t in range(LT):
                ps = full(act, "ret_out", hd, t)
                if hd + t:
                    act.wait_ge(sem("ret_squared"), hd * LT + t)
                A(junk[:, 0:W], ps, ACT.Square, accum_out=stats[:, 44 + t:45 + t]).then_inc(sem("ret_squared"), 1)
            act.wait_ge(sem("ret_var"), hd + 1)
            A(stats[:, 52:56], stats[:, 48:52], ACT.Sqrt).then_inc(sem("ret_std"), 1)
        ret_turn(RET_HEADS - 1)

        for n in range(2):
            for b, (dst, bias) in enumerate(((gate_r, "b_gate_r"), (gate_a, "b_gate_a"))):
                for f in range(4):
                    ps = full(act, "mix_gate", b, n, f)
                    free(A(dst[:, 4 * n + f, :], ps, ACT.Sigmoid, bias=col(bias, 4 * n + f)), "mix_gate", b, n, f)
        for n in range(2):
            for t in range(LT):
                free(A(F_mix[:, t, n * W:(n + 1) * W], full(act, "mix_o", n, t), ACT.Copy), "mix_o", n, t)
        post("mix")

        norm("mlp")
        for f in range(D_FF // P):
            ps = full(act, "up", f)
            ins = A(ffT[:, f, :], ps, ACT.Relu)
            free(ins, "up", f)
            taken(act, "up", f)
            A(ffT[:, f, :], ffT[:, f, :], ACT.Square).then_inc(sem("ff_squared"), 1)
        for n in range(2):
            for t in range(LT):
                free(A(F_mlp[:, t, n * W:(n + 1) * W], full(act, "down", n, t), ACT.Copy), "down", n, t)
        post("mlp")

        norm("ple")
        for d in range(PLE // P):
            free(A(pT[:, d, :], full(act, "ple_turn", d), ACT.Copy), "ple_turn", d)
        for n in range(2):
            for t in range(LT):
                free(A(gate_p[:, t, n * W:(n + 1) * W], full(act, "ple_gate", n, t), ACT.Sigmoid), "ple_gate", n, t)
        post("ple")

        A(cond[:, :, :], cols[:, COLUMNS["cond"][0]:COLUMNS["cond"][0] + 2 * KD].rearrange("p (s k) -> p s k", s=2),
          ACT.Silu).then_inc(sem("cond_ready"), 1)
        for l in range(2):
            ps = full(act, "ada_turn", l)[:, 0:96]
            free(A(mod[:, l].rearrange("p s j k -> p (s j k)"), ps, ACT.Copy), "ada_turn", l)

        norm("na")
        for i in range(NA_STEPS + 2):
            if i < NA_STEPS:
                if i >= 2:
                    full(act, "na_turn", i - 2)
                ps = full(act, "na_proj", i)
                A(na_p[:, i % 2, :], ps, ACT.Square).then_inc(sem("na_squared"), 1)
                free(A(na_s[:, i % 2, :], ps, ACT.Copy), "na_proj", i)
                act.wait_ge(sem("na_var"), i + 1)
                A(stats[:, 16 + 8 * (i % 2):24 + 8 * (i % 2)], stats[:, 8 * (i % 2):8 * (i % 2) + 8], ACT.Sqrt).then_inc(sem("na_std"), 1)
            if i >= 2:
                j = i - 2
                half, t = divmod(j, NT)
                ps = full(act, "na_turn", j).rearrange("p (f t) -> p f t", f=4)
                dst, g = (naq, "na_q_g") if half < 2 else (nak, "na_k_g")
                f0 = 4 * (half % 2)
                if half < 2 and t < LT:
                    for r in range(2):
                        to = dst[:, f0:f0 + 4, 0:SEQ].rearrange("p f (j r c) -> p f j r c", j=BLOCKS, r=ROWS)[:, :, :, 2 * t + r, :]
                        ins = A(to, ps.rearrange("p f (r j c) -> p f r j c", r=2, j=BLOCKS)[:, :, r], ACT.Copy, scale=col(g))
                else:
                    ins = A(dst[:, f0:f0 + 4, t * P:(t + 1) * P], ps, ACT.Copy, scale=col(g))
                free(ins, "na_turn", j)
        for n in range(2):
            if n == 1:
                act.wait_ge(sem("na_strips_landed"), 16 * 2 * BLOCKS * LT)
            for t in range(NT):
                ps = full(act, "na_v", n, t)
                dst = na_v[:, t, :] if t < LT else na_vc[:, t - LT, n * W:(n + 1) * W]
                free(A(dst, ps, ACT.Copy), "na_v", n, t)
        for i in range(NA_UNITS + 1):
            if i < NA_UNITS:
                nk = W if i % NT < BLOCKS else CTX
                act.wait_ge(sem("na_max"), i + 1)
                A(na_s[:, i % 2, 0:nk], na_s[:, i % 2, 0:nk], ACT.Exp, bias=stats[:, 40 + i % 2:41 + i % 2],
                  accum_out=stats[:, 42 + i % 2:43 + i % 2]).then_inc(sem("na_exp"), 1)
            if i >= 1:
                nk = W if (i - 1) % NT < BLOCKS else CTX
                ps = full(act, "na_pt", i - 1)[:, 0:nk]
                if i >= 3:
                    full(act, "na_out", i - 3)
                free(A(na_p[:, (i - 1) % 2, 0:nk], ps, ACT.Copy), "na_pt", i - 1)
        for t in range(NT):
            ps = full(act, "na_ot", t)
            if t < BLOCKS:
                for f in range(KD):
                    dst = na_oT[:, f, 0:SEQ].rearrange("p (r c) -> p r c", c=GRID)[:, :, 16 * t:16 * t + 16]
                    ins = A(dst, ps[:, f * P:(f + 1) * P].rearrange("p (r c) -> p r c", c=16), ACT.Copy)
            else:
                ins = A(na_oT[:, :, t * P:(t + 1) * P], ps.rearrange("p (f c) -> p f c", f=KD), ACT.Copy)
            free(ins, "na_ot", t)

        def experts(l):
            use = f"moe{l}"
            norm(use)
            act.wait_ge(sem("moe_logit_less_max"), l + 1)
            A(logit, logit, ACT.Exp).then_inc(sem("moe_exp"), 1)

            def gather(e):
                b = e % 2
                for half in range(2):
                    ps = full(act, "moe_gather", l, e, half).rearrange("p (k s) -> p k s", k=4)
                    if half == 0 and e >= 2:
                        full(act, "moe_h3", l, e - 2, 1)
                    for k in range(4):
                        for s in range(1 if l else 2):
                            lo, hi = (0, CAP_L) if s == 0 else (CAP_L, SLOTS)
                            scale, shift = modulation(use, s, 4 * half + k)
                            ins = A(xinT[:, b, 4 * half + k, lo:hi], ps[:, k, lo:hi], ACT.Identity, bias=shift, scale=scale)
                    free(ins, "moe_gather", l, e, half)
                ps = full(act, "moe_selt", l, e)[:, 0:TILES[l] * P]
                if e >= 2:
                    full(act, "moe_add", l, e - 2, TILES[l] - 1, 1)
                n = SLOTS if l == 0 else CAP_L
                free(A(selT[0:n, b, 0:TILES[l] * P], ps[0:n, :], ACT.Copy), "moe_selt", l, e)

            gather(0)
            m = SLOTS if l == 0 else CAP_L
            for e in range(EXPERTS):
                for n in range(2):
                    ps = full(act, "moe_h1", l, e, n)
                    if e >= 1:
                        taken(act, "moe_h3", l, e - 1, n)
                    free(A(s1[0:m, n * W:(n + 1) * W], ps[0:m, :], ACT.Silu), "moe_h1", l, e, n)
                if e + 1 < EXPERTS:
                    gather(e + 1)
                ps = full(act, "moe_ht", l, e).rearrange("p (k s) -> p k s", k=KD)
                free(A(hidT[:, :, 0:m], ps[:, :, 0:m], ACT.Copy), "moe_ht", l, e)
                for n in range(2):
                    ps = full(act, "moe_y", l, e, n)
                    if e >= 2:
                        full(act, "moe_add", l, e - 2, TILES[l] - 1, 1)
                    free(A(y_moe[0:m, e % 2, n * W:(n + 1) * W], ps[0:m, :], ACT.Copy), "moe_y", l, e, n)

        experts(0)

        norm("rw")
        count = [0]

        def stage(ins_of, key):
            i = count[0]
            if i >= 4:
                act.wait_ge(sem(f"spilled_{i % 4}"), 16 * (i // 4))
            free(ins_of(staging[:, i % 4, :]), *key)
            count[0] += 1

        for q in "rkv":
            for n in range(2):
                for t in range(LT if q == "r" else NT):
                    ps = full(act, "rw_proj", q, n, t)
                    stage(lambda dst: A(dst, ps, ACT.Copy), ("rw_proj", q, n, t))
        for q in "wag":
            ps = full(act, "rw_low", q)[:, 0:TOK]
            free(A(lowT, ps, {"w": ACT.Tanh, "a": ACT.Copy, "g": ACT.Sigmoid}[q]), "rw_low", q)
            for z in range(1 if q == "g" else 2):
                for n in range(2):
                    for t in range(LT if q == "g" else NT):
                        ps = full(act, "rw_high", q, z, n, t)
                        stage(lambda dst: A(dst, ps, ACT.Copy if q == "g" else ACT.Sigmoid), ("rw_high", q, z, n, t))

        def flat(x):
            return x.rearrange("p a b -> p (a b)")

        def sums(p, z):
            ps = full(act, "rw_sum", p, z)[:, 0:TOK]
            if z == 0 and p >= 1:
                taken(act, "rw_tgv", p - 1, RW_GROUPS - 1, RW_CHAINS - 1)
                full(act, "rw_tgv", p - 1, RW_GROUPS - 1, RW_CHAINS - 1)
            if z == 1:
                act.wait_ge(sem("rw_scaled"), 2 * p + 1)
            A(flat(e_neg), ps, ACT.Exp, scale=-1.0)
            free(A(flat(e_pos), ps, ACT.Exp), "rw_sum", p, z)
            ps = full(act, "rw_sum_ex", p, z)[:, 0:TOK]
            free(A(flat(e_ex), ps, ACT.Exp, scale=-1.0), "rw_sum_ex", p, z)
            ps = full(act, "rw_end", p, z)[:, 0:RW_STEPS]
            free(A(w_end[p % 2][z], ps, ACT.Exp, scale=-1.0), "rw_end", p, z)

        def turn_factors(p, z):
            for x, dst in enumerate((KT[z], BT[z], TT[z], RT[p % 2][z])):
                ps = full(act, "rw_turn", p, z, x)[:, 0:SEQ if x == 3 else TOK]
                free(A(dst, ps, ACT.Copy), "rw_turn", p, z, x)

        def scan(p, i):
            for z in range(2):
                t, c = rw_chunk(i, z)
                if p >= 0 and t < LT:
                    if p >= 1:
                        act.wait_ge(sem("rw_read_out"), p)
                    ps = full(act, "rw_y", p, i, z)[:, 0:P]
                    rows = slice(c * CH, (c + 1) * CH)
                    free(A(yz[z][rows, t, :], ps[rows, :], ACT.Copy), "rw_y", p, i, z)

        def read_out(p):
            act.wait_ge(sem("rw_y_var"), p + 1)
            A(rw_s[:, 32:40], rw_s[:, 24:32], ACT.Sqrt).then_inc(sem("rw_y_std"), 1)

        for p in range(RW_PAIRS):
            act.wait_ge(sem("rw_kk_squared"), p + 1)
            A(rw_s[:, 12:24], rw_s[:, 0:12], ACT.Sqrt).then_inc(sem("rw_kk_norm"), 1)
            sums(p, 0)
            scan(p - 1, RW_STEPS - 4)
            turn_factors(p, 0)
            sums(p, 1)
            scan(p - 1, RW_STEPS - 3)
            scan(p - 1, RW_STEPS - 2)
            turn_factors(p, 1)
            scan(p - 1, RW_STEPS - 1)
            for g in range(RW_GROUPS):
                for c in range(RW_CHAINS):
                    ps = full(act, "rw_gv", p, g, c)[:, 0:P]
                    free(A(gv[c], ps, ACT.Copy), "rw_gv", p, g, c)
                for lv in range(1, RW_LEVELS):
                    if rw_step_beside(g, lv) is not None:
                        scan(p, rw_step_beside(g, lv))
                    if g == 0 and p >= 1 and lv == RW_READ_STD:
                        read_out(p - 1)
                for c in range(RW_CHAINS):
                    t, z = rw_tile(g, c)
                    ps = full(act, "rw_tk", p, g, c)[:, 0:P]
                    free(A(tkT[z][:, t, :], ps, ACT.Copy), "rw_tk", p, g, c)
                for c in range(RW_CHAINS):
                    t, z = rw_tile(g, c)
                    ps = full(act, "rw_tgv", p, g, c)[:, 0:P]
                    free(A(tgv[z][:, t, :], ps, ACT.Copy), "rw_tgv", p, g, c)
                if g == 0 and p >= 1:
                    free(A(zT(p - 1), full(act, "rw_ot", p - 1), ACT.Copy), "rw_ot", p - 1)
        for i in range(RW_STEPS - 4, RW_STEPS):
            scan(RW_PAIRS - 1, i)
        read_out(RW_PAIRS - 1)
        free(A(zT(RW_PAIRS - 1), full(act, "rw_ot", RW_PAIRS - 1), ACT.Copy), "rw_ot", RW_PAIRS - 1)
        experts(1)

    @block.vector
    def _(dve):
        V = nc.vector
        dve_step = [0]

        def link(ins):
            dve_step[0] += 1
            ins.then_inc(sem("dve_step"), 1)
            dve.wait_ge(sem("dve_step"), dve_step[0])

        def norm(use):
            xn, _ = norm_of[use]
            t0, nt = tiles_before[use], NORMS[use]
            dve.wait_ge(sem("norm_squared"), t0 + nt)
            V.tensor_scalar(stats[:, 8:8 + nt], stats[:, 0:nt], 1.0 / D, EPS, ALU.mult, ALU.add).then_inc(sem("norm_var"), 1)
            dve.wait_ge(sem("norm_std"), USES.index(use) + 1)
            link(V.reciprocal(stats[:, 0:nt], stats[:, 16:16 + nt]))
            for t in range(nt):
                V.tensor_scalar(xn[:, t, :], h[:, t, :], stats[:, t:t + 1], None, ALU.mult).then_inc(sem("normed"), 1)

        def post(use):
            F, gb = post_of[use]
            i = POSTS.index(use)
            dve.wait_ge(sem("post_squared"), (i + 1) * LT)
            V.tensor_scalar(stats[:, 28:32], stats[:, 24:28], 1.0 / D, EPS, ALU.mult, ALU.add).then_inc(sem("post_var"), 1)
            dve.wait_ge(sem("post_std"), i + 1)
            link(V.reciprocal(stats[:, 36:40], stats[:, 32:36]))
            dve.wait_ge(sem("post_gain_landed"), 16 * (i + 1))
            for t in range(LT):
                link(V.scalar_tensor_tensor(F[:, t, :], F[:, t, :], stats[:, 36 + t:37 + t], gb, ALU.mult, ALU.mult))
                V.tensor_tensor(h[:, t, :], h[:, t, :], F[:, t, :], ALU.add).then_inc(sem("post_added"), 1)

        dve.wait_ge(sem("const_landed"), 16 * 6)
        V.tensor_copy(pos_f, pos_i)
        link(V.tensor_copy(pos_cf, pos_ci))
        V.tensor_scalar(ang[:, 0:SEQ], pos_f, ret_freq, None, ALU.mult)
        for c in range(DIL_STRIDE):
            ins = V.tensor_scalar(ang[:, SEQ + 8 * c:SEQ + 8 * c + 8], dil_freq, pos_cf[:, c:c + 1], None, ALU.mult)
        link(ins)
        ROUND = 1.5 * 2.0 ** 23
        link(V.tensor_scalar(turns, ang, float(np.float32(1 / (2 * np.pi))), ROUND, ALU.mult, ALU.add))
        link(V.tensor_scalar(turns, turns, ROUND, None, ALU.subtract))
        part1 = 6.28125
        part2 = float(np.float32(np.float64(2 * np.pi) - part1).astype(np.float16))
        part3 = float(np.float32(2 * np.pi - part1 - part2))
        for x in (part1, part2, part3):
            link(V.scalar_tensor_tensor(ang, turns, -x, ang, ALU.mult, ALU.add))
        lim = float(np.nextafter(np.float32(np.pi), np.float32(0)))
        V.tensor_scalar(ang, ang, lim, -lim, ALU.min, ALU.max).then_inc(sem("angle_reduced"), 1)
        dve.wait_ge(sem("angle_sin"), 1)
        link(V.tensor_tensor(turns, turns, turns, ALU.mult))
        V.tensor_copy(ret_sin, angs[:, 0:SEQ])
        V.tensor_copy(dil_sin.rearrange("p a b -> p (a b)"), angs[:, SEQ:544])
        V.tensor_scalar(ret_cos, turns[:, 0:SEQ], -2.0, 1.0, ALU.mult, ALU.add)
        link(V.tensor_scalar(dil_cos.rearrange("p a b -> p (a b)"), turns[:, SEQ:544], -2.0, 1.0, ALU.mult, ALU.add))
        norm("dil")

        n_rot = 0
        for i, (g, kind) in enumerate(DIL_STEPS):
            if kind == 2:
                continue
            for c in range(DIL_STRIDE):
                taken(dve, "dil_proj", i, c)
                x = dil_tmp[:, c, :].rearrange("p (h d) -> p h d", d=HD)
                x1, x2 = x[:, :, 0:ROPE8], x[:, :, ROPE8:2 * ROPE8]
                cos = dil_cos[:, c, :].unsqueeze(1).to_broadcast([P, DIL_SLOTS, ROPE8])
                sin = dil_sin[:, c, :].unsqueeze(1).to_broadcast([P, DIL_SLOTS, ROPE8])
                if n_rot >= 2:
                    dve.wait_ge(sem("dil_rotated"), n_rot - 1)
                r = [dil_rot[:, q, n_rot % 2] for q in range(4)]
                V.tensor_tensor(r[0], x1, cos, ALU.mult)
                V.tensor_tensor(r[1], x2, sin, ALU.mult)
                V.tensor_tensor(r[2], x2, cos, ALU.mult)
                link(V.tensor_tensor(r[3], x1, sin, ALU.mult))
                V.tensor_tensor(x1, r[0], r[1], ALU.subtract)
                V.tensor_tensor(x2, r[2], r[3], ALU.add).then_inc(sem("dil_rotated"), 1)
                n_rot += 1
        dve.wait_ge(sem("mask_landed"), 16)
        for i in range(DIL_TILES + 2):
            if i < DIL_TILES:
                s, c = divmod(i, DIL_STRIDE)
                ps = full(dve, "dil_score", i)[:, 0:6 * P]
                if i >= 2:
                    full(dve, "dil_pt", i - 2)
                    dve.wait_ge(sem("dil_exp"), i - 1)
                x = V.tensor_tensor_reduce(out=dil_s[:, i % 2, :], in0=ps, in1=dil_mask[:, c, :], scale=HD ** -0.5,
                                           scalar=-3e38, op0=ALU.add, op1=ALU.max, accum_out=stats[:, 56 + i % 2:57 + i % 2])
                free(x, "dil_score", i)
                taken(dve, "dil_score", i)
                V.tensor_scalar(stats[:, 40 + i % 2:41 + i % 2], stats[:, 56 + i % 2:57 + i % 2], -1.0, None,
                                ALU.mult).then_inc(sem("dil_max"), 1)
            if 1 <= i <= DIL_TILES:
                j = i - 1
                dve.wait_ge(sem("dil_exp"), j + 1)
                if j >= 2:
                    taken(dve, "dil_out", j - 2)
                link(V.reciprocal(stats[:, 58 + j % 2:59 + j % 2], stats[:, 42 + j % 2:43 + j % 2]))
            if i >= 2:
                j = i - 2
                s, c = divmod(j, DIL_STRIDE)
                ps = full(dve, "dil_out", j)[:, 0:HD]
                free(V.tensor_scalar(dil_o[:, c, s * HD:(s + 1) * HD], ps, stats[:, 58 + j % 2:59 + j % 2], None, ALU.mult),
                     "dil_out", j)

        dve.wait_ge(sem("decay_landed"), 16)
        for hd in range(RET_HEADS):
            for b, dst in enumerate((rqT, rkT)):
                if hd + b:
                    dve.wait_ge(sem("ret_rotated"), 2 * hd + b)
                p0 = full(dve, "ret_qk", hd, 2 * b)
                V.tensor_tensor(dst[:, 0, :], p0, ret_cos, ALU.mult)
                free(V.tensor_tensor(rot_b, p0, ret_sin, ALU.mult), "ret_qk", hd, 2 * b)
                p1 = full(dve, "ret_qk", hd, 2 * b + 1)
                V.tensor_tensor(rot_a, p1, ret_sin, ALU.mult)
                x = V.tensor_tensor(dst[:, 1, :], p1, ret_cos, ALU.mult)
                free(x, "ret_qk", hd, 2 * b + 1)
                taken(dve, "ret_qk", hd, 2 * b + 1)
                V.tensor_tensor(dst[:, 0, :], dst[:, 0, :], rot_a, ALU.subtract)
                V.tensor_tensor(dst[:, 1, :], dst[:, 1, :], rot_b, ALU.add).then_inc(sem("ret_rotated"), 1)
            for j in range(LT):
                n = SEQ - j * P
                ps = full(dve, "ret_score", hd, j)[:, 0:n]
                free(V.tensor_tensor(rs[:, j, 0:n], ps, decay[:, hd, 0:n], ALU.mult), "ret_score", hd, j)
            dve.wait_ge(sem("ret_squared"), (hd + 1) * LT)
            V.tensor_scalar(stats[:, 48:52], stats[:, 44:48], 1.0 / RET_V, EPS, ALU.mult, ALU.add).then_inc(sem("ret_var"), 1)
            dve.wait_ge(sem("ret_std"), hd + 1)
            link(V.reciprocal(stats[:, 60:64], stats[:, 52:56]))
            for t in range(LT):
                taken(dve, "ret_g", hd, t)
                ps = full(dve, "ret_out", hd, t)
                free(V.scalar_tensor_tensor(ry[:, t, :], ps, stats[:, 60 + t:61 + t], rg[:, t, :], ALU.mult, ALU.mult),
                     "ret_out", hd, t)

        for n in range(2):
            for f in range(4):
                taken(dve, "mix_gate", 0, n, f)
                ps = full(dve, "mix_ret", n, f)
                free(V.tensor_tensor(mixT[:, 4 * n + f, :], ps, gate_r[:, 4 * n + f, :], ALU.mult), "mix_ret", n, f)
        for f in range(KD):
            taken(dve, "mix_gate", 1, f // 4, f % 4)
            if f:
                dve.wait_ge(sem("mixed"), f)
            ps = full(dve, "mix_dil", f)
            free(V.tensor_tensor(mix_t, ps, gate_a[:, f, :], ALU.mult), "mix_dil", f)
            taken(dve, "mix_dil", f)
            V.tensor_tensor(mixT[:, f, :], mixT[:, f, :], mix_t, ALU.add).then_inc(sem("mixed"), 1)
        post("mix")

        norm("mlp")
        post("mlp")

        norm("ple")
        for n in range(2):
            for t in range(LT):
                taken(dve, "ple_gate", n, t)
                ps = full(dve, "ple_in", n, t)
                sl = slice(n * W, (n + 1) * W)
                free(V.tensor_tensor(F_ple[:, t, sl], ps, gate_p[:, t, sl], ALU.mult), "ple_in", n, t)
        post("ple")

        dve.wait_ge(sem("ada_bias_landed"), 32)
        for l in range(2):
            for n in range(6 * D // W):
                ps = full(dve, "ada", l, n)
                m = ada_m[0:2, l, n * W:(n + 1) * W]
                free(V.tensor_tensor(m, ps[0:2, :], m, ALU.add), "ada", l, n)
        for l in range(2):
            taken(dve, "ada_turn", l)
            for s in range(2):
                for n in range(2):
                    at = COLUMNS["norm_g"][0] + (2 * l + n) * KD
                    ins = V.scalar_tensor_tensor(mod_a[:, l, s, n, :], mod[:, l, s, 3 * n + 1, :], 1.0, cols[:, at:at + KD], ALU.add, ALU.mult)
            ins.then_inc(sem("modulation"), 1)

        norm("na")
        for i in range(NA_STEPS):
            b = i % 2
            dve.wait_ge(sem("na_squared"), i + 1)
            if i >= 2:
                dve.wait_ge(sem("na_normed"), i - 1)
            link(V.tensor_reduce(rw_s[:, 8 * b:8 * b + 8], na_p[:, b, :].rearrange("p (h d) -> p h d", d=HD), AX, ALU.add))
            V.tensor_scalar(stats[:, 8 * b:8 * b + 8], rw_s[:, 8 * b:8 * b + 8], 1.0 / HD, EPS, ALU.mult, ALU.add).then_inc(sem("na_var"), 1)
            dve.wait_ge(sem("na_std"), i + 1)
            link(V.reciprocal(rw_s[:, 16 + 8 * b:24 + 8 * b], stats[:, 16 + 8 * b:24 + 8 * b]))
            taken(dve, "na_proj", i)
            x = na_s[:, b, :].rearrange("p (h d) -> p h d", d=HD)
            V.tensor_tensor(x, x, rw_s[:, 16 + 8 * b:24 + 8 * b].unsqueeze(2).to_broadcast([P, 8, HD]), ALU.mult).then_inc(sem("na_normed"), 1)
        dve.wait_ge(sem("na_zeroed"), 2)
        dve.wait_ge(sem("na_strips_landed"), 16 * 4 * BLOCKS * LT)
        dve.wait_ge(sem("na_mask_landed"), 16)
        for i in range(NA_UNITS + 2):
            if i < NA_UNITS:
                hd, un = divmod(i, NT)
                bias = na_bias[hd % 2]
                if un == 0:
                    dve.wait_ge(sem(f"na_bias_landed_{hd % 2}"), 16 * ROWS * (hd // 2 + 1))
                    link(V.scalar_tensor_tensor(bias[:, 0:3, :], bias[:, 0:3, :], HD ** 0.5, na_mask, ALU.mult, ALU.add))
                nk = W if un < BLOCKS else CTX
                ps = full(dve, "na_score", i)[:, 0:nk]
                if i >= 2:
                    full(dve, "na_pt", i - 2)
                    dve.wait_ge(sem("na_exp"), i - 1)
                s_ = na_s[:, i % 2, 0:nk]
                mx = stats[:, 56 + i % 2:57 + i % 2]
                if un < BLOCKS:
                    kind = (0, 1, 1, 2)[un]
                    ins = V.tensor_tensor_reduce(out=s_.rearrange("p (a b) -> p a b", a=2), in0=ps.rearrange("p (a b) -> p a b", a=2),
                                                 in1=bias[:, kind::3 - kind, :], scale=HD ** -0.5, scalar=-3e38, op0=ALU.add, op1=ALU.max,
                                                 accum_out=mx)
                else:
                    ins = V.tensor_tensor_reduce(out=s_, in0=ps, in1=bias[:, 3, :], scale=HD ** -0.5, scalar=-3e38, op0=ALU.add,
                                                 op1=ALU.max, accum_out=mx)
                free(ins, "na_score", i)
                taken(dve, "na_score", i)
                V.tensor_scalar(stats[:, 40 + i % 2:41 + i % 2], mx, -1.0, None, ALU.mult).then_inc(sem("na_max"), 1)
            if 1 <= i <= NA_UNITS:
                j = i - 1
                dve.wait_ge(sem("na_exp"), j + 1)
                if j >= 2:
                    taken(dve, "na_out", j - 2)
                link(V.reciprocal(stats[:, 58 + j % 2:59 + j % 2], stats[:, 42 + j % 2:43 + j % 2]))
            if i >= 2:
                j = i - 2
                hd, un = divmod(j, NT)
                ps = full(dve, "na_out", j)[:, 0:HD]
                free(V.tensor_scalar(na_o[:, un, hd * HD:(hd + 1) * HD], ps, stats[:, 58 + j % 2:59 + j % 2], None, ALU.mult), "na_out", j)
        dve.wait_ge(sem("na_gate_landed"), 32)
        for n in range(2):
            for t in range(NT):
                i = n * NT + t
                ps = full(dve, "na_o", n, t)
                sl = slice(n * W, (n + 1) * W)
                if i >= 2:
                    dve.wait_ge(sem("na_added"), i - 1)
                free(V.tensor_tensor(na_t[:, i % 2, :], ps, na_gate[:, int(t >= LT), sl], ALU.mult), "na_o", n, t)
                taken(dve, "na_o", n, t)
                V.tensor_tensor(h[:, t, sl], h[:, t, sl], na_t[:, i % 2, :], ALU.add).then_inc(sem("na_added"), 1)

        def experts(l):
            nt, tok = TILES[l], TILES[l] * P
            streams = [(0, SEQ, CAP_L)] + ([(SEQ, TOK, CAP_C)] if l == 0 else [])
            norm(f"moe{l}")
            ps = full(dve, "moe_logit", l)[:, 0:nt * EXPERTS].rearrange("p (t e) -> p t e", e=EXPERTS)
            link(V.tensor_reduce(stats[:, 24:24 + nt], ps, AX, ALU.max))
            free(V.tensor_tensor(logit[:, 0:nt], ps, stats[:, 24:24 + nt].unsqueeze(2).to_broadcast([P, nt, EXPERTS]), ALU.subtract), "moe_logit", l)
            if l == 1:
                V.memset(logit[:, nt:NT, :], 0.0)
            taken(dve, "moe_logit", l)
            V.memset(sel_g[:, :, :], 0.0).then_inc(sem("moe_logit_less_max"), 1)
            dve.wait_ge(sem("moe_exp"), l + 1)
            link(V.tensor_reduce(stats[:, 32:32 + nt], logit[:, 0:nt], AX, ALU.add))
            link(V.reciprocal(stats[:, 24:24 + nt], stats[:, 32:32 + nt]))
            V.tensor_tensor(aff[:, 0:nt], logit[:, 0:nt], stats[:, 24:24 + nt].unsqueeze(2).to_broadcast([P, nt, EXPERTS]),
                            ALU.mult).then_inc(sem("moe_affinity"), 1)
            E = slice(0, EXPERTS)
            ps = full(dve, "moe_afft", l)[E, 0:tok]
            free(V.tensor_copy(workT[E, 0:tok], ps), "moe_afft", l)
            taken(dve, "moe_afft", l)
            for lo, hi, cap in streams:
                for _ in range(cap // 8):
                    link(V.max(top8[E, :], workT[E, lo:hi]))
                    link(V.match_replace(affT[E, lo:hi], top8[E, :], workT[E, lo:hi], -1.0))
                    link(V.tensor_copy(workT[E, lo:hi], affT[E, lo:hi]))
            link(V.tensor_scalar(workT[E, 0:tok], workT[E, 0:tok], 0.0, None, ALU.is_lt))
            for lo, hi, cap in streams:
                ins = V.tensor_tensor_scan(sumT[E, lo:hi], ones[E, 0:1].to_broadcast([EXPERTS, hi - lo]), workT[E, lo:hi], 0.0,
                                           ALU.mult, ALU.add)
            link(ins)
            link(V.tensor_tensor(sumT[E, 0:tok], sumT[E, 0:tok], workT[E, 0:tok], ALU.mult))
            V.tensor_scalar(sumT[E, 0:tok], sumT[E, 0:tok], -1.0, None, ALU.add).then_inc(sem("moe_numbered"), 1)
            ps = full(dve, "moe_slot", l)[:, 0:nt * EXPERTS]
            free(V.tensor_copy(slot[:, 0:nt].rearrange("p t e -> p (t e)"), ps), "moe_slot", l)
            taken(dve, "moe_slot", l)
            dve.wait_ge(sem("moe_landed"), 64 * (l + 1))

            def select(e):
                if e >= 1:
                    full(dve, "moe_gather", l, e - 1, 1)
                    full(dve, "moe_selt", l, e - 1)
                for t in range(nt):
                    lat = t < LT
                    cap = CAP_L if lat else CAP_C
                    lo = 0 if lat else CAP_L
                    one = slot[:, t, e:e + 1]
                    dst = sel_l[:, t, :] if lat else sel_c[:, t - LT, :]
                    V.tensor_scalar(dst, slot_no[:, 0:cap], one, None, ALU.is_equal)
                    ins = V.tensor_scalar(sel_g[:, t, lo:lo + cap], slot_no[:, 0:cap], one, aff[:, t, e:e + 1], ALU.is_equal, ALU.mult)
                ins.then_inc(sem("moe_selected"), 1)

            def scatter(e):
                for t in range(nt):
                    for n in range(2):
                        ps = full(dve, "moe_add", l, e, t, n)
                        x = acc[:, t, n * W:(n + 1) * W]
                        if e == 0:
                            ins = V.tensor_copy(x, ps)
                        else:
                            taken(dve, "moe_add", l, e - 1, t, n)
                            ins = V.tensor_tensor(x, x, ps, ALU.add)
                        free(ins, "moe_add", l, e, t, n)

            m = SLOTS if l == 0 else CAP_L
            select(0)
            for e in range(EXPERTS):
                if e + 1 < EXPERTS:
                    select(e + 1)
                for n in range(2):
                    taken(dve, "moe_h1", l, e, n)
                    ps = full(dve, "moe_h3", l, e, n)
                    if e >= 1:
                        full(dve, "moe_ht", l, e - 1)
                    free(V.tensor_tensor(hid[0:m, n * W:(n + 1) * W], ps[0:m, :], s1[0:m, n * W:(n + 1) * W], ALU.mult), "moe_h3", l, e, n)
                if e >= 1:
                    scatter(e - 1)
            scatter(EXPERTS - 1)
            for t in range(nt):
                taken(dve, "moe_add", l, EXPERTS - 1, t, 1)
                link(V.tensor_tensor(acc[:, t, :], acc[:, t, :], moe_gate[:, int(t >= LT), :], ALU.mult))
                V.tensor_tensor(h[:, t, :], h[:, t, :], acc[:, t, :], ALU.add).then_inc(sem("moe_added"), 1)

        experts(0)

        norm("rw")
        taken(dve, "turn", "rw", 1, KD - 1)
        for lo, hi in ((0, SEQ), (SEQ, TOK)):
            V.tensor_tensor(xx[:, :, lo + 1:hi - 1], hT_rw[:, :, lo:hi - 2], hT_rw[:, :, lo + 2:hi], ALU.add)
            V.tensor_copy(xx[:, :, lo:lo + 1], hT_rw[:, :, lo + 1:lo + 2])
            ins = V.tensor_copy(xx[:, :, hi - 1:hi], hT_rw[:, :, hi - 2:hi - 1])
        link(ins)
        link(V.scalar_tensor_tensor(xx, xx, 0.5, hT_rw, ALU.mult, ALU.subtract))
        order = "rkvwag"
        for i, q in enumerate(order):
            if i >= 2:
                o = order[i - 2]
                full(dve, *(("rw_proj", o, 1, (LT if o == "r" else NT) - 1) if o in "rkv" else ("rw_low", o)))
            for k in range(KD):
                c = "rwkvag".index(q) * KD + k
                V.scalar_tensor_tensor(xs[i % 2][:, k, :], xx[:, k, :], col("rw_mix", c), hT_rw[:, k, :], ALU.mult, ALU.add
                                       ).then_inc(sem("rw_mixed"), 1)

        def over(row, nt):
            return row.unsqueeze(1).to_broadcast([P, nt, P])

        def heads(x):
            return x.rearrange("p t (h d) -> p (t h) d", d=HD)

        def by_head(x, n):
            return x.unsqueeze(2).to_broadcast([P, n, HD])

        def pair(p):
            return {q: v[p % 2] for q, v in RW_IN.items()}, [rw_rows[:, p % 2, x, :] for x in range(5)]

        def unit_keys(p):
            I, (k_k, *_) = pair(p)
            dve.wait_ge(sem(f"rw_in_landed_{p % 2}"), 16 * 9 * (p // 2 + 1))
            if p >= 1:
                taken(dve, "rw_tgv", p - 1, RW_GROUPS - 1, RW_CHAINS - 1)
                full(dve, "rw_tgv", p - 1, RW_GROUPS - 1, RW_CHAINS - 1)
            link(V.tensor_tensor(kk, I["k"], over(k_k, NT), ALU.mult))
            link(V.tensor_tensor(rw_t, kk, kk, ALU.mult))
            V.tensor_reduce(rw_s[:, 0:12], heads(rw_t), AX, ALU.add).then_inc(sem("rw_kk_squared"), 1)
            dve.wait_ge(sem("rw_kk_norm"), p + 1)
            link(V.tensor_scalar(rw_s[:, 12:24], rw_s[:, 12:24], 1e-12, None, ALU.max))
            link(V.reciprocal(rw_s[:, 0:12], rw_s[:, 12:24]))
            link(V.tensor_tensor(heads(kk), heads(kk), by_head(rw_s[:, 0:12], 12), ALU.mult))

        def factors(p, z):
            I, (_, k_a, *_) = pair(p)
            az, B, T = I[f"a{z}"], bh[p % 2][z], th[p % 2][z]
            if z == 1:
                full(dve, "rw_turn", p, 0, 3)
            V.tensor_tensor(B, kk, az, ALU.mult)
            link(V.scalar_tensor_tensor(rw_t, az, -1.0, over(k_a, NT), ALU.add, ALU.mult))
            link(V.scalar_tensor_tensor(T, rw_t, 1.0, I["k"], ALU.add, ALU.mult))

        def scale(p, z):
            I, _ = pair(p)
            B, T = bh[p % 2][z], th[p % 2][z]
            taken(dve, "rw_sum_ex", p, z)
            V.tensor_tensor(kh[z], kk, e_ex, ALU.mult)
            V.tensor_tensor(B, B, e_pos, ALU.mult)
            V.tensor_tensor(T, T, e_pos, ALU.mult)
            V.tensor_tensor(rw_t[:, 0:LT], I["r"], e_neg[:, 0:LT], ALU.mult).then_inc(sem("rw_scaled"), 1)

        def scan_u(p, i):
            for z in range(2):
                t, c = rw_chunk(i, z)
                rows = slice(c * CH, (c + 1) * CH)
                ps = full(dve, "rw_u", p, i, z)[:, 0:P]
                taken(dve, "rw_tgv", p, i // 4, 2 * (i // 2 % 2) + z)
                free(V.scalar_tensor_tensor(u[z][rows, :], ps[rows, :], -1.0, tgv[z][rows, t, :], ALU.mult, ALU.subtract), "rw_u", p, i, z)

        def scan_state(p, i):
            if i + 1 == RW_STEPS:
                return
            for z in range(2):
                t, c = rw_chunk(i, z)
                ps = full(dve, "rw_state", p, i, z)[:, 0:P]
                new = state[z][:, (i + 1) % 2, :]
                if i == 0:
                    dve.wait_ge(sem("rw_state_zeroed"), p + 1)
                else:
                    taken(dve, "rw_state", p, i - 1, z)
                if i >= 1 and rw_chunk(i - 1, z)[0] < LT:
                    full(dve, "rw_y", p, i - 1, z)
                link(V.tensor_tensor(new, ps, state[z][:, i % 2, :], ALU.add))
                end = w_end[p % 2][z][:, 2 * t + c:2 * t + c + 1]
                free(V.scalar_tensor_tensor(new, new, end, c_blocks, ALU.mult, ALU.mult), "rw_state", p, i, z)

        def scan(p, i):
            if p >= 0:
                scan_u(p, i)
                scan_state(p, i)

        def zero_states(p):
            if p >= 1:
                for z in range(2):
                    full(dve, "rw_y", p - 1, RW_STEPS - 1, z)
                    taken(dve, "rw_state", p - 1, RW_STEPS - 2, z)
            V.memset(state[0][:, 0, :], 0.0)
            V.memset(state[1][:, 0, :], 0.0).then_inc(sem("rw_state_zeroed"), 1)

        def chain_start(p, g, c):
            t, z = rw_tile(g, c)
            if last_unit(p, g, c):
                full(dve, "rw_tgv", *last_unit(p, g, c))
            mask = [c_mask[:, z, x:x + 1, :].to_broadcast([P, 2, P]) for x in range(2)]
            ps = full(dve, "rw_ab", p, g, c).rearrange("p (h x s) -> p h x s", h=2, x=4)
            V.tensor_tensor(aT[c], ps[:, :, 0, :], mask[0], ALU.mult).then_inc(sem("rw_at"), 1)
            T = inv[c][:, :, 0, :]
            pa = full(dve, "rw_a", p, g, c).rearrange("p (h s) -> p h s", h=2)[:, :, 0:P]
            link(V.tensor_tensor(T, pa, c_pairs[:, z, 0:1, :].to_broadcast([P, 2, P]), ALU.mult))
            if t < LT:
                for rows in (slice(0, CH), slice(CH, P)):
                    own = c_mask[rows, z, 1:2, rows].to_broadcast([CH, 2, CH])
                    V.tensor_tensor(rbT[z][rows, t], ps[rows, :, 1, rows], own, ALU.mult)
                    V.tensor_tensor(rtT[z][rows, t], ps[rows, :, 3, rows], own, ALU.mult)
            free(V.tensor_tensor(gT[c], ps[:, :, 2, :], mask[0], ALU.mult), "rw_ab", p, g, c)
            free(V.tensor_tensor(T, T, ident[:, :].unsqueeze(1).to_broadcast([P, 2, P]), ALU.add), "rw_a", p, g, c)

        def read_out(p, part):
            I, (k_k, k_a, r_k, ln_g, ln_b) = pair(p)
            y, d = yd
            w = yz[0]
            if part == 1:
                for z in range(2):
                    taken(dve, "rw_y", p, RW_STEPS - 1, z)
                if p >= 1:
                    full(dve, "rw_ot", p - 1)
                link(V.tensor_tensor(y, yz[0], yz[1], ALU.add))
                link(V.tensor_reduce(rw_s[:, 24:32], heads(y), AX, ALU.add))
                link(V.tensor_scalar(rw_s[:, 24:32], rw_s[:, 24:32], 1.0 / HD, None, ALU.mult))
                link(V.tensor_tensor(heads(d), heads(y), by_head(rw_s[:, 24:32], 8), ALU.subtract))
                link(V.tensor_tensor(y, d, d, ALU.mult))
            elif part == 2:
                link(V.tensor_reduce(rw_s[:, 40:48], heads(y), AX, ALU.add))
                V.tensor_scalar(rw_s[:, 24:32], rw_s[:, 40:48], 1.0 / HD, GN_EPS, ALU.mult, ALU.add).then_inc(sem("rw_y_var"), 1)
                link(V.tensor_tensor(w, I["a0"][:, 0:LT], I["a1"][:, 0:LT], ALU.add))
                link(V.scalar_tensor_tensor(w, w, -2.0, over(k_a, LT), ALU.add, ALU.mult))
                link(V.scalar_tensor_tensor(w, w, 2.0, I["k"][:, 0:LT], ALU.add, ALU.mult))
            elif part == 3:
                link(V.tensor_tensor(w, w, I["r"], ALU.mult))
                link(V.tensor_tensor(w, w, over(r_k, LT), ALU.mult))
                link(V.tensor_reduce(rw_s[:, 40:48], heads(w), AX, ALU.add))
                link(V.tensor_tensor(heads(w), heads(I["v"][:, 0:LT]), by_head(rw_s[:, 40:48], 8), ALU.mult))
            elif part == 4:
                dve.wait_ge(sem("rw_y_std"), p + 1)
                link(V.reciprocal(rw_s[:, 40:48], rw_s[:, 32:40]))
                link(V.tensor_tensor(heads(d), heads(d), by_head(rw_s[:, 40:48], 8), ALU.mult))
                link(V.tensor_tensor(d, d, over(ln_g, LT), ALU.mult))
                link(V.tensor_tensor(d, d, over(ln_b, LT), ALU.add))
            else:
                link(V.tensor_tensor(d, d, w, ALU.add))
                V.tensor_tensor(d, d, I["g"], ALU.mult).then_inc(sem("rw_read_out"), 1)

        dve.wait_ge(sem("rw_const_landed"), 16 * 7)
        units = 0
        for p in range(RW_PAIRS):
            unit_keys(p)
            factors(p, 0)
            scale(p, 0)
            scan(p - 1, RW_STEPS - 4)
            factors(p, 1)
            scan(p - 1, RW_STEPS - 3)
            scale(p, 1)
            scan(p - 1, RW_STEPS - 2)
            scan(p - 1, RW_STEPS - 1)
            zero_states(p)
            for g in range(RW_GROUPS):
                for c in range(RW_CHAINS):
                    chain_start(p, g, c)
                for lv in range(1, RW_LEVELS):
                    i = rw_step_beside(g, lv)
                    for c in range(RW_CHAINS):
                        z = c % 2
                        ps = full(dve, "rw_x", p, g, c, lv)[:, 0:2 * P].rearrange("p (h s) -> p h s", h=2)
                        free(V.tensor_tensor(xl[c], ps, c_join[:, z, lv - 1:lv, :].to_broadcast([P, 2, P]), ALU.mult), "rw_x", p, g, c, lv)
                    if i is not None:
                        scan_u(p, i)
                    for c in range(RW_CHAINS):
                        z = c % 2
                        ps = full(dve, "rw_join", p, g, c, lv)[:, 0:4 * CH].rearrange("p (h x a b) -> p h x a b", h=2, x=2, b=1 << lv)
                        T = halves(inv[c][:, :, 0, :], lv, z)
                        M = halves(inv[c][:, :, 1, :], lv, z, True)
                        if lv == 1:
                            taken(dve, "rw_a", p, g, c)
                            dve.wait_ge(sem("rw_off"), units + c + 1)
                        else:
                            taken(dve, "rw_join", p, g, c, lv - 1)
                        if lv < RW_LEVELS - 1:
                            V.tensor_tensor(T, T, ps[:, :, 0], ALU.subtract)
                        free(V.tensor_tensor(M, M, ps[:, :, 1], ALU.subtract), "rw_join", p, g, c, lv)
                    if i is not None:
                        scan_state(p, i)
                    if g == 0 and p >= 1:
                        read_out(p - 1, lv)
                units += RW_CHAINS
        for i in range(RW_STEPS - 4, RW_STEPS):
            scan(RW_PAIRS - 1, i)
        for part in range(1, RW_LEVELS):
            read_out(RW_PAIRS - 1, part)
        dve.wait_ge(sem("rw_gate_landed"), 16)
        for n in range(2):
            for t in range(LT):
                i = n * LT + t
                ps = full(dve, "rw_o", n, t)
                sl = slice(n * W, (n + 1) * W)
                if i >= 2:
                    dve.wait_ge(sem("rw_added"), i - 1)
                free(V.tensor_tensor(rw_ot[:, i % 2, :], ps, rw_gate[:, sl], ALU.mult), "rw_o", n, t)
                taken(dve, "rw_o", n, t)
                V.tensor_tensor(h[:, t, sl], h[:, t, sl], rw_ot[:, i % 2, :], ALU.add).then_inc(sem("rw_added"), 1)
        experts(1)

    @block.tensor
    def _(pe):
        mm, turn = nc.tensor.matmul, nc.tensor.transpose
        load_no = [0]

        def weights(name, k=KD, n=W):
            i = load_no[0]
            assert loads[i][0] == name, (loads[i][0], name)
            pe.wait_ge(landed[i % RING], landed_at[i])
            load_no[0] += 1
            return ring[:, i % RING, 0:k * n].rearrange("p (k n) -> p k n", n=n)

        def open_(*key):
            for before in plan[key].before:
                pe.wait_ge(freed[before.engine], before.count)
            return bank(plan[key])

        def close(ins, *key):
            assert done["pe"] == plan[key].number, (key, done["pe"], plan[key].number)
            done["pe"] += 1
            ins.then_inc(filled, 1)

        def product(key, lhs, rhs, nk, ncol=W, first=True):
            ps = open_(*key)
            for k in range(nk):
                ins = mm(ps[:, 0:ncol], lhs(k), rhs(k), start=(k == 0 and first), stop=(k == nk - 1))
            return ins

        def norm(use):
            xn, _ = norm_of[use]
            t0 = tiles_before[use]
            for k in range(KD):
                ps = open_("turn", use, 0, k)
                for t in range(LT):
                    pe.wait_ge(sem("normed"), t0 + t + 1)
                    ins = turn(ps[:, t * P:(t + 1) * P], xn[:, t, k * P:(k + 1) * P], ident[:, :])
                close(ins, "turn", use, 0, k)
            if NORMS[use] == NT:
                for k in range(KD):
                    ps = open_("turn", use, 1, k)
                    for t in range(LT, NT):
                        pe.wait_ge(sem("normed"), t0 + t + 1)
                        ins = turn(ps[:, (t - LT) * P:(t - LT + 1) * P], xn[:, t, k * P:(k + 1) * P], ident[:, :])
                    close(ins, "turn", use, 1, k)
            taken(pe, "turn", use, int(NORMS[use] == NT), KD - 1)

        pe.wait_ge(sem("const_landed"), 16 * 6)
        norm("dil")
        n_rot = 0
        for i in range(len(DIL_STEPS) + 1):
            if i < len(DIL_STEPS):
                w = weights("dil_proj")
                for c in range(DIL_STRIDE):
                    ins = product(("dil_proj", i, c), lambda k: uT[:, k, c::DIL_STRIDE], lambda k: w[:, k, :], KD)
                    close(ins, "dil_proj", i, c)
            if i >= 1 and DIL_STEPS[i - 1][1] < 2:
                for c in range(DIL_STRIDE):
                    n_rot += 1
                    pe.wait_ge(sem("dil_rotated"), n_rot)
                    ps = open_("dil_turn", i - 1, c)
                    for f in range(4):
                        ins = turn(ps[:, f * P:(f + 1) * P], dil_tmp[:, c, f * P:(f + 1) * P], ident[:, :])
                    close(ins, "dil_turn", i - 1, c)
        taken(pe, "dil_turn", len(DIL_STEPS) - 2, DIL_STRIDE - 1)
        taken(pe, "dil_proj", len(DIL_STEPS) - 1, DIL_STRIDE - 1)
        for i in range(DIL_TILES + 2):
            if i < DIL_TILES:
                s, c = divmod(i, DIL_STRIDE)
                rows = slice(s % 2 * HD, s % 2 * HD + HD)
                ps = open_("dil_score", i)
                f = [4 * g + s // 2 for g in range(DIL_GROUPS)]
                own = slice(c * P, (c + 1) * P)
                mm(ps[:, 0:SEQ], qT[rows, f[0], own], kT[rows, f[0], :], start=True, stop=True)
                for g in (1, 2):
                    ins = mm(ps[:, SEQ + (g - 1) * P:SEQ + g * P], qT[rows, f[g], own], kT[rows, f[g], own], start=True, stop=True)
                close(ins, "dil_score", i)
            if 1 <= i <= DIL_TILES:
                j = i - 1
                ps = open_("dil_pt", j)
                pe.wait_ge(sem("dil_exp"), j + 1)
                for b in range(6):
                    ins = turn(ps[:, b * P:(b + 1) * P], dil_s[:, j % 2, b * P:(b + 1) * P], ident[:, :])
                close(ins, "dil_pt", j)
            if i >= 2:
                j = i - 2
                s, c = divmod(j, DIL_STRIDE)
                ps = open_("dil_out", j)
                taken(pe, "dil_pt", j)
                for b in range(6):
                    g, tile = (0, b) if b < 4 else (b - 3, c)
                    ins = mm(ps[:, 0:HD], dil_p[:, j % 2, b * P:(b + 1) * P], vR[:, tile, g * W + s * HD:g * W + (s + 1) * HD],
                             start=(b == 0), stop=(b == 5))
                close(ins, "dil_out", j)
        taken(pe, "dil_out", DIL_TILES - 1)
        for c in range(DIL_STRIDE):
            ps = open_("dil_ot", c)
            for f in range(4):
                ins = turn(ps[:, f * P:(f + 1) * P], dil_o[:, c, f * P:(f + 1) * P], ident[:, :])
            close(ins, "dil_ot", c)

        def ret_turn(hd):
            taken(pe, "ret_out", hd, LT - 1)
            for f in range(4):
                ps = open_("ret_turn", hd, f)
                for t in range(LT):
                    ins = turn(ps[:, t * P:(t + 1) * P], ry[:, t, f * P:(f + 1) * P], ident[:, :])
                close(ins, "ret_turn", hd, f)

        for hd in range(RET_HEADS):
            w = weights("ret_qk", 2 * KD, RET_QK)
            for mt in range(4):
                b, d = divmod(mt, 2)
                ins = product(("ret_qk", hd, mt), lambda k: w[:, b * KD + k, d * P:(d + 1) * P], lambda k: uT[:, k, :], KD)
                close(ins, "ret_qk", hd, mt)
            for name in ("ret_v", "ret_g"):
                w = weights(name)
                for t in range(LT):
                    ins = product((name, hd, t), lambda k: uT[:, k, t * P:(t + 1) * P], lambda k: w[:, k, :], KD)
                    close(ins, name, hd, t)
            if hd >= 1:
                ret_turn(hd - 1)
            pe.wait_ge(sem("ret_rotated"), 2 * (hd + 1))
            for j in range(LT):
                ins = product(("ret_score", hd, j), lambda d: rkT[:, d, j * P:(j + 1) * P], lambda d: rqT[:, d, j * P:SEQ], 2,
                              ncol=SEQ - j * P)
                close(ins, "ret_score", hd, j)
            taken(pe, "ret_v", hd, LT - 1)
            for t in range(LT):
                taken(pe, "ret_score", hd, t)
                ins = product(("ret_out", hd, t), lambda j: rs[:, j, (t - j) * P:(t - j + 1) * P], lambda j: rv[:, j, :], t + 1)
                close(ins, "ret_out", hd, t)
        ret_turn(RET_HEADS - 1)
        taken(pe, "ret_turn", RET_HEADS - 1, 3)

        for n in range(2):
            for b in range(2):
                w = weights("mix_gate")
                for f in range(4):
                    ins = product(("mix_gate", b, n, f), lambda k: w[:, k, f * P:(f + 1) * P], lambda k: uT[:, k, :], KD)
                    close(ins, "mix_gate", b, n, f)
            for half in range(2):
                w = weights("mix_ret")
                for f in range(4):
                    ps = open_("mix_ret", n, f) if half == 0 else bank(plan["mix_ret", n, f])
                    for k in range(KD):
                        ins = mm(ps, w[:, k, f * P:(f + 1) * P], yrT[:, half * KD + k, :], start=(half == 0 and k == 0),
                                 stop=(half == 1 and k == KD - 1))
                    if half == 1:
                        close(ins, "mix_ret", n, f)
                if half == 0:
                    ins.then_inc(used, 1)
        w = weights("mix_dil", 4, D)
        for f in range(KD):
            ins = product(("mix_dil", f), lambda k: w[:, k, f * P:(f + 1) * P], lambda k: yaT[:, k, :], 4)
            close(ins, "mix_dil", f)
        pe.wait_ge(sem("mixed"), KD)
        for n in range(2):
            w = weights("mix_o")
            for t in range(LT):
                ins = product(("mix_o", n, t), lambda k: mixT[:, k, t * P:(t + 1) * P], lambda k: w[:, k, :], KD)
                close(ins, "mix_o", n, t)

        norm("mlp")
        for l in range(D_FF // W):
            w = weights("up")
            for f in range(4):
                ins = product(("up", 4 * l + f), lambda k: w[:, k, f * P:(f + 1) * P], lambda k: vT[:, k, :], KD)
                close(ins, "up", 4 * l + f)
        for n in range(2):
            for q in range(4):
                w = weights("down")
                for t in range(LT):
                    ps = open_("down", n, t) if q == 0 else bank(plan["down", n, t])
                    for k in range(KD):
                        pe.wait_ge(sem("ff_squared"), q * KD + k + 1)
                        ins = mm(ps, ffT[:, q * KD + k, t * P:(t + 1) * P], w[:, k, :], start=(q == 0 and k == 0),
                                 stop=(q == 3 and k == KD - 1))
                    if q == 3:
                        close(ins, "down", n, t)
                if q < 3:
                    ins.then_inc(used, 1)

        norm("ple")
        pe.wait_ge(sem("ple_landed"), 32)
        pe.wait_ge(sem("ones_set"), 1)
        for d in range(PLE // P):
            ps = open_("ple_turn", d)
            for t in range(LT):
                ins = turn(ps[:, t * P:(t + 1) * P], pR[:, t, d * P:(d + 1) * P], ident[:, :])
            close(ins, "ple_turn", d)
        for n in range(2):
            w = weights("ple_gate")
            for t in range(LT):
                ps = open_("ple_gate", n, t)
                mm(ps, ones[0:1, :], b_ple[0:1, n * W:(n + 1) * W], start=True, stop=False)
                for k in range(KD):
                    ins = mm(ps, wT[:, k, t * P:(t + 1) * P], w[:, k, :], start=False, stop=(k == KD - 1))
                close(ins, "ple_gate", n, t)
        taken(pe, "ple_turn", PLE // P - 1)
        w = weights("ple_in", 2, D)
        for n in range(2):
            for t in range(LT):
                ins = product(("ple_in", n, t), lambda k: pT[:, k, t * P:(t + 1) * P], lambda k: w[:, k, n * W:(n + 1) * W], 2)
                close(ins, "ple_in", n, t)

        pe.wait_ge(sem("cond_ready"), 1)
        for l in range(2):
            for n in range(6 * D // W):
                w = weights("ada")
                ps = open_("ada", l, n)
                for k in range(KD):
                    ins = mm(ps[0:2, :], cond[:, :, k], w[:, k, :], start=(k == 0), stop=(k == KD - 1))
                close(ins, "ada", l, n)
        for l in range(2):
            ps = open_("ada_turn", l)
            pe.wait_ge(sem("mod_rows_landed"), 16 * (l + 1))
            close(turn(ps[:, 0:96], mod_rows[0:96, l, :], ident[0:96, 0:96]), "ada_turn", l)

        norm("na")
        for i in range(NA_STEPS + 2):
            if i < NA_STEPS:
                half, t = divmod(i, NT)
                if t == 0:
                    w = weights("na_proj")
                ins = product(("na_proj", i), lambda k: hT_na[:, k, t * P:(t + 1) * P], lambda k: w[:, k, :], KD)
                close(ins, "na_proj", i)
            if i >= 2:
                j = i - 2
                ps = open_("na_turn", j)
                pe.wait_ge(sem("na_normed"), j + 1)
                for f in range(4):
                    ins = turn(ps[:, f * P:(f + 1) * P], na_s[:, j % 2, f * P:(f + 1) * P], ident[:, :])
                close(ins, "na_turn", j)

        def grid(x, c0, n):
            return x[:, 0:SEQ].rearrange("p (r c) -> p r c", c=GRID)[:, :, c0:c0 + n]

        for n in range(2):
            w = weights("na_v")
            for t in range(NT):
                ins = product(("na_v", n, t), lambda k: hT_na[:, k, t * P:(t + 1) * P], lambda k: w[:, k, :], KD)
                close(ins, "na_v", n, t)
        taken(pe, "na_turn", NA_STEPS - 1)
        taken(pe, "na_v", 1, NT - 1)
        pe.wait_ge(sem("na_strips_landed"), 16 * 4 * BLOCKS * LT)
        for i in range(NA_UNITS + 2):
            if i < NA_UNITS:
                hd, un = divmod(i, NT)
                rows, f = slice(hd % 2 * HD, hd % 2 * HD + HD), hd // 2
                ps = open_("na_score", i)
                if un < BLOCKS:
                    q = naq[rows, f, un * P:(un + 1) * P]
                    mm(ps[:, 0:2 * P], q, grid(nak[rows, f, :], strip0[un], STRIP), start=True, stop=True)
                    ins = mm(ps[:, 2 * P:W], q, nak[rows, f, SEQ:TOK], start=True, stop=True)
                else:
                    ins = mm(ps[:, 0:CTX], naq[rows, f, un * P:(un + 1) * P], nak[rows, f, SEQ:TOK], start=True, stop=True)
                close(ins, "na_score", i)
            if 1 <= i <= NA_UNITS:
                j = i - 1
                ps = open_("na_pt", j)
                pe.wait_ge(sem("na_exp"), j + 1)
                for b in range(4 if j % NT < BLOCKS else CT):
                    ins = turn(ps[:, b * P:(b + 1) * P], na_s[:, j % 2, b * P:(b + 1) * P], ident[:, :])
                close(ins, "na_pt", j)
            if i >= 2:
                j = i - 2
                hd, un = divmod(j, NT)
                ps = open_("na_out", j)
                taken(pe, "na_pt", j)
                d = slice(hd * HD, (hd + 1) * HD)
                vals = [na_vc[:, c, d] for c in range(CT)]
                if un < BLOCKS:
                    vals = [na_vs[:, 2 * un + half, d] for half in range(2)] + vals
                for b, v in enumerate(vals):
                    ins = mm(ps[:, 0:HD], na_p[:, j % 2, b * P:(b + 1) * P], v, start=(b == 0), stop=(b == len(vals) - 1))
                close(ins, "na_out", j)
        taken(pe, "na_out", NA_UNITS - 1)
        for t in range(NT):
            ps = open_("na_ot", t)
            for f in range(KD):
                ins = turn(ps[:, f * P:(f + 1) * P], na_o[:, t, f * P:(f + 1) * P], ident[:, :])
            close(ins, "na_ot", t)
        taken(pe, "na_ot", NT - 1)
        for n in range(2):
            w = weights("na_o")
            for t in range(NT):
                ins = product(("na_o", n, t), lambda k: na_oT[:, k, t * P:(t + 1) * P], lambda k: w[:, k, :], KD)
                close(ins, "na_o", n, t)

        def experts(l):
            nt, m = TILES[l], SLOTS if l == 0 else CAP_L
            norm(f"moe{l}")
            pe.wait_ge(sem("moe_landed"), 64 * (l + 1))
            ps = open_("moe_logit", l)
            for t in range(nt):
                for k in range(KD):
                    ins = mm(ps[:, t * EXPERTS:(t + 1) * EXPERTS], hT_moe[:, k, t * P:(t + 1) * P], router[:, k, :],
                             start=(k == 0), stop=(k == KD - 1))
            close(ins, "moe_logit", l)
            ps = open_("moe_afft", l)
            pe.wait_ge(sem("moe_affinity"), l + 1)
            for t in range(nt):
                ins = turn(ps[0:EXPERTS, t * P:(t + 1) * P], aff[:, t, :], ident[:, :])
            close(ins, "moe_afft", l)
            ps = open_("moe_slot", l)
            pe.wait_ge(sem("moe_numbered"), l + 1)
            for t in range(nt):
                ins = turn(ps[:, t * EXPERTS:(t + 1) * EXPERTS], sumT[0:EXPERTS, t * P:(t + 1) * P], ident[0:EXPERTS, 0:EXPERTS])
            close(ins, "moe_slot", l)

            def gather(e):
                pe.wait_ge(sem("moe_selected"), l * EXPERTS + e + 1)
                for half in range(2):
                    ps = open_("moe_gather", l, e, half).rearrange("p (k s) -> p k s", k=4)
                    for k in range(4):
                        d = slice((4 * half + k) * P, (4 * half + k + 1) * P)
                        for t in range(LT):
                            ins = mm(ps[:, k, 0:CAP_L], xn_moe[:, t, d], sel_l[:, t, :], start=(t == 0), stop=(t == LT - 1))
                        for t in range(LT, nt):
                            ins = mm(ps[:, k, CAP_L:SLOTS], xn_moe[:, t, d], sel_c[:, t - LT, :], start=(t == LT), stop=(t == nt - 1))
                    close(ins, "moe_gather", l, e, half)
                ps = open_("moe_selt", l, e)
                for t in range(nt):
                    ins = turn(ps[0:m, t * P:(t + 1) * P], sel_g[:, t, 0:m], ident[:, :])
                close(ins, "moe_selt", l, e)

            def scatter(e):
                taken(pe, "moe_selt", l, e)
                taken(pe, "moe_y", l, e, 1)
                for t in range(nt):
                    for n in range(2):
                        ps = open_("moe_add", l, e, t, n)
                        close(mm(ps, selT[0:m, e % 2, t * P:(t + 1) * P], y_moe[0:m, e % 2, n * W:(n + 1) * W], start=True, stop=True),
                              "moe_add", l, e, t, n)

            gather(0)
            for e in range(EXPERTS):
                taken(pe, "moe_gather", l, e, 1)
                for n in range(2):
                    for name, key in (("moe_w1", "moe_h1"), ("moe_w3", "moe_h3")):
                        w = weights(name)
                        ps = open_(key, l, e, n)
                        for k in range(KD):
                            ins = mm(ps[0:m, :], xinT[:, e % 2, k, 0:m], w[:, k, :], start=(k == 0), stop=(k == KD - 1))
                        close(ins, key, l, e, n)
                if e >= 1:
                    scatter(e - 1)
                if e + 1 < EXPERTS:
                    gather(e + 1)
                taken(pe, "moe_h3", l, e, 1)
                ps = open_("moe_ht", l, e).rearrange("p (k s) -> p k s", k=KD)
                for k in range(KD):
                    ins = turn(ps[:, k, 0:m], hid[0:m, k * P:(k + 1) * P], ident[0:m, 0:m])
                close(ins, "moe_ht", l, e)
                taken(pe, "moe_ht", l, e)
                for n in range(2):
                    w = weights("moe_w2")
                    ps = open_("moe_y", l, e, n)
                    for k in range(KD):
                        ins = mm(ps[0:m, :], hidT[:, k, 0:m], w[:, k, :], start=(k == 0), stop=(k == KD - 1))
                    close(ins, "moe_y", l, e, n)
            scatter(EXPERTS - 1)

        experts(0)

        norm("rw")
        for i, q in enumerate("rkvwag"):
            x = xs[i % 2]
            if q in "rkv":
                for n in range(2):
                    w = weights("rw_proj")
                    for t in range(LT if q == "r" else NT):
                        pe.wait_ge(sem("rw_mixed"), (i + 1) * KD)
                        ins = product(("rw_proj", q, n, t), lambda k: x[:, k, t * P:(t + 1) * P], lambda k: w[:, k, :], KD)
                        close(ins, "rw_proj", q, n, t)
                continue
            w = weights(f"rw_low_{q}", 1, SLOT)[:, 0, :]
            pe.wait_ge(sem("rw_mixed"), (i + 1) * KD)
            ps = open_("rw_low", q)
            for lo, hi in ((0, SEQ), (SEQ, TOK)):
                for k in range(KD):
                    ins = mm(ps[:, lo:hi], w[:, k * P:(k + 1) * P], x[:, k, lo:hi], start=(k == 0), stop=(k == KD - 1))
            close(ins, "rw_low", q)
            taken(pe, "rw_low", q)
            for z in range(1 if q == "g" else 2):
                rows = slice(0, P) if q == "g" else slice(z * CH, (z + 1) * CH)
                for n in range(2):
                    at = KD * P + n * W
                    for t in range(LT if q == "g" else NT):
                        ps = open_("rw_high", q, z, n, t)
                        if q != "g":
                            mm(ps, ones[z * CH:z * CH + 1, :], w[z * CH:z * CH + 1, at + D:at + D + W], start=True, stop=False)
                        ins = mm(ps, lowT[rows, t * P:(t + 1) * P], w[rows, at:at + W], start=(q == "g"), stop=True)
                        close(ins, "rw_high", q, z, n, t)

        def sums(p, z):
            pe.wait_ge(sem(f"rw_in_landed_{p % 2}"), 16 * 9 * (p // 2 + 1))
            lam = RW_IN[f"w{z}"][p % 2]
            lam_f = lam.rearrange("p t d -> p (t d)")
            for key, c in (("rw_sum", c_sum), ("rw_sum_ex", c_sum_ex)):
                ps = open_(key, p, z)
                for lo, hi in ((0, SEQ), (SEQ, TOK)):
                    ins = mm(ps[:, lo:hi], c[:, z, :], lam_f[:, lo:hi], start=True, stop=True)
                close(ins, key, p, z)
            ps = open_("rw_end", p, z)
            for t in range(NT):
                ins = mm(ps[:, 2 * t:2 * t + 2], lam[:, t, :], c_ind, start=True, stop=True)
            close(ins, "rw_end", p, z)

        def turn_factors(p, z):
            pe.wait_ge(sem("rw_scaled"), 2 * p + z + 1)
            for x, src in enumerate((kh[z], bh[p % 2][z], th[p % 2][z], rw_t)):
                ps = open_("rw_turn", p, z, x)
                for t in range(LT if x == 3 else NT):
                    ins = turn(ps[:, t * P:(t + 1) * P], src[:, t, :], ident[:, :])
                close(ins, "rw_turn", p, z, x)

        def scan_u(p, i):
            for z in range(2):
                t, c = rw_chunk(i, z)
                ps = open_("rw_u", p, i, z)
                if i == 0:
                    pe.wait_ge(sem("rw_state_zeroed"), p + 1)
                else:
                    taken(pe, "rw_state", p, i - 1, z)
                taken(pe, "rw_tk", p, i // 4, 2 * (i // 2 % 2) + z)
                close(mm(ps[:, 0:P], tkT[z][:, t, :], state[z][:, i % 2, :], start=True, stop=True), "rw_u", p, i, z)

        def scan_state(p, i):
            V_ = RW_IN["v"][p % 2]
            for z in range(2):
                t, c = rw_chunk(i, z)
                rows = slice(c * CH, (c + 1) * CH)
                taken(pe, "rw_u", p, i, z)
                if i + 1 < RW_STEPS:
                    ps = open_("rw_state", p, i, z)[:, 0:P]
                    mm(ps, th[p % 2][z][rows, t, :], V_[rows, t, :], start=True, stop=False)
                    close(mm(ps, bh[p % 2][z][rows, t, :], u[z][rows, :], start=False, stop=True), "rw_state", p, i, z)
                if t < LT:
                    ps = open_("rw_y", p, i, z)[rows, 0:P]
                    mm(ps, RT[p % 2][z][:, t * P + c * CH:t * P + (c + 1) * CH], state[z][:, i % 2, :], start=True, stop=False)
                    for hd in range(2):
                        d = slice(hd * CH, (hd + 1) * CH)
                        mm(ps[:, d], rtT[z][rows, t, hd, :], V_[rows, t, d], start=False, stop=False)
                        ins = mm(ps[:, d], rbT[z][rows, t, hd, :], u[z][rows, d], start=False, stop=(hd == 1))
                    close(ins, "rw_y", p, i, z)

        def scan(p, i):
            if p >= 0:
                scan_u(p, i)
                scan_state(p, i)

        def products(p, g, c):
            t, z = rw_tile(g, c)
            tile = slice(t * P, (t + 1) * P)
            to_r = TOK + p % 2 * SEQ
            kr = xT[z][:, 0:2 * to_r].rearrange("p (x s) -> p x s", x=2)[:, 0:2 if t < LT else 1, tile]
            n = 2 * P if t < LT else P
            ps = open_("rw_ab", p, g, c).rearrange("p (h s) -> p h s", h=2)
            for hd in range(2):
                rows = slice(hd * CH, (hd + 1) * CH)
                mm(ps[:, hd, 0:n], BT[z][rows, tile], kr[rows], start=True, stop=True)
                ins = mm(ps[:, hd, 2 * P:2 * P + n], TT[z][rows, tile], kr[rows], start=True, stop=True)
            close(ins, "rw_ab", p, g, c)
            ps = open_("rw_a", p, g, c).rearrange("p (h s) -> p h s", h=2)
            for hd in range(2):
                rows = slice(hd * CH, (hd + 1) * CH)
                ins = mm(ps[:, hd, 0:P], KT[z][rows, tile], BT[z][rows, tile], start=True, stop=True)
            close(ins, "rw_a", p, g, c)

        def read_out(p):
            ps = open_("rw_ot", p)
            pe.wait_ge(sem("rw_read_out"), p + 1)
            for t in range(LT):
                ins = turn(ps[:, t * P:(t + 1) * P], yd[1][:, t, :], ident[:, :])
            close(ins, "rw_ot", p)

        units = 0
        pe.wait_ge(sem("rw_const_landed"), 16 * 7)
        for p in range(RW_PAIRS):
            sums(p, 0)
            scan(p - 1, RW_STEPS - 4)
            turn_factors(p, 0)
            sums(p, 1)
            scan(p - 1, RW_STEPS - 3)
            scan(p - 1, RW_STEPS - 2)
            turn_factors(p, 1)
            scan(p - 1, RW_STEPS - 1)
            taken(pe, "rw_turn", p, 1, 3)
            for g in range(RW_GROUPS):
                for c in range(RW_CHAINS):
                    products(p, g, c)
                for c in range(RW_CHAINS):
                    t, z = rw_tile(g, c)
                    ps = open_("rw_gv", p, g, c)
                    taken(pe, "rw_ab", p, g, c)
                    for hd in range(2):
                        d = slice(hd * CH, (hd + 1) * CH)
                        ins = mm(ps[:, d], gT[c][:, hd, :], RW_IN["v"][p % 2][:, t, d], start=True, stop=True)
                    close(ins, "rw_gv", p, g, c)
                for lv in range(1, RW_LEVELS):
                    i = rw_step_beside(g, lv)
                    for c in range(RW_CHAINS):
                        ps = open_("rw_x", p, g, c, lv)
                        if lv == 1:
                            taken(pe, "rw_a", p, g, c)
                            pe.wait_ge(sem("rw_off"), units + c + 1)
                        else:
                            taken(pe, "rw_join", p, g, c, lv - 1)
                        for hd in range(2):
                            ins = mm(ps[:, hd * P:(hd + 1) * P], aT[c][:, hd, :], inv[c][:, hd, 0, :], start=True, stop=True)
                        close(ins, "rw_x", p, g, c, lv)
                    if i is not None:
                        scan_u(p, i)
                    for c in range(RW_CHAINS):
                        z = c % 2
                        ps = open_("rw_join", p, g, c, lv)[:, 0:4 * CH].rearrange("p (h x s) -> p h x s", h=2, x=2)
                        taken(pe, "rw_x", p, g, c, lv)
                        X = halves(xl[c], lv, z)
                        M = halves(inv[c][:, :, 1, :], lv, z, True)
                        for hd in range(2):
                            if lv < RW_LEVELS - 1:
                                mm(ps[:, hd, 0, :], inv[c][:, hd, 1, :], X[:, hd], start=True, stop=True)
                            ins = mm(ps[:, hd, 1, :], xl[c][:, hd, :], M[:, hd], start=True, stop=True)
                        close(ins, "rw_join", p, g, c, lv)
                    if i is not None:
                        scan_state(p, i)
                for c in range(RW_CHAINS):
                    t, z = rw_tile(g, c)
                    ps = open_("rw_tk", p, g, c)
                    taken(pe, "rw_join", p, g, c, RW_LEVELS - 1)
                    for hd in range(2):
                        d = slice(hd * CH, (hd + 1) * CH)
                        ins = mm(ps[d, 0:P], kh[z][:, t, d], inv[c][:, hd, 1, :], start=True, stop=True)
                    close(ins, "rw_tk", p, g, c)
                for c in range(RW_CHAINS):
                    t, z = rw_tile(g, c)
                    ps = open_("rw_tgv", p, g, c)
                    taken(pe, "rw_gv", p, g, c)
                    for hd in range(2):
                        d = slice(hd * CH, (hd + 1) * CH)
                        ins = mm(ps[:, d], inv[c][:, hd, 1, :], gv[c][:, d], start=True, stop=True)
                    close(ins, "rw_tgv", p, g, c)
                if g == 0 and p >= 1:
                    read_out(p - 1)
                units += RW_CHAINS
        for i in range(RW_STEPS - 4, RW_STEPS):
            scan(RW_PAIRS - 1, i)
        read_out(RW_PAIRS - 1)
        taken(pe, "rw_ot", RW_PAIRS - 1)
        for n in range(2):
            w = weights("rw_o")
            for t in range(LT):
                ins = product(("rw_o", n, t), lambda k: zT(k)[:, t * P:(t + 1) * P], lambda k: w[:, k, :], KD)
                close(ins, "rw_o", n, t)
        experts(1)


def columns_of(x):
    x = np.asarray(x).reshape(-1, P)
    return x.T


def kernel(**inputs):
    from concourse import bacc
    from concourse.bass_utils import run_bass_kernel_spmd

    nc = bacc.Bacc("TRN2", target_bir_lowering=False, num_devices=1)
    i = {k: np.asarray(v) for k, v in inputs.items()}
    arrays = dict(constants())
    vectors = {"g_pre_mix": i["g_pre_mix"], "b_gate_r": i["b_gate"][0, 0], "b_gate_a": i["b_gate"][0, 1],
               "g_pre_mlp": i["g_pre_mlp"], "g_pre_ple": i["g_pre_ple"],
               "norm_g": np.stack([i["norm1_g_2"], i["norm2_g_2"]], 1), "na_q_g": np.tile(i["na_q_g_2"][0], 2),
               "na_k_g": np.tile(i["na_k_g_2"][0], 2), "rw_mix": i["rw_mix_2"][0], "cond": np.stack([i["c_2"][0], i["c_ctx_2"]])}
    arrays["cols"] = np.concatenate([columns_of(vectors[k]) for k in COLUMNS], 1)
    arrays["x"] = i["x"][0]
    arrays["p"] = i["p"][0, 0]
    arrays["pos_row"] = np.broadcast_to(i["positions"], (P, SEQ))
    arrays["pos_col"] = i["positions"].reshape(P, DIL_STRIDE)
    for k in ("w_in", "w_ret_out", "w_dil_out", "w_o", "w_up", "w_down", "w_ple_gate", "w_ple_in", "g_post_mix", "g_post_mlp",
              "g_post_ple", "b_ple_gate"):
        arrays[k] = i[k][0]
    arrays["ctx"] = i["ctx_2"][0]
    for k in ("ada_w", "ada_b", "moe_router", "moe_w1", "moe_w3", "moe_w2"):
        arrays[k] = i[k + "_2"]
    for k in ("na_w_qkv", "na_w_o", "rw_w_r", "rw_w_k", "rw_w_v", "rw_w0", "rw_a0", "rw_g1", "rw_g2", "rw_w_o"):
        arrays[k] = i[k + "_2"][0]
    arrays["na_rpb"] = np.pad(i["na_rpb_2"][0], ((0, 0), (0, 0), (RPB_PAD, RPB_PAD)))
    for q in "wa":
        arrays[f"rw_{q}1"] = i[f"rw_{q}1_2"][0].transpose(1, 0, 2).reshape(D, 2 * CH)
        arrays[f"rw_{q}2"] = i[f"rw_{q}2_2"][0].reshape(2 * CH, D)
    arrays["rw_rows"] = np.stack([i["rw_k_k_2"][0], i["rw_k_a_2"][0], i["rw_r_k_2"][0].reshape(D), i["rw_ln_g_2"][0], i["rw_ln_b_2"][0]])
    arrays = {f"in_{k}": np.ascontiguousarray(v) for k, v in arrays.items()}
    a = {k[3:]: nc.dram_tensor(k, v.shape, mybir.dt.from_np(v.dtype), kind="ExternalInput").ap() for k, v in arrays.items()}
    out = nc.dram_tensor("out", (SEQ, D), F32, kind="ExternalOutput").ap()
    build(nc, a, out)
    got = run_bass_kernel_spmd(nc, [arrays], core_ids=[0])
    return got.results[0]["out"].reshape(1, SEQ, D)
```

```python
from contextlib import ExitStack

import numpy as np
import concourse.bass as bass
from concourse import mybir

F32 = mybir.dt.float32
F32R = mybir.dt.float32r
BF16 = mybir.dt.bfloat16
I32 = mybir.dt.int32
ALU = mybir.AluOpType
ACT = mybir.ActivationFunctionType
AX = mybir.AxisListType.X

P = 128
D = 1024
KD = D // P
SEQ = 512
LT = SEQ // P
CTX = 256
CT = CTX // P
NT = LT + CT
TOK = SEQ + CTX
W = 512
EPS = 1e-6
BIG = 1e30

RET_HEADS, RET_QK, RET_V = 4, 256, 512
DIL_SLOTS, DIL_GROUPS, HD = 8, 3, 64
DIL_STRIDE = 4
ROPE8 = 8
D_FF = 4096
PLE = 256
COL_RQ, COL_RK, COL_RV, COL_RG = 0, 1024, 2048, 4096
COL_DIL = 6144
COL_GATE = COL_DIL + 3 * DIL_GROUPS * DIL_SLOTS * HD

NA_HEADS = 16
STRIP = 32
BLOCKS = 4
GRID = 64
ROWS = SEQ // GRID

NA_LAG = 1
NA_BUFFERS = 2
ADA_COLS = [W, W // 2]
ADA_JOBS = [6 * D // n for n in ADA_COLS]

EXPERTS = 16
CAP_L, CAP_C = 2 * SEQ // EXPERTS, 2 * CTX // EXPERTS
SLOTS = CAP_L + CAP_C
D_EXP = 1024

RW_PAIRS = 8
CH = 64
RW_LEVELS = 6
RW_CHAINS = 4
RW_GROUPS = NT * 2 // RW_CHAINS
RW_STEPS = 2 * NT
RW_READ_STD = 3
RW_STAGES = 6
GN_EPS = 64e-5
RPB_PAD = 32
RING = 3
SLOT = KD * W
PIECE = 2 * W
PIECES_RAW, PIECES_HIGH = 7, 5
JOB_PIECES = D // P // 2
EXPERT_JOBS = 6
POOL_PIECES = (1, 3)
DVE_PIECES = (0, 2)
assert (PIECES_RAW + PIECES_HIGH) * PIECE == RING * SLOT


def constants():
    c = {}
    eye = np.eye(P, dtype=np.float64)
    c["ident"] = eye
    f = np.arange(P)
    c["ret_freq"] = (1.0 / (10000.0 ** (f / (P - 1.0))))[:, None]
    c["dil_freq"] = np.broadcast_to(500000.0 ** (-np.arange(0, 16, 2) / 16.0), (P, ROPE8))
    dec = np.zeros((P, RET_HEADS, SEQ))
    for h in range(RET_HEADS):
        g = np.log1p(-(2.0 ** (-5.0 - h)))
        dist = np.arange(SEQ)[None, :] - np.arange(P)[:, None]
        dec[:, h] = np.where(dist >= 0, np.exp(np.maximum(dist, 0) * g), 0.0) * RET_QK ** -0.5
    c["ret_decay"] = dec
    m = np.full((P, DIL_STRIDE, 6, P), -BIG)
    l = np.arange(P)
    for s in range(DIL_STRIDE):
        t = DIL_STRIDE * l + s
        for s2 in range(DIL_STRIDE):
            d = t[:, None] - (DIL_STRIDE * l + s2)[None, :]
            m[:, s, s2][(d >= 0) & (d <= 128)] = 0
        d = l[:, None] - l[None, :]
        m[:, s, 4][d >= 0] = 0
        m[:, s, 5][(d >= 0) & (d % 4 == 0)] = 0
    c["dil_mask"] = m
    m = np.full((P, 3, ROWS, STRIP), -BIG)
    cc = np.arange(P) % 16
    kk = np.arange(STRIP)[None, :]
    for n, j in enumerate((0, 1, 3)):
        qcol = 16 * j + cc
        lo = np.clip(qcol - 8, 0, GRID - 16) - np.clip(16 * j - 8, 0, GRID - STRIP)
        ok = (kk >= lo[:, None]) & (kk < lo[:, None] + 16)
        m[:, n][np.broadcast_to(ok[:, None, :], (P, ROWS, STRIP))] = 0
    c["na_mask"] = m
    c["slot_no"] = np.broadcast_to(np.arange(CAP_L), (P, CAP_L))
    a, b = np.arange(P)[:, None], np.arange(P)[None, :]
    same = a // CH == b // CH
    k = np.exp(-0.5)
    c["rw_sum"] = np.stack([(same & (a <= b)) * k, (same & (a >= b)) * k], 1)
    c["rw_sum_ex"] = np.stack([(same & (a < b)) * k, (same & (a > b)) * k], 1)
    c["rw_blocks"] = same
    c["rw_ind"] = np.stack([(f // CH == n) * k for n in range(2)], 1)
    c["rw_mask"] = np.stack([np.stack([same & (a < b), same & (a <= b)], 1), np.stack([same & (a > b), same & (a >= b)], 1)], 1)
    joins = np.zeros((P, 2, RW_LEVELS, P))
    for n in range(RW_LEVELS):
        half = 1 << n
        join = (a // (2 * half) == b // (2 * half)) & (a // half % 2 == 1) & (b // half % 2 == 0)
        joins[:, 0, n], joins[:, 1, n] = join, join.T
    c["rw_join"] = joins[:, :, 1:]
    c["rw_pairs"] = -np.stack([joins[:, :, 0], joins[:, ::-1, 0]], 2)
    return {k: np.ascontiguousarray(np.asarray(v, np.float32).reshape(P, -1)) for k, v in c.items()}


class Job:

    def __init__(self, number, bank, width, engine, count, before):
        self.number, self.bank, self.width = number, bank, width
        self.engine, self.count, self.before = engine, count, before


class JobPlan:

    def __init__(self):
        self.jobs, self.at, self.holder, self.taken = {}, 0, [None] * 8, {"act": 0, "dve": 0}

    def add(self, engine, *key, width=1):
        if width == 2 and self.at % 2:
            self.at += 1
        bank = self.at % 8
        before = [self.holder[bank + i] for i in range(width) if self.holder[bank + i]]
        self.taken[engine] += 1
        job = Job(len(self.jobs), bank, width, engine, self.taken[engine], before)
        for i in range(width):
            self.holder[bank + i] = job
        self.at += width
        assert key not in self.jobs, key
        self.jobs[key] = job

    def __getitem__(self, key):
        return self.jobs[key]


DIL_STEPS = [(g, kind) for g in range(DIL_GROUPS) for kind in range(3)]
DIL_TILES = DIL_SLOTS * DIL_STRIDE
TILES = [NT, LT]
NA_STEPS = 4 * NT
NA_UNITS = NA_HEADS * NT
NORMS = {"dil": LT, "mlp": LT, "ple": LT, "na": NT, "moe0": NT, "rw": NT, "moe1": LT}


def ada_beside_dil(i):
    return i // 3 if i % 3 == 0 and i // 3 < ADA_JOBS[0] else None


def ada_beside_na(i):
    return i // 4 if i % 4 == 3 and i // 4 < ADA_JOBS[1] else None


def plan_jobs():
    plan = JobPlan()

    def norm(use):
        for k in range(KD):
            plan.add("act", "turn", use, 0, k)
        if NORMS[use] == NT:
            for k in range(KD):
                plan.add("act", "turn", use, 1, k)

    norm("dil")
    for i in range(len(DIL_STEPS) + 1):
        if i < len(DIL_STEPS):
            for c in range(DIL_STRIDE):
                plan.add("act", "dil_proj", i, c)
        if i >= 1 and DIL_STEPS[i - 1][1] < 2:
            for c in range(DIL_STRIDE):
                plan.add("act", "dil_turn", i - 1, c)
    for i in range(DIL_TILES + 2):
        if i < DIL_TILES:
            plan.add("dve", "dil_score", i, width=2)
        if 1 <= i <= DIL_TILES:
            plan.add("act", "dil_pt", i - 1, width=2)
        if i >= 2:
            plan.add("dve", "dil_out", i - 2)
        if ada_beside_dil(i) is not None:
            plan.add("dve", "ada", 0, ada_beside_dil(i))
    for c in range(DIL_STRIDE):
        plan.add("act", "dil_ot", c)

    for h in range(RET_HEADS):
        for m in range(4):
            plan.add("dve", "ret_qk", h, m)
        for t in range(LT):
            plan.add("act", "ret_v", h, t)
        for t in range(LT):
            plan.add("act", "ret_g", h, t)
        if h >= 1:
            for f in range(4):
                plan.add("act", "ret_turn", h - 1, f)
        for j in range(LT):
            plan.add("dve", "ret_score", h, j)
        for t in range(LT):
            plan.add("dve", "ret_out", h, t)
    for f in range(4):
        plan.add("act", "ret_turn", RET_HEADS - 1, f)

    for n in range(2):
        for b in range(2):
            for f in range(4):
                plan.add("act", "mix_gate", b, n, f)
        for f in range(4):
            plan.add("dve", "mix_ret", n, f)
    for f in range(KD):
        plan.add("dve", "mix_dil", f)
    for n in range(2):
        for t in range(LT):
            plan.add("act", "mix_o", n, t)

    norm("mlp")
    for f in range(D_FF // P):
        plan.add("act", "up", f)
    for n in range(2):
        for t in range(LT):
            plan.add("act", "down", n, t)

    norm("ple")
    for d in range(PLE // P):
        plan.add("act", "ple_turn", d)
    for n in range(2):
        for t in range(LT):
            plan.add("act", "ple_gate", n, t)
    for n in range(2):
        for t in range(LT):
            plan.add("dve", "ple_in", n, t)

    plan.add("act", "ada_turn", 0)
    norm("na")
    for i in range(NA_STEPS + 2):
        if i < NA_STEPS:
            plan.add("act", "na_proj", i)
        if i >= 2:
            plan.add("act", "na_turn", i - 2)
    for n in range(2):
        for t in range(NT):
            plan.add("act", "na_v", n, t)
    for i in range(NA_UNITS + 2 * NA_LAG):
        if i < NA_UNITS:
            plan.add("dve", "na_score", i)
        if 0 <= i - NA_LAG < NA_UNITS:
            plan.add("act", "na_pt", i - NA_LAG)
        if i >= 2 * NA_LAG:
            plan.add("dve", "na_out", i - 2 * NA_LAG)
        if ada_beside_na(i) is not None:
            plan.add("dve", "ada", 1, ada_beside_na(i))
    for t in range(NT):
        plan.add("act", "na_ot", t, width=2)
    plan.add("act", "ada_turn", 1)
    for n in range(2):
        for t in range(NT):
            plan.add("dve", "na_o", n, t)
    plan_experts(plan, norm, 0)
    plan_recurrence(plan, norm)
    plan_experts(plan, norm, 1)
    return plan


def plan_experts(plan, norm, l):
    norm(f"moe{l}")
    plan.add("dve", "moe_logit", l)
    plan.add("dve", "moe_afft", l, width=2)
    plan.add("dve", "moe_slot", l)

    def gather(e):
        for half in range(2):
            plan.add("act", "moe_gather", l, e, half)
        plan.add("act", "moe_selt", l, e, width=2)
        plan.add("dve", "moe_gates", l, e)

    def scatter(e):
        for t in range(TILES[l]):
            for n in range(2):
                plan.add("dve", "moe_add", l, e, t, n)

    gather(0)
    for e in range(EXPERTS):
        for n in range(2):
            plan.add("act", "moe_h1", l, e, n)
            plan.add("dve", "moe_h3", l, e, n)
        if e >= 1:
            scatter(e - 1)
        plan.add("dve", "moe_ht", l, e, width=2)
        if e + 1 < EXPERTS:
            gather(e + 1)
        for n in range(2):
            plan.add("dve", "moe_y", l, e, n)
    scatter(EXPERTS - 1)


def expert_job(no):
    e, r = divmod(no, EXPERT_JOBS)
    l, e = divmod(e, EXPERTS)
    return ("moe_h1", l, e, r // 2) if r in (0, 2) else ("moe_h3", l, e, r // 2) if r in (1, 3) else ("moe_y", l, e, r - 4)


def expert_piece(a, no):
    job, q = divmod(no, JOB_PIECES)
    key, l, e, n = expert_job(job)
    w = a[{"moe_h1": "moe_w1", "moe_h3": "moe_w3", "moe_y": "moe_w2"}[key]][l, e]
    return w[2 * q * P:2 * (q + 1) * P, n * W:(n + 1) * W].rearrange("(k p) n -> p k n", p=P)


RW_RANK = {"w": 2 * CH, "a": 2 * CH, "g": P}


def plan_recurrence(plan, norm):
    norm("rw")
    for q in "rkv":
        for n in range(2):
            for t in range(LT if q == "r" else NT):
                plan.add("act", "rw_proj", q, n, t)
    for q in "wag":
        plan.add("act", "rw_low", q, width=2)
        for z in range(1 if q == "g" else 2):
            for n in range(2):
                for t in range(LT if q == "g" else NT):
                    plan.add("act" if q == "g" else "dve", "rw_high", q, z, n, t)

    def sums(p, z):
        plan.add("act", "rw_sum", p, z, width=2)
        plan.add("act", "rw_sum_ex", p, z, width=2)
        plan.add("act", "rw_end", p, z)

    def turn_factors(p, z):
        for x in range(4):
            plan.add("act", "rw_turn", p, z, x, width=2)

    def scan_u(p, i):
        for z in range(2):
            plan.add("dve", "rw_u", p, i, z)

    def scan_state(p, i):
        for z in range(2):
            if i + 1 < RW_STEPS:
                plan.add("dve", "rw_state", p, i, z)
            if rw_chunk(i, z)[0] < LT:
                plan.add("act", "rw_y", p, i, z)

    def scan(p, i):
        if p >= 0:
            scan_u(p, i)
            scan_state(p, i)

    for p in range(RW_PAIRS):
        sums(p, 0)
        scan(p - 1, RW_STEPS - 4)
        turn_factors(p, 0)
        sums(p, 1)
        scan(p - 1, RW_STEPS - 3)
        scan(p - 1, RW_STEPS - 2)
        turn_factors(p, 1)
        scan(p - 1, RW_STEPS - 1)
        for g in range(RW_GROUPS):
            for c in range(RW_CHAINS):
                plan.add("dve", "rw_ab", p, g, c, width=2)
                plan.add("dve", "rw_a", p, g, c, width=2)
            for c in range(RW_CHAINS):
                plan.add("act", "rw_gv", p, g, c)
            for lv in range(1, RW_LEVELS):
                i = rw_step_beside(g, lv)
                for c in range(RW_CHAINS):
                    plan.add("dve", "rw_x", p, g, c, lv)
                if i is not None:
                    scan_u(p, i)
                for c in range(RW_CHAINS):
                    plan.add("dve", "rw_join", p, g, c, lv)
                if i is not None:
                    scan_state(p, i)
            for c in range(RW_CHAINS):
                plan.add("act", "rw_tk", p, g, c)
            for c in range(RW_CHAINS):
                plan.add("act", "rw_tgv", p, g, c)
            if g == 0 and p >= 1:
                plan.add("act", "rw_ot", p - 1)
    for i in range(RW_STEPS - 4, RW_STEPS):
        scan(RW_PAIRS - 1, i)
    plan.add("act", "rw_ot", RW_PAIRS - 1)
    for n in range(2):
        for t in range(LT):
            plan.add("dve", "rw_o", n, t)


def rw_chunk(i, z):
    tile, c = divmod(i, 2)
    if z == 0:
        return (LT + tile, c) if tile < CT else (tile - CT, c)
    return (LT + CT - 1 - tile, 1 - c) if tile < CT else (LT - 1 - (tile - CT), 1 - c)


def rw_tile(g, c):
    return rw_chunk(2 * (2 * g + c // 2), c % 2)[0], c % 2


def rw_step_beside(g, lv):
    return 4 * (g - 1) + lv - 1 if g and lv <= 4 else None


def plan_weights(a):
    def square(w, n):
        return [(w[:, n * W:(n + 1) * W].rearrange("(k p) n -> p k n", p=P), 0, KD, W)]

    loads = []
    w_in = a["w_in"]
    for i, (g, kind) in enumerate(DIL_STEPS):
        c0 = COL_DIL + kind * DIL_GROUPS * W + g * W
        loads.append(("dil_proj", square(w_in[:, c0:c0 + W], 0), ("dil_proj", i, DIL_STRIDE - 1)))
    def modulation(l):
        for n in range(ADA_JOBS[l]):
            w = a["ada_w"][l][:, n * ADA_COLS[l]:(n + 1) * ADA_COLS[l]].rearrange("(k p) n -> p k n", p=P)
            loads.append(("ada", [(w, 0, KD, ADA_COLS[l])], ("ada", l, n)))

    modulation(0)
    for h in range(RET_HEADS):
        q, k = (w_in[:, c + h * RET_QK:c + (h + 1) * RET_QK].rearrange("(k p) n -> p k n", p=P) for c in (COL_RQ, COL_RK))
        loads.append(("ret_qk", [(q, 0, KD, RET_QK), (k, KD * RET_QK, KD, RET_QK)], ("ret_qk", h, 3)))
        loads.append(("ret_v", square(w_in[:, COL_RV:], h), ("ret_v", h, LT - 1)))
        loads.append(("ret_g", square(w_in[:, COL_RG:], h), ("ret_g", h, LT - 1)))
    for n in range(2):
        loads.append(("mix_gate", square(w_in[:, COL_GATE:], n), ("mix_gate", 0, n, 3)))
        loads.append(("mix_gate", square(w_in[:, COL_GATE + D:], n), ("mix_gate", 1, n, 3)))
        for half in range(2):
            loads.append(("mix_ret", square(a["w_ret_out"][half * D:(half + 1) * D], n), ("mix_ret", n, 3) if half else None))
    loads.append(("mix_dil", [(a["w_dil_out"].rearrange("(k p) n -> p k n", p=P), 0, 4, D)], ("mix_dil", KD - 1)))
    for n in range(2):
        loads.append(("mix_o", square(a["w_o"], n), ("mix_o", n, LT - 1)))
    for n in range(D_FF // W):
        loads.append(("up", square(a["w_up"], n), ("up", 4 * n + 3)))
    for n in range(2):
        for part in range(4):
            loads.append(("down", square(a["w_down"][part * D:(part + 1) * D], n), ("down", n, LT - 1) if part == 3 else None))
    for n in range(2):
        loads.append(("ple_gate", square(a["w_ple_gate"], n), ("ple_gate", n, LT - 1)))
    loads.append(("ple_in", [(a["w_ple_in"].rearrange("(k p) n -> p k n", p=P), 0, 2, D)], ("ple_in", 1, LT - 1)))
    for n in range(4):
        loads.append(("na_proj", square(a["na_w_qkv"], n), ("na_proj", (n + 1) * NT - 1)))
    for n in range(2):
        loads.append(("na_v", square(a["na_w_qkv"][:, 2 * D:], n), ("na_v", n, NT - 1)))
    modulation(1)
    for n in range(2):
        loads.append(("na_o", square(a["na_w_o"], n), ("na_o", n, NT - 1)))

    for q in "rkv":
        for n in range(2):
            loads.append(("rw_proj", square(a[f"rw_w_{q}"], n), ("rw_proj", q, n, (LT if q == "r" else NT) - 1)))
    for q in "wa":
        pieces = [(a[f"rw_{q}1"].rearrange("(k p) r -> p k r", p=P), 0, KD, 2 * CH),
                  (a[f"rw_{q}2"].rearrange("r (o d) -> r o d", o=1), KD * 2 * CH, 1, D)]
        pieces += [(a[f"rw_{q}0"][z].partition_broadcast(P).rearrange("p (o d) -> p o d", o=1), KD * 2 * CH + (1 + z) * D, 1, D) for z in range(2)]
        loads.append((f"rw_low_{q}", pieces, ("rw_high", q, 1, 1, NT - 1)))
    loads.append(("rw_low_g", [(a["rw_g1"].rearrange("(k p) r -> p k r", p=P), 0, KD, P),
                               (a["rw_g2"].rearrange("r (o d) -> r o d", o=1), KD * P, 1, D)], ("rw_high", "g", 0, 1, LT - 1)))
    for n in range(2):
        loads.append(("rw_o", square(a["rw_w_o"], n), ("rw_o", n, LT - 1)))
    return loads


COLUMNS = {}
for _name, _n in (("g_pre_mix", KD), ("b_gate_r", KD), ("b_gate_a", KD), ("g_pre_mlp", KD), ("g_pre_ple", KD),
                  ("norm_g", 4 * KD), ("na_q_g", 1), ("na_k_g", 1), ("rw_mix", 6 * KD), ("cond", 2 * KD)):
    COLUMNS[_name] = (sum(n for _, n in COLUMNS.values()), _n)
N_COLUMNS = sum(n for _, n in COLUMNS.values())


def build(nc, a, out, debug=None):
    plan = plan_jobs()
    loads = plan_weights(a)
    ctx = ExitStack()
    signals = {}

    def sem(name):
        if name not in signals:
            signals[name] = nc.alloc_semaphore(name)
        return signals[name]

    def sb(name, *shape, dt=F32):
        return ctx.enter_context(nc.sbuf_tensor(name, [P, *shape], dt))

    h = sb("h", NT, D)
    ring = sb("ring", RING, SLOT)
    ring_at = nc.sbuf_base - 4 * RING * SLOT
    ident = sb("ident", P)
    ring_flat = ring[:, :, :].rearrange("p a b -> p (a b)")
    ones = sb("ones", P)
    cols = sb("cols", N_COLUMNS)
    stats = sb("stats", 64)
    psum = [ctx.enter_context(nc.psum_tensor(f"bank{i}", [P, 2 * W], F32)) for i in range(4)]
    ARENA = 32768
    arena = sb("arena", ARENA)
    arena_at = nc.sbuf_base - 4 * ARENA

    def rounded(name, at, *shape):
        v = nc.alloc_sbuf_tensor_at(name, [P, int(np.prod(shape))], F32R, offset=at)[:, :]
        names = "abcd"[:len(shape)]
        return v.rearrange(f"p ({' '.join(names)}) -> p {' '.join(names)}", **dict(zip(names[1:], shape[1:])))

    class Carve:

        def __init__(self, at=0):
            self.at = at

        def take(self, *shape, dt=F32):
            n = int(np.prod(shape))
            assert self.at + n <= ARENA, (self.at, n)
            v = arena[:, self.at:self.at + n]
            self.at += n
            if dt != F32:
                v = v.bitcast(dt)
            names = "abcd"[:len(shape)]
            if len(shape) > 1:
                v = v.rearrange(f"p ({' '.join(names)}) -> p {' '.join(names)}", **dict(zip(names[1:], shape[1:])))
            return v

    def col(name, k=0):
        at, _ = COLUMNS[name]
        return cols[:, at + k:at + k + 1]

    def bank(job):
        lo = job.bank % 2 * W
        return psum[job.bank // 2][:, lo:lo + job.width * W]

    filled = sem("psum_filled")
    freed = {"act": sem("psum_freed_act"), "dve": sem("psum_freed_dve")}
    landed = [sem(f"weights_landed_{i}") for i in range(RING)]
    used = sem("weights_used")

    def full(eng, *key):
        eng.wait_ge(filled, plan[key].number + 1)
        return bank(plan[key])

    def taken(eng, *key):
        eng.wait_ge(freed[plan[key].engine], plan[key].count)

    def free(ins, *key):
        done[plan[key].engine] += 1
        assert done[plan[key].engine] == plan[key].count, key
        ins.then_inc(freed[plan[key].engine], 1)

    done = {"act": 0, "dve": 0, "pe": 0}

    n_pieces = 2 * EXPERTS * EXPERT_JOBS * JOB_PIECES
    piece_landed = [sem(f"piece_landed_{i}") for i in range(PIECES_RAW)]
    piece_used = sem("piece_used")
    piece_high = sem("piece_high")
    piece_low = {"dve": sem("piece_low_dve"), "pool": sem("piece_low_pool")}

    def raw_piece(i):
        return ring_flat[:, i % PIECES_RAW * PIECE:(i % PIECES_RAW + 1) * PIECE]

    low_pieces = rounded("low_pieces", ring_at, PIECES_RAW, PIECE)
    high_pieces = rounded("high_pieces", ring_at + 4 * PIECES_RAW * PIECE, PIECES_HIGH, PIECE)

    def low_piece(i):
        return low_pieces[:, i % PIECES_RAW, :]

    def high_piece(i):
        return high_pieces[:, i % PIECES_HIGH, :]

    def piece_free(eng, i):
        job, q = divmod(i, JOB_PIECES)
        if q == JOB_PIECES - 1:
            full(eng, *expert_job(job))
        else:
            eng.wait_ge(piece_used, (JOB_PIECES - 1) * job + q + 1)

    def piece_split(eng, i):
        job, q = divmod(i, JOB_PIECES)
        name, own = ("pool", POOL_PIECES) if q in POOL_PIECES else ("dve", DVE_PIECES)
        eng.wait_ge(piece_low[name], len(own) * job + own.index(q) + 1)

    def low_part(eng, engine, name, i):
        eng.wait_ge(piece_high, i + 1)
        engine.tensor_tensor(low_piece(i), raw_piece(i), high_piece(i).bitcast(F32), ALU.subtract).then_inc(piece_low[name], 1)

    m = Carve()
    uT = m.take(KD, SEQ)
    yaT = h[:, LT:NT, :].rearrange("p t (f c) -> p (t f) c", f=2)
    ret_cos, ret_sin = m.take(SEQ), m.take(SEQ)
    dil_cos, dil_sin = m.take(DIL_STRIDE, ROPE8), m.take(DIL_STRIDE, ROPE8)
    part = m.at
    n = Carve(part)
    ang, turns, angs = n.take(544), n.take(544), n.take(544)
    pos_i, pos_f = n.take(SEQ, dt=I32), n.take(SEQ)
    pos_ci, pos_cf = n.take(DIL_STRIDE, dt=I32), n.take(DIL_STRIDE)
    ret_freq, dil_freq = n.take(1), n.take(ROPE8)
    n = Carve(part)
    dil_tmp = n.take(DIL_STRIDE, W)
    dil_rot = n.take(4, 2, DIL_SLOTS, ROPE8)
    dil_o = dil_tmp
    qT, kT = n.take(12, SEQ), n.take(12, SEQ)
    v_at = n.at
    vR = n.take(DIL_STRIDE, 3 * W)
    xn_dil = Carve(v_at).take(LT, D)
    dil_mask = n.take(DIL_STRIDE, 6 * P)
    dil_s = n.take(2, 6 * P)
    dil_p = n.take(2, 6 * P)
    n = Carve(part)
    yrT = n.take(16, SEQ)
    mix_from = n.at
    rqT, rkT = n.take(2, SEQ), n.take(2, SEQ)
    rot_a, rot_b = n.take(SEQ), n.take(SEQ)
    rv, rg, rs, ry = (n.take(LT, W) for _ in range(4))
    decay = n.take(RET_HEADS, SEQ)
    n = Carve(mix_from)
    gate_r, gate_a, mixT = n.take(KD, SEQ), n.take(KD, SEQ), n.take(KD, SEQ)
    mix_t = n.take(SEQ)
    F_mix = n.take(LT, D)
    gb_mix = n.take(D)
    n = Carve()
    vT = n.take(KD, SEQ)
    xn_mlp = n.take(LT, D)
    ffT = n.take(D_FF // P, SEQ)
    F_mlp = n.take(LT, D)
    gb_mlp = n.take(D)
    n = Carve()
    wT = n.take(KD, SEQ)
    xn_ple = n.take(LT, D)
    pR, pT = n.take(LT, PLE), n.take(PLE // P, SEQ)
    gate_p = n.take(LT, D)
    F_ple = n.take(LT, D)
    gb_ple = n.take(D)
    b_ple = n.take(D)
    junk = sb("junk", D)
    cond = sb("cond", 2, KD)
    mod = sb("mod", 2, 2, 6, KD)
    mod_a = sb("mod_a", 2, 2, 2, KD)
    n = Carve()
    xn_na, hT_na = n.take(NT, D), n.take(KD, TOK)
    mod_rows = [n.take(P)]
    n = Carve()
    naq = n.take(KD, TOK)
    n.take(KD, TOK)
    na_o = hT_na.rearrange("p k t -> p (k t)").rearrange("p (t d) -> p t d", d=D)
    nak = n.take(KD, TOK)
    na_vs = n.take(2 * BLOCKS, D)
    na_vc = n.take(CT, D)
    na_v = Carve(n.at).take(LT, W)
    na_s, na_p = n.take(2, W), n.take(2, W)
    na_bias = [n.take(4, 2 * P), junk[:, :].rearrange("p (a b) -> p a b", a=4)]
    ada_rows = [[junk[0:2, b * W:(b + 1) * W] for b in range(2)], [n.take(ADA_COLS[1])[0:2, :]]]
    na_mask = n.take(3, 2 * P)
    mod_rows.append(na_s[:, 0, 0:P])
    at_max, at_neg, at_sum, at_rec = (stats[:, NA_BUFFERS * i:NA_BUFFERS * (i + 1)] for i in range(4))
    na_oT = naq
    na_gate = nak.rearrange("p k t -> p (k t)")[:, 0:2 * D].rearrange("p (s d) -> p s d", d=D)
    na_t = nak.rearrange("p k t -> p (k t)")[:, 2 * D:3 * D].rearrange("p (s d) -> p s d", d=W)
    def half_size(*shape):
        v = n.take(int(np.prod(shape)) // 2).bitcast(BF16)
        names = "abcd"[:len(shape)]
        return v.rearrange(f"p ({' '.join(names)}) -> p {' '.join(names)}", **dict(zip(names[1:], shape[1:])))

    n = Carve()
    xn_moe = n.take(NT, D)
    hT_moe = n.take(KD, TOK)
    x_part = [half_size(NT, D) for _ in range(3)]
    router = n.take(KD, EXPERTS)
    logit, aff = n.take(NT, EXPERTS), n.take(NT, EXPERTS)
    aff_part = half_size(NT, EXPERTS, 3)
    ident_b = half_size(P)
    top8, slot, slot_no = n.take(8), n.take(NT, EXPERTS), n.take(CAP_L)
    gates = n.take(2)
    sel = [half_size(NT, SLOTS) for _ in range(2)]
    def take_rounded(name, *shape):
        n.at = -(-n.at // 8) * 8
        return rounded(name, arena_at + 4 * n.at, *shape), n.take(*shape)

    x_high, _ = take_rounded("x_high", 2, KD, SLOTS)
    x_low, x_whole = take_rounded("x_low", 2, KD, SLOTS)
    hid_high, _ = take_rounded("hid_high", KD, SLOTS)
    hid_low, _ = take_rounded("hid_low", KD, SLOTS)
    keep = n.at
    selT, _ = take_rounded("chosen", 2, TOK)
    s1 = n.take(D)
    acc = hT_moe.rearrange("p k t -> p (k t)").rearrange("p (t d) -> p t d", d=D)
    n = Carve(keep)
    affT, workT, sumT = n.take(TOK), n.take(TOK), n.take(TOK)
    n = Carve(0)
    y_high, _ = take_rounded("y_high", 2, D)
    y_low, _ = take_rounded("y_low", 2, D)
    moe_gate = n.take(2, D)
    n = Carve()
    hT_rw = n.take(KD, TOK)
    xx = n.take(KD, TOK)
    xs = [n.take(KD, TOK), n.take(KD, TOK)]
    xn_rw = xs[1].rearrange("p k t -> p (k t)").rearrange("p (t d) -> p t d", d=D)
    lowT = n.take(TOK)
    staging = n.take(RW_STAGES, W)
    RW_IN, at = {}, 0
    for q in ("r", "g", "k", "v", "w0", "w1", "a0", "a1"):
        nt = LT if q in "rg" else NT
        RW_IN[q] = [ring_flat[:, b * 5632 + at:b * 5632 + at + nt * P].rearrange("p (t d) -> p t d", d=P) for b in range(2)]
        at += nt * P
    assert at == 5632
    n = Carve()
    c_sum, c_sum_ex, c_ind = n.take(2, P), n.take(2, P), n.take(2)
    c_mask, c_join, c_pairs = n.take(2, 2, P), n.take(2, RW_LEVELS - 1, P), n.take(2, 2, P)
    c_blocks = n.take(P)
    rw_rows = n.take(2, 5, P)
    kh = [n.take(NT, P) for _ in range(2)]
    bh, th = ([[n.take(NT, P) for _ in range(2)] for _ in range(2)] for _ in range(2))
    xT = [n.take(2 * TOK + 2 * SEQ) for _ in range(2)]
    TT = [n.take(TOK) for _ in range(2)]
    KT, BT = ([x[:, lo:lo + TOK] for x in xT] for lo in (0, TOK + 2 * SEQ))
    RT = [[x[:, TOK + b * SEQ:TOK + (b + 1) * SEQ] for x in xT] for b in range(2)]
    tkT, tgv = ([n.take(NT, P) for _ in range(2)] for _ in range(2))
    rbT, rtT = ([n.take(LT, 2, CH) for _ in range(2)] for _ in range(2))
    w_end = [[n.take(RW_STEPS) for _ in range(2)] for _ in range(2)]
    state, u = [n.take(2, P) for _ in range(2)], [n.take(P) for _ in range(2)]
    zT_hi = n.take(4, SEQ)
    temp = n.at
    e_neg, e_pos, e_ex, kk, rw_t = (n.take(NT, P) for _ in range(5))
    n = Carve(temp)
    aT, gT = ([n.take(2, P) for _ in range(RW_CHAINS)] for _ in range(2))
    gv = [n.take(P) for _ in range(RW_CHAINS)]
    inv = [n.take(2, 2, P) for _ in range(RW_CHAINS)]
    xl = [n.take(2, P) for _ in range(RW_CHAINS)]
    zT_lo = h[:, LT:NT, :].rearrange("p t (f c) -> p (t f) c", f=2)
    yz = [junk[:, z * SEQ:(z + 1) * SEQ].rearrange("p (t d) -> p t d", d=P) for z in range(2)]
    yd = [ring_flat[:, RING * SLOT - (z + 1) * SEQ:RING * SLOT - z * SEQ].rearrange("p (t d) -> p t d", d=P) for z in range(2)]
    rw_s = sb("rw_s", 48)
    n = Carve(ARENA - 4 * SEQ - 2 * D - D)
    rw_gate, rw_ot = n.take(D), n.take(2, W)

    def zT(f):
        return zT_lo[:, f, :] if f < 4 else zT_hi[:, f - 4, :]

    mod_dram = nc.dram_tensor("mod_dram", [2, 2, 6 * D], F32).ap()
    spill = {q: nc.dram_tensor(f"spill_{q}", [LT if q in "rg" else NT, P, D], F32).ap()
             for q in ("r", "g", "k", "v", "w0", "w1", "a0", "a1")}
    rpb_strip = nc.dram_tensor("rpb_strip", [NA_HEADS, 3, 16, 15 * STRIP], F32).ap()

    norm_of = {"dil": (xn_dil, uT), "mlp": (xn_mlp, vT), "ple": (xn_ple, wT), "na": (xn_na, hT_na), "moe0": (xn_moe, hT_moe),
               "rw": (xn_rw, hT_rw), "moe1": (xn_moe, hT_moe)}
    norm_mod = {"na": (0, 0), "moe0": (0, 1), "rw": (1, 0), "moe1": (1, 1)}

    def modulation(use, s, k):
        l, n = norm_mod[use]
        return mod_a[:, l, s, n, k:k + 1], mod[:, l, s, 3 * n, k:k + 1]

    norm_scale = {"dil": "g_pre_mix", "mlp": "g_pre_mlp", "ple": "g_pre_ple"}
    USES = list(NORMS)
    tiles_before = {u: sum(NORMS[x] for x in USES[:i]) for i, u in enumerate(USES)}
    POSTS = ["mix", "mlp", "ple"]
    post_of = {"mix": (F_mix, gb_mix), "mlp": (F_mlp, gb_mlp), "ple": (F_ple, gb_ple)}
    last_job = {"mix": "mix_o", "mlp": "down", "ple": "ple_in"}

    def h_ready(eng, use, t):
        i = USES.index(use)
        if i == 0:
            eng.wait_ge(sem("x_landed"), 16)
        elif use == "na" and t >= LT:
            eng.wait_ge(sem("ctx_landed"), 16)
        elif i <= len(POSTS):
            eng.wait_ge(sem("post_added"), (i - 1) * LT + t + 1)
        elif use == "moe0":
            eng.wait_ge(sem("na_added"), 2 * NT)
        elif use == "rw":
            eng.wait_ge(sem("moe_added"), t + 1)
        else:
            eng.wait_ge(sem("rw_added"), LT + t + 1)

    strip0 = [int(np.clip(16 * j - 8, 0, GRID - STRIP)) for j in range(BLOCKS)]

    def spilled_jobs():
        for q in "rkv":
            for n in range(2):
                for t in range(LT if q == "r" else NT):
                    yield q, n, t, ("rw_proj", q, n, t)
        for q in "wag":
            for z in range(1 if q == "g" else 2):
                for n in range(2):
                    for t in range(LT if q == "g" else NT):
                        yield (q if q == "g" else f"{q}{z}"), n, t, ("rw_high", q, z, n, t)

    def chains():
        for i in range(RW_PAIRS * RW_GROUPS * RW_CHAINS):
            yield (i, i // (RW_GROUPS * RW_CHAINS), i // RW_CHAINS % RW_GROUPS, i % RW_CHAINS)

    def last_unit(p, g, c):
        i = p * RW_GROUPS + g - 1
        return (i // RW_GROUPS, i % RW_GROUPS, c) if i >= 0 else None

    low_slot = {q: [name for name, _, _ in loads].index(f"rw_low_{q}") % RING for q in "wa"}

    def halves(x, lv, z, transposed=False):
        b = 1 << lv
        v = x.rearrange("p h (a two b) -> p h a two b", two=2, b=b)
        return v[:, :, :, (z + transposed) % 2, :]

    block = ctx.enter_context(nc.Block())
    first_rw, first_rw_o = ([name for name, _, _ in loads].index(x) for x in ("rw_proj", "rw_o"))

    @block.sync
    def _(sp):
        sp.dma_start(h[:, 0:LT, :], a["x"].rearrange("(t p) d -> p t d", p=P)).then_inc(sem("x_landed"), 16)
        sp.wait_ge(sem("const_landed"), 16 * 6)
        goes_on = 0

        def experts(l):
            n = n_pieces // 2
            full(sp, *(("na_o", 1, NT - 1) if l == 0 else ("rw_o", 1, LT - 1)))
            for i in range(l * n, (l + 1) * n):
                if i >= l * n + PIECES_RAW:
                    piece_free(sp, i - PIECES_RAW)
                sp.dma_start(raw_piece(i).rearrange("p (k n) -> p k n", n=W), expert_piece(a, i)).then_inc(piece_landed[i % PIECES_RAW], 16)

        for i, (_, pieces, _) in enumerate(loads):
            if i == first_rw:
                experts(0)
            if first_rw <= i < first_rw + RING:
                full(sp, "moe_y", 0, EXPERTS - 1, 1)
            elif i >= RING:
                last = loads[i - RING][2]
                if last:
                    full(sp, *last)
                else:
                    goes_on += 1
                    sp.wait_ge(used, goes_on)
            if i == first_rw_o:
                taken(sp, "rw_ot", RW_PAIRS - 1)
            for src, at, k, n in pieces:
                dst = ring[:, i % RING, at:at + k * n].rearrange("p (k n) -> p k n", n=n)
                sp.dma_start(dst, src).then_inc(landed[i % RING], 16)
        experts(1)
        for t in range(LT):
            sp.wait_ge(sem("moe_added"), NT + t + 1)
            sp.dma_start(out[t * P:(t + 1) * P, :], h[:, t, :]).then_inc(sem("out_stored"), 16)
        sp.wait_ge(sem("out_stored"), 16 * LT)

    slot_count, landed_at = [0] * RING, []
    for i, (_, pieces, _) in enumerate(loads):
        slot_count[i % RING] += 16 * len(pieces)
        landed_at.append(slot_count[i % RING])

    @block.gpsimd
    def _(pool):
        def load(dst, name, signal):
            pool.dma_start(dst, a[name]).then_inc(sem(signal), 16)

        nc.gpsimd.memset(ones[:, :], 1.0).then_inc(sem("ones_set"), 1)
        load(ident[:, :], "ident", "const_landed")
        load(cols[:, :], "cols", "const_landed")
        load(pos_i, "pos_row", "const_landed")
        load(pos_ci, "pos_col", "const_landed")
        load(ret_freq, "ret_freq", "const_landed")
        load(dil_freq, "dil_freq", "const_landed")
        load(dil_mask.rearrange("p a b -> p (a b)"), "dil_mask", "mask_landed")
        def load_bias(l, n):
            rows = ada_rows[l][n % len(ada_rows[l])]
            pool.dma_start(rows, a["ada_b"][l, n * ADA_COLS[l]:(n + 1) * ADA_COLS[l]].partition_broadcast(2)).then_inc(sem(f"ada_bias_landed_{n % len(ada_rows[l])}"), 16)

        def store_mod(l, n):
            ways = len(ada_rows[l])
            taken(pool, "ada", l, n)
            pool.dma_start(mod_dram[l][:, n * ADA_COLS[l]:(n + 1) * ADA_COLS[l]], ada_rows[l][n % ways]).then_inc(sem("mod_stored"), 16)
            pool.wait_ge(sem("mod_stored"), 16 * (l * ADA_JOBS[0] + n + 1))
            if n + ways < ADA_JOBS[l]:
                load_bias(l, n + ways)

        def load_mod(l):
            pool.dma_start(mod_rows[l][0:96, :], mod_dram[l].rearrange("s (r c) -> (s r) c", c=P)).then_inc(sem("mod_rows_landed"), 16)

        load_bias(0, 0)
        load_bias(0, 1)
        for n in range(ADA_JOBS[0]):
            store_mod(0, n)
        taken(pool, "dil_ot", DIL_STRIDE - 1)
        load(decay.rearrange("p a b -> p (a b)"), "ret_decay", "decay_landed")
        for u in POSTS:
            if u == "mix":
                taken(pool, "ret_turn", RET_HEADS - 1, 3)
            else:
                pool.wait_ge(sem("post_added"), POSTS.index(u) * LT)
            pool.dma_start(post_of[u][1], a[f"g_post_{u}"].partition_broadcast(P)).then_inc(sem("post_gain_landed"), 16)
            if u == "ple":
                pool.dma_start(pR, a["p"].rearrange("(t p) d -> p t d", p=P)).then_inc(sem("ple_landed"), 16)
                pool.dma_start(b_ple[0:1, :], a["b_ple_gate"].rearrange("(o d) -> o d", o=1)).then_inc(sem("ple_landed"), 16)
            if u == "mlp":
                pool.dma_start(h[:, LT:NT, :], a["ctx"].rearrange("(t p) d -> p t d", p=P)).then_inc(sem("ctx_landed"), 16)
        for n, j in enumerate((0, 1, 3)):
            off = int(np.clip(16 * j - 8, 0, GRID - STRIP)) - 16 * j
            for cc in range(16):
                lo = off - cc + 15 + RPB_PAD
                pool.dma_start(rpb_strip[:, n, cc, :].rearrange("h (r k) -> h r k", k=STRIP),
                               a["na_rpb"][:, :, lo:lo + STRIP]).then_inc(sem("strip_stored"), 16)
        pool.wait_ge(sem("post_added"), 3 * LT)
        load_mod(0)
        taken(pool, "ada_turn", 0)
        for n in range(2):
            for t in range(LT):
                taken(pool, "na_v", n, t)
                for j in range(BLOCKS):
                    for r in range(2):
                        to = (2 * t + r) % 4 * STRIP
                        pool.dma_start(na_vs[to:to + STRIP, 2 * j + t // 2, n * W:(n + 1) * W],
                                       na_v[r * GRID + strip0[j]:r * GRID + strip0[j] + STRIP, t, :]).then_inc(sem("na_strips_landed"), 16)
        pool.dma_start(na_mask.rearrange("p a b -> p (a b)"), a["na_mask"]).then_inc(sem("na_mask_landed"), 16)
        for b in range(2):
            nc.gpsimd.memset(na_bias[b][:, 3, :], 0.0).then_inc(sem("na_zeroed"), 1)
        load_bias(1, 0)
        pool.wait_ge(sem("strip_stored"), 16 * 48)
        pool.wait_ge(sem("na_mask_landed"), 16)
        def load_rpb(hd):
            if hd >= 2:
                taken(pool, "na_score", (hd - 1) * NT - 1)
            for r in range(ROWS):
                pool.dma_start(na_bias[hd % 2][16 * r:16 * r + 16, 0:3, :],
                               rpb_strip[hd, :, :, (7 - r) * STRIP:(15 - r) * STRIP].rearrange("n c k -> c n k")
                               ).then_inc(sem(f"na_bias_landed_{hd % 2}"), 16)

        load_rpb(0)
        for i in range(NA_UNITS):
            if i % NT == 0 and i // NT + 1 < NA_HEADS:
                load_rpb(i // NT + 1)
            if ada_beside_na(i) is not None:
                store_mod(1, ada_beside_na(i))
        taken(pool, "na_out", NA_UNITS - 1)
        load_mod(1)
        for s in range(2):
            pool.dma_start(na_gate[:, s, :], mod_dram[0, s, 2 * D:3 * D].partition_broadcast(P)).then_inc(sem("na_gate_landed"), 16)

        def experts(l):
            use = f"moe{l}"
            nt = TILES[l]
            h_ready(pool, use, nt - 1)
            pool.dma_start(router, a["moe_router"][l].rearrange("(k p) e -> p k e", p=P)).then_inc(sem("moe_landed"), 16)
            pool.dma_start(slot_no, a["slot_no"]).then_inc(sem("moe_landed"), 16)
            full(pool, "turn", use, int(nt == NT), KD - 1)
            for part in range(2):
                for t in range(nt):
                    pool.wait_ge(sem("moe_part"), 3 * (l * NT) + part * nt + t + 1)
                    if part:
                        pool.wait_ge(sem("moe_rest"), 2 * (l * NT) + t + 1)
                    nc.gpsimd.tensor_tensor(xn_moe[:, t, :], xn_moe[:, t, :], x_part[part][:, t, :], ALU.subtract).then_inc(sem("moe_rest"), 1)
            pool.wait_ge(sem("moe_part"), 3 * (l * NT + nt))
            for s in range(2):
                pool.dma_start(moe_gate[:, s, :], mod_dram[l, s, 5 * D:6 * D].partition_broadcast(P)).then_inc(sem("moe_gate_landed"), 16)
            for job in range(l * EXPERTS * EXPERT_JOBS, (l + 1) * EXPERTS * EXPERT_JOBS):
                for q in POOL_PIECES:
                    low_part(pool, nc.gpsimd, "pool", job * JOB_PIECES + q)

        experts(0)
        squashed = 0
        uses = [0] * RW_STAGES
        for i, (q, n, t, key) in enumerate(spilled_jobs()):
            if q[0] in "wa":
                squashed += 1
                pool.wait_ge(sem("rw_squashed"), squashed)
            else:
                taken(pool, *key)
            pool.dma_start(spill[q][t, :, n * W:(n + 1) * W], staging[:, i % RW_STAGES, :]).then_inc(sem(f"spilled_{i % RW_STAGES}"), 16)
            uses[i % RW_STAGES] += 16
        for i in range(RW_STAGES):
            pool.wait_ge(sem(f"spilled_{i}"), uses[i])
        taken(pool, "rw_low", "g")
        for dst, name in ((c_sum, "rw_sum"), (c_sum_ex, "rw_sum_ex"), (c_ind, "rw_ind"), (c_mask, "rw_mask"), (c_join, "rw_join"),
                          (c_pairs, "rw_pairs"), (c_blocks, "rw_blocks")):
            pool.dma_start(dst if len(dst.shape) == 2 else dst.rearrange("p a b -> p (a b)") if len(dst.shape) == 3 else
                           dst.rearrange("p a b c -> p (a b c)"), a[name]).then_inc(sem("rw_const_landed"), 16)

        def load_pair(p):
            for q in RW_IN:
                pool.dma_start(RW_IN[q][p % 2], spill[q][:, :, p * P:(p + 1) * P].rearrange("t p d -> p t d")
                               ).then_inc(sem(f"rw_in_landed_{p % 2}"), 16)
            pool.dma_start(rw_rows[:, p % 2], a["rw_rows"][:, p * P:(p + 1) * P].partition_broadcast(P)
                           ).then_inc(sem(f"rw_in_landed_{p % 2}"), 16)

        load_pair(0)
        load_pair(1)
        pool.wait_ge(sem("rw_const_landed"), 16 * 7)
        for i, p, g, c in chains():
            z = c % 2
            pool.wait_ge(sem("rw_at"), i + 1)
            if last_unit(p, g, c):
                full(pool, "rw_tgv", *last_unit(p, g, c))
            M = inv[c][:, :, 1, :]
            nc.gpsimd.tensor_tensor(M, aT[c], c_pairs[:, z, 1:2, :].to_broadcast([P, 2, P]), ALU.mult).then_inc(sem("rw_pool_step"), 1)
            pool.wait_ge(sem("rw_pool_step"), i + 1)
            nc.gpsimd.tensor_tensor(M, M, ident[:, :].unsqueeze(1).to_broadcast([P, 2, P]), ALU.add).then_inc(sem("rw_off"), 1)
            if (g, c) == (0, RW_CHAINS - 1) and 1 <= p < RW_PAIRS - 1:
                taken(pool, "rw_ot", p - 1)
                load_pair(p + 1)
        taken(pool, "rw_ot", RW_PAIRS - 1)
        pool.dma_start(rw_gate, mod_dram[1, 0, 2 * D:3 * D].partition_broadcast(P)).then_inc(sem("rw_gate_landed"), 16)
        experts(1)

    @block.scalar
    def _(act):
        A = nc.scalar.activation
        act_step = [0]

        def link(ins):
            act_step[0] += 1
            ins.then_inc(sem("act_step"), 1)
            act.wait_ge(sem("act_step"), act_step[0])

        def norm(use):
            xn, dst = norm_of[use]
            t0, nt = tiles_before[use], NORMS[use]
            for t in range(nt):
                h_ready(act, use, t)
                A(xn[:, t, :], h[:, t, :], ACT.Square, accum_out=stats[:, t:t + 1]).then_inc(sem("norm_squared"), 1)
            act.wait_ge(sem("norm_var"), USES.index(use) + 1)
            A(stats[:, 16:16 + nt], stats[:, 8:8 + nt], ACT.Sqrt).then_inc(sem("norm_std"), 1)
            if use in norm_mod:
                act.wait_ge(sem("modulation"), norm_mod[use][0] + 1)
                for s in range(1 if nt == LT else 2):
                    for k in range(KD):
                        scale, shift = modulation(use, s, k)
                        n0, n1 = (0, SEQ) if s == 0 else (SEQ, TOK)
                        ps = full(act, "turn", use, s, k)[:, 0:n1 - n0]
                        free(A(dst[:, k, n0:n1], ps, ACT.Identity, bias=shift, scale=scale), "turn", use, s, k)
                return
            for k in range(KD):
                ps = full(act, "turn", use, 0, k)
                free(A(dst[:, k, 0:SEQ], ps, ACT.Copy, scale=col(norm_scale[use], k)), "turn", use, 0, k)

        def post_square(use, t):
            F, _ = post_of[use]
            taken(act, last_job[use], 1, t)
            if t:
                act.wait_ge(sem("post_squared"), POSTS.index(use) * LT + t)
            A(junk[:, :], F[:, t, :], ACT.Square, accum_out=stats[:, 24 + t:25 + t]).then_inc(sem("post_squared"), 1)

        def post(use):
            act.wait_ge(sem("post_var"), POSTS.index(use) + 1)
            A(stats[:, 32:36], stats[:, 28:32], ACT.Sqrt).then_inc(sem("post_std"), 1)

        norm("dil")
        act.wait_ge(sem("angle_reduced"), 1)
        A(angs, ang, ACT.Sin)
        A(turns, ang, ACT.Sin, scale=0.5).then_inc(sem("angle_sin"), 1)
        A(cond[:, :, :], cols[:, COLUMNS["cond"][0]:COLUMNS["cond"][0] + 2 * KD].rearrange("p (s k) -> p s k", s=2),
          ACT.Silu).then_inc(sem("cond_ready"), 1)
        act.wait_ge(sem("angles_used"), 1)

        for i in range(len(DIL_STEPS) + 1):
            if i < len(DIL_STEPS):
                g, kind = DIL_STEPS[i]
                for c in range(DIL_STRIDE):
                    ps = full(act, "dil_proj", i, c)
                    if kind == 2:
                        dst = vR[:, c, g * W:(g + 1) * W]
                    else:
                        dst = dil_tmp[:, c, :]
                        if i >= 1 and DIL_STEPS[i - 1][1] < 2:
                            full(act, "dil_turn", i - 1, c)
                    free(A(dst, ps, ACT.Copy), "dil_proj", i, c)
            if i >= 1 and DIL_STEPS[i - 1][1] < 2:
                g, kind = DIL_STEPS[i - 1]
                for c in range(DIL_STRIDE):
                    ps = full(act, "dil_turn", i - 1, c).rearrange("p (f l) -> p f l", f=4)
                    dst = (qT, kT)[kind][:, 4 * g:4 * g + 4, c * P:(c + 1) * P]
                    free(A(dst, ps, ACT.Copy), "dil_turn", i - 1, c)
        for i in range(DIL_TILES + 1):
            if i < DIL_TILES:
                act.wait_ge(sem("dil_max"), i + 1)
                A(dil_s[:, i % 2, :], dil_s[:, i % 2, :], ACT.Exp, bias=stats[:, 40 + i % 2:41 + i % 2],
                  accum_out=stats[:, 42 + i % 2:43 + i % 2]).then_inc(sem("dil_exp"), 1)
            if i >= 1:
                ps = full(act, "dil_pt", i - 1)[:, 0:6 * P]
                if i >= 3:
                    full(act, "dil_out", i - 3)
                free(A(dil_p[:, (i - 1) % 2, :], ps, ACT.Copy), "dil_pt", i - 1)
        for c in range(DIL_STRIDE):
            ps = full(act, "dil_ot", c).rearrange("p (f l) -> p f l", f=4)
            free(A(yaT[:, :, c::DIL_STRIDE], ps, ACT.Copy), "dil_ot", c)

        def ret_turn(hd):
            for f in range(4):
                ps = full(act, "ret_turn", hd, f)
                free(A(yrT[:, 4 * hd + f, :], ps, ACT.Copy), "ret_turn", hd, f)

        for hd in range(RET_HEADS):
            for t in range(LT):
                free(A(rv[:, t, :], full(act, "ret_v", hd, t), ACT.Copy), "ret_v", hd, t)
            if hd >= 1:
                taken(act, "ret_out", hd - 1, LT - 1)
            for t in range(LT):
                free(A(rg[:, t, :], full(act, "ret_g", hd, t), ACT.Silu), "ret_g", hd, t)
            if hd >= 1:
                ret_turn(hd - 1)
            for t in range(LT):
                ps = full(act, "ret_out", hd, t)
                if hd + t:
                    act.wait_ge(sem("ret_squared"), hd * LT + t)
                A(junk[:, 0:W], ps, ACT.Square, accum_out=stats[:, 44 + t:45 + t]).then_inc(sem("ret_squared"), 1)
            act.wait_ge(sem("ret_var"), hd + 1)
            A(stats[:, 52:56], stats[:, 48:52], ACT.Sqrt).then_inc(sem("ret_std"), 1)
        ret_turn(RET_HEADS - 1)

        for n in range(2):
            for b, (dst, bias) in enumerate(((gate_r, "b_gate_r"), (gate_a, "b_gate_a"))):
                for f in range(4):
                    ps = full(act, "mix_gate", b, n, f)
                    free(A(dst[:, 4 * n + f, :], ps, ACT.Sigmoid, bias=col(bias, 4 * n + f)), "mix_gate", b, n, f)
        for n in range(2):
            for t in range(LT):
                free(A(F_mix[:, t, n * W:(n + 1) * W], full(act, "mix_o", n, t), ACT.Copy), "mix_o", n, t)
                if n == 1:
                    post_square("mix", t)
        post("mix")

        norm("mlp")
        for f in range(D_FF // P):
            ps = full(act, "up", f)
            ins = A(ffT[:, f, :], ps, ACT.Relu)
            free(ins, "up", f)
            taken(act, "up", f)
            A(ffT[:, f, :], ffT[:, f, :], ACT.Square).then_inc(sem("ff_squared"), 1)
        for n in range(2):
            for t in range(LT):
                free(A(F_mlp[:, t, n * W:(n + 1) * W], full(act, "down", n, t), ACT.Copy), "down", n, t)
                if n == 1:
                    post_square("mlp", t)
        post("mlp")

        norm("ple")
        for d in range(PLE // P):
            free(A(pT[:, d, :], full(act, "ple_turn", d), ACT.Copy), "ple_turn", d)
        for n in range(2):
            for t in range(LT):
                free(A(gate_p[:, t, n * W:(n + 1) * W], full(act, "ple_gate", n, t), ACT.Sigmoid), "ple_gate", n, t)
        for t in range(LT):
            post_square("ple", t)
        post("ple")

        def turn_mod(l):
            ps = full(act, "ada_turn", l)[:, 0:96]
            free(A(mod[:, l].rearrange("p s j k -> p (s j k)"), ps, ACT.Copy), "ada_turn", l)

        turn_mod(0)
        norm("na")
        for i in range(NA_STEPS + 2):
            if i < NA_STEPS:
                if i >= 2:
                    full(act, "na_turn", i - 2)
                ps = full(act, "na_proj", i)
                A(na_p[:, i % 2, :], ps, ACT.Square).then_inc(sem("na_squared"), 1)
                free(A(na_s[:, i % 2, :], ps, ACT.Copy), "na_proj", i)
                act.wait_ge(sem("na_var"), i + 1)
                A(stats[:, 16 + 8 * (i % 2):24 + 8 * (i % 2)], stats[:, 8 * (i % 2):8 * (i % 2) + 8], ACT.Sqrt).then_inc(sem("na_std"), 1)
            if i >= 2:
                j = i - 2
                half, t = divmod(j, NT)
                ps = full(act, "na_turn", j).rearrange("p (f t) -> p f t", f=4)
                dst, g = (naq, "na_q_g") if half < 2 else (nak, "na_k_g")
                f0 = 4 * (half % 2)
                if half < 2 and t < LT:
                    for r in range(2):
                        to = dst[:, f0:f0 + 4, 0:SEQ].rearrange("p f (j r c) -> p f j r c", j=BLOCKS, r=ROWS)[:, :, :, 2 * t + r, :]
                        ins = A(to, ps.rearrange("p f (r j c) -> p f r j c", r=2, j=BLOCKS)[:, :, r], ACT.Copy, scale=col(g))
                else:
                    ins = A(dst[:, f0:f0 + 4, t * P:(t + 1) * P], ps, ACT.Copy, scale=col(g))
                free(ins, "na_turn", j)
        for n in range(2):
            if n == 1:
                act.wait_ge(sem("na_strips_landed"), 16 * 2 * BLOCKS * LT)
            for t in range(NT):
                ps = full(act, "na_v", n, t)
                dst = na_v[:, t, :] if t < LT else na_vc[:, t - LT, n * W:(n + 1) * W]
                free(A(dst, ps, ACT.Copy), "na_v", n, t)
        for i in range(NA_UNITS + NA_LAG):
            if i < NA_UNITS:
                nk, b = W if i % NT < BLOCKS else CTX, i % NA_BUFFERS
                act.wait_ge(sem("na_max"), i + 1)
                A(na_s[:, b, 0:nk], na_s[:, b, 0:nk], ACT.Exp, bias=at_neg[:, b:b + 1], accum_out=at_sum[:, b:b + 1]).then_inc(sem("na_exp"), 1)
            j = i - NA_LAG
            if j >= 0:
                nk, b = W if j % NT < BLOCKS else CTX, j % NA_BUFFERS
                ps = full(act, "na_pt", j)[:, 0:nk]
                if j >= NA_BUFFERS:
                    full(act, "na_out", j - NA_BUFFERS)
                free(A(na_p[:, b, 0:nk], ps, ACT.Copy), "na_pt", j)
        for t in range(NT):
            ps = full(act, "na_ot", t)
            if t < BLOCKS:
                for f in range(KD):
                    dst = na_oT[:, f, 0:SEQ].rearrange("p (r c) -> p r c", c=GRID)[:, :, 16 * t:16 * t + 16]
                    ins = A(dst, ps[:, f * P:(f + 1) * P].rearrange("p (r c) -> p r c", c=16), ACT.Copy)
            else:
                ins = A(na_oT[:, :, t * P:(t + 1) * P], ps.rearrange("p (f c) -> p f c", f=KD), ACT.Copy)
            free(ins, "na_ot", t)
        turn_mod(1)

        next_high = [0]

        def high_to(i):
            while next_high[0] <= min(i, n_pieces - 1):
                j = next_high[0]
                act.wait_ge(piece_landed[j % PIECES_RAW], 16 * (j // PIECES_RAW + 1))
                if j >= PIECES_HIGH:
                    piece_free(act, j - PIECES_HIGH)
                A(high_piece(j), raw_piece(j), ACT.Copy).then_inc(piece_high, 1)
                next_high[0] += 1

        def experts(l):
            use = f"moe{l}"
            nt, m = TILES[l], SLOTS if l == 0 else CAP_L
            norm(use)
            A(ident_b, ident[:, :], ACT.Copy).then_inc(sem("moe_ident"), 1)
            for part in range(3):
                if part == 1:
                    act.wait_ge(sem("moe_logit_less_max"), l + 1)
                    A(logit, logit, ACT.Exp).then_inc(sem("moe_exp"), 1)
                for t in range(nt):
                    if part:
                        act.wait_ge(sem("moe_rest"), 2 * (l * NT) + (part - 1) * nt + t + 1)
                    else:
                        act.wait_ge(sem("normed"), tiles_before[use] + t + 1)
                    A(x_part[part][:, t, :], xn_moe[:, t, :], ACT.Copy).then_inc(sem("moe_part"), 1)

            def gather(e):
                b = e % 2
                for half in range(2):
                    ps = full(act, "moe_gather", l, e, half).rearrange("p (k s) -> p k s", k=4)
                    for k in range(4):
                        for s in range(1 if l else 2):
                            lo, hi = (0, CAP_L) if s == 0 else (CAP_L, SLOTS)
                            scale, shift = modulation(use, s, 4 * half + k)
                            ins = A(x_whole[:, b, 4 * half + k, lo:hi], ps[:, k, lo:hi], ACT.Identity, bias=shift, scale=scale)
                    free(ins, "moe_gather", l, e, half)
                taken(act, "moe_gather", l, e, 1)
                A(x_high[:, b, :, 0:m], x_whole[:, b, :, 0:m], ACT.Copy).then_inc(sem("moe_x_high"), 1)
                ps = full(act, "moe_selt", l, e)[:, 0:nt * P]
                free(A(selT[0:m, b, 0:nt * P], ps[0:m, :], ACT.Copy), "moe_selt", l, e)

            gather(0)
            for e in range(EXPERTS):
                job = (l * EXPERTS + e) * EXPERT_JOBS
                for n in range(2):
                    high_to(JOB_PIECES * (job + 2 * n + 2) - 1)
                    ps = full(act, "moe_h1", l, e, n)
                    free(A(s1[0:m, n * W:(n + 1) * W], ps[0:m, :], ACT.Silu), "moe_h1", l, e, n)
                high_to(JOB_PIECES * (job + 5))
                ps = full(act, "moe_ht", l, e).rearrange("p (k s) -> p k s", k=KD)[:, :, 0:m]
                A(hid_high[:, :, 0:m], ps, ACT.Copy).then_inc(sem("moe_hid_high"), 1)
                if e + 1 < EXPERTS:
                    gather(e + 1)
                for n in range(2):
                    high_to(min(JOB_PIECES * (job + n + 6) - 1, (l + 1) * n_pieces // 2 - 1))
                    ps = full(act, "moe_y", l, e, n)
                    A(y_high[0:m, e % 2, n * W:(n + 1) * W], ps[0:m, :], ACT.Copy, scale=gates[0:m, e % 2:e % 2 + 1]
                      ).then_inc(sem("moe_y_high"), 1)

        experts(0)

        norm("rw")
        low_act = {"w": ACT.Tanh, "a": ACT.Copy, "g": ACT.Sigmoid}
        low_done = set()
        for i, (q, n, t, key) in enumerate(spilled_jobs()):
            if q[0] in "wag" and q[0] not in low_done:
                low_done.add(q[0])
                free(A(lowT, full(act, "rw_low", q[0])[:, 0:TOK], low_act[q[0]]), "rw_low", q[0])
            dst = staging[:, i % RW_STAGES, :]
            if q[0] in "wa":
                taken(act, *key)
                A(dst, dst, ACT.Sigmoid).then_inc(sem("rw_squashed"), 1)
                continue
            if i >= RW_STAGES:
                act.wait_ge(sem(f"spilled_{i % RW_STAGES}"), 16 * (i // RW_STAGES))
            free(A(dst, full(act, *key), ACT.Copy), *key)

        def flat(x):
            return x.rearrange("p a b -> p (a b)")

        def sums(p, z):
            ps = full(act, "rw_sum", p, z)[:, 0:TOK]
            if z == 0 and p >= 1:
                taken(act, "rw_tgv", p - 1, RW_GROUPS - 1, RW_CHAINS - 1)
                full(act, "rw_tgv", p - 1, RW_GROUPS - 1, RW_CHAINS - 1)
            if z == 1:
                act.wait_ge(sem("rw_scaled"), 2 * p + 1)
            A(flat(e_neg), ps, ACT.Exp, scale=-1.0)
            free(A(flat(e_pos), ps, ACT.Exp), "rw_sum", p, z)
            ps = full(act, "rw_sum_ex", p, z)[:, 0:TOK]
            free(A(flat(e_ex), ps, ACT.Exp, scale=-1.0), "rw_sum_ex", p, z)
            ps = full(act, "rw_end", p, z)[:, 0:RW_STEPS]
            free(A(w_end[p % 2][z], ps, ACT.Exp, scale=-1.0), "rw_end", p, z)

        def turn_factors(p, z):
            for x, dst in enumerate((KT[z], BT[z], TT[z], RT[p % 2][z])):
                ps = full(act, "rw_turn", p, z, x)[:, 0:SEQ if x == 3 else TOK]
                free(A(dst, ps, ACT.Copy), "rw_turn", p, z, x)

        def scan(p, i):
            for z in range(2):
                t, c = rw_chunk(i, z)
                if p >= 0 and t < LT:
                    if p >= 1:
                        act.wait_ge(sem("rw_read_out"), p)
                    ps = full(act, "rw_y", p, i, z)[:, 0:P]
                    rows = slice(c * CH, (c + 1) * CH)
                    free(A(yz[z][rows, t, :], ps[rows, :], ACT.Copy), "rw_y", p, i, z)

        def read_out(p):
            act.wait_ge(sem("rw_y_var"), p + 1)
            A(rw_s[:, 32:40], rw_s[:, 24:32], ACT.Sqrt).then_inc(sem("rw_y_std"), 1)

        for p in range(RW_PAIRS):
            act.wait_ge(sem("rw_kk_squared"), p + 1)
            A(rw_s[:, 12:24], rw_s[:, 0:12], ACT.Sqrt).then_inc(sem("rw_kk_norm"), 1)
            sums(p, 0)
            scan(p - 1, RW_STEPS - 4)
            turn_factors(p, 0)
            sums(p, 1)
            scan(p - 1, RW_STEPS - 3)
            scan(p - 1, RW_STEPS - 2)
            turn_factors(p, 1)
            scan(p - 1, RW_STEPS - 1)
            for g in range(RW_GROUPS):
                for c in range(RW_CHAINS):
                    ps = full(act, "rw_gv", p, g, c)[:, 0:P]
                    free(A(gv[c], ps, ACT.Copy), "rw_gv", p, g, c)
                for lv in range(1, RW_LEVELS):
                    if rw_step_beside(g, lv) is not None:
                        scan(p, rw_step_beside(g, lv))
                    if g == 0 and p >= 1 and lv == RW_READ_STD:
                        read_out(p - 1)
                for c in range(RW_CHAINS):
                    t, z = rw_tile(g, c)
                    ps = full(act, "rw_tk", p, g, c)[:, 0:P]
                    free(A(tkT[z][:, t, :], ps, ACT.Copy), "rw_tk", p, g, c)
                for c in range(RW_CHAINS):
                    t, z = rw_tile(g, c)
                    ps = full(act, "rw_tgv", p, g, c)[:, 0:P]
                    free(A(tgv[z][:, t, :], ps, ACT.Copy), "rw_tgv", p, g, c)
                if g == 0 and p >= 1:
                    free(A(zT(p - 1), full(act, "rw_ot", p - 1), ACT.Copy), "rw_ot", p - 1)
        for i in range(RW_STEPS - 4, RW_STEPS):
            scan(RW_PAIRS - 1, i)
        read_out(RW_PAIRS - 1)
        free(A(zT(RW_PAIRS - 1), full(act, "rw_ot", RW_PAIRS - 1), ACT.Copy), "rw_ot", RW_PAIRS - 1)
        experts(1)

    @block.vector
    def _(dve):
        V = nc.vector
        dve_step = [0]

        def link(ins):
            dve_step[0] += 1
            ins.then_inc(sem("dve_step"), 1)
            dve.wait_ge(sem("dve_step"), dve_step[0])

        def norm(use):
            xn, _ = norm_of[use]
            t0, nt = tiles_before[use], NORMS[use]
            dve.wait_ge(sem("norm_squared"), t0 + nt)
            V.tensor_scalar(stats[:, 8:8 + nt], stats[:, 0:nt], 1.0 / D, EPS, ALU.mult, ALU.add).then_inc(sem("norm_var"), 1)
            dve.wait_ge(sem("norm_std"), USES.index(use) + 1)
            link(V.reciprocal(stats[:, 0:nt], stats[:, 16:16 + nt]))
            for t in range(nt):
                V.tensor_scalar(xn[:, t, :], h[:, t, :], stats[:, t:t + 1], None, ALU.mult).then_inc(sem("normed"), 1)

        def post(use):
            F, gb = post_of[use]
            i = POSTS.index(use)
            dve.wait_ge(sem("post_gain_landed"), 16 * (i + 1))
            for t in range(LT):
                dve.wait_ge(sem("post_squared"), i * LT + t + 1)
                if t == LT - 1:
                    V.tensor_scalar(stats[:, 28:32], stats[:, 24:28], 1.0 / D, EPS, ALU.mult, ALU.add).then_inc(sem("post_var"), 1)
                ins = V.tensor_tensor(F[:, t, :], F[:, t, :], gb, ALU.mult)
            link(ins)
            dve.wait_ge(sem("post_std"), i + 1)
            link(V.reciprocal(stats[:, 36:40], stats[:, 32:36]))
            for t in range(LT):
                V.scalar_tensor_tensor(h[:, t, :], F[:, t, :], stats[:, 36 + t:37 + t], h[:, t, :], ALU.mult, ALU.add).then_inc(sem("post_added"), 1)

        def ada(l, n):
            ways = len(ada_rows[l])
            before = ADA_JOBS[0] // len(ada_rows[0]) if l else 0
            dve.wait_ge(sem(f"ada_bias_landed_{n % ways}"), 16 * (before + n // ways + 1))
            ps = full(dve, "ada", l, n)
            rows = ada_rows[l][n % ways]
            free(V.tensor_tensor(rows, ps[0:2, 0:ADA_COLS[l]], rows, ALU.add), "ada", l, n)

        norm("dil")
        dve.wait_ge(sem("const_landed"), 16 * 6)
        V.tensor_copy(pos_f, pos_i)
        link(V.tensor_copy(pos_cf, pos_ci))
        V.tensor_scalar(ang[:, 0:SEQ], pos_f, ret_freq, None, ALU.mult)
        for c in range(DIL_STRIDE):
            ins = V.tensor_scalar(ang[:, SEQ + 8 * c:SEQ + 8 * c + 8], dil_freq, pos_cf[:, c:c + 1], None, ALU.mult)
        link(ins)
        ROUND = 1.5 * 2.0 ** 23
        link(V.tensor_scalar(turns, ang, float(np.float32(1 / (2 * np.pi))), ROUND, ALU.mult, ALU.add))
        link(V.tensor_scalar(turns, turns, ROUND, None, ALU.subtract))
        part1 = 6.28125
        part2 = float(np.float32(np.float64(2 * np.pi) - part1).astype(np.float16))
        part3 = float(np.float32(2 * np.pi - part1 - part2))
        for x in (part1, part2, part3):
            link(V.scalar_tensor_tensor(ang, turns, -x, ang, ALU.mult, ALU.add))
        lim = float(np.nextafter(np.float32(np.pi), np.float32(0)))
        V.tensor_scalar(ang, ang, lim, -lim, ALU.min, ALU.max).then_inc(sem("angle_reduced"), 1)
        dve.wait_ge(sem("angle_sin"), 1)
        link(V.tensor_tensor(turns, turns, turns, ALU.mult))
        V.tensor_copy(ret_sin, angs[:, 0:SEQ])
        V.tensor_copy(dil_sin.rearrange("p a b -> p (a b)"), angs[:, SEQ:544])
        V.tensor_scalar(ret_cos, turns[:, 0:SEQ], -2.0, 1.0, ALU.mult, ALU.add)
        V.tensor_scalar(dil_cos.rearrange("p a b -> p (a b)"), turns[:, SEQ:544], -2.0, 1.0, ALU.mult, ALU.add).then_inc(sem("angles_used"), 1)
        dve.wait_ge(sem("angles_used"), 1)

        n_rot = 0
        for i, (g, kind) in enumerate(DIL_STEPS):
            if kind == 2:
                continue
            for c in range(DIL_STRIDE):
                taken(dve, "dil_proj", i, c)
                x = dil_tmp[:, c, :].rearrange("p (h d) -> p h d", d=HD)
                x1, x2 = x[:, :, 0:ROPE8], x[:, :, ROPE8:2 * ROPE8]
                cos = dil_cos[:, c, :].unsqueeze(1).to_broadcast([P, DIL_SLOTS, ROPE8])
                sin = dil_sin[:, c, :].unsqueeze(1).to_broadcast([P, DIL_SLOTS, ROPE8])
                if n_rot >= 2:
                    dve.wait_ge(sem("dil_rotated"), n_rot - 1)
                r = [dil_rot[:, q, n_rot % 2] for q in range(4)]
                V.tensor_tensor(r[0], x1, cos, ALU.mult)
                V.tensor_tensor(r[1], x2, sin, ALU.mult)
                V.tensor_tensor(r[2], x2, cos, ALU.mult)
                link(V.tensor_tensor(r[3], x1, sin, ALU.mult))
                V.tensor_tensor(x1, r[0], r[1], ALU.subtract)
                V.tensor_tensor(x2, r[2], r[3], ALU.add).then_inc(sem("dil_rotated"), 1)
                n_rot += 1
        dve.wait_ge(sem("mask_landed"), 16)
        for i in range(DIL_TILES + 2):
            if i < DIL_TILES:
                s, c = divmod(i, DIL_STRIDE)
                ps = full(dve, "dil_score", i)[:, 0:6 * P]
                if i >= 2:
                    full(dve, "dil_pt", i - 2)
                    dve.wait_ge(sem("dil_exp"), i - 1)
                x = V.tensor_tensor_reduce(out=dil_s[:, i % 2, :], in0=ps, in1=dil_mask[:, c, :], scale=HD ** -0.5,
                                           scalar=-3e38, op0=ALU.add, op1=ALU.max, accum_out=stats[:, 56 + i % 2:57 + i % 2])
                free(x, "dil_score", i)
                taken(dve, "dil_score", i)
                V.tensor_scalar(stats[:, 40 + i % 2:41 + i % 2], stats[:, 56 + i % 2:57 + i % 2], -1.0, None,
                                ALU.mult).then_inc(sem("dil_max"), 1)
            if 1 <= i <= DIL_TILES:
                j = i - 1
                dve.wait_ge(sem("dil_exp"), j + 1)
                if j >= 2:
                    taken(dve, "dil_out", j - 2)
                link(V.reciprocal(stats[:, 58 + j % 2:59 + j % 2], stats[:, 42 + j % 2:43 + j % 2]))
            if i >= 2:
                j = i - 2
                s, c = divmod(j, DIL_STRIDE)
                ps = full(dve, "dil_out", j)[:, 0:HD]
                free(V.tensor_scalar(dil_o[:, c, s * HD:(s + 1) * HD], ps, stats[:, 58 + j % 2:59 + j % 2], None, ALU.mult),
                     "dil_out", j)
            if ada_beside_dil(i) is not None:
                ada(0, ada_beside_dil(i))

        dve.wait_ge(sem("decay_landed"), 16)
        for hd in range(RET_HEADS):
            for b, dst in enumerate((rqT, rkT)):
                if hd + b:
                    dve.wait_ge(sem("ret_rotated"), 2 * hd + b)
                p0 = full(dve, "ret_qk", hd, 2 * b)
                V.tensor_tensor(dst[:, 0, :], p0, ret_cos, ALU.mult)
                free(V.tensor_tensor(rot_b, p0, ret_sin, ALU.mult), "ret_qk", hd, 2 * b)
                p1 = full(dve, "ret_qk", hd, 2 * b + 1)
                V.tensor_tensor(rot_a, p1, ret_sin, ALU.mult)
                x = V.tensor_tensor(dst[:, 1, :], p1, ret_cos, ALU.mult)
                free(x, "ret_qk", hd, 2 * b + 1)
                taken(dve, "ret_qk", hd, 2 * b + 1)
                V.tensor_tensor(dst[:, 0, :], dst[:, 0, :], rot_a, ALU.subtract)
                V.tensor_tensor(dst[:, 1, :], dst[:, 1, :], rot_b, ALU.add).then_inc(sem("ret_rotated"), 1)
            for j in range(LT):
                n = SEQ - j * P
                ps = full(dve, "ret_score", hd, j)[:, 0:n]
                free(V.tensor_tensor(rs[:, j, 0:n], ps, decay[:, hd, 0:n], ALU.mult), "ret_score", hd, j)
            dve.wait_ge(sem("ret_squared"), (hd + 1) * LT)
            V.tensor_scalar(stats[:, 48:52], stats[:, 44:48], 1.0 / RET_V, EPS, ALU.mult, ALU.add).then_inc(sem("ret_var"), 1)
            dve.wait_ge(sem("ret_std"), hd + 1)
            link(V.reciprocal(stats[:, 60:64], stats[:, 52:56]))
            for t in range(LT):
                taken(dve, "ret_g", hd, t)
                ps = full(dve, "ret_out", hd, t)
                free(V.scalar_tensor_tensor(ry[:, t, :], ps, stats[:, 60 + t:61 + t], rg[:, t, :], ALU.mult, ALU.mult),
                     "ret_out", hd, t)

        for n in range(2):
            for f in range(4):
                taken(dve, "mix_gate", 0, n, f)
                ps = full(dve, "mix_ret", n, f)
                free(V.tensor_tensor(mixT[:, 4 * n + f, :], ps, gate_r[:, 4 * n + f, :], ALU.mult), "mix_ret", n, f)
        for f in range(KD):
            taken(dve, "mix_gate", 1, f // 4, f % 4)
            if f:
                dve.wait_ge(sem("mixed"), f)
            ps = full(dve, "mix_dil", f)
            free(V.tensor_tensor(mix_t, ps, gate_a[:, f, :], ALU.mult), "mix_dil", f)
            taken(dve, "mix_dil", f)
            V.tensor_tensor(mixT[:, f, :], mixT[:, f, :], mix_t, ALU.add).then_inc(sem("mixed"), 1)
        post("mix")

        norm("mlp")
        post("mlp")

        norm("ple")
        for n in range(2):
            for t in range(LT):
                taken(dve, "ple_gate", n, t)
                ps = full(dve, "ple_in", n, t)
                sl = slice(n * W, (n + 1) * W)
                free(V.tensor_tensor(F_ple[:, t, sl], ps, gate_p[:, t, sl], ALU.mult), "ple_in", n, t)
        post("ple")

        def modulation_gain(l):
            taken(dve, "ada_turn", l)
            for s in range(2):
                for n in range(2):
                    at = COLUMNS["norm_g"][0] + (2 * l + n) * KD
                    ins = V.scalar_tensor_tensor(mod_a[:, l, s, n, :], mod[:, l, s, 3 * n + 1, :], 1.0, cols[:, at:at + KD], ALU.add, ALU.mult)
            ins.then_inc(sem("modulation"), 1)

        modulation_gain(0)

        norm("na")
        for i in range(NA_STEPS):
            b = i % 2
            dve.wait_ge(sem("na_squared"), i + 1)
            if i >= 2:
                dve.wait_ge(sem("na_normed"), i - 1)
            link(V.tensor_reduce(rw_s[:, 8 * b:8 * b + 8], na_p[:, b, :].rearrange("p (h d) -> p h d", d=HD), AX, ALU.add))
            V.tensor_scalar(stats[:, 8 * b:8 * b + 8], rw_s[:, 8 * b:8 * b + 8], 1.0 / HD, EPS, ALU.mult, ALU.add).then_inc(sem("na_var"), 1)
            dve.wait_ge(sem("na_std"), i + 1)
            link(V.reciprocal(rw_s[:, 16 + 8 * b:24 + 8 * b], stats[:, 16 + 8 * b:24 + 8 * b]))
            taken(dve, "na_proj", i)
            x = na_s[:, b, :].rearrange("p (h d) -> p h d", d=HD)
            V.tensor_tensor(x, x, rw_s[:, 16 + 8 * b:24 + 8 * b].unsqueeze(2).to_broadcast([P, 8, HD]), ALU.mult).then_inc(sem("na_normed"), 1)
        dve.wait_ge(sem("na_zeroed"), 2)
        dve.wait_ge(sem("na_strips_landed"), 16 * 4 * BLOCKS * LT)
        dve.wait_ge(sem("na_mask_landed"), 16)
        full(dve, "na_v", 1, NT - 1)
        for i in range(NA_UNITS + 2 * NA_LAG):
            if i < NA_UNITS:
                hd, un = divmod(i, NT)
                bias, b = na_bias[hd % 2], i % NA_BUFFERS
                if un == 0:
                    dve.wait_ge(sem(f"na_bias_landed_{hd % 2}"), 16 * ROWS * (hd // 2 + 1))
                    link(V.scalar_tensor_tensor(bias[:, 0:3, :], bias[:, 0:3, :], HD ** 0.5, na_mask, ALU.mult, ALU.add))
                nk = W if un < BLOCKS else CTX
                ps = full(dve, "na_score", i)[:, 0:nk]
                if i >= NA_BUFFERS:
                    full(dve, "na_pt", i - NA_BUFFERS)
                    dve.wait_ge(sem("na_exp"), i - NA_BUFFERS + 1)
                s_, mx = na_s[:, b, 0:nk], at_max[:, b:b + 1]
                if un < BLOCKS:
                    kind = (0, 1, 1, 2)[un]
                    ins = V.tensor_tensor_reduce(out=s_.rearrange("p (a b) -> p a b", a=2), in0=ps.rearrange("p (a b) -> p a b", a=2),
                                                 in1=bias[:, kind::3 - kind, :], scale=HD ** -0.5, scalar=-3e38, op0=ALU.add, op1=ALU.max,
                                                 accum_out=mx)
                else:
                    ins = V.tensor_tensor_reduce(out=s_, in0=ps, in1=bias[:, 3, :], scale=HD ** -0.5, scalar=-3e38, op0=ALU.add,
                                                 op1=ALU.max, accum_out=mx)
                free(ins, "na_score", i)
                taken(dve, "na_score", i)
                V.tensor_scalar(at_neg[:, b:b + 1], mx, -1.0, None, ALU.mult).then_inc(sem("na_max"), 1)
            j = i - NA_LAG
            if 0 <= j < NA_UNITS:
                b = j % NA_BUFFERS
                dve.wait_ge(sem("na_exp"), j + 1)
                if j >= NA_BUFFERS:
                    taken(dve, "na_out", j - NA_BUFFERS)
                V.reciprocal(at_rec[:, b:b + 1], at_sum[:, b:b + 1]).then_inc(sem("na_reciprocal"), 1)
            j = i - 2 * NA_LAG
            if j >= 0:
                hd, un = divmod(j, NT)
                b = j % NA_BUFFERS
                ps = full(dve, "na_out", j)[:, 0:HD]
                dve.wait_ge(sem("na_reciprocal"), j + 1)
                free(V.tensor_scalar(na_o[:, un, hd * HD:(hd + 1) * HD], ps, at_rec[:, b:b + 1], None, ALU.mult), "na_out", j)
            if ada_beside_na(i) is not None:
                ada(1, ada_beside_na(i))
        modulation_gain(1)
        dve.wait_ge(sem("na_gate_landed"), 32)
        for n in range(2):
            for t in range(NT):
                i = n * NT + t
                ps = full(dve, "na_o", n, t)
                sl = slice(n * W, (n + 1) * W)
                if i >= 2:
                    dve.wait_ge(sem("na_added"), i - 1)
                free(V.tensor_tensor(na_t[:, i % 2, :], ps, na_gate[:, int(t >= LT), sl], ALU.mult), "na_o", n, t)
                taken(dve, "na_o", n, t)
                V.tensor_tensor(h[:, t, sl], h[:, t, sl], na_t[:, i % 2, :], ALU.add).then_inc(sem("na_added"), 1)

        def experts(l):
            nt, tok = TILES[l], TILES[l] * P
            streams = [(0, SEQ, CAP_L)] + ([(SEQ, TOK, CAP_C)] if l == 0 else [])
            norm(f"moe{l}")
            ps = full(dve, "moe_logit", l)[:, 0:nt * EXPERTS].rearrange("p (t e) -> p t e", e=EXPERTS)
            link(V.tensor_reduce(stats[:, 24:24 + nt], ps, AX, ALU.max))
            free(V.tensor_tensor(logit[:, 0:nt], ps, stats[:, 24:24 + nt].unsqueeze(2).to_broadcast([P, nt, EXPERTS]), ALU.subtract), "moe_logit", l)
            if l == 1:
                V.memset(logit[:, nt:NT, :], 0.0)
            taken(dve, "moe_logit", l)
            V.memset(sel[0], 0.0)
            V.memset(sel[1], 0.0).then_inc(sem("moe_logit_less_max"), 1)
            dve.wait_ge(sem("moe_exp"), l + 1)
            link(V.tensor_reduce(stats[:, 32:32 + nt], logit[:, 0:nt], AX, ALU.add))
            link(V.reciprocal(stats[:, 24:24 + nt], stats[:, 32:32 + nt]))
            V.tensor_tensor(aff[:, 0:nt], logit[:, 0:nt], stats[:, 24:24 + nt].unsqueeze(2).to_broadcast([P, nt, EXPERTS]),
                            ALU.mult).then_inc(sem("moe_affinity"), 1)
            dve.wait_ge(sem("moe_affinity"), l + 1)
            rest = aff[:, 0:nt]
            for part in range(3):
                link(V.tensor_copy(aff_part[:, 0:nt, :, part], rest))
                if part < 2:
                    link(V.tensor_tensor(logit[:, 0:nt], rest, aff_part[:, 0:nt, :, part], ALU.subtract))
                    rest = logit[:, 0:nt]
            E = slice(0, EXPERTS)
            ps = full(dve, "moe_afft", l)[E, 0:tok]
            free(V.tensor_copy(workT[E, 0:tok], ps), "moe_afft", l)
            taken(dve, "moe_afft", l)
            for lo, hi, cap in streams:
                left, then = workT, affT
                for _ in range(cap // 8):
                    link(V.max(top8[E, :], left[E, lo:hi]))
                    link(V.match_replace(then[E, lo:hi], top8[E, :], left[E, lo:hi], -1.0))
                    left, then = then, left
                assert left is workT
            link(V.tensor_scalar(workT[E, 0:tok], workT[E, 0:tok], 0.0, None, ALU.is_lt))
            for lo, hi, cap in streams:
                ins = V.tensor_tensor_scan(sumT[E, lo:hi], ones[E, 0:1].to_broadcast([EXPERTS, hi - lo]), workT[E, lo:hi], 0.0,
                                           ALU.mult, ALU.add)
            link(ins)
            link(V.tensor_tensor(sumT[E, 0:tok], sumT[E, 0:tok], workT[E, 0:tok], ALU.mult))
            V.tensor_scalar(sumT[E, 0:tok], sumT[E, 0:tok], -1.0, None, ALU.add).then_inc(sem("moe_numbered"), 1)
            ps = full(dve, "moe_slot", l)[:, 0:nt * EXPERTS]
            free(V.tensor_copy(slot[:, 0:nt].rearrange("p t e -> p (t e)"), ps), "moe_slot", l)
            taken(dve, "moe_slot", l)
            dve.wait_ge(sem("moe_landed"), 32 * (l + 1))

            next_low = [l * n_pieces // 2]

            def low_to(i):
                while next_low[0] <= min(i, (l + 1) * n_pieces // 2 - 1):
                    if next_low[0] % JOB_PIECES in DVE_PIECES:
                        low_part(dve, V, "dve", next_low[0])
                    next_low[0] += 1

            def select(e):
                if e >= 2:
                    full(dve, "moe_gates", l, e - 2)
                for t in range(nt):
                    lo, cap = (0, CAP_L) if t < LT else (CAP_L, CAP_C)
                    ins = V.tensor_scalar(sel[e % 2][:, t, lo:lo + cap], slot_no[:, 0:cap], slot[:, t, e:e + 1], None, ALU.is_equal)
                ins.then_inc(sem("moe_selected"), 1)

            def gathered(e):
                ps = full(dve, "moe_gates", l, e)[0:m, 0:3]
                free(V.tensor_reduce(gates[0:m, e % 2:e % 2 + 1], ps, AX, ALU.add), "moe_gates", l, e)
                dve.wait_ge(sem("moe_x_high"), l * EXPERTS + e + 1)
                V.tensor_tensor(x_low[:, e % 2, :, 0:m], x_whole[:, e % 2, :, 0:m], x_high[:, e % 2, :, 0:m].bitcast(F32), ALU.subtract).then_inc(sem("moe_x_low"), 1)

            def scatter(e):
                for t in range(nt):
                    for n in range(2):
                        ps = full(dve, "moe_add", l, e, t, n)
                        x = acc[:, t, n * W:(n + 1) * W]
                        if e == 0:
                            ins = V.tensor_copy(x, ps)
                        else:
                            taken(dve, "moe_add", l, e - 1, t, n)
                            ins = V.tensor_tensor(x, x, ps, ALU.add)
                        free(ins, "moe_add", l, e, t, n)

            m = SLOTS if l == 0 else CAP_L
            select(0)
            select(1)
            gathered(0)
            for e in range(EXPERTS):
                job = (l * EXPERTS + e) * EXPERT_JOBS
                for n in range(2):
                    low_to(JOB_PIECES * (job + 2 * n + 3) - 1)
                    taken(dve, "moe_h1", l, e, n)
                    ps = full(dve, "moe_h3", l, e, n)
                    x = s1[0:m, n * W:(n + 1) * W]
                    free(V.tensor_tensor(x, ps[0:m, :], x, ALU.mult), "moe_h3", l, e, n)
                if e >= 1:
                    scatter(e - 1)
                low_to(JOB_PIECES * (job + 5))
                ps = full(dve, "moe_ht", l, e).rearrange("p (k s) -> p k s", k=KD)[:, :, 0:m]
                dve.wait_ge(sem("moe_hid_high"), l * EXPERTS + e + 1)
                free(V.tensor_tensor(hid_low[:, :, 0:m], ps, hid_high[:, :, 0:m].bitcast(F32), ALU.subtract), "moe_ht", l, e)
                if e + 2 < EXPERTS:
                    select(e + 2)
                if e + 1 < EXPERTS:
                    gathered(e + 1)
                for n in range(2):
                    low_to(JOB_PIECES * (job + n + 6) - 1)
                    ps = full(dve, "moe_y", l, e, n)
                    dve.wait_ge(sem("moe_y_high"), 2 * (l * EXPERTS + e) + n + 1)
                    sl = slice(n * W, (n + 1) * W)
                    free(V.scalar_tensor_tensor(y_low[0:m, e % 2, sl], ps[0:m, :], gates[0:m, e % 2:e % 2 + 1],
                                                y_high[0:m, e % 2, sl].bitcast(F32), ALU.mult, ALU.subtract), "moe_y", l, e, n)
            scatter(EXPERTS - 1)
            dve.wait_ge(sem("moe_gate_landed"), 32 * (l + 1))
            for t in range(nt):
                taken(dve, "moe_add", l, EXPERTS - 1, t, 1)
                link(V.tensor_tensor(acc[:, t, :], acc[:, t, :], moe_gate[:, int(t >= LT), :], ALU.mult))
                V.tensor_tensor(h[:, t, :], h[:, t, :], acc[:, t, :], ALU.add).then_inc(sem("moe_added"), 1)

        experts(0)

        norm("rw")
        for s, (lo, hi) in enumerate(((0, SEQ), (SEQ, TOK))):
            taken(dve, "turn", "rw", s, KD - 1)
            V.tensor_tensor(xx[:, :, lo + 1:hi - 1], hT_rw[:, :, lo:hi - 2], hT_rw[:, :, lo + 2:hi], ALU.add)
            V.tensor_copy(xx[:, :, lo:lo + 1], hT_rw[:, :, lo + 1:lo + 2])
            ins = V.tensor_copy(xx[:, :, hi - 1:hi], hT_rw[:, :, hi - 2:hi - 1])
        link(ins)
        order = "rkvwag"
        for i, q in enumerate(order):
            if i >= 2:
                o = order[i - 2]
                full(dve, *(("rw_proj", o, 1, (LT if o == "r" else NT) - 1) if o in "rkv" else ("rw_low", o)))
            if i == 0:
                V.scalar_tensor_tensor(xx[:, 0, :], xx[:, 0, :], 0.5, hT_rw[:, 0, :], ALU.mult, ALU.subtract).then_inc(sem("rw_shifted"), 1)
            for k in range(KD):
                if i == 0 and k + 1 < KD:
                    V.scalar_tensor_tensor(xx[:, k + 1, :], xx[:, k + 1, :], 0.5, hT_rw[:, k + 1, :], ALU.mult, ALU.subtract
                                           ).then_inc(sem("rw_shifted"), 1)
                if i == 0:
                    dve.wait_ge(sem("rw_shifted"), k + 1)
                c = "rwkvag".index(q) * KD + k
                V.scalar_tensor_tensor(xs[i % 2][:, k, :], xx[:, k, :], col("rw_mix", c), hT_rw[:, k, :], ALU.mult, ALU.add
                                       ).then_inc(sem("rw_mixed"), 1)

        for i, (q, n, t, key) in enumerate(spilled_jobs()):
            if q[0] in "wa":
                if i >= RW_STAGES:
                    dve.wait_ge(sem(f"spilled_{i % RW_STAGES}"), 16 * (i // RW_STAGES))
                at = KD * 2 * CH + (1 + int(q[1])) * D + n * W
                bias = ring[:, low_slot[q[0]], at:at + W]
                free(V.tensor_tensor(staging[:, i % RW_STAGES, :], full(dve, *key), bias, ALU.add), *key)

        def over(row, nt):
            return row.unsqueeze(1).to_broadcast([P, nt, P])

        def heads(x):
            return x.rearrange("p t (h d) -> p (t h) d", d=HD)

        def by_head(x, n):
            return x.unsqueeze(2).to_broadcast([P, n, HD])

        def pair(p):
            return {q: v[p % 2] for q, v in RW_IN.items()}, [rw_rows[:, p % 2, x, :] for x in range(5)]

        def unit_keys(p):
            I, (k_k, *_) = pair(p)
            dve.wait_ge(sem(f"rw_in_landed_{p % 2}"), 16 * 9 * (p // 2 + 1))
            if p >= 1:
                taken(dve, "rw_tgv", p - 1, RW_GROUPS - 1, RW_CHAINS - 1)
                full(dve, "rw_tgv", p - 1, RW_GROUPS - 1, RW_CHAINS - 1)
            link(V.tensor_tensor(kk, I["k"], over(k_k, NT), ALU.mult))
            link(V.tensor_tensor(rw_t, kk, kk, ALU.mult))
            V.tensor_reduce(rw_s[:, 0:12], heads(rw_t), AX, ALU.add).then_inc(sem("rw_kk_squared"), 1)
            dve.wait_ge(sem("rw_kk_norm"), p + 1)
            link(V.tensor_scalar(rw_s[:, 12:24], rw_s[:, 12:24], 1e-12, None, ALU.max))
            link(V.reciprocal(rw_s[:, 0:12], rw_s[:, 12:24]))
            link(V.tensor_tensor(heads(kk), heads(kk), by_head(rw_s[:, 0:12], 12), ALU.mult))

        def factors(p, z):
            I, (_, k_a, *_) = pair(p)
            az, B, T = I[f"a{z}"], bh[p % 2][z], th[p % 2][z]
            if z == 1:
                full(dve, "rw_turn", p, 0, 3)
            V.tensor_tensor(B, kk, az, ALU.mult)
            link(V.scalar_tensor_tensor(rw_t, az, -1.0, over(k_a, NT), ALU.add, ALU.mult))
            link(V.scalar_tensor_tensor(T, rw_t, 1.0, I["k"], ALU.add, ALU.mult))

        def scale(p, z):
            I, _ = pair(p)
            B, T = bh[p % 2][z], th[p % 2][z]
            taken(dve, "rw_sum_ex", p, z)
            V.tensor_tensor(kh[z], kk, e_ex, ALU.mult)
            V.tensor_tensor(B, B, e_pos, ALU.mult)
            V.tensor_tensor(T, T, e_pos, ALU.mult)
            V.tensor_tensor(rw_t[:, 0:LT], I["r"], e_neg[:, 0:LT], ALU.mult).then_inc(sem("rw_scaled"), 1)

        def scan_u(p, i):
            for z in range(2):
                t, c = rw_chunk(i, z)
                rows = slice(c * CH, (c + 1) * CH)
                ps = full(dve, "rw_u", p, i, z)[:, 0:P]
                taken(dve, "rw_tgv", p, i // 4, 2 * (i // 2 % 2) + z)
                free(V.scalar_tensor_tensor(u[z][rows, :], ps[rows, :], -1.0, tgv[z][rows, t, :], ALU.mult, ALU.subtract), "rw_u", p, i, z)

        def scan_state(p, i):
            if i + 1 == RW_STEPS:
                return
            for z in range(2):
                t, c = rw_chunk(i, z)
                ps = full(dve, "rw_state", p, i, z)[:, 0:P]
                new = state[z][:, (i + 1) % 2, :]
                if i == 0:
                    dve.wait_ge(sem("rw_state_zeroed"), p + 1)
                else:
                    taken(dve, "rw_state", p, i - 1, z)
                if i >= 1 and rw_chunk(i - 1, z)[0] < LT:
                    full(dve, "rw_y", p, i - 1, z)
                link(V.tensor_tensor(new, ps, state[z][:, i % 2, :], ALU.add))
                end = w_end[p % 2][z][:, 2 * t + c:2 * t + c + 1]
                free(V.scalar_tensor_tensor(new, new, end, c_blocks, ALU.mult, ALU.mult), "rw_state", p, i, z)

        def scan(p, i):
            if p >= 0:
                scan_u(p, i)
                scan_state(p, i)

        def zero_states(p):
            if p >= 1:
                for z in range(2):
                    full(dve, "rw_y", p - 1, RW_STEPS - 1, z)
                    taken(dve, "rw_state", p - 1, RW_STEPS - 2, z)
            V.memset(state[0][:, 0, :], 0.0)
            V.memset(state[1][:, 0, :], 0.0).then_inc(sem("rw_state_zeroed"), 1)

        def chain_start(p, g, c):
            t, z = rw_tile(g, c)
            if last_unit(p, g, c):
                full(dve, "rw_tgv", *last_unit(p, g, c))
            mask = [c_mask[:, z, x:x + 1, :].to_broadcast([P, 2, P]) for x in range(2)]
            ps = full(dve, "rw_ab", p, g, c).rearrange("p (h x s) -> p h x s", h=2, x=4)
            V.tensor_tensor(aT[c], ps[:, :, 0, :], mask[0], ALU.mult).then_inc(sem("rw_at"), 1)
            T = inv[c][:, :, 0, :]
            pa = full(dve, "rw_a", p, g, c).rearrange("p (h s) -> p h s", h=2)[:, :, 0:P]
            link(V.tensor_tensor(T, pa, c_pairs[:, z, 0:1, :].to_broadcast([P, 2, P]), ALU.mult))
            if t < LT:
                for rows in (slice(0, CH), slice(CH, P)):
                    own = c_mask[rows, z, 1:2, rows].to_broadcast([CH, 2, CH])
                    V.tensor_tensor(rbT[z][rows, t], ps[rows, :, 1, rows], own, ALU.mult)
                    V.tensor_tensor(rtT[z][rows, t], ps[rows, :, 3, rows], own, ALU.mult)
            free(V.tensor_tensor(gT[c], ps[:, :, 2, :], mask[0], ALU.mult), "rw_ab", p, g, c)
            free(V.tensor_tensor(T, T, ident[:, :].unsqueeze(1).to_broadcast([P, 2, P]), ALU.add), "rw_a", p, g, c)

        def read_out(p, part):
            I, (k_k, k_a, r_k, ln_g, ln_b) = pair(p)
            y, d = yd
            w = yz[0]
            if part == 1:
                for z in range(2):
                    taken(dve, "rw_y", p, RW_STEPS - 1, z)
                if p >= 1:
                    full(dve, "rw_ot", p - 1)
                link(V.tensor_tensor(y, yz[0], yz[1], ALU.add))
                link(V.tensor_reduce(rw_s[:, 24:32], heads(y), AX, ALU.add))
                link(V.tensor_scalar(rw_s[:, 24:32], rw_s[:, 24:32], 1.0 / HD, None, ALU.mult))
                link(V.tensor_tensor(heads(d), heads(y), by_head(rw_s[:, 24:32], 8), ALU.subtract))
                link(V.tensor_tensor(y, d, d, ALU.mult))
            elif part == 2:
                link(V.tensor_reduce(rw_s[:, 40:48], heads(y), AX, ALU.add))
                V.tensor_scalar(rw_s[:, 24:32], rw_s[:, 40:48], 1.0 / HD, GN_EPS, ALU.mult, ALU.add).then_inc(sem("rw_y_var"), 1)
                link(V.tensor_tensor(w, I["a0"][:, 0:LT], I["a1"][:, 0:LT], ALU.add))
                link(V.scalar_tensor_tensor(w, w, -2.0, over(k_a, LT), ALU.add, ALU.mult))
                link(V.scalar_tensor_tensor(w, w, 2.0, I["k"][:, 0:LT], ALU.add, ALU.mult))
            elif part == 3:
                link(V.tensor_tensor(w, w, I["r"], ALU.mult))
                link(V.tensor_tensor(w, w, over(r_k, LT), ALU.mult))
                link(V.tensor_reduce(rw_s[:, 40:48], heads(w), AX, ALU.add))
                link(V.tensor_tensor(heads(w), heads(I["v"][:, 0:LT]), by_head(rw_s[:, 40:48], 8), ALU.mult))
            elif part == 4:
                dve.wait_ge(sem("rw_y_std"), p + 1)
                link(V.reciprocal(rw_s[:, 40:48], rw_s[:, 32:40]))
                link(V.tensor_tensor(heads(d), heads(d), by_head(rw_s[:, 40:48], 8), ALU.mult))
                link(V.tensor_tensor(d, d, over(ln_g, LT), ALU.mult))
                link(V.tensor_tensor(d, d, over(ln_b, LT), ALU.add))
            else:
                link(V.tensor_tensor(d, d, w, ALU.add))
                V.tensor_tensor(d, d, I["g"], ALU.mult).then_inc(sem("rw_read_out"), 1)

        dve.wait_ge(sem("rw_const_landed"), 16 * 7)
        units = 0
        for p in range(RW_PAIRS):
            unit_keys(p)
            factors(p, 0)
            scale(p, 0)
            scan(p - 1, RW_STEPS - 4)
            factors(p, 1)
            scan(p - 1, RW_STEPS - 3)
            scale(p, 1)
            scan(p - 1, RW_STEPS - 2)
            scan(p - 1, RW_STEPS - 1)
            zero_states(p)
            for g in range(RW_GROUPS):
                for c in range(RW_CHAINS):
                    chain_start(p, g, c)
                for lv in range(1, RW_LEVELS):
                    i = rw_step_beside(g, lv)
                    for c in range(RW_CHAINS):
                        z = c % 2
                        ps = full(dve, "rw_x", p, g, c, lv)[:, 0:2 * P].rearrange("p (h s) -> p h s", h=2)
                        free(V.tensor_tensor(xl[c], ps, c_join[:, z, lv - 1:lv, :].to_broadcast([P, 2, P]), ALU.mult), "rw_x", p, g, c, lv)
                    if i is not None:
                        scan_u(p, i)
                    for c in range(RW_CHAINS):
                        z = c % 2
                        ps = full(dve, "rw_join", p, g, c, lv)[:, 0:4 * CH].rearrange("p (h x a b) -> p h x a b", h=2, x=2, b=1 << lv)
                        T = halves(inv[c][:, :, 0, :], lv, z)
                        M = halves(inv[c][:, :, 1, :], lv, z, True)
                        if lv == 1:
                            taken(dve, "rw_a", p, g, c)
                            dve.wait_ge(sem("rw_off"), units + c + 1)
                        else:
                            taken(dve, "rw_join", p, g, c, lv - 1)
                        if lv < RW_LEVELS - 1:
                            V.tensor_tensor(T, T, ps[:, :, 0], ALU.subtract)
                        free(V.tensor_tensor(M, M, ps[:, :, 1], ALU.subtract), "rw_join", p, g, c, lv)
                    if i is not None:
                        scan_state(p, i)
                    if g == 0 and p >= 1:
                        read_out(p - 1, lv)
                units += RW_CHAINS
        for i in range(RW_STEPS - 4, RW_STEPS):
            scan(RW_PAIRS - 1, i)
        for part in range(1, RW_LEVELS):
            read_out(RW_PAIRS - 1, part)
        dve.wait_ge(sem("rw_gate_landed"), 16)
        for n in range(2):
            for t in range(LT):
                i = n * LT + t
                ps = full(dve, "rw_o", n, t)
                sl = slice(n * W, (n + 1) * W)
                if i >= 2:
                    dve.wait_ge(sem("rw_added"), i - 1)
                free(V.tensor_tensor(rw_ot[:, i % 2, :], ps, rw_gate[:, sl], ALU.mult), "rw_o", n, t)
                taken(dve, "rw_o", n, t)
                V.tensor_tensor(h[:, t, sl], h[:, t, sl], rw_ot[:, i % 2, :], ALU.add).then_inc(sem("rw_added"), 1)
        experts(1)

    @block.tensor
    def _(pe):
        mm, turn = nc.tensor.matmul, nc.tensor.transpose
        load_no = [0]

        def weights(name, k=KD, n=W):
            i = load_no[0]
            assert loads[i][0] == name, (loads[i][0], name)
            pe.wait_ge(landed[i % RING], landed_at[i])
            load_no[0] += 1
            return ring[:, i % RING, 0:k * n].rearrange("p (k n) -> p k n", n=n)

        def open_(*key):
            for before in plan[key].before:
                pe.wait_ge(freed[before.engine], before.count)
            return bank(plan[key])

        def close(ins, *key):
            assert done["pe"] == plan[key].number, (key, done["pe"], plan[key].number)
            done["pe"] += 1
            ins.then_inc(filled, 1)

        def product(key, lhs, rhs, nk, ncol=W, first=True):
            ps = open_(*key)
            for k in range(nk):
                ins = mm(ps[:, 0:ncol], lhs(k), rhs(k), start=(k == 0 and first), stop=(k == nk - 1))
            return ins

        def norm(use):
            xn, _ = norm_of[use]
            t0 = tiles_before[use]
            for k in range(KD):
                ps = open_("turn", use, 0, k)
                for t in range(LT):
                    pe.wait_ge(sem("normed"), t0 + t + 1)
                    ins = turn(ps[:, t * P:(t + 1) * P], xn[:, t, k * P:(k + 1) * P], ident[:, :])
                close(ins, "turn", use, 0, k)
            if NORMS[use] == NT:
                for k in range(KD):
                    ps = open_("turn", use, 1, k)
                    for t in range(LT, NT):
                        pe.wait_ge(sem("normed"), t0 + t + 1)
                        ins = turn(ps[:, (t - LT) * P:(t - LT + 1) * P], xn[:, t, k * P:(k + 1) * P], ident[:, :])
                    close(ins, "turn", use, 1, k)
            taken(pe, "turn", use, int(NORMS[use] == NT), KD - 1)

        def ada(l, n):
            pe.wait_ge(sem("cond_ready"), 1)
            w = weights("ada", KD, ADA_COLS[l])
            ps = open_("ada", l, n)
            for k in range(KD):
                ins = mm(ps[0:2, 0:ADA_COLS[l]], cond[:, :, k], w[:, k, :], start=(k == 0), stop=(k == KD - 1))
            close(ins, "ada", l, n)

        def turn_mod(l):
            ps = open_("ada_turn", l)
            pe.wait_ge(sem("mod_rows_landed"), 16 * (l + 1))
            close(turn(ps[:, 0:96], mod_rows[l][0:96, :], ident[0:96, 0:96]), "ada_turn", l)

        pe.wait_ge(sem("const_landed"), 16 * 6)
        norm("dil")
        n_rot = 0
        for i in range(len(DIL_STEPS) + 1):
            if i < len(DIL_STEPS):
                w = weights("dil_proj")
                for c in range(DIL_STRIDE):
                    ins = product(("dil_proj", i, c), lambda k: uT[:, k, c::DIL_STRIDE], lambda k: w[:, k, :], KD)
                    close(ins, "dil_proj", i, c)
            if i >= 1 and DIL_STEPS[i - 1][1] < 2:
                for c in range(DIL_STRIDE):
                    n_rot += 1
                    pe.wait_ge(sem("dil_rotated"), n_rot)
                    ps = open_("dil_turn", i - 1, c)
                    for f in range(4):
                        ins = turn(ps[:, f * P:(f + 1) * P], dil_tmp[:, c, f * P:(f + 1) * P], ident[:, :])
                    close(ins, "dil_turn", i - 1, c)
        taken(pe, "dil_turn", len(DIL_STEPS) - 2, DIL_STRIDE - 1)
        taken(pe, "dil_proj", len(DIL_STEPS) - 1, DIL_STRIDE - 1)
        for i in range(DIL_TILES + 2):
            if i < DIL_TILES:
                s, c = divmod(i, DIL_STRIDE)
                rows = slice(s % 2 * HD, s % 2 * HD + HD)
                ps = open_("dil_score", i)
                f = [4 * g + s // 2 for g in range(DIL_GROUPS)]
                own = slice(c * P, (c + 1) * P)
                mm(ps[:, 0:SEQ], qT[rows, f[0], own], kT[rows, f[0], :], start=True, stop=True)
                for g in (1, 2):
                    ins = mm(ps[:, SEQ + (g - 1) * P:SEQ + g * P], qT[rows, f[g], own], kT[rows, f[g], own], start=True, stop=True)
                close(ins, "dil_score", i)
            if 1 <= i <= DIL_TILES:
                j = i - 1
                ps = open_("dil_pt", j)
                pe.wait_ge(sem("dil_exp"), j + 1)
                for b in range(6):
                    ins = turn(ps[:, b * P:(b + 1) * P], dil_s[:, j % 2, b * P:(b + 1) * P], ident[:, :])
                close(ins, "dil_pt", j)
            if i >= 2:
                j = i - 2
                s, c = divmod(j, DIL_STRIDE)
                ps = open_("dil_out", j)
                taken(pe, "dil_pt", j)
                for b in range(6):
                    g, tile = (0, b) if b < 4 else (b - 3, c)
                    ins = mm(ps[:, 0:HD], dil_p[:, j % 2, b * P:(b + 1) * P], vR[:, tile, g * W + s * HD:g * W + (s + 1) * HD],
                             start=(b == 0), stop=(b == 5))
                close(ins, "dil_out", j)
            if ada_beside_dil(i) is not None:
                ada(0, ada_beside_dil(i))
        taken(pe, "dil_out", DIL_TILES - 1)
        for c in range(DIL_STRIDE):
            ps = open_("dil_ot", c)
            for f in range(4):
                ins = turn(ps[:, f * P:(f + 1) * P], dil_o[:, c, f * P:(f + 1) * P], ident[:, :])
            close(ins, "dil_ot", c)

        def ret_turn(hd):
            taken(pe, "ret_out", hd, LT - 1)
            for f in range(4):
                ps = open_("ret_turn", hd, f)
                for t in range(LT):
                    ins = turn(ps[:, t * P:(t + 1) * P], ry[:, t, f * P:(f + 1) * P], ident[:, :])
                close(ins, "ret_turn", hd, f)

        for hd in range(RET_HEADS):
            w = weights("ret_qk", 2 * KD, RET_QK)
            for mt in range(4):
                b, d = divmod(mt, 2)
                ins = product(("ret_qk", hd, mt), lambda k: w[:, b * KD + k, d * P:(d + 1) * P], lambda k: uT[:, k, :], KD)
                close(ins, "ret_qk", hd, mt)
            for name in ("ret_v", "ret_g"):
                w = weights(name)
                for t in range(LT):
                    ins = product((name, hd, t), lambda k: uT[:, k, t * P:(t + 1) * P], lambda k: w[:, k, :], KD)
                    close(ins, name, hd, t)
            if hd >= 1:
                ret_turn(hd - 1)
            pe.wait_ge(sem("ret_rotated"), 2 * (hd + 1))
            for j in range(LT):
                ins = product(("ret_score", hd, j), lambda d: rkT[:, d, j * P:(j + 1) * P], lambda d: rqT[:, d, j * P:SEQ], 2,
                              ncol=SEQ - j * P)
                close(ins, "ret_score", hd, j)
            taken(pe, "ret_v", hd, LT - 1)
            for t in range(LT):
                taken(pe, "ret_score", hd, t)
                ins = product(("ret_out", hd, t), lambda j: rs[:, j, (t - j) * P:(t - j + 1) * P], lambda j: rv[:, j, :], t + 1)
                close(ins, "ret_out", hd, t)
        ret_turn(RET_HEADS - 1)
        taken(pe, "ret_turn", RET_HEADS - 1, 3)

        for n in range(2):
            for b in range(2):
                w = weights("mix_gate")
                for f in range(4):
                    ins = product(("mix_gate", b, n, f), lambda k: w[:, k, f * P:(f + 1) * P], lambda k: uT[:, k, :], KD)
                    close(ins, "mix_gate", b, n, f)
            for half in range(2):
                w = weights("mix_ret")
                for f in range(4):
                    ps = open_("mix_ret", n, f) if half == 0 else bank(plan["mix_ret", n, f])
                    for k in range(KD):
                        ins = mm(ps, w[:, k, f * P:(f + 1) * P], yrT[:, half * KD + k, :], start=(half == 0 and k == 0),
                                 stop=(half == 1 and k == KD - 1))
                    if half == 1:
                        close(ins, "mix_ret", n, f)
                if half == 0:
                    ins.then_inc(used, 1)
        w = weights("mix_dil", 4, D)
        for f in range(KD):
            ins = product(("mix_dil", f), lambda k: w[:, k, f * P:(f + 1) * P], lambda k: yaT[:, k, :], 4)
            close(ins, "mix_dil", f)
        pe.wait_ge(sem("mixed"), KD)
        for n in range(2):
            w = weights("mix_o")
            for t in range(LT):
                ins = product(("mix_o", n, t), lambda k: mixT[:, k, t * P:(t + 1) * P], lambda k: w[:, k, :], KD)
                close(ins, "mix_o", n, t)

        norm("mlp")
        for l in range(D_FF // W):
            w = weights("up")
            for f in range(4):
                ins = product(("up", 4 * l + f), lambda k: w[:, k, f * P:(f + 1) * P], lambda k: vT[:, k, :], KD)
                close(ins, "up", 4 * l + f)
        for n in range(2):
            for q in range(4):
                w = weights("down")
                for t in range(LT):
                    ps = open_("down", n, t) if q == 0 else bank(plan["down", n, t])
                    for k in range(KD):
                        pe.wait_ge(sem("ff_squared"), q * KD + k + 1)
                        ins = mm(ps, ffT[:, q * KD + k, t * P:(t + 1) * P], w[:, k, :], start=(q == 0 and k == 0),
                                 stop=(q == 3 and k == KD - 1))
                    if q == 3:
                        close(ins, "down", n, t)
                if q < 3:
                    ins.then_inc(used, 1)

        norm("ple")
        pe.wait_ge(sem("ple_landed"), 32)
        pe.wait_ge(sem("ones_set"), 1)
        for d in range(PLE // P):
            ps = open_("ple_turn", d)
            for t in range(LT):
                ins = turn(ps[:, t * P:(t + 1) * P], pR[:, t, d * P:(d + 1) * P], ident[:, :])
            close(ins, "ple_turn", d)
        for n in range(2):
            w = weights("ple_gate")
            for t in range(LT):
                ps = open_("ple_gate", n, t)
                mm(ps, ones[0:1, :], b_ple[0:1, n * W:(n + 1) * W], start=True, stop=False)
                for k in range(KD):
                    ins = mm(ps, wT[:, k, t * P:(t + 1) * P], w[:, k, :], start=False, stop=(k == KD - 1))
                close(ins, "ple_gate", n, t)
        taken(pe, "ple_turn", PLE // P - 1)
        w = weights("ple_in", 2, D)
        for n in range(2):
            for t in range(LT):
                ins = product(("ple_in", n, t), lambda k: pT[:, k, t * P:(t + 1) * P], lambda k: w[:, k, n * W:(n + 1) * W], 2)
                close(ins, "ple_in", n, t)

        turn_mod(0)

        norm("na")
        for i in range(NA_STEPS + 2):
            if i < NA_STEPS:
                half, t = divmod(i, NT)
                if t == 0:
                    w = weights("na_proj")
                ins = product(("na_proj", i), lambda k: hT_na[:, k, t * P:(t + 1) * P], lambda k: w[:, k, :], KD)
                close(ins, "na_proj", i)
            if i >= 2:
                j = i - 2
                ps = open_("na_turn", j)
                pe.wait_ge(sem("na_normed"), j + 1)
                for f in range(4):
                    ins = turn(ps[:, f * P:(f + 1) * P], na_s[:, j % 2, f * P:(f + 1) * P], ident[:, :])
                close(ins, "na_turn", j)

        def grid(x, c0, n):
            return x[:, 0:SEQ].rearrange("p (r c) -> p r c", c=GRID)[:, :, c0:c0 + n]

        for n in range(2):
            w = weights("na_v")
            for t in range(NT):
                ins = product(("na_v", n, t), lambda k: hT_na[:, k, t * P:(t + 1) * P], lambda k: w[:, k, :], KD)
                close(ins, "na_v", n, t)
        taken(pe, "na_turn", NA_STEPS - 1)
        taken(pe, "na_v", 1, NT - 1)
        pe.wait_ge(sem("na_strips_landed"), 16 * 4 * BLOCKS * LT)
        for i in range(NA_UNITS + 2 * NA_LAG):
            if i < NA_UNITS:
                hd, un = divmod(i, NT)
                rows, f = slice(hd % 2 * HD, hd % 2 * HD + HD), hd // 2
                ps = open_("na_score", i)
                if un < BLOCKS:
                    q = naq[rows, f, un * P:(un + 1) * P]
                    mm(ps[:, 0:2 * P], q, grid(nak[rows, f, :], strip0[un], STRIP), start=True, stop=True)
                    ins = mm(ps[:, 2 * P:W], q, nak[rows, f, SEQ:TOK], start=True, stop=True)
                else:
                    ins = mm(ps[:, 0:CTX], naq[rows, f, un * P:(un + 1) * P], nak[rows, f, SEQ:TOK], start=True, stop=True)
                close(ins, "na_score", i)
            j = i - NA_LAG
            if 0 <= j < NA_UNITS:
                ps = open_("na_pt", j)
                pe.wait_ge(sem("na_exp"), j + 1)
                for b in range(4 if j % NT < BLOCKS else CT):
                    ins = turn(ps[:, b * P:(b + 1) * P], na_s[:, j % NA_BUFFERS, b * P:(b + 1) * P], ident[:, :])
                close(ins, "na_pt", j)
            j = i - 2 * NA_LAG
            if j >= 0:
                hd, un = divmod(j, NT)
                ps = open_("na_out", j)
                taken(pe, "na_pt", j)
                d = slice(hd * HD, (hd + 1) * HD)
                vals = [na_vc[:, c, d] for c in range(CT)]
                if un < BLOCKS:
                    vals = [na_vs[:, 2 * un + half, d] for half in range(2)] + vals
                for b, v in enumerate(vals):
                    ins = mm(ps[:, 0:HD], na_p[:, j % NA_BUFFERS, b * P:(b + 1) * P], v, start=(b == 0), stop=(b == len(vals) - 1))
                close(ins, "na_out", j)
            if ada_beside_na(i) is not None:
                ada(1, ada_beside_na(i))
        taken(pe, "na_out", NA_UNITS - 1)
        for t in range(NT):
            ps = open_("na_ot", t)
            for f in range(KD):
                ins = turn(ps[:, f * P:(f + 1) * P], na_o[:, t, f * P:(f + 1) * P], ident[:, :])
            close(ins, "na_ot", t)
        turn_mod(1)
        taken(pe, "na_ot", NT - 1)
        for n in range(2):
            w = weights("na_o")
            for t in range(NT):
                ins = product(("na_o", n, t), lambda k: na_oT[:, k, t * P:(t + 1) * P], lambda k: w[:, k, :], KD)
                close(ins, "na_o", n, t)

        def experts(l):
            nt, m = TILES[l], SLOTS if l == 0 else CAP_L
            norm(f"moe{l}")
            pe.wait_ge(sem("moe_landed"), 32 * (l + 1))
            ps = open_("moe_logit", l)
            for t in range(nt):
                for k in range(KD):
                    ins = mm(ps[:, t * EXPERTS:(t + 1) * EXPERTS], hT_moe[:, k, t * P:(t + 1) * P], router[:, k, :],
                             start=(k == 0), stop=(k == KD - 1))
            close(ins, "moe_logit", l)
            ps = open_("moe_afft", l)
            pe.wait_ge(sem("moe_affinity"), l + 1)
            for t in range(nt):
                ins = turn(ps[0:EXPERTS, t * P:(t + 1) * P], aff[:, t, :], ident[:, :])
            close(ins, "moe_afft", l)
            ps = open_("moe_slot", l)
            pe.wait_ge(sem("moe_numbered"), l + 1)
            for t in range(nt):
                ins = turn(ps[:, t * EXPERTS:(t + 1) * EXPERTS], sumT[0:EXPERTS, t * P:(t + 1) * P], ident[0:EXPERTS, 0:EXPERTS])
            close(ins, "moe_slot", l)

            def gather(e):
                b = e % 2
                pe.wait_ge(sem("moe_selected"), l * EXPERTS + e + 1)
                for half in range(2):
                    ps = open_("moe_gather", l, e, half).rearrange("p (k s) -> p k s", k=4)
                    for k in range(4):
                        d = slice((4 * half + k) * P, (4 * half + k + 1) * P)
                        for tiles, slots in ((range(LT), slice(0, CAP_L)), (range(LT, nt), slice(CAP_L, SLOTS))):
                            for t in tiles:
                                for part in range(3):
                                    ins = mm(ps[:, k, slots], x_part[part][:, t, d], sel[b][:, t, slots],
                                             start=(t == tiles[0] and part == 0), stop=(t == tiles[-1] and part == 2))
                    close(ins, "moe_gather", l, e, half)
                ps = open_("moe_selt", l, e)
                for t in range(nt):
                    ins = mm(ps[0:m, t * P:(t + 1) * P], sel[b][:, t, 0:m], ident_b, start=True, stop=True)
                close(ins, "moe_selt", l, e)
                ps = open_("moe_gates", l, e)
                for t in range(nt):
                    ins = mm(ps[0:m, 0:3], sel[b][:, t, 0:m], aff_part[:, t, e, :], start=(t == 0), stop=(t == nt - 1))
                close(ins, "moe_gates", l, e)

            def scatter(e):
                b = e % 2
                taken(pe, "moe_selt", l, e)
                taken(pe, "moe_y", l, e, 1)
                for t in range(nt):
                    for n in range(2):
                        ps = open_("moe_add", l, e, t, n)
                        one, sl = selT[0:m, b, t * P:(t + 1) * P], slice(n * W, (n + 1) * W)
                        mm(ps, one, y_high[0:m, b, sl], start=True, stop=False)
                        close(mm(ps, one, y_low[0:m, b, sl], start=False, stop=True), "moe_add", l, e, t, n)

            def expert(job, x_hi, x_lo):
                key = expert_job(job)
                ps = open_(*key)[0:m, :]
                for q in range(JOB_PIECES):
                    i = job * JOB_PIECES + q
                    piece_split(pe, i)
                    w_hi, w_lo = (x.rearrange("p (k n) -> p k n", n=W) for x in (high_piece(i), low_piece(i)))
                    for kk in range(2):
                        k = 2 * q + kk
                        mm(ps, x_hi[:, k, :], w_hi[:, kk, :], start=(k == 0), stop=False)
                        mm(ps, x_hi[:, k, :], w_lo[:, kk, :], start=False, stop=False)
                        ins = mm(ps, x_lo[:, k, :], w_hi[:, kk, :], start=False, stop=(k == KD - 1))
                    if q < JOB_PIECES - 1:
                        ins.then_inc(piece_used, 1)
                close(ins, *key)

            pe.wait_ge(sem("moe_part"), 3 * (l * NT + nt))
            gather(0)
            for e in range(EXPERTS):
                job = (l * EXPERTS + e) * EXPERT_JOBS
                pe.wait_ge(sem("moe_x_low"), l * EXPERTS + e + 1)
                x_hi, x_lo = (x[:, e % 2, :, 0:m] for x in (x_high, x_low))
                for r in range(4):
                    expert(job + r, x_hi, x_lo)
                if e >= 1:
                    scatter(e - 1)
                taken(pe, "moe_h3", l, e, 1)
                ps = open_("moe_ht", l, e).rearrange("p (k s) -> p k s", k=KD)[:, :, 0:m]
                for k in range(KD):
                    ins = turn(ps[:, k, :], s1[0:m, k * P:(k + 1) * P], ident[0:m, 0:m])
                close(ins, "moe_ht", l, e)
                if e + 1 < EXPERTS:
                    gather(e + 1)
                taken(pe, "moe_ht", l, e)
                for r in range(4, EXPERT_JOBS):
                    expert(job + r, hid_high[:, :, 0:m], hid_low[:, :, 0:m])
            scatter(EXPERTS - 1)

        experts(0)

        norm("rw")
        for i, q in enumerate("rkvwag"):
            x = xs[i % 2]
            if q in "rkv":
                for n in range(2):
                    w = weights("rw_proj")
                    for t in range(LT if q == "r" else NT):
                        def mixed(k):
                            if n + t == 0:
                                pe.wait_ge(sem("rw_mixed"), i * KD + k + 1)
                            return x[:, k, t * P:(t + 1) * P]

                        ins = product(("rw_proj", q, n, t), mixed, lambda k: w[:, k, :], KD)
                        close(ins, "rw_proj", q, n, t)
                continue
            w = weights(f"rw_low_{q}", 1, SLOT)[:, 0, :]
            pe.wait_ge(sem("rw_mixed"), (i + 1) * KD)
            ps = open_("rw_low", q)
            for lo, hi in ((0, SEQ), (SEQ, TOK)):
                for k in range(KD):
                    ins = mm(ps[:, lo:hi], w[:, k * P:(k + 1) * P], x[:, k, lo:hi], start=(k == 0), stop=(k == KD - 1))
            close(ins, "rw_low", q)
            taken(pe, "rw_low", q)
            for z in range(1 if q == "g" else 2):
                rows = slice(0, P) if q == "g" else slice(z * CH, (z + 1) * CH)
                for n in range(2):
                    at = KD * P + n * W
                    for t in range(LT if q == "g" else NT):
                        ps = open_("rw_high", q, z, n, t)
                        ins = mm(ps, lowT[rows, t * P:(t + 1) * P], w[rows, at:at + W], start=True, stop=True)
                        close(ins, "rw_high", q, z, n, t)

        def sums(p, z):
            pe.wait_ge(sem(f"rw_in_landed_{p % 2}"), 16 * 9 * (p // 2 + 1))
            lam = RW_IN[f"w{z}"][p % 2]
            lam_f = lam.rearrange("p t d -> p (t d)")
            for key, c in (("rw_sum", c_sum), ("rw_sum_ex", c_sum_ex)):
                ps = open_(key, p, z)
                for lo, hi in ((0, SEQ), (SEQ, TOK)):
                    ins = mm(ps[:, lo:hi], c[:, z, :], lam_f[:, lo:hi], start=True, stop=True)
                close(ins, key, p, z)
            ps = open_("rw_end", p, z)
            for t in range(NT):
                ins = mm(ps[:, 2 * t:2 * t + 2], lam[:, t, :], c_ind, start=True, stop=True)
            close(ins, "rw_end", p, z)

        def turn_factors(p, z):
            pe.wait_ge(sem("rw_scaled"), 2 * p + z + 1)
            for x, src in enumerate((kh[z], bh[p % 2][z], th[p % 2][z], rw_t)):
                ps = open_("rw_turn", p, z, x)
                for t in range(LT if x == 3 else NT):
                    ins = turn(ps[:, t * P:(t + 1) * P], src[:, t, :], ident[:, :])
                close(ins, "rw_turn", p, z, x)

        def scan_u(p, i):
            for z in range(2):
                t, c = rw_chunk(i, z)
                ps = open_("rw_u", p, i, z)
                if i == 0:
                    pe.wait_ge(sem("rw_state_zeroed"), p + 1)
                else:
                    taken(pe, "rw_state", p, i - 1, z)
                taken(pe, "rw_tk", p, i // 4, 2 * (i // 2 % 2) + z)
                close(mm(ps[:, 0:P], tkT[z][:, t, :], state[z][:, i % 2, :], start=True, stop=True), "rw_u", p, i, z)

        def scan_state(p, i):
            V_ = RW_IN["v"][p % 2]
            for z in range(2):
                t, c = rw_chunk(i, z)
                rows = slice(c * CH, (c + 1) * CH)
                taken(pe, "rw_u", p, i, z)
                if i + 1 < RW_STEPS:
                    ps = open_("rw_state", p, i, z)[:, 0:P]
                    mm(ps, th[p % 2][z][rows, t, :], V_[rows, t, :], start=True, stop=False)
                    close(mm(ps, bh[p % 2][z][rows, t, :], u[z][rows, :], start=False, stop=True), "rw_state", p, i, z)
                if t < LT:
                    ps = open_("rw_y", p, i, z)[rows, 0:P]
                    mm(ps, RT[p % 2][z][:, t * P + c * CH:t * P + (c + 1) * CH], state[z][:, i % 2, :], start=True, stop=False)
                    for hd in range(2):
                        d = slice(hd * CH, (hd + 1) * CH)
                        mm(ps[:, d], rtT[z][rows, t, hd, :], V_[rows, t, d], start=False, stop=False)
                        ins = mm(ps[:, d], rbT[z][rows, t, hd, :], u[z][rows, d], start=False, stop=(hd == 1))
                    close(ins, "rw_y", p, i, z)

        def scan(p, i):
            if p >= 0:
                scan_u(p, i)
                scan_state(p, i)

        def products(p, g, c):
            t, z = rw_tile(g, c)
            tile = slice(t * P, (t + 1) * P)
            to_r = TOK + p % 2 * SEQ
            kr = xT[z][:, 0:2 * to_r].rearrange("p (x s) -> p x s", x=2)[:, 0:2 if t < LT else 1, tile]
            n = 2 * P if t < LT else P
            ps = open_("rw_ab", p, g, c).rearrange("p (h s) -> p h s", h=2)
            for hd in range(2):
                rows = slice(hd * CH, (hd + 1) * CH)
                mm(ps[:, hd, 0:n], BT[z][rows, tile], kr[rows], start=True, stop=True)
                ins = mm(ps[:, hd, 2 * P:2 * P + n], TT[z][rows, tile], kr[rows], start=True, stop=True)
            close(ins, "rw_ab", p, g, c)
            ps = open_("rw_a", p, g, c).rearrange("p (h s) -> p h s", h=2)
            for hd in range(2):
                rows = slice(hd * CH, (hd + 1) * CH)
                ins = mm(ps[:, hd, 0:P], KT[z][rows, tile], BT[z][rows, tile], start=True, stop=True)
            close(ins, "rw_a", p, g, c)

        def read_out(p):
            ps = open_("rw_ot", p)
            pe.wait_ge(sem("rw_read_out"), p + 1)
            for t in range(LT):
                ins = turn(ps[:, t * P:(t + 1) * P], yd[1][:, t, :], ident[:, :])
            close(ins, "rw_ot", p)

        units = 0
        pe.wait_ge(sem("rw_const_landed"), 16 * 7)
        for p in range(RW_PAIRS):
            sums(p, 0)
            scan(p - 1, RW_STEPS - 4)
            turn_factors(p, 0)
            sums(p, 1)
            scan(p - 1, RW_STEPS - 3)
            scan(p - 1, RW_STEPS - 2)
            turn_factors(p, 1)
            scan(p - 1, RW_STEPS - 1)
            taken(pe, "rw_turn", p, 1, 3)
            for g in range(RW_GROUPS):
                for c in range(RW_CHAINS):
                    products(p, g, c)
                for c in range(RW_CHAINS):
                    t, z = rw_tile(g, c)
                    ps = open_("rw_gv", p, g, c)
                    taken(pe, "rw_ab", p, g, c)
                    for hd in range(2):
                        d = slice(hd * CH, (hd + 1) * CH)
                        ins = mm(ps[:, d], gT[c][:, hd, :], RW_IN["v"][p % 2][:, t, d], start=True, stop=True)
                    close(ins, "rw_gv", p, g, c)
                for lv in range(1, RW_LEVELS):
                    i = rw_step_beside(g, lv)
                    for c in range(RW_CHAINS):
                        ps = open_("rw_x", p, g, c, lv)
                        if lv == 1:
                            taken(pe, "rw_a", p, g, c)
                            pe.wait_ge(sem("rw_off"), units + c + 1)
                        else:
                            taken(pe, "rw_join", p, g, c, lv - 1)
                        for hd in range(2):
                            ins = mm(ps[:, hd * P:(hd + 1) * P], aT[c][:, hd, :], inv[c][:, hd, 0, :], start=True, stop=True)
                        close(ins, "rw_x", p, g, c, lv)
                    if i is not None:
                        scan_u(p, i)
                    for c in range(RW_CHAINS):
                        z = c % 2
                        ps = open_("rw_join", p, g, c, lv)[:, 0:4 * CH].rearrange("p (h x s) -> p h x s", h=2, x=2)
                        taken(pe, "rw_x", p, g, c, lv)
                        X = halves(xl[c], lv, z)
                        M = halves(inv[c][:, :, 1, :], lv, z, True)
                        for hd in range(2):
                            if lv < RW_LEVELS - 1:
                                mm(ps[:, hd, 0, :], inv[c][:, hd, 1, :], X[:, hd], start=True, stop=True)
                            ins = mm(ps[:, hd, 1, :], xl[c][:, hd, :], M[:, hd], start=True, stop=True)
                        close(ins, "rw_join", p, g, c, lv)
                    if i is not None:
                        scan_state(p, i)
                for c in range(RW_CHAINS):
                    t, z = rw_tile(g, c)
                    ps = open_("rw_tk", p, g, c)
                    taken(pe, "rw_join", p, g, c, RW_LEVELS - 1)
                    for hd in range(2):
                        d = slice(hd * CH, (hd + 1) * CH)
                        ins = mm(ps[d, 0:P], kh[z][:, t, d], inv[c][:, hd, 1, :], start=True, stop=True)
                    close(ins, "rw_tk", p, g, c)
                for c in range(RW_CHAINS):
                    t, z = rw_tile(g, c)
                    ps = open_("rw_tgv", p, g, c)
                    taken(pe, "rw_gv", p, g, c)
                    for hd in range(2):
                        d = slice(hd * CH, (hd + 1) * CH)
                        ins = mm(ps[:, d], inv[c][:, hd, 1, :], gv[c][:, d], start=True, stop=True)
                    close(ins, "rw_tgv", p, g, c)
                if g == 0 and p >= 1:
                    read_out(p - 1)
                units += RW_CHAINS
        for i in range(RW_STEPS - 4, RW_STEPS):
            scan(RW_PAIRS - 1, i)
        read_out(RW_PAIRS - 1)
        taken(pe, "rw_ot", RW_PAIRS - 1)
        for n in range(2):
            w = weights("rw_o")
            for t in range(LT):
                ins = product(("rw_o", n, t), lambda k: zT(k)[:, t * P:(t + 1) * P], lambda k: w[:, k, :], KD)
                close(ins, "rw_o", n, t)
        experts(1)


def columns_of(x):
    x = np.asarray(x).reshape(-1, P)
    return x.T


def kernel(**inputs):
    from concourse import bacc
    from concourse.bass_utils import run_bass_kernel_spmd

    nc = bacc.Bacc("TRN2", target_bir_lowering=False, num_devices=1)
    i = {k: np.asarray(v) for k, v in inputs.items()}
    arrays = dict(constants())
    vectors = {"g_pre_mix": i["g_pre_mix"], "b_gate_r": i["b_gate"][0, 0], "b_gate_a": i["b_gate"][0, 1],
               "g_pre_mlp": i["g_pre_mlp"], "g_pre_ple": i["g_pre_ple"],
               "norm_g": np.stack([i["norm1_g_2"], i["norm2_g_2"]], 1), "na_q_g": np.tile(i["na_q_g_2"][0], 2),
               "na_k_g": np.tile(i["na_k_g_2"][0], 2), "rw_mix": i["rw_mix_2"][0], "cond": np.stack([i["c_2"][0], i["c_ctx_2"]])}
    arrays["cols"] = np.concatenate([columns_of(vectors[k]) for k in COLUMNS], 1)
    arrays["x"] = i["x"][0]
    arrays["p"] = i["p"][0, 0]
    arrays["pos_row"] = np.broadcast_to(i["positions"], (P, SEQ))
    arrays["pos_col"] = i["positions"].reshape(P, DIL_STRIDE)
    for k in ("w_in", "w_ret_out", "w_dil_out", "w_o", "w_up", "w_down", "w_ple_gate", "w_ple_in", "g_post_mix", "g_post_mlp",
              "g_post_ple", "b_ple_gate"):
        arrays[k] = i[k][0]
    arrays["ctx"] = i["ctx_2"][0]
    for k in ("ada_w", "ada_b", "moe_router", "moe_w1", "moe_w3", "moe_w2"):
        arrays[k] = i[k + "_2"]
    for k in ("na_w_qkv", "na_w_o", "rw_w_r", "rw_w_k", "rw_w_v", "rw_w0", "rw_a0", "rw_g1", "rw_g2", "rw_w_o"):
        arrays[k] = i[k + "_2"][0]
    arrays["na_rpb"] = np.pad(i["na_rpb_2"][0], ((0, 0), (0, 0), (RPB_PAD, RPB_PAD)))
    for q in "wa":
        arrays[f"rw_{q}1"] = i[f"rw_{q}1_2"][0].transpose(1, 0, 2).reshape(D, 2 * CH)
        arrays[f"rw_{q}2"] = i[f"rw_{q}2_2"][0].reshape(2 * CH, D)
    arrays["rw_rows"] = np.stack([i["rw_k_k_2"][0], i["rw_k_a_2"][0], i["rw_r_k_2"][0].reshape(D), i["rw_ln_g_2"][0], i["rw_ln_b_2"][0]])
    arrays = {f"in_{k}": np.ascontiguousarray(v) for k, v in arrays.items()}
    a = {k[3:]: nc.dram_tensor(k, v.shape, mybir.dt.from_np(v.dtype), kind="ExternalInput").ap() for k, v in arrays.items()}
    out = nc.dram_tensor("out", (SEQ, D), F32, kind="ExternalOutput").ap()
    build(nc, a, out)
    got = run_bass_kernel_spmd(nc, [arrays], core_ids=[0])
    return got.results[0]["out"].reshape(1, SEQ, D)
```
